# Optimizing a Trainium2 kernel written in Bass

```python
import jax, jax.numpy as jnp
from jax import lax
import numpy as np

D_MODEL = 1024
BATCH = 1
SEQ = 2048
DEPTH = 1
DEC_BATCH = 8
DEC_SEQ = 1
PAST_LEN = 2048
PAGE_SIZE = 128

N_MIXERS = 4
W_GROUP = D_MODEL // N_MIXERS
D_MIX = N_MIXERS * W_GROUP
SC_WIDTH = 3
SSD_HEADS = 4
SSD_HEAD_DIM = W_GROUP // SSD_HEADS
SSD_GROUPS = 2
SSD_STATE = 128
SSD_CONV = 4
SSD_CHUNK = 128
SSD_CONV_DIM = W_GROUP + 2 * SSD_GROUPS * SSD_STATE
CF_WIDTH = 31
NSA_HEADS = 4
NSA_HEAD_DIM = W_GROUP // NSA_HEADS
CMP_STRIDE = 16
CMP_BLOCK = 2 * CMP_STRIDE
CMP_HIDDEN = 128
SEL_BLOCK = 64
SEL_TOPN = 16
SEL_LOCAL = 2
WINDOW = 512
Q_BLOCK = 128
KV_SLOTS = 4
NEG = -1e30
EPS = 1e-6

SPLITS = (W_GROUP, W_GROUP, W_GROUP, W_GROUP,
          W_GROUP, SSD_CONV_DIM, SSD_HEADS,
          2 * W_GROUP, W_GROUP,
          W_GROUP, 6 * NSA_HEAD_DIM, W_GROUP, 3 * NSA_HEADS)
D_IN = sum(SPLITS)

kernel_name = 'hymba_sconv_ssd_conformer_nsa_step'

def rmsnorm(x, g):
    x32 = x.astype(jnp.float32)
    y = x32 * lax.rsqrt(jnp.mean(x32 * x32, axis=-1, keepdims=True) + EPS)
    return y.astype(x.dtype) * g

def layernorm(x, g, b):
    x32 = x.astype(jnp.float32)
    mu = jnp.mean(x32, axis=-1, keepdims=True)
    var = jnp.mean(jnp.square(x32 - mu), axis=-1, keepdims=True)
    return ((x32 - mu) * lax.rsqrt(var + EPS)).astype(x.dtype) * g + b

def causal_dwconv(u, prev, w, b=None):
    full = jnp.concatenate([prev.astype(u.dtype), u], axis=1)
    y = lax.conv_general_dilated(full, w[:, None, :].astype(u.dtype), (1,), 'VALID',
                                 dimension_numbers=('NWC', 'WIO', 'NWC'),
                                 feature_group_count=u.shape[-1])
    if b is not None:
        y = y + b
    return y, full[:, full.shape[1] - (w.shape[0] - 1):]

def ssd_scan(x, dt, A, Bm, Cm, h0):
    f32 = jnp.float32
    n, l, hh, p = x.shape
    q = min(SSD_CHUNK, l)
    lp = -(-l // q) * q
    pad4 = ((0, 0), (0, lp - l), (0, 0), (0, 0))
    xf = jnp.pad(x.astype(f32), pad4)
    bf = jnp.pad(Bm.astype(f32), pad4)
    cf = jnp.pad(Cm.astype(f32), pad4)
    dtf = jnp.pad(dt, ((0, 0), (0, lp - l), (0, 0)))
    nc = lp // q
    xf = xf.reshape(n, nc, q, hh, p)
    bf = bf.reshape(n, nc, q, hh, -1)
    cf = cf.reshape(n, nc, q, hh, -1)
    dtf = dtf.reshape(n, nc, q, hh)
    acs = jnp.cumsum(jnp.moveaxis(dtf * A, 3, 1), axis=-1)
    causal = jnp.tril(jnp.ones((q, q), dtype=bool))
    decay = jnp.exp(jnp.where(causal, acs[..., :, None] - acs[..., None, :], -jnp.inf))
    xdt = xf * dtf[..., None]
    scores = jnp.einsum('nclhs,ncmhs->nhclm', cf, bf) * decay
    y_diag = jnp.einsum('nhclm,ncmhp->nclhp', scores, xdt)
    to_end = jnp.exp(acs[..., -1:] - acs)
    chunk_states = jnp.einsum('nclhs,nhcl,nclhp->nchps', bf, to_end, xdt)
    chunk_decay = jnp.exp(acs[..., -1])

    def step(h, inp):
        d, s = inp
        return d[:, :, None, None] * h + s, h

    h_fin, h_prev = lax.scan(step, h0.astype(f32),
                             (jnp.moveaxis(chunk_decay, 2, 0), jnp.moveaxis(chunk_states, 1, 0)))
    y_off = jnp.einsum('nclhs,cnhps,nhcl->nclhp', cf, h_prev, jnp.exp(acs))
    y = (y_diag + y_off).reshape(n, lp, hh, p)[:, :l]
    return y.astype(x.dtype), h_fin.astype(h0.dtype)

def masked_softmax(s, mask):
    p = jax.nn.softmax(jnp.where(mask, s, NEG), axis=-1)
    return jnp.where(mask, p, 0.0)

def compress_rows(rows, pe, w1, b1, w2, b2):
    n, s, d = rows.shape
    ch = rows.reshape(n, s // CMP_STRIDE, CMP_STRIDE, d)
    first = jnp.einsum('nmjd,jdf->nmf', ch, w1[:CMP_STRIDE])
    second = jnp.einsum('nmjd,jdf->nmf', ch, w1[CMP_STRIDE:])
    pe_term = jnp.einsum('jd,jdf->f', pe, w1)
    hid = jax.nn.silu(first[:, :-1] + second[:, 1:] + pe_term + b1)
    return hid @ w2 + b2

def compress_kv(k_raw, v_raw, lp):
    kc = compress_rows(k_raw, lp['cmp_pe'][0], lp['cmp_w1'][0], lp['cmp_b1'][0], lp['cmp_w2'][0], lp['cmp_b2'][0])
    vc = compress_rows(v_raw, lp['cmp_pe'][1], lp['cmp_w1'][1], lp['cmp_b1'][1], lp['cmp_w2'][1], lp['cmp_b2'][1])
    return rmsnorm(kc, lp['k_g'][0]), vc

def block_importance(pg, n_blocks):
    r = SEL_BLOCK // CMP_STRIDE
    nb = CMP_BLOCK // CMP_STRIDE - 1
    nc = pg.shape[-1]
    p = jnp.pad(pg, ((0, 0), (0, 0), (nb, r * n_blocks - nc)))
    total = None
    for o in range(-nb, r):
        w = (min(CMP_STRIDE * o + CMP_BLOCK, SEL_BLOCK) - max(CMP_STRIDE * o, 0)) / CMP_BLOCK
        start = o + nb
        term = w * p[..., start:start + r * (n_blocks - 1) + 1:r]
        total = term if total is None else total + term
    return total

def nsa_core(q, qpos, kc, vc, ks, vs, kw, vw, kpos, gates):
    n, tq = q.shape[:2]
    scale = NSA_HEAD_DIM ** -0.5
    nc = kc.shape[1]
    cvalid = (jnp.arange(nc) * CMP_STRIDE + CMP_BLOCK - 1)[None, :] <= qpos[:, None]
    s_c = jnp.einsum('nqhd,ncd->nqhc', q, kc).astype(jnp.float32) * scale
    p_c = masked_softmax(s_c, cvalid[None, :, None, :])
    o_c = jnp.einsum('nqhc,ncd->nqhd', p_c.astype(vc.dtype), vc)
    ns = ks.shape[1] // SEL_BLOCK
    p_sel = block_importance(p_c.sum(axis=2), ns)
    cur = qpos // SEL_BLOCK
    j = jnp.arange(ns)
    valid = j[None, :] <= cur[:, None]
    forced = valid & ((j[None, :] == 0) | (j[None, :] > cur[:, None] - SEL_LOCAL))
    score = jnp.where(forced, jnp.inf, jnp.where(valid, p_sel, -jnp.inf))
    n_sel = min(SEL_TOPN, ns)
    _, idx = lax.top_k(score, n_sel)
    tok = (idx[..., None] * SEL_BLOCK + jnp.arange(SEL_BLOCK)).reshape(n, tq, n_sel * SEL_BLOCK)
    ksel = jax.vmap(lambda k, t: k[t])(ks, tok)
    vsel = jax.vmap(lambda v, t: v[t])(vs, tok)
    smask = (tok <= qpos[None, :, None])[:, :, None, :]
    s_s = jnp.einsum('nqhd,nqkd->nqhk', q, ksel).astype(jnp.float32) * scale
    p_s = masked_softmax(s_s, smask)
    o_s = jnp.einsum('nqhk,nqkd->nqhd', p_s.astype(vsel.dtype), vsel)
    dpos = qpos[:, None] - kpos[None, :]
    wmask = (dpos >= 0) & (dpos <= WINDOW) & (kpos[None, :] >= 0)
    s_w = jnp.einsum('nqhd,nkd->nqhk', q, kw).astype(jnp.float32) * scale
    p_w = masked_softmax(s_w, wmask[None, :, None, :])
    o_w = jnp.einsum('nqhk,nkd->nqhd', p_w.astype(vw.dtype), vw)
    return gates[..., 0:1] * o_c + gates[..., 1:2] * o_s + gates[..., 2:3] * o_w

def attend_prompt(q, rows, win_rows, gates, lp):
    n, l = q.shape[:2]
    kc, vc = compress_kv(rows[:, :, 0], rows[:, :, 1], lp)
    ks, vs = rows[:, :, 2], rows[:, :, 3]
    kw_pad = jnp.pad(win_rows, ((0, 0), (WINDOW, 0), (0, 0), (0, 0)))

    def block(b):
        s0 = b * Q_BLOCK
        qb = lax.dynamic_slice_in_dim(q, s0, Q_BLOCK, axis=1)
        gb = lax.dynamic_slice_in_dim(gates, s0, Q_BLOCK, axis=1)
        kwb = lax.dynamic_slice_in_dim(kw_pad, s0, WINDOW + Q_BLOCK, axis=1)
        qpos = s0 + jnp.arange(Q_BLOCK)
        kpos = s0 - WINDOW + jnp.arange(WINDOW + Q_BLOCK)
        return nsa_core(qb, qpos, kc, vc, ks, vs, kwb[:, :, 0], kwb[:, :, 1], kpos, gb)

    o = lax.map(block, jnp.arange(l // Q_BLOCK))
    o = jnp.moveaxis(o, 0, 1).reshape(n, l, NSA_HEADS, NSA_HEAD_DIM)
    new_pages = rows.reshape(n * l // PAGE_SIZE, PAGE_SIZE, KV_SLOTS, NSA_HEAD_DIM)
    new_win = win_rows[:, l - min(WINDOW, l):]
    return o, (new_pages, new_win)

def make_attend_sample(cache_kv_l, cache_win_l, page_table):
    def attend(q, rows, win_rows, gates, lp):
        n, l = q.shape[:2]
        past = cache_kv_l[page_table].reshape(n, -1, KV_SLOTS, NSA_HEAD_DIM)
        p_len = past.shape[1]
        full = jnp.concatenate([past.astype(rows.dtype), rows], axis=1)
        t = p_len + l
        s = -(-t // SEL_BLOCK) * SEL_BLOCK
        full = jnp.pad(full, ((0, 0), (0, s - t), (0, 0), (0, 0)))
        kc, vc = compress_kv(full[:, :, 0], full[:, :, 1], lp)
        kw = jnp.concatenate([cache_win_l.astype(win_rows.dtype), win_rows], axis=1)
        wb = cache_win_l.shape[1]
        qpos = p_len + jnp.arange(l)
        kpos = p_len - wb + jnp.arange(wb + l)
        o = nsa_core(q, qpos, kc, vc, full[:, :, 2], full[:, :, 3], kw[:, :, 0], kw[:, :, 1], kpos, gates)
        return o, (rows, kw[:, l:])
    return attend

def trunk_layer(x, c, lp, prev_sc, prev_bconv, h0, prev_cf, attend):
    n, l, _ = x.shape
    ada = jax.nn.silu(c) @ lp['w_ada'] + lp['b_ada']
    shift, scale, ada_gate = jnp.split(ada, 3, axis=-1)
    h = rmsnorm(x, lp['norm_g']) * (1 + scale[:, None]) + shift[:, None]
    proj = h @ lp['w_in']
    offs = np.cumsum(SPLITS)[:-1].tolist()
    (a_h, a_b, a_c, a_g, b_z, b_xbc, b_dt, c_glu, c_g, d_q, d_kv, d_g, d_bg) = jnp.split(proj, offs, axis=-1)
    u_a, st_sc = causal_dwconv(a_c * a_h, prev_sc, lp['sc_w'])
    y_a = jax.nn.silu(a_g) * a_b * u_a
    xbc, st_bconv = causal_dwconv(b_xbc, prev_bconv, lp['ssd_conv_w'], lp['ssd_conv_b'])
    xbc = jax.nn.silu(xbc)
    xs, bs, cs = jnp.split(xbc, [W_GROUP, W_GROUP + SSD_GROUPS * SSD_STATE], axis=-1)
    rep = SSD_HEADS // SSD_GROUPS
    xs = xs.reshape(n, l, SSD_HEADS, SSD_HEAD_DIM)
    bs = jnp.repeat(bs.reshape(n, l, SSD_GROUPS, SSD_STATE), rep, axis=2)
    cs = jnp.repeat(cs.reshape(n, l, SSD_GROUPS, SSD_STATE), rep, axis=2)
    dt = jax.nn.softplus((b_dt + lp['ssd_dt_bias']).astype(jnp.float32))
    a_neg = -jnp.exp(lp['ssd_A_log'].astype(jnp.float32))
    y_ssd, st_h = ssd_scan(xs, dt, a_neg, bs, cs, h0)
    y_b = (y_ssd + lp['ssd_D'][:, None] * xs).reshape(n, l, W_GROUP)
    y_b = rmsnorm(y_b * jax.nn.silu(b_z), lp['ssd_norm_g'])
    glu_a, glu_b = jnp.split(c_glu, 2, axis=-1)
    u_c, st_cf = causal_dwconv(glu_a * jax.nn.sigmoid(glu_b), prev_cf, lp['cf_w'], lp['cf_b'])
    y_c = jax.nn.silu(c_g) * jax.nn.silu(layernorm(u_c, lp['cf_ln_g'], lp['cf_ln_b']))
    q = rmsnorm(d_q.reshape(n, l, NSA_HEADS, NSA_HEAD_DIM), lp['q_g'])
    kv = d_kv.reshape(n, l, 6, NSA_HEAD_DIM)
    k_slc = rmsnorm(kv[:, :, 2], lp['k_g'][1])
    k_win = rmsnorm(kv[:, :, 4], lp['k_g'][2])
    rows = jnp.stack([kv[:, :, 0], kv[:, :, 1], k_slc, kv[:, :, 3]], axis=2)
    win_rows = jnp.stack([k_win, kv[:, :, 5]], axis=2)
    gates = jax.nn.sigmoid(d_bg.reshape(n, l, NSA_HEADS, 3))
    o, st_attn = attend(q, rows, win_rows, gates, lp)
    y_d = jax.nn.silu(d_g) * o.reshape(n, l, W_GROUP)
    out = jnp.concatenate([y_a, y_b, y_c, y_d], axis=-1) @ lp['w_out']
    x = x + ada_gate[:, None] * out
    return x, st_attn + (st_sc, st_bconv, st_h, st_cf)

def setup_inputs(seed: int = 0) -> dict:
    key = jax.random.key(seed)
    keys = iter(jax.random.split(key, 48))
    f32 = jnp.float32

    def nrm(shape, s):
        return jax.random.normal(next(keys), shape, f32) * s

    n_pages = PAST_LEN // PAGE_SIZE
    n_pool = (5 * DEC_BATCH * n_pages) // 4
    win_buf = min(WINDOW, PAST_LEN)
    perm = jax.random.permutation(next(keys), n_pool)[:DEC_BATCH * n_pages]
    page_table = perm.reshape(DEC_BATCH, n_pages).astype(jnp.int32)
    dt_init = jnp.exp(jax.random.uniform(next(keys), (DEPTH, SSD_HEADS), f32, float(np.log(1e-3)), float(np.log(1e-1))))
    ssd_dt_bias = dt_init + jnp.log(-jnp.expm1(-dt_init))
    ssd_A_log = jnp.log(jax.random.uniform(next(keys), (DEPTH, SSD_HEADS), f32, 1.0, 16.0))
    return {
        'x_prompt': nrm((BATCH, SEQ, D_MODEL), 1.0),
        'x_sample': nrm((DEC_BATCH, DEC_SEQ, D_MODEL), 1.0),
        'cache_kv': nrm((DEPTH, n_pool, PAGE_SIZE, KV_SLOTS, NSA_HEAD_DIM), 1.0),
        'cache_win': nrm((DEPTH, DEC_BATCH, win_buf, 2, NSA_HEAD_DIM), 1.0),
        'state_sconv': nrm((DEPTH, DEC_BATCH, SC_WIDTH - 1, W_GROUP), 1.0),
        'state_ssm_conv': nrm((DEPTH, DEC_BATCH, SSD_CONV - 1, SSD_CONV_DIM), 1.0),
        'state_ssm': nrm((DEPTH, DEC_BATCH, SSD_HEADS, SSD_HEAD_DIM, SSD_STATE), 0.5),
        'state_cconv': nrm((DEPTH, DEC_BATCH, CF_WIDTH - 1, W_GROUP), 1.0),
        'page_table': page_table,
        'c_prompt': nrm((BATCH, D_MODEL), 1.0),
        'c_sample': nrm((DEC_BATCH, D_MODEL), 1.0),
        'norm_g': 1.0 + nrm((DEPTH, D_MODEL), 0.05),
        'w_ada': nrm((DEPTH, D_MODEL, 3 * D_MODEL), D_MODEL ** -0.5),
        'b_ada': nrm((DEPTH, 3 * D_MODEL), 0.02),
        'w_in': nrm((DEPTH, D_MODEL, D_IN), D_MODEL ** -0.5),
        'w_out': nrm((DEPTH, D_MIX, D_MODEL), D_MIX ** -0.5),
        'sc_w': nrm((DEPTH, SC_WIDTH, W_GROUP), SC_WIDTH ** -0.5),
        'ssd_conv_w': nrm((DEPTH, SSD_CONV, SSD_CONV_DIM), SSD_CONV ** -0.5),
        'ssd_conv_b': nrm((DEPTH, SSD_CONV_DIM), 0.02),
        'ssd_dt_bias': ssd_dt_bias,
        'ssd_A_log': ssd_A_log,
        'ssd_D': 1.0 + nrm((DEPTH, SSD_HEADS), 0.1),
        'ssd_norm_g': 1.0 + nrm((DEPTH, W_GROUP), 0.05),
        'cf_w': nrm((DEPTH, CF_WIDTH, W_GROUP), CF_WIDTH ** -0.5),
        'cf_b': nrm((DEPTH, W_GROUP), 0.02),
        'cf_ln_g': 1.0 + nrm((DEPTH, W_GROUP), 0.05),
        'cf_ln_b': nrm((DEPTH, W_GROUP), 0.02),
        'q_g': 1.0 + nrm((DEPTH, NSA_HEAD_DIM), 0.05),
        'k_g': 1.0 + nrm((DEPTH, 3, NSA_HEAD_DIM), 0.05),
        'cmp_pe': nrm((DEPTH, 2, CMP_BLOCK, NSA_HEAD_DIM), 0.1),
        'cmp_w1': nrm((DEPTH, 2, CMP_BLOCK, NSA_HEAD_DIM, CMP_HIDDEN), (CMP_BLOCK * NSA_HEAD_DIM) ** -0.5),
        'cmp_b1': nrm((DEPTH, 2, CMP_HIDDEN), 0.02),
        'cmp_w2': nrm((DEPTH, 2, CMP_HIDDEN, NSA_HEAD_DIM), CMP_HIDDEN ** -0.5),
        'cmp_b2': nrm((DEPTH, 2, NSA_HEAD_DIM), 0.02),
    }

def reference(x_prompt, x_sample, cache_kv, cache_win, state_sconv, state_ssm_conv, state_ssm, state_cconv,
              page_table, c_prompt, c_sample, norm_g, w_ada, b_ada, w_in, w_out, sc_w, ssd_conv_w, ssd_conv_b,
              ssd_dt_bias, ssd_A_log, ssd_D, ssd_norm_g, cf_w, cf_b, cf_ln_g, cf_ln_b, q_g, k_g,
              cmp_pe, cmp_w1, cmp_b1, cmp_w2, cmp_b2):
    nb = x_prompt.shape[0]
    dt = x_prompt.dtype
    z_sc = jnp.zeros((nb, SC_WIDTH - 1, W_GROUP), dt)
    z_bc = jnp.zeros((nb, SSD_CONV - 1, SSD_CONV_DIM), dt)
    z_h = jnp.zeros((nb, SSD_HEADS, SSD_HEAD_DIM, SSD_STATE), dt)
    z_cf = jnp.zeros((nb, CF_WIDTH - 1, W_GROUP), dt)
    yp, ys = x_prompt, x_sample
    acc_p, acc_s = [], []
    for l in range(DEPTH):
        lp = {'norm_g': norm_g[l], 'w_ada': w_ada[l], 'b_ada': b_ada[l], 'w_in': w_in[l], 'w_out': w_out[l],
              'sc_w': sc_w[l], 'ssd_conv_w': ssd_conv_w[l], 'ssd_conv_b': ssd_conv_b[l],
              'ssd_dt_bias': ssd_dt_bias[l], 'ssd_A_log': ssd_A_log[l], 'ssd_D': ssd_D[l],
              'ssd_norm_g': ssd_norm_g[l], 'cf_w': cf_w[l], 'cf_b': cf_b[l], 'cf_ln_g': cf_ln_g[l],
              'cf_ln_b': cf_ln_b[l], 'q_g': q_g[l], 'k_g': k_g[l], 'cmp_pe': cmp_pe[l], 'cmp_w1': cmp_w1[l],
              'cmp_b1': cmp_b1[l], 'cmp_w2': cmp_w2[l], 'cmp_b2': cmp_b2[l]}
        yp, st_p = trunk_layer(yp, c_prompt, lp, z_sc, z_bc, z_h, z_cf, attend_prompt)
        ys, st_s = trunk_layer(ys, c_sample, lp, state_sconv[l], state_ssm_conv[l], state_ssm[l], state_cconv[l],
                               make_attend_sample(cache_kv[l], cache_win[l], page_table))
        acc_p.append(st_p)
        acc_s.append(st_s)
    kv_p, win_p, sc_p, bc_p, h_p, cf_p = [jnp.stack(a) for a in zip(*acc_p)]
    kv_s, win_s, sc_s, bc_s, h_s, cf_s = [jnp.stack(a) for a in zip(*acc_s)]
    return (yp, ys, kv_p, kv_s, win_p, win_s, sc_p, sc_s, bc_p, bc_s, h_p, h_s, cf_p, cf_s)


_drawn_inputs = setup_inputs


def setup_inputs(seed=0):
    import zlib

    import numpy as np

    out = dict(_drawn_inputs(seed))
    spreads = {}
    factors = {'cache_kv': 5.652,
     'ssd_D': 41.731,
     'ssd_norm_g': 5.199,
     'cf_b': 8.0,
     'cf_ln_g': 8.0,
     'cf_ln_b': 40.949,
     'q_g': 8.0,
     'cmp_pe': 8.0,
     'cmp_b1': 37.026,
     'cmp_b2': 36.243}
    for name, (base, spread) in spreads.items():
        noise = np.random.default_rng([zlib.crc32(name.encode()), seed]).standard_normal(out[name].shape)
        drawn = base * np.exp(spread * noise) if base else spread * noise
        out[name] = __import__('jax').numpy.asarray(drawn.astype(out[name].dtype))
    for name, factor in factors.items():
        out[name] = (out[name] * factor).astype(out[name].dtype)
    return out
```

```python
from contextlib import ExitStack

import concourse.bass as bass
from concourse import mybir

F32 = mybir.dt.float32
I32 = mybir.dt.int32
ALU = mybir.AluOpType
ACT = mybir.ActivationFunctionType
AX = mybir.AxisListType

P = 128
D = 1024
KT = D // P
W = 256
T = 2048
NC = T // P
NS = 8
TT = T + NS
GT = 512
NG = T // GT
SH, SP, SST = 4, 64, 128
CV = 768
KCF = 31
H, HD = 4, 64
PAST = 2048
PAGES = PAST // P
NCMP = T // 16 - 1
NBLK = T // 64
EPS = 1e-6
NEG = -1e30
BIG = 1e30
SCALE = HD ** -0.5

COL_A = 0
COL_Z = 4 * W
COL_XBC = COL_Z + W
COL_DT = COL_XBC + CV
COL_GLU = COL_DT + SH
COL_CG = COL_GLU + 2 * W
COL_Q = COL_CG + W
COL_KV = COL_Q + W
COL_DG = COL_KV + 6 * HD
COL_BG = COL_DG + W
TM = W + 6 * HD + 3 * H

PA_ROWS, PB_ROWS, PC_ROWS = 5, 38, 4
PA = 0
PB = PA + 6 * PA_ROWS
PC = PB + 2 * PB_ROWS
PEND = PC + 8 * PC_ROWS
B_SC, B_CF, B_CFB, B_LNG, B_LNB, B_SSDG = 0, 3, 34, 35, 36, 37


class Shared:

    def __init__(self, io):
        self.io = io


def chain(eng, sem):
    count = [0]

    def link(ins):
        count[0] += 1
        ins.then_inc(sem, 1)
        eng.wait_ge(sem, count[0])
    return link


def stage_prepare(nc, k, sem):
    NV = NS + 1
    WB = 512
    NB = 3 * D // WB
    with ExitStack() as ctx:
        def sb(name, shape, dt=F32):
            return ctx.enter_context(nc.sbuf_tensor(name, shape, dt))
        c_rows, c_silu = sb("c_rows", [NV, D]), sb("c_silu", [NV, D])
        rows_a, rows_b, rows_c = sb("rows_a", [PA_ROWS, CV]), sb("rows_b", [PB_ROWS, W]), sb("rows_c", [PC_ROWS, D])
        cT = sb("cT", [P, KT, NV])
        w_ada = k.hview(0, 2 * KT * WB).rearrange("p (b k n) -> p b k n", b=2, k=KT)
        pick_prompt = sb("pick_prompt", [NV, P])
        b_gate = sb("b_gate", [NV, D])
        gates = sb("gates", [NV, D])
        blk_rows = k.hview(2 * KT * WB, T)[0:NBLK, :]
        rows_in, c_in, bg_in, w_in, silu_done, tr_done, cp_done, w_used, ada_done, gate_done, gsum_done, bc_done, g_done = (
            sem(n) for n in ("rows_in", "c_in", "bg_in", "wada_in", "csilu", "ptr_done", "pcp_done", "wada_used",
                             "ada_done", "gate_done", "gsum_done", "bc_done", "pconst_done"))
        w_in1 = sem("wada_in1")
        blk_sent = sem("blk_sent")
        block = ctx.enter_context(nc.Block())
        par_ps, cT_ps = k.ps[:, 0, 0:PEND], k.ps[:, 1, 0:KT * NV]
        ada_ps = k.ps[:, 2, 0:2 * KT * NV]

        @block.sync
        def _(sp):
            sp.dma_start(c_rows[0:NS, :], k.io["c_sample"]).then_inc(c_in, 16)
            sp.dma_start(c_rows[NS:NV, :], k.io["c_prompt"]).then_inc(c_in, 16)
            for b in range(NB):
                if b >= 2:
                    sp.wait_ge(w_used, b - 1)
                sp.dma_start(w_ada[:, b % 2], k.io["w_ada"][0].rearrange("(k p) n -> p k n", p=P)[:, :, b * WB:(b + 1) * WB]
                             ).then_inc(w_in1 if b % 2 else w_in, 16)

        @block.scalar
        def _(act):
            sc = k.io["sc_w"][0], k.io["cf_w"][0]
            act.dma_start(rows_a[0:4, :], k.io["ssd_conv_w"][0]).then_inc(rows_in, 16)
            act.dma_start(rows_a[4:5, :], k.io["ssd_conv_b"]).then_inc(rows_in, 16)
            act.dma_start(rows_b[B_SC:B_SC + 3, :], sc[0]).then_inc(rows_in, 16)
            act.dma_start(rows_b[B_CF:B_CF + KCF, :], sc[1]).then_inc(rows_in, 16)
            for r, a in ((B_CFB, k.io["cf_b"]), (B_LNG, k.io["cf_ln_g"]), (B_LNB, k.io["cf_ln_b"]), (B_SSDG, k.io["ssd_norm_g"])):
                act.dma_start(rows_b[r:r + 1, :], a).then_inc(rows_in, 16)
            act.dma_start(rows_c[0:1, :], k.io["norm_g"]).then_inc(rows_in, 16)
            act.dma_start(rows_c[1:4, :], k.io["b_ada"][0].rearrange("(r d) -> r d", r=3)).then_inc(rows_in, 16)
            act.dma_start(b_gate[:, :], k.io["b_ada"][0:1, 2 * D:3 * D].broadcast_to([NV, D])).then_inc(bg_in, 16)
            act.wait_ge(c_in, 32)
            nc.scalar.activation(c_silu[:, :], c_rows[:, :], ACT.Silu).then_inc(silu_done, 1)

        @block.gpsimd
        def _(pool):
            g = nc.gpsimd
            link = chain(pool, g_done)
            link(g.memset(k.ones[:, :], 1.0))

            def select(t, src, pattern, base, mult, fill, op=ALU.is_ge):
                link(g.affine_select(out=t, in_=src, pattern=pattern, compare_op=op, fill=fill, base=base,
                                     channel_multiplier=mult))
            one = k.ones[:, :]
            select(k.ident[:, :], one, [[-1, P]], 0, 1, 0.0, ALU.is_equal)
            select(k.upper[:, :], one, [[1, P]], 0, -1, 0.0)
            select(k.below[:, :], one, [[-1, P]], -1, 1, 0.0)
            link(g.memset(k.neg_upper[:, :], 0.0))
            for h in range(SH):
                v = k.neg_upper[:, h * P:(h + 1) * P]
                select(v, v, [[1, P]], 0, -1, NEG)
            link(g.memset(k.causal[:, :], 0.0))
            select(k.causal[:, :], k.causal[:, :], [[-1, P]], 0, 1, NEG)
            link(g.memset(k.win_low[:, :], 0.0))
            select(k.win_low[:, :], k.win_low[:, :], [[1, P]], 0, -1, NEG)
            link(g.memset(k.cmp_mask[:, :], 0.0))
            select(k.cmp_mask[:, :], k.cmp_mask[:, :], [[-16, 2 * P]], 16 * P - 31, 1, NEG)
            link(g.memset(k.sel_mask[:, :], BIG))
            select(k.sel_mask[:, :], k.sel_mask[:, :], [[64, 2 * NBLK]], 64 * (2 - NBLK) - 1, -1, 0.0)
            select(k.sel_mask[:, :], k.sel_mask[:, :], [[-64, 2 * NBLK]], 64 * NBLK, 1, NEG)
            link(g.memset(blk_rows[:, :], 1.0))
            select(blk_rows[:, :], blk_rows[:, :], [[1, T]], 0, -64, 0.0)
            select(blk_rows[:, :], blk_rows[:, :], [[-1, T]], 63, 64, 0.0)
            pool.dma_start(k.blk_dram[:, :], blk_rows[:, :]).then_inc(blk_sent, 16)
            link(g.memset(pick_prompt[:, :], 1.0))
            select(pick_prompt[:, :], pick_prompt[:, :], [[0, P]], -NS, 1, 0.0)
            for j in range(2):
                v = k.head_pick[:, j, :]
                link(g.memset(v, 1.0))
                select(v, v, [[1, P]], 2 * j * SP, -SP, 0.0)
                select(v, v, [[-1, P]], -2 * j * SP + SP - 1, SP, 0.0)
            pool.wait_ge(blk_sent, 16)

        n_const = 1 + 3 + 1 + SH + 2 + 2 + 2 + 3 + 3 + 2 + 6

        @block.tensor
        def _(pe):
            m = nc.tensor
            pe.wait_ge(g_done, n_const)
            pe.wait_ge(rows_in, 160)
            for n in range(6):
                m.transpose(par_ps[:, PA + n * PA_ROWS:PA + (n + 1) * PA_ROWS], rows_a[:, n * P:(n + 1) * P],
                            k.ident[0:PA_ROWS, 0:PA_ROWS])
            for n in range(2):
                m.transpose(par_ps[:, PB + n * PB_ROWS:PB + (n + 1) * PB_ROWS], rows_b[:, n * P:(n + 1) * P],
                            k.ident[0:PB_ROWS, 0:PB_ROWS])
            for n in range(8):
                last = m.transpose(par_ps[:, PC + n * PC_ROWS:PC + (n + 1) * PC_ROWS], rows_c[:, n * P:(n + 1) * P],
                                   k.ident[0:PC_ROWS, 0:PC_ROWS])
            last.then_inc(tr_done, 1)
            pe.wait_ge(silu_done, 1)
            for n in range(KT):
                last = m.transpose(cT_ps[:, n * NV:(n + 1) * NV], c_silu[:, n * P:(n + 1) * P], k.ident[0:NV, 0:NV])
            last.then_inc(tr_done, 1)
            pe.wait_ge(cp_done, 2)
            for b in range(NB):
                pe.wait_ge(w_in1 if b % 2 else w_in, 16 * (b // 2 + 1))
                if b < 4:
                    for n in range(4):
                        for kk in range(KT):
                            last = m.matmul(ada_ps[:, (4 * b + n) * NV:(4 * b + n + 1) * NV],
                                            w_ada[:, b % 2, kk, n * P:(n + 1) * P], cT[:, kk, :],
                                            start=(kk == 0), stop=(kk == KT - 1))
                    last.then_inc(w_used, 1)
                else:
                    for kk in range(KT):
                        last = m.matmul(k.ps[0:NV, b - 1, :], cT[:, kk, :], w_ada[:, b % 2, kk, :],
                                        start=(kk == 0), stop=(kk == KT - 1))
                    last.then_inc(w_used, 1)
            pe.wait_ge(gsum_done, 1)
            for n in range(2):
                last = m.matmul(k.ps[:, 5 + n, :], pick_prompt[:, :], gates[:, n * 512:(n + 1) * 512], start=True, stop=True)
            last.then_inc(bc_done, 1)

        @block.vector
        def _(dve):
            v = nc.vector
            dve.wait_ge(tr_done, 1)
            v.tensor_copy(k.par[:, :], par_ps).then_inc(cp_done, 1)
            dve.wait_ge(tr_done, 2)
            v.tensor_copy(cT[:, :, :].rearrange("p k n -> p (k n)"), cT_ps).then_inc(cp_done, 1)
            dve.wait_ge(w_used, 4)
            dve.wait_ge(cp_done, 2)
            pc = k.par[:, PC:PEND].rearrange("p (n r) -> p n r", r=PC_ROWS)
            ada = ada_ps.rearrange("p (n v) -> p n v", v=NV)
            v.tensor_tensor(k.shift[:, :, :], ada[:, 0:KT, :], pc[:, :, 1:2].broadcast_to([P, KT, NV]), ALU.add)
            link = chain(dve, ada_done)
            link(v.tensor_tensor(k.scale[:, :, :], ada[:, KT:2 * KT, :], pc[:, :, 2:3].broadcast_to([P, KT, NV]), ALU.add))
            link(v.tensor_scalar(k.scale[:, :, :], k.scale[:, :, :], 1.0, None, ALU.add))
            link(v.tensor_tensor(k.scale[:, :, :], k.scale[:, :, :], pc[:, :, 0:1].broadcast_to([P, KT, NV]), ALU.mult))
            dve.wait_ge(w_used, NB)
            dve.wait_ge(bg_in, 16)
            link(v.tensor_tensor(gates[:, 0:512], k.ps[0:NV, 3, :], b_gate[:, 0:512], ALU.add))
            v.tensor_tensor(gates[:, 512:D], k.ps[0:NV, 4, :], b_gate[:, 512:D], ALU.add).then_inc(gsum_done, 1)
            dve.wait_ge(gsum_done, 1)
            v.tensor_copy(k.gate_s[:, :], gates[0:NS, :])
            dve.wait_ge(bc_done, 1)
            v.tensor_copy(k.gate_p[:, 0:512], k.ps[:, 5, :])
            v.tensor_copy(k.gate_p[:, 512:D], k.ps[:, 6, :])


def stage_norm(nc, k, sem):
    NX = 3
    with ExitStack() as ctx:
        def sb(name, shape, dt=F32):
            return ctx.enter_context(nc.sbuf_tensor(name, shape, dt))
        x_in = sb("x_in", [P, NX, D])
        x_n = sb("x_n", [P, 2, D])
        junk = sb("junk", [P, D])
        stat = sb("stat", [P, NC + 1, 4])
        x_in0 = [sem(f"x_in{i}") for i in range(NX)]
        sq_done, var_done, root_done, xn_done, tr_done, ev_v, ev_a, link_s, aux = (
            sem(n) for n in ("sq_done", "var_done", "root_done", "xn_done", "xtr_done", "hev_v", "hev_a", "nlink", "naux"))
        block = ctx.enter_context(nc.Block())
        rows = [P] * NC + [NS]

        @block.sync
        def _(sp):
            for t in range(NC + 1):
                if t >= NX:
                    sp.wait_ge(xn_done, t - NX + 1)
                src = k.io["x_prompt"][0, t * P:(t + 1) * P, :] if t < NC else k.io["x_sample"][:, 0, :]
                sp.dma_start(x_in[0:rows[t], t % NX, :], src).then_inc(x_in0[t % NX], 16)

        @block.scalar
        def _(act):
            def head(t):
                r = rows[t]
                act.wait_ge(x_in0[t % NX], 16 * (t // NX + 1))
                if t:
                    act.wait_ge(sq_done, t)
                nc.scalar.activation(junk[0:r, :], x_in[0:r, t % NX, :], ACT.Square,
                                     accum_out=stat[0:r, t, 0:1]).then_inc(sq_done, 1)
                act.wait_ge(var_done, t + 1)
                nc.scalar.activation(stat[0:r, t, 3:4], stat[0:r, t, 2:3], ACT.Sqrt).then_inc(root_done, 1)

            head(0)
            for t in range(NC):
                head(t + 1)
                act.wait_ge(tr_done, t + 1)
                for kk in range(4, 8):
                    last = nc.scalar.activation(k.hT[:, kk, t * P:(t + 1) * P], k.ps[:, 2 * (t % 2) + 1, (kk - 4) * P:(kk - 3) * P],
                                                ACT.Identity, bias=k.shift[:, kk, NS:NS + 1], scale=k.scale[:, kk, NS:NS + 1])
                last.then_inc(ev_a, 1)

        @block.tensor
        def _(pe):
            for t in range(NC + 1):
                r = rows[t]
                pe.wait_ge(xn_done, t + 1)
                if t >= 2:
                    pe.wait_ge(ev_v, t - 1)
                    pe.wait_ge(ev_a, t - 1)
                for kk in range(KT):
                    last = nc.tensor.transpose(k.ps[:, 2 * (t % 2) + kk // 4, (kk % 4) * r:(kk % 4 + 1) * r],
                                               x_n[0:r, t % 2, kk * P:(kk + 1) * P], k.ident[0:r, 0:r])
                last.then_inc(tr_done, 1)

        @block.vector
        def _(dve):
            v = nc.vector
            link = chain(dve, link_s)

            def head(t):
                r = rows[t]
                dve.wait_ge(sq_done, t + 1)
                link(v.tensor_scalar(stat[0:r, t, 1:2], stat[0:r, t, 0:1], 1.0 / D, EPS, ALU.mult, ALU.add))
                v.reciprocal(stat[0:r, t, 2:3], stat[0:r, t, 1:2]).then_inc(var_done, 1)
                dve.wait_ge(root_done, t + 1)
                if t >= 2:
                    dve.wait_ge(tr_done, t - 1)
                v.tensor_scalar(x_n[0:r, t % 2, :], x_in[0:r, t % NX, :], stat[0:r, t, 3:4], None,
                                ALU.mult).then_inc(xn_done, 1)

            head(0)
            for t in range(NC):
                head(t + 1)
                dve.wait_ge(tr_done, t + 1)
                for kk in range(4):
                    last = v.tensor_scalar(k.hT[:, kk, t * P:(t + 1) * P], k.ps[:, 2 * (t % 2), kk * P:(kk + 1) * P],
                                           k.scale[:, kk, NS:NS + 1], k.shift[:, kk, NS:NS + 1], ALU.mult, ALU.add)
                last.then_inc(ev_v, 1)
            dve.wait_ge(tr_done, NC + 1)
            for half in range(2):
                src = k.ps[:, 2 * (NC % 2) + half, 0:4 * NS].rearrange("p (k n) -> p k n", n=NS)
                dst = k.hT[:, 4 * half:4 * half + 4, T:TT]
                link(v.tensor_tensor(dst, src, k.scale[:, 4 * half:4 * half + 4, 0:NS], ALU.mult))
                link(v.tensor_tensor(dst, dst, k.shift[:, 4 * half:4 * half + 4, 0:NS], ALU.add))


def channel_projection(nc, k, eng, cols, w_buf, w_ready, used, unit_done, unit_free):
    for i, c in enumerate(cols):
        eng.wait_ge(w_ready[i % 2], 16 * (i // 2 + 1))
        for g in range(NG + 1):
            u = i * (NG + 1) + g
            if u >= 8:
                unit_free(eng, u - 8)
            n, t0 = (GT, g * GT) if g < NG else (NS, T)
            for kk in range(KT):
                last = nc.tensor.matmul(k.ps[:, u % 8, 0:n], w_buf[:, i % 2, kk, :], k.hT[:, kk, t0:t0 + n],
                                        start=(kk == 0), stop=(kk == KT - 1))
            last.then_inc(unit_done, 1)


def load_tiles(k, sp, cols, w_buf, w_ready, unit_done):
    for i, c in enumerate(cols):
        if i >= 2:
            sp.wait_ge(unit_done, (i - 1) * (NG + 1))
        sp.dma_start(w_buf[:, i % 2], k.io["w_in"][0].rearrange("(k p) n -> p k n", p=P)[:, :, c:c + P]).then_inc(w_ready[i % 2], 16)


def stage_ssd_inputs(nc, k, sem):
    cols = [COL_XBC + P * j for j in range(6)] + [COL_Z, COL_Z + P]
    NJ = 6
    with ExitStack() as ctx:
        def sb(name, shape, dt=F32):
            return ctx.enter_context(nc.sbuf_tensor(name, shape, dt))
        w_buf = sb("w_buf", [P, 2, KT, P])
        w_dt = sb("w_dt", [P, KT, SH])
        raw = sb("raw_xbc", [P, 2, 3 + TT])
        prev_rows = sb("prev_rows", [3 * NS, CV])
        prev = sb("prev_xbc", [P, 6, NS, 3])
        tail = sb("tail_xbc", [P, 2, 3 + NS])
        tails = sb("tails_xbc", [3 + NS, CV])
        w_ready = [sem("wx_ready0"), sem("wx_ready1")]
        dt_in, prev_in, unit_done, evac, conv, silu, link_s, zero, prev_tr, prev_cp, tail_cp, tail_tr, tails_cp, stored, dt_done = (
            sem(n) for n in ("dt_in", "prev_in", "xunit", "xevac", "xconv", "xsilu", "xlink", "xzero", "xprev_tr", "xprev_cp",
                             "xtail_cp", "xtail_tr", "xtails_cp", "xstored", "dt_done"))
        block = ctx.enter_context(nc.Block())
        U = NG + 1

        @block.sync
        def _(sp):
            sp.dma_start(prev_rows[:, :], k.io["state_ssm_conv"][0].rearrange("s r c -> (s r) c")).then_inc(prev_in, 16)
            with nc.allow_non_contiguous_dma(reason="four columns of the projection"):
                sp.dma_start(w_dt[:, :, :], k.io["w_in"][0].rearrange("(k p) n -> p k n", p=P)[:, :, COL_DT:COL_DT + SH]).then_inc(dt_in, 16)
            load_tiles(k, sp, cols, w_buf, w_ready, unit_done)
            sp.dma_start(k.io["ssm_conv_s"][0, :, 0:2, :], k.io["state_ssm_conv"][0, :, 1:3, :]).then_inc(stored, 16)
            sp.wait_ge(tails_cp, 1)
            sp.dma_start(k.io["ssm_conv_p"][0, 0], tails[0:3, :]).then_inc(stored, 16)
            sp.dma_start(k.io["ssm_conv_s"][0, :, 2, :], tails[3:3 + NS, :]).then_inc(stored, 16)
            sp.wait_ge(stored, 48)

        @block.tensor
        def _(pe):
            m = nc.tensor
            pe.wait_ge(prev_in, 16)
            for j in range(NJ):
                last = m.transpose(k.ps[:, 7, j * 24:(j + 1) * 24], prev_rows[:, j * P:(j + 1) * P], k.ident[0:24, 0:24])
            last.then_inc(prev_tr, 1)
            pe.wait_ge(dt_in, 16)
            for t in range(NC + 1):
                r = P if t < NC else NS
                for kk in range(KT):
                    last = m.matmul(k.ps[0:r, 6, t * SH:(t + 1) * SH], k.hT[:, kk, t * P:t * P + r], w_dt[:, kk, :],
                                    start=(kk == 0), stop=(kk == KT - 1))
            last.then_inc(dt_done, 1)
            pe.wait_ge(prev_cp, 3)

            def free(eng, u):
                eng.wait_ge(evac, u + 1)
            channel_projection(nc, k, pe, cols, w_buf, w_ready, None, unit_done, free)
            pe.wait_ge(evac, len(cols) * U)
            for j in range(NJ):
                pe.wait_ge(tail_cp, j + 1)
                m.transpose(k.ps[0:3 + NS, j // 4, (j % 4) * P:(j % 4 + 1) * P], k.tails_T[:, j, :], k.ident[:, :]).then_inc(tail_tr, 1)

        @block.scalar
        def _(act):
            for i in range(len(cols)):
                for g in range(U):
                    n, t0 = (GT, g * GT) if g < NG else (NS, T)
                    u = i * U + g
                    act.wait_ge(unit_done, u + 1)
                    if i < NJ:
                        if i >= 2 and g == 0:
                            act.wait_ge(conv, i - 1)
                            act.wait_ge(tail_cp, i - 1)
                        nc.scalar.copy(raw[:, i % 2, 3 + t0:3 + t0 + n], k.ps[:, u % 8, 0:n]).then_inc(evac, 1)
                    else:
                        nc.scalar.activation(k.yT[i - NJ][:, t0:t0 + n], k.ps[:, u % 8, 0:n], ACT.Silu).then_inc(evac, 1)
                if 1 <= i <= NJ:
                    act.wait_ge(conv, i)
                    b = PA + (i - 1) * PA_ROWS + 4
                    nc.scalar.activation(k.xbc[:, i - 1, :], k.xbc[:, i - 1, :], ACT.Silu, bias=k.par[:, b:b + 1]).then_inc(silu, 1)

        @block.vector
        def _(dve):
            v = nc.vector
            link = chain(dve, link_s)
            link(v.memset(raw[:, :, 0:3], 0.0))
            link(v.memset(k.dt[:, :], 0.0))
            dve.wait_ge(prev_tr, 1)
            v.tensor_copy(prev[:, :, :, :].rearrange("p j s r -> p (j s r)"), k.ps[:, 7, 0:6 * 24]).then_inc(prev_cp, 1)
            dve.wait_ge(dt_done, 1)
            v.tensor_copy(k.dt[:, 0:NC * SH], k.ps[:, 6, 0:NC * SH]).then_inc(prev_cp, 1)
            dve.wait_ge(prev_cp, 2)
            v.tensor_copy(k.dt[0:NS, NC * SH:(NC + 1) * SH], k.ps[0:NS, 6, NC * SH:(NC + 1) * SH]).then_inc(prev_cp, 1)
            dve.wait_ge(prev_cp, 3)
            for j in range(NJ):
                dve.wait_ge(evac, (j + 1) * U)
                wc = [k.par[:, PA + j * PA_ROWS + q:PA + j * PA_ROWS + q + 1] for q in range(4)]
                r = raw[:, j % 2, :]
                o = k.xbc[:, j, 0:T]
                link(v.tensor_scalar(o, r[:, 3:3 + T], wc[3], None, ALU.mult))
                for q in range(3):
                    link(v.scalar_tensor_tensor(out=o, in0=r[:, q:q + T], scalar=wc[q], in1=o, op0=ALU.mult, op1=ALU.add))
                s = k.xbc[:, j, T:TT]
                link(v.tensor_scalar(s, r[:, 3 + T:3 + TT], wc[3], None, ALU.mult))
                for q in range(3):
                    ins = v.scalar_tensor_tensor(out=s, in0=prev[:, j, :, q], scalar=wc[q], in1=s, op0=ALU.mult, op1=ALU.add)
                    if q < 2:
                        link(ins)
                    else:
                        ins.then_inc(conv, 1)
                v.tensor_copy(k.tails_T[:, j, :], r[:, T:3 + TT]).then_inc(tail_cp, 1)
            dve.wait_ge(tail_tr, NJ)
            link(v.tensor_copy(tails[:, 0:512], k.ps[0:3 + NS, 0, :]))
            v.tensor_copy(tails[:, 512:CV], k.ps[0:3 + NS, 1, 0:256]).then_inc(tails_cp, 1)


def stage_ssd(nc, k, sem):
    NT = (NC + 1) * SH
    with ExitStack() as ctx:
        def sb(name, shape, dt=F32):
            return ctx.enter_context(nc.sbuf_tensor(name, shape, dt))
        bias_b, a_neg, d_col = sb("dt_bias_b", [P, SH]), sb("a_neg", [P, SH]), sb("ssd_d_col", [P, 2])
        e_abs, u1, um, zero_m, lnu, da = (sb(n, [P, NT]) for n in ("e_abs", "u1", "um", "zero_m", "lnu", "da"))
        da_exp = sb("da_exp", [NS, SH])
        aU = sb("aU", [P, SH, P])
        dec = sb("dec", [P, 2, SH, P])
        grow = sb("grow", [P, 2, SH, P])
        xdt, xde = sb("xdt", [P, SH, SP]), sb("xde", [P, SH, SP])
        b_tm = sb("b_tm", [P, 2, P])
        mix = sb("mix", [P, SH, P])
        cgrow = sb("cgrow", [P, SH, P])
        state = sb("ssd_state", [P, SH, SP])
        y_sum = sb("y_sum", [P, 2, P])
        st_out = sb("st_out", [P, 2, P])
        h0 = sb("h0", [P, NS, P])
        diag = sb("diag", [P, NS, P])
        hb = sb("hb", [P, NS, P])
        dtT = sb("dtT", [SH, 2, NS])
        dtb = sb("dtb", [P, 2, 2, NS])
        y_s = sb("y_s", [P, NS])
        coef = sb("coef_s", [P, NS])
        small_in, h0_in, dt_a, dt_v, link_s, tr, bt, xd, au, logs, scr, expd, expg, mixd, cg, yd, stn, std, y_fin, fin_tr, fin_cp, stored = (
            sem("s_" + n) for n in ("small_in", "h0_in", "dt_a", "dt_v", "link", "tr", "bt", "xd", "au", "logs", "scr", "expd",
                                    "expg", "mixd", "cg", "yd", "stn", "std", "y_fin", "fin_tr", "fin_cp", "stored"))
        d_pe, d_v, d_alink, h_new = sem("s_d_pe"), sem("s_d_v"), sem("s_alink"), sem("s_h_new")
        h_used = sem("s_h_used")
        btp = k.ps[:, 6, :]
        block = ctx.enter_context(nc.Block())
        tp, sc_ps, log_ps, grow_ps, y_ps, new_ps = (k.ps[:, b, :] for b in range(6))

        @block.sync
        def _(sp):
            sp.dma_start(bias_b[:, :], k.io["ssd_dt_bias"].broadcast_to([P, SH])).then_inc(small_in, 16)
            sp.dma_start(a_neg[:, :], k.io["ssd_A_log"].broadcast_to([P, SH])).then_inc(small_in, 16)
            for h in range(SH):
                sp.dma_start(d_col[(h % 2) * SP:(h % 2 + 1) * SP, h // 2:h // 2 + 1],
                             k.io["ssd_D"][0:1, h:h + 1].broadcast_to([SP, 1])).then_inc(small_in, 16)
            for j in range(2):
                if j:
                    sp.wait_ge(stored, 16)
                    sp.wait_ge(h_used, 1)
                sp.dma_start(h0[:, :, :], k.io["state_ssm"][0].rearrange("n (j h) p s -> j (h p) n s", j=2)[j]).then_inc(h0_in, 16)
                sp.wait_ge(h_new, j + 1)
                sp.dma_start(k.io["ssm_s"][0].rearrange("n (j h) p s -> j (h p) n s", j=2)[j], h0[:, :, :]).then_inc(stored, 16)
            sp.wait_ge(fin_cp, 1)
            sp.dma_start(k.io["ssm_p"][0, 0].rearrange("(j h) p s -> (h p) j s", j=2), st_out[:, :, :]).then_inc(stored, 16)
            sp.wait_ge(stored, 48)

        @block.scalar
        def _(act):
            link = chain(act, d_alink)
            act.wait_ge(dt_v, 1)
            link(nc.scalar.activation(e_abs[:, :], k.dt[:, :], ACT.Abs))
            link(nc.scalar.activation(e_abs[:, :], e_abs[:, :], ACT.Exp, scale=-1.0))
            nc.scalar.activation(a_neg[:, :], a_neg[:, :], ACT.Exp).then_inc(dt_a, 1)
            act.wait_ge(dt_v, 2)
            nc.scalar.activation(lnu[:, :], u1[:, :], ACT.Ln).then_inc(dt_a, 1)
            act.wait_ge(dt_v, 3)
            nc.scalar.activation(da_exp[:, :], da[0:NS, NC * SH:NT], ACT.Exp).then_inc(dt_a, 1)
            for c in range(NC):
                act.wait_ge(tr, c + 1)
                if c:
                    act.wait_ge(stn, c)
                nc.scalar.copy(b_tm[:, :, :].rearrange("p g s -> p (g s)"), btp[:, 0:2 * P]).then_inc(bt, 1)
                act.wait_ge(logs, c + 1)
                if c >= 2:
                    act.wait_ge(std, c - 1)
                nc.scalar.activation(dec[:, c % 2].rearrange("p h l -> p (h l)"), log_ps, ACT.Exp).then_inc(expd, 1)
                nc.scalar.activation(grow[:, c % 2].rearrange("p h l -> p (h l)"), grow_ps, ACT.Exp).then_inc(expg, 1)

        @block.tensor
        def _(pe):
            m = nc.tensor
            for c in range(NC):
                t0 = c * P
                if c:
                    pe.wait_ge(bt, c)
                    pe.wait_ge(xd, c)
                for j in range(4):
                    last = m.transpose((tp if j < 2 else btp)[:, (j % 2) * P:(j % 2 + 1) * P], k.xbc[:, j, t0:t0 + P], k.ident[:, :])
                last.then_inc(tr, 1)
                pe.wait_ge(au, c + 1)
                if c:
                    pe.wait_ge(expg, c)
                m.matmul(log_ps, k.below[:, :], aU[:, :, :].rearrange("p h l -> p (h l)"), start=True, stop=False)
                m.matmul(log_ps, k.ident[:, :], k.neg_upper[:, :], start=False, stop=True)
                m.matmul(grow_ps, k.ones[:, :], aU[:, :, :].rearrange("p h l -> p (h l)"), start=True, stop=True).then_inc(logs, 1)
                if c:
                    pe.wait_ge(mixd, c)
                for g in range(2):
                    last = m.matmul(sc_ps[:, g * P:(g + 1) * P], k.xbc[:, 2 + g, t0:t0 + P], k.xbc[:, 4 + g, t0:t0 + P],
                                    start=True, stop=True)
                last.then_inc(scr, 1)
                pe.wait_ge(mixd, c + 1)
                pe.wait_ge(cg, c + 1)
                if c:
                    pe.wait_ge(yd, c)
                for h in range(SH):
                    o = y_ps[(h % 2) * SP:(h % 2 + 1) * SP, (h // 2) * P:(h // 2 + 1) * P]
                    m.matmul(o, xdt[:, h, :], mix[:, h, :], start=True, stop=(c == 0))
                    if c:
                        m.matmul(o, state[:, h, :], cgrow[:, h, :], start=False, stop=True)
                m.matmul(new_ps[:, 0:P], b_tm[:, 0, :], xde[:, 0:2, :].rearrange("p h s -> p (h s)"), start=True, stop=True)
                m.matmul(new_ps[:, P:2 * P], b_tm[:, 1, :], xde[:, 2:4, :].rearrange("p h s -> p (h s)"),
                         start=True, stop=True).then_inc(stn, 1)
            pe.wait_ge(std, NC)
            for j in range(2):
                last = m.transpose(new_ps[:, j * P:(j + 1) * P], state[:, 2 * j:2 * j + 2, :].rearrange("p h s -> p (h s)"), k.ident[:, :])
            last.then_inc(fin_tr, 1)
            m.transpose(sc_ps[0:SH, 0:NS], k.dt[0:NS, NC * SH:NT], k.ident[0:NS, 0:NS])
            pe.wait_ge(dt_a, 3)
            m.transpose(sc_ps[0:SH, NS:2 * NS], da_exp[:, :], k.ident[0:NS, 0:NS]).then_inc(d_pe, 1)
            pe.wait_ge(d_v, 1)
            for j in range(2):
                last = m.matmul(tp[:, j * 2 * NS:(j + 1) * 2 * NS], k.head_pick[0:SH, j, :], dtT[:, :, :].rearrange("h a n -> h (a n)"),
                                start=True, stop=True)
            last.then_inc(d_pe, 1)
            for n in range(4):
                pe.wait_ge(d_v, 3 + n)
                for half in range(2):
                    last = m.matmul(k.ps[:, 1 + half + 2 * (n % 2), :], k.ones[:, :],
                                    diag[:, 4 * half:4 * half + 4, :].rearrange("p n s -> p (n s)"), start=True, stop=True)
                last.then_inc(d_pe, 1)

        @block.vector
        def _(dve):
            v = nc.vector
            link = chain(dve, link_s)
            dve.wait_ge(small_in, 96)
            dt3 = k.dt[:, :].rearrange("p (t h) -> p t h", h=SH)
            v.tensor_tensor(dt3, dt3, bias_b[:, :].rearrange("p (o h) -> p o h", o=1).broadcast_to([P, NC + 1, SH]), ALU.add).then_inc(dt_v, 1)
            dve.wait_ge(dt_a, 1)
            v.tensor_scalar(u1[:, :], e_abs[:, :], 1.0, None, ALU.add).then_inc(dt_v, 1)
            dve.wait_ge(dt_v, 2)
            link(v.tensor_scalar(um[:, :], u1[:, :], -1.0, None, ALU.add))
            link(v.tensor_scalar(zero_m[:, :], um[:, :], 0.0, None, ALU.is_equal))
            link(v.tensor_tensor(um[:, :], um[:, :], zero_m[:, :], ALU.add))
            link(v.reciprocal(um[:, :], um[:, :]))
            dve.wait_ge(dt_a, 2)
            link(v.tensor_tensor(lnu[:, :], lnu[:, :], zero_m[:, :], ALU.add))
            link(v.tensor_tensor(lnu[:, :], lnu[:, :], um[:, :], ALU.mult))
            link(v.tensor_tensor(lnu[:, :], lnu[:, :], e_abs[:, :], ALU.mult))
            link(v.tensor_scalar(k.dt[:, :], k.dt[:, :], 0.0, None, ALU.max))
            link(v.tensor_tensor(k.dt[:, :], k.dt[:, :], lnu[:, :], ALU.add))
            link(v.tensor_scalar(a_neg[:, :], a_neg[:, :], -1.0, None, ALU.mult))
            da3 = da[:, :].rearrange("p (t h) -> p t h", h=SH)
            v.tensor_tensor(da3, dt3, a_neg[:, :].rearrange("p (o h) -> p o h", o=1).broadcast_to([P, NC + 1, SH]), ALU.mult).then_inc(dt_v, 1)
            dve.wait_ge(dt_v, 3)
            for c in range(NC):
                dtc = k.dt[:, c * SH:(c + 1) * SH].rearrange("p (h o) -> p h o", o=1)
                dac = da3[:, c, :].rearrange("p (h o) -> p h o", o=1)
                if c:
                    dve.wait_ge(logs, c)
                v.tensor_tensor(aU[:, :, :], k.upper[:, :].rearrange("p (o l) -> p o l", o=1).broadcast_to([P, SH, P]),
                                dac.broadcast_to([P, SH, P]), ALU.mult).then_inc(au, 1)
                dve.wait_ge(tr, c + 1)
                if c:
                    dve.wait_ge(stn, c)
                v.tensor_tensor(xdt[:, :, :], tp[:, 0:2 * P].rearrange("p (h s) -> p h s", h=SH),
                                dtc.broadcast_to([P, SH, SP]), ALU.mult).then_inc(xd, 1)
                dve.wait_ge(expd, c + 1)
                dve.wait_ge(scr, c + 1)
                dc, gc = dec[:, c % 2], grow[:, c % 2]
                for g in range(2):
                    last = v.tensor_tensor(mix[:, 2 * g:2 * g + 2, :], sc_ps[:, g * P:(g + 1) * P].rearrange("p (o l) -> p o l", o=1).broadcast_to([P, 2, P]),
                                           dc[:, 2 * g:2 * g + 2, :], ALU.mult)
                last.then_inc(mixd, 1)
                dve.wait_ge(xd, c + 1)
                v.tensor_tensor(xde[:, :, :], xdt[:, :, :], dc[:, :, P - 1:P].broadcast_to([P, SH, SP]), ALU.mult)
                dve.wait_ge(expg, c + 1)
                for g in range(2):
                    last = v.tensor_tensor(cgrow[:, 2 * g:2 * g + 2, :],
                                           k.xbc[:, 4 + g, c * P:(c + 1) * P].rearrange("p (o l) -> p o l", o=1).broadcast_to([P, 2, P]),
                                           gc[:, 2 * g:2 * g + 2, :], ALU.mult)
                last.then_inc(cg, 1)
                dve.wait_ge(stn, c + 1)
                for j in range(2):
                    last = v.scalar_tensor_tensor(out=y_sum[:, j, :], in0=k.xbc[:, j, c * P:(c + 1) * P], scalar=d_col[:, j:j + 1],
                                                  in1=y_ps[:, j * P:(j + 1) * P], op0=ALU.mult, op1=ALU.add)
                last.then_inc(yd, 1)
                if c:
                    link(v.tensor_tensor(state[:, :, :], state[:, :, :], gc[:, :, P - 1:P].broadcast_to([P, SH, SP]), ALU.mult))
                    v.tensor_tensor(state[:, :, :], state[:, :, :], new_ps[:, 0:2 * P].rearrange("p (h s) -> p h s", h=SH), ALU.add).then_inc(std, 1)
                else:
                    v.tensor_copy(state[:, :, :], new_ps[:, 0:2 * P].rearrange("p (h s) -> p h s", h=SH)).then_inc(std, 1)
                dve.wait_ge(yd, c + 1)
                for j in range(2):
                    y = k.yT[j][:, c * P:(c + 1) * P]
                    last = v.tensor_tensor(y, y_sum[:, j, :], y, ALU.mult)
                link(last)
                dve.wait_ge(std, c + 1)
            dve.wait_ge(fin_tr, 1)
            v.tensor_copy(st_out[:, :, :].rearrange("p j s -> p (j s)"), new_ps[:, 0:2 * P]).then_inc(fin_cp, 1)
            dve.wait_ge(d_pe, 1)
            v.tensor_copy(dtT[:, :, :].rearrange("h a n -> h (a n)"), sc_ps[0:SH, 0:2 * NS]).then_inc(d_v, 1)
            dve.wait_ge(d_pe, 2)
            v.tensor_copy(dtb[:, :, :, :].rearrange("p j a n -> p (j a n)"), tp[:, 0:4 * NS]).then_inc(d_v, 1)
            dve.wait_ge(d_v, 2)
            idb = k.ident[:, :].rearrange("p (o s) -> p o s", o=1).broadcast_to([P, NS, P])

            def spread(tile, n):
                if n:
                    dve.wait_ge(d_pe, 2 + n)
                v.tensor_tensor(diag[:, :, :], idb, k.xbc[:, tile, T:TT].rearrange("p (n o) -> p n o", o=1).broadcast_to([P, NS, P]),
                                ALU.mult).then_inc(d_v, 1)

            spread(2, 0)
            for j in range(2):
                xs = k.xbc[:, j, T:TT]
                spread(4 + j, 2 * j + 1)
                dve.wait_ge(h0_in, 16 * (j + 1))
                link(v.tensor_tensor(h0[:, :, :], h0[:, :, :], dtb[:, j, 1, :].rearrange("p (n o) -> p n o", o=1).broadcast_to([P, NS, P]), ALU.mult))
                link(v.tensor_tensor(coef[:, :], xs, dtb[:, j, 0, :], ALU.mult))
                cf = coef[:, :].rearrange("p (n o) -> p n o", o=1)
                for half in range(2):
                    ns = slice(4 * half, 4 * half + 4)
                    last = v.tensor_tensor(hb[:, ns, :], k.ps[:, 1 + half, :].rearrange("p (n s) -> p n s", s=P),
                                           cf[:, ns, :].broadcast_to([P, 4, P]), ALU.mult)
                link(last)
                v.tensor_tensor(h0[:, :, :], h0[:, :, :], hb[:, :, :], ALU.add).then_inc(h_new, 1)
                dve.wait_ge(h_new, j + 1)
                dve.wait_ge(d_pe, 4 + 2 * j)
                if j == 0:
                    spread(3, 2)
                for half in range(2):
                    ns = slice(4 * half, 4 * half + 4)
                    last = v.tensor_tensor(hb[:, ns, :], h0[:, ns, :], k.ps[:, 3 + half, :].rearrange("p (n s) -> p n s", s=P), ALU.mult)
                last.then_inc(h_used, 1)
                dve.wait_ge(h_used, j + 1)
                link(v.tensor_reduce(y_s[:, :], hb[:, :, :], AX.X, ALU.add))
                link(v.scalar_tensor_tensor(out=y_s[:, :], in0=xs, scalar=d_col[:, j:j + 1], in1=y_s[:, :], op0=ALU.mult, op1=ALU.add))
                y = k.yT[j][:, T:TT]
                link(v.tensor_tensor(y, y_s[:, :], y, ALU.mult))


def column_sums(k, pe, m, src, out, n):
    for j in range(2):
        last = m.matmul(out, k.ones[:, :], src[j], start=(j == 0), stop=(j == 1))
    return last


def stage_ssd_norm(nc, k, sem):
    with ExitStack() as ctx:
        sq = ctx.enter_context(nc.sbuf_tensor("rms_sq", [P, 2, 2, GT], F32))
        inv = ctx.enter_context(nc.sbuf_tensor("rms_inv", [P, 2, GT], F32))
        sqd, summed, var, root, link_s = (sem("r_" + n) for n in ("sqd", "summed", "var", "root", "link"))
        block = ctx.enter_context(nc.Block())
        groups = [(g * GT, GT) for g in range(NG)] + [(T, NS)]

        @block.scalar
        def _(act):
            def square(g):
                t0, n = groups[g]
                if g >= 2:
                    act.wait_ge(summed, g - 1)
                for j in range(2):
                    last = nc.scalar.activation(sq[:, g % 2, j, 0:n], k.yT[j][:, t0:t0 + n], ACT.Square)
                last.then_inc(sqd, 1)
            square(0)
            for g, (t0, n) in enumerate(groups):
                if g + 1 < len(groups):
                    square(g + 1)
                act.wait_ge(var, g + 1)
                nc.scalar.activation(inv[:, g % 2, 0:n], inv[:, g % 2, 0:n], ACT.Sqrt).then_inc(root, 1)

        @block.tensor
        def _(pe):
            for g, (t0, n) in enumerate(groups):
                pe.wait_ge(sqd, g + 1)
                if g >= 2:
                    pe.wait_ge(var, g - 1)
                column_sums(k, pe, nc.tensor, [sq[:, g % 2, j, 0:n] for j in range(2)], k.ps[:, g % 2, 0:n], n).then_inc(summed, 1)

        @block.vector
        def _(dve):
            v = nc.vector
            link = chain(dve, link_s)
            for g, (t0, n) in enumerate(groups):
                dve.wait_ge(summed, g + 1)
                link(v.tensor_scalar(inv[:, g % 2, 0:n], k.ps[:, g % 2, 0:n], 1.0 / W, EPS, ALU.mult, ALU.add))
                v.reciprocal(inv[:, g % 2, 0:n], inv[:, g % 2, 0:n]).then_inc(var, 1)
                dve.wait_ge(root, g + 1)
                for j in range(2):
                    y = k.yT[j][:, t0:t0 + n]
                    b = PB + j * PB_ROWS + B_SSDG
                    last = v.scalar_tensor_tensor(out=y, in0=y, scalar=k.par[:, b:b + 1], in1=inv[:, g % 2, 0:n],
                                                  op0=ALU.mult, op1=ALU.mult)
                link(last)


def stage_convs(nc, k, sem):
    cols, kinds = [], []
    for j in range(2):
        cols += [COL_GLU + j * P, COL_GLU + W + j * P, COL_CG + j * P]
        kinds += [("u", j, 0), ("sig", j, 0), ("gate", j, 4)]
    for j in range(2):
        cols += [COL_A + j * P, COL_A + 2 * W + j * P, COL_A + W + j * P, COL_A + 3 * W + j * P]
        kinds += [("u", j, 2), ("v", j, 2), ("b", j, 2), ("gate", j, 2)]
    cols += [COL_DG, COL_DG + P]
    kinds += [("gate", 0, 6), ("gate", 1, 6)]
    U = NG + 1
    PADC = KCF - 1
    with ExitStack() as ctx:
        def sb(name, shape, dt=F32):
            return ctx.enter_context(nc.sbuf_tensor(name, shape, dt))
        w_buf = sb("w_buf2", [P, 2, KT, P])
        first = sb("first", [P, TT])
        second = sb("second", [P, TT])
        padded = sb("padded", [P, PADC + TT])
        acc = k.conf
        prev_rows = sb("prev_rows2", [120, 2, W])
        prev_a_rows = sb("prev_a_rows", [2 * NS, W])
        prev_c = sb("prev_c", [P, 2, NS * PADC])
        prev_a = sb("prev_a", [P, 2, NS, 2])
        prod = sb("prod_c", [P, NS, PADC])
        tailc = sb("tailc", [P, 2, PADC + NS])
        taila = sb("taila", [P, 2, 2 + NS])
        outc = sb("outc", [PADC + NS, W])
        outa = sb("outa", [2 + NS, W])
        w_ready = [sem("wc_ready0"), sem("wc_ready1")]
        prev_in, prev_tr, prev_cp, unit_done, evac, link_s, u_done, convd, tail_cp, tail_tr, tails_cp, stored, pad_free, gated = (
            sem("c_" + n) for n in ("prev_in", "prev_tr", "prev_cp", "unit", "evac", "link", "u_done", "convd", "tail_cp",
                                    "tail_tr", "tails_cp", "stored", "pad_free", "gated"))
        block = ctx.enter_context(nc.Block())

        @block.sync
        def _(sp):
            st = k.io["state_cconv"][0].rearrange("(a s) r c -> (s r) a c", a=2)
            sp.dma_start(prev_rows[:, :, :], st).then_inc(prev_in, 16)
            sp.dma_start(prev_a_rows[:, :], k.io["state_sconv"][0].rearrange("s r c -> (s r) c")).then_inc(prev_in, 16)
            load_tiles(k, sp, cols, w_buf, w_ready, unit_done)
            sp.dma_start(k.io["cconv_s"][0, :, 0:PADC - 1, :], k.io["state_cconv"][0, :, 1:PADC, :]).then_inc(stored, 16)
            sp.dma_start(k.io["sconv_s"][0, :, 0:1, :], k.io["state_sconv"][0, :, 1:2, :]).then_inc(stored, 16)
            sp.wait_ge(tails_cp, 1)
            sp.dma_start(k.io["cconv_p"][0, 0], outc[0:PADC, :]).then_inc(stored, 16)
            sp.dma_start(k.io["cconv_s"][0, :, PADC - 1, :], outc[PADC:PADC + NS, :]).then_inc(stored, 16)
            sp.dma_start(k.io["sconv_p"][0, 0], outa[0:2, :]).then_inc(stored, 16)
            sp.dma_start(k.io["sconv_s"][0, :, 1, :], outa[2:2 + NS, :]).then_inc(stored, 16)
            sp.wait_ge(stored, 96)

        @block.tensor
        def _(pe):
            m = nc.tensor
            pe.wait_ge(prev_in, 32)
            for j in range(2):
                for a in range(2):
                    m.transpose(k.ps[:, 7, (2 * j + a) * 120:(2 * j + a + 1) * 120], prev_rows[:, a, j * P:(j + 1) * P], k.ident[0:120, 0:120])
                last = m.transpose(k.ps[:, 6, j * 16:(j + 1) * 16], prev_a_rows[:, j * P:(j + 1) * P], k.ident[0:16, 0:16])
            last.then_inc(prev_tr, 1)
            pe.wait_ge(prev_cp, 2)

            def free(eng, u):
                eng.wait_ge(evac, u + 1)
            channel_projection(nc, k, pe, cols, w_buf, w_ready, None, unit_done, free)
            pe.wait_ge(evac, len(cols) * U)
            pe.wait_ge(tail_cp, 4)
            for j in range(2):
                m.transpose(k.ps[0:PADC + NS, 0, j * P:(j + 1) * P], tailc[:, j, :], k.ident[:, :])
                last = m.transpose(k.ps[0:2 + NS, 1, j * P:(j + 1) * P], taila[:, j, :], k.ident[:, :])
            last.then_inc(tail_tr, 1)

        @block.scalar
        def _(act):
            nu = 0
            nb = 0
            for i, (kind, j, y0) in enumerate(kinds):
                if kind == "u" and nu:
                    act.wait_ge(u_done, nu)
                if kind == "u" and y0 == 2 and j == 1:
                    act.wait_ge(convd, 3)
                for g in range(U):
                    n, t0 = (GT, g * GT) if g < NG else (NS, T)
                    u = i * U + g
                    act.wait_ge(unit_done, u + 1)
                    src = k.ps[:, u % 8, 0:n]
                    if kind == "u":
                        ins = nc.scalar.copy(first[:, t0:t0 + n], src)
                    elif kind == "v":
                        if g == 0 and j:
                            act.wait_ge(gated, j)
                        ins = nc.scalar.copy(second[:, t0:t0 + n], src)
                    elif kind == "sig":
                        ins = nc.scalar.activation(second[:, t0:t0 + n], src, ACT.Sigmoid)
                    elif kind == "b":
                        if g == 0:
                            act.wait_ge(u_done, nu)
                        ins = nc.scalar.copy(first[:, t0:t0 + n], src)
                    else:
                        ins = nc.scalar.activation(k.yT[y0 + j][:, t0:t0 + n], src, ACT.Silu)
                    ins.then_inc(evac, 1)
                if kind == "u":
                    nu += 1

        @block.vector
        def _(dve):
            v = nc.vector
            link = chain(dve, link_s)
            dve.wait_ge(prev_tr, 1)
            v.tensor_copy(prev_c[:, :, :].rearrange("p j n -> p (j n)"), k.ps[:, 7, 0:480]).then_inc(prev_cp, 1)
            v.tensor_copy(prev_a[:, :, :, :].rearrange("p j s r -> p (j s r)"), k.ps[:, 6, 0:32]).then_inc(prev_cp, 1)
            dve.wait_ge(prev_cp, 2)
            link(v.memset(padded[:, 0:PADC], 0.0))
            for j in range(2):
                cw = [k.par[:, PB + j * PB_ROWS + B_CF + q:PB + j * PB_ROWS + B_CF + q + 1] for q in range(KCF)]
                cb = PB + j * PB_ROWS + B_CFB
                dve.wait_ge(evac, (3 * j + 2) * U)
                v.tensor_tensor(padded[:, PADC:PADC + TT], first[:, :], second[:, :], ALU.mult).then_inc(u_done, 1)
                dve.wait_ge(u_done, j + 1)
                v.tensor_copy(tailc[:, j, :], padded[:, T:T + PADC + NS]).then_inc(tail_cp, 1)
                o, s = acc[:, j, 0:T], acc[:, j, T:TT]
                link(v.tensor_scalar(o, padded[:, PADC:PADC + T], cw[KCF - 1], k.par[:, cb:cb + 1], ALU.mult, ALU.add))
                for q in range(KCF - 1):
                    link(v.scalar_tensor_tensor(out=o, in0=padded[:, q:q + T], scalar=cw[q], in1=o, op0=ALU.mult, op1=ALU.add))
                b = PB + j * PB_ROWS + B_CF
                link(v.tensor_tensor(prod[:, :, :], prev_c[:, j, :].rearrange("p (s r) -> p s r", r=PADC),
                                     k.par[:, b:b + PADC].rearrange("p (o r) -> p o r", o=1).broadcast_to([P, NS, PADC]), ALU.mult))
                link(v.tensor_reduce(s, prod[:, :, :], AX.X, ALU.add))
                link(v.tensor_scalar(s, s, k.par[:, cb:cb + 1], None, ALU.add))
                v.scalar_tensor_tensor(out=s, in0=padded[:, PADC + T:PADC + TT], scalar=cw[KCF - 1], in1=s,
                                       op0=ALU.mult, op1=ALU.add).then_inc(convd, 1)
                dve.wait_ge(convd, j + 1)
            for j in range(2):
                i0 = 6 + 4 * j
                aw = [k.par[:, PB + j * PB_ROWS + B_SC + q:PB + j * PB_ROWS + B_SC + q + 1] for q in range(3)]
                dve.wait_ge(evac, (i0 + 2) * U)
                v.tensor_tensor(padded[:, PADC:PADC + TT], first[:, :], second[:, :], ALU.mult).then_inc(u_done, 1)
                dve.wait_ge(u_done, 3 + j)
                v.tensor_copy(taila[:, j, :], padded[:, T + PADC - 2:T + PADC + NS]).then_inc(tail_cp, 1)
                o, s = second[:, 0:T], second[:, T:TT]
                link(v.tensor_scalar(o, padded[:, PADC:PADC + T], aw[2], None, ALU.mult))
                for q in range(2):
                    link(v.scalar_tensor_tensor(out=o, in0=padded[:, PADC - 2 + q:PADC - 2 + q + T], scalar=aw[q], in1=o,
                                                op0=ALU.mult, op1=ALU.add))
                link(v.tensor_scalar(s, padded[:, PADC + T:PADC + TT], aw[2], None, ALU.mult))
                for q in range(2):
                    link(v.scalar_tensor_tensor(out=s, in0=prev_a[:, j, :, q], scalar=aw[q], in1=s, op0=ALU.mult, op1=ALU.add))
                dve.wait_ge(evac, (i0 + 4) * U)
                y = k.yT[2 + j]
                v.tensor_tensor(second[:, :], second[:, :], first[:, :], ALU.mult).then_inc(convd, 1)
                dve.wait_ge(convd, 3 + j)
                v.tensor_tensor(y[:, :], y[:, :], second[:, :], ALU.mult).then_inc(gated, 1)
            dve.wait_ge(tail_tr, 1)
            v.tensor_copy(outc[:, :], k.ps[0:PADC + NS, 0, 0:W])
            v.tensor_copy(outa[:, :], k.ps[0:2 + NS, 1, 0:W]).then_inc(tails_cp, 1)


def stage_conformer_norm(nc, k, sem):
    with ExitStack() as ctx:
        sq = ctx.enter_context(nc.sbuf_tensor("ln_sq", [P, 2, GT], F32))
        inv = ctx.enter_context(nc.sbuf_tensor("ln_inv", [P, GT], F32))
        mean = ctx.enter_context(nc.sbuf_tensor("ln_mean", [P, GT], F32))
        summed, cen, sqd, sq_sum, var, root, scaled, swished, link_s = (
            sem("ln_" + n) for n in ("summed", "cen", "sqd", "sq_sum", "var", "root", "scaled", "swished", "link"))
        block = ctx.enter_context(nc.Block())
        groups = [(g * GT, GT) for g in range(NG)] + [(T, NS)]
        acc = k.conf

        @block.tensor
        def _(pe):
            for g, (t0, n) in enumerate(groups):
                if g:
                    pe.wait_ge(cen, g)
                column_sums(k, pe, nc.tensor, [acc[:, j, t0:t0 + n] for j in range(2)], k.ps[:, 0, 0:n], n).then_inc(summed, 1)
                pe.wait_ge(sqd, g + 1)
                if g:
                    pe.wait_ge(var, g)
                column_sums(k, pe, nc.tensor, [sq[:, j, 0:n] for j in range(2)], k.ps[:, 1, 0:n], n).then_inc(sq_sum, 1)

        @block.scalar
        def _(act):
            for g, (t0, n) in enumerate(groups):
                act.wait_ge(cen, g + 1)
                if g:
                    act.wait_ge(sq_sum, g)
                for j in range(2):
                    last = nc.scalar.activation(sq[:, j, 0:n], acc[:, j, t0:t0 + n], ACT.Square)
                last.then_inc(sqd, 1)
                act.wait_ge(var, g + 1)
                nc.scalar.activation(inv[:, 0:n], inv[:, 0:n], ACT.Sqrt).then_inc(root, 1)
            act.wait_ge(scaled, len(groups))
            for j in range(2):
                b = PB + j * PB_ROWS
                nc.scalar.activation(acc[:, j, :], acc[:, j, :], ACT.Silu, bias=k.par[:, b + B_LNB:b + B_LNB + 1],
                                     scale=k.par[:, b + B_LNG:b + B_LNG + 1]).then_inc(swished, 1)

        @block.vector
        def _(dve):
            v = nc.vector
            link = chain(dve, link_s)
            for g, (t0, n) in enumerate(groups):
                dve.wait_ge(summed, g + 1)
                link(v.tensor_scalar(mean[:, 0:n], k.ps[:, 0, 0:n], 1.0 / W, None, ALU.mult))
                for j in range(2):
                    last = v.tensor_tensor(acc[:, j, t0:t0 + n], acc[:, j, t0:t0 + n], mean[:, 0:n], ALU.subtract)
                last.then_inc(cen, 1)
                dve.wait_ge(sq_sum, g + 1)
                link(v.tensor_scalar(inv[:, 0:n], k.ps[:, 1, 0:n], 1.0 / W, EPS, ALU.mult, ALU.add))
                v.reciprocal(inv[:, 0:n], inv[:, 0:n]).then_inc(var, 1)
                dve.wait_ge(root, g + 1)
                dve.wait_ge(cen, g + 1)
                for j in range(2):
                    last = v.tensor_tensor(acc[:, j, t0:t0 + n], acc[:, j, t0:t0 + n], inv[:, 0:n], ALU.mult)
                last.then_inc(scaled, 1)
                dve.wait_ge(scaled, g + 1)
            for j in range(2):
                dve.wait_ge(swished, j + 1)
                y = k.yT[4 + j]
                v.tensor_tensor(y[:, :], y[:, :], acc[:, j, :], ALU.mult)


def stage_token_major(nc, k, sem):
    parts = [(0, 384), (384, TM)]
    with ExitStack() as ctx:
        def sb(name, shape, dt=F32):
            return ctx.enter_context(nc.sbuf_tensor(name, shape, dt))
        w_tm = sb("w_tm", [P, KT, 384])
        gains = sb("qk_gains", [P, 6, HD])
        sq = sb("qk_sq", [P, 6, HD])
        ss = sb("qk_ss", [P, (NC + 1) * 6])
        w_in_s, g_in, proj, evac, link_s, ss_done, root, rows_done, stored, mem = (
            sem("t_" + n) for n in ("w_in", "g_in", "proj", "evac", "link", "ss_done", "root", "rows_done", "stored", "mem"))
        block = ctx.enter_context(nc.Block())
        N1 = NC + 1

        @block.sync
        def _(sp):
            for h in range(H):
                sp.dma_start(gains[:, h, :], k.io["q_g"].broadcast_to([P, HD])).then_inc(g_in, 16)
            for i in range(2):
                sp.dma_start(gains[:, H + i, :], k.io["k_g"][0, 1 + i:2 + i, :].broadcast_to([P, HD])).then_inc(g_in, 16)
            wv = k.io["w_in"][0].rearrange("(k p) n -> p k n", p=P)
            sp.dma_start(w_tm[:, :, 0:384], wv[:, :, COL_Q:COL_Q + 384]).then_inc(w_in_s, 16)
            sp.wait_ge(proj, N1)
            sp.dma_start(w_tm[:, :, 0:256], wv[:, :, COL_Q + 384:COL_Q + 640]).then_inc(w_in_s, 16)
            sp.dma_start(w_tm[:, :, 256:268], wv[:, :, COL_BG:COL_BG + 12]).then_inc(w_in_s, 16)
            sp.dma_start(k.io["win_s"][0, :, 0:511], k.io["cache_win"][0, :, 1:512]).then_inc(stored, 16)
            sp.wait_ge(rows_done, 1)
            rows = k.io["kv_p"][0].rearrange("t p s d -> p t (s d)")
            sp.dma_start(rows, k.tm[:, 0:NC, W:W + 256]).then_inc(stored, 16)
            sp.dma_start(k.io["win_p"][0, 0].rearrange("(t p) s d -> p t (s d)", p=P), k.tm[:, NC - 4:NC, 512:640]).then_inc(stored, 16)
            sp.dma_start(k.io["kv_s"][0, :, 0].rearrange("n s d -> n (s d)"), k.tm[0:NS, NC, W:W + 256]).then_inc(stored, 16)
            sp.dma_start(k.io["win_s"][0, :, 511].rearrange("n s d -> n (s d)"), k.tm[0:NS, NC, 512:640]).then_inc(stored, 16)
            sp.wait_ge(stored, 80)

        @block.tensor
        def _(pe):
            for i, (c0, c1) in enumerate(parts):
                pe.wait_ge(w_in_s, 16 if i == 0 else 48)
                for t in range(N1):
                    u = i * N1 + t
                    r = P if t < NC else NS
                    if u >= 4:
                        pe.wait_ge(evac, u - 3)
                    for kk in range(KT):
                        last = nc.tensor.matmul(k.ps[0:r, u % 4, 0:c1 - c0], k.hT[:, kk, t * P:t * P + r], w_tm[:, kk, 0:c1 - c0],
                                                start=(kk == 0), stop=(kk == KT - 1))
                    last.then_inc(proj, 1)

        @block.scalar
        def _(act):
            act.wait_ge(mem, 1)
            for i, (c0, c1) in enumerate(parts):
                for t in range(N1):
                    u = i * N1 + t
                    r = P if t < NC else NS
                    act.wait_ge(proj, u + 1)
                    nc.scalar.copy(k.tm[0:r, t, c0:c1], k.ps[0:r, u % 4, 0:c1 - c0]).then_inc(evac, 1)
            act.wait_ge(ss_done, 1)
            nc.scalar.activation(ss[:, :], ss[:, :], ACT.Sqrt).then_inc(root, 1)
            g = k.tm[:, :, 640:652]
            act.wait_ge(evac, 2 * N1)
            nc.scalar.activation(g, g, ACT.Sigmoid)

        @block.vector
        def _(dve):
            v = nc.vector
            link = chain(dve, link_s)
            v.memset(k.tm[:, NC, :], 0.0).then_inc(mem, 1)
            for t in range(N1):
                q = k.tm[:, t, 0:W]
                kk = k.tm[:, t, 384:640].rearrange("p (i d) -> p i d", d=2 * HD)[:, :, 0:HD]
                dve.wait_ge(evac, N1 + t + 1)
                v.tensor_tensor(sq[:, 0:H, :].rearrange("p h d -> p (h d)"), q, q, ALU.mult)
                link(v.tensor_tensor(sq[:, H:6, :], kk, kk, ALU.mult))
                link(v.tensor_reduce(ss[:, t * 6:(t + 1) * 6], sq[:, :, :], AX.X, ALU.add))
            link(v.tensor_scalar(ss[:, :], ss[:, :], 1.0 / HD, EPS, ALU.mult, ALU.add))
            v.reciprocal(ss[:, :], ss[:, :]).then_inc(ss_done, 1)
            dve.wait_ge(root, 1)
            dve.wait_ge(g_in, 96)
            for t in range(N1):
                q = k.tm[:, t, 0:W].rearrange("p (h d) -> p h d", d=HD)
                kk = k.tm[:, t, 384:640].rearrange("p (i d) -> p i d", d=2 * HD)[:, :, 0:HD]
                s3 = ss[:, t * 6:(t + 1) * 6].rearrange("p (h o) -> p h o", o=1)
                v.tensor_tensor(q, q, s3[:, 0:H, :].broadcast_to([P, H, HD]), ALU.mult)
                link(v.tensor_tensor(kk, kk, s3[:, H:6, :].broadcast_to([P, 2, HD]), ALU.mult))
                v.tensor_tensor(q, q, gains[:, 0:H, :], ALU.mult)
                link(v.tensor_tensor(kk, kk, gains[:, H:6, :], ALU.mult))
            v.memset(sq[:, 0, 0:1], 0.0).then_inc(rows_done, 1)


def stage_compress(nc, k, sem):
    NQ = 1 + NS
    with ExitStack() as ctx:
        def sb(name, shape, dt=F32):
            return ctx.enter_context(nc.sbuf_tensor(name, shape, dt))
        rawT = k.hview(2 * T, 2 * T).rearrange("p (b t) -> p b t", b=2)
        w1 = k.hview(4 * T, 2 * T).rearrange("p (j f) -> p j f", j=32)
        page = k.hview(6 * T, 2 * T).rearrange("p (b g c) -> p b g c", b=2, c=P)
        table = sb("table", [1, NS * PAGES], I32)
        pe_rows = sb("pe_rows", [32, P])
        b1_rows = sb("b1_rows", [2, P])
        peT = sb("peT", [P, 32])
        bias1 = sb("bias1", [P, 2])
        b1T = sb("b1T", [P, 2])
        w2 = sb("w2", [P, 2, HD])
        b2 = sb("b2", [P, 2, HD])
        kg = sb("kg", [P, HD])
        hid = sb("hid", [P, 2, 2, P])
        kc = sb("kc", [P, 2, HD])
        sq = sb("kc_sq", [P, HD])
        st = sb("kc_st", [P, 2])
        table_in, par_in, blk_in, page_in0, page_in1, pt, pcp, bias_d, rcp, hidp, hidd, cmp_d, kcd, kct, kcc, link_s, root, root_in, loaded = (
            sem("k_" + n) for n in ("table_in", "par_in", "blk_in", "page_in0", "page_in1", "pt", "pcp", "bias_d", "rcp",
                                    "hidp", "hidd", "cmp_d", "kcd", "kct", "kcc", "link", "root", "root_in", "loaded"))
        ktr, kcp, kcp2 = sem("k_ktr"), sem("k_kcp"), sem("k_kcp2")
        block = ctx.enter_context(nc.Block())
        M = NCMP
        page_in = [page_in0, page_in1]

        @block.sync
        def _(sp):
            sp.dma_start(table[:, :], k.io["page_table"].rearrange("n g -> (n g)").rearrange("(o m) -> o m", o=1)).then_inc(table_in, 16)
            sp.dma_start(w1[0:HD], k.io["cmp_w1"][0, 0].rearrange("j d f -> d j f")).then_inc(par_in, 16)
            sp.dma_start(w1[HD:P], k.io["cmp_w1"][0, 1].rearrange("j d f -> d j f")).then_inc(par_in, 16)
            for i in range(2):
                sp.dma_start(pe_rows[:, i * HD:(i + 1) * HD], k.io["cmp_pe"][0, i]).then_inc(par_in, 16)
            sp.dma_start(b1_rows[:, :], k.io["cmp_b1"][0]).then_inc(par_in, 16)
            sp.dma_start(w2[:, :, :], k.io["cmp_w2"][0].rearrange("i f d -> f i d")).then_inc(par_in, 16)
            for i in range(2):
                sp.dma_start(b2[:, i, :], k.io["cmp_b2"][0, i:i + 1, :].broadcast_to([P, HD])).then_inc(par_in, 16)
            sp.dma_start(kg[:, :], k.io["k_g"][0, 0:1, :].broadcast_to([P, HD])).then_inc(par_in, 16)
            sp.dma_start(k.ksel[HD:HD + NBLK, :], k.blk_dram[:, :]).then_inc(blk_in, 16)
            sp.wait_ge(table_in, 16)
            for n in range(NS):
                if n >= 2:
                    sp.wait_ge(ktr, NC + 4 * n)
                for g in range(PAGES):
                    i = sp.value_load(table[0:1, n * PAGES + g:n * PAGES + g + 1], min_val=0, max_val=k.n_pool - 1)
                    sp.dma_start(page[:, n % 2, g, :], k.io["cache_kv"][0, bass.DynSlice(i, 1), :, 0:2, :].rearrange("o p s d -> (o p) (s d)")
                                 ).then_inc(page_in[n % 2], 16)
            sp.wait_ge(blk_in, 16)

        @block.tensor
        def _(pe):
            m = nc.tensor
            pe.wait_ge(par_in, 144)
            m.transpose(k.ps[:, 0, 0:32], pe_rows[:, :], k.ident[0:32, 0:32])
            m.transpose(k.ps[:, 0, 32:34], b1_rows[:, :], k.ident[0:2, 0:2]).then_inc(pt, 1)
            pe.wait_ge(pcp, 1)
            for i in range(2):
                for j in range(32):
                    r = slice(i * HD, (i + 1) * HD)
                    last = m.matmul(k.ps[:, 1 + i, 0:1], w1[r, j, :], peT[r, j:j + 1], start=(j == 0), stop=(j == 31))
            last.then_inc(pt, 1)
            pe.wait_ge(bias_d, 1)
            for t in range(NC):
                if t >= 2:
                    pe.wait_ge(kcp, t - 1)
                b = k.ps[:, 3 + t % 2, :]
                m.transpose(b[0:HD, 0:P], k.tm[:, t, 384:448], k.ident[:, :])
                m.transpose(b[0:HD, P:2 * P], k.tm[:, t, 512:576], k.ident[:, :]).then_inc(ktr, 1)
            pe.wait_ge(kcp, NC)

            def raw_transposes(q):
                if q:
                    pe.wait_ge(page_in[(q - 1) % 2], 16 * PAGES * ((q - 1) // 2 + 1))
                for b4 in range(4):
                    e = q * 4 + b4
                    if e >= 2:
                        pe.wait_ge(rcp, e - 1)
                    for n in range(4):
                        t = 4 * b4 + n
                        src = k.tm[:, t, W:W + P] if q == 0 else page[:, (q - 1) % 2, t, :]
                        last = m.transpose(k.ps[:, 3 + e % 2, n * P:(n + 1) * P], src, k.ident[:, :])
                    last.then_inc(ktr, 1)

            raw_transposes(0)
            for q in range(NQ):
                if q + 1 < NQ:
                    raw_transposes(q + 1)
                pe.wait_ge(rcp, 4 * (q + 1))
                if q:
                    pe.wait_ge(hidd, 2 * q)
                for i in range(2):
                    r = slice(i * HD, (i + 1) * HD)
                    for j in range(32):
                        last = m.matmul(k.ps[:, 1 + i, 0:M], w1[r, j, :], rawT[r, q % 2, j:j + 16 * (M - 1) + 1:16],
                                        start=(j == 0), stop=(j == 31))
                    last.then_inc(hidp, 1)
                if q:
                    pe.wait_ge(kcc, q)
                for i in range(2):
                    pe.wait_ge(hidd, 2 * q + i + 1)
                    last = m.matmul(k.ps[0:M, 5, i * HD:(i + 1) * HD], hid[:, q % 2, i, 0:M], w2[:, i, :], start=True, stop=True)
                last.then_inc(cmp_d, 1)
                pe.wait_ge(kcd, q + 1)
                m.transpose(k.ps[0:HD, 6, 0:M], kc[0:M, q % 2, :], k.ident[0:M, 0:M]).then_inc(kct, 1)

        @block.scalar
        def _(act):
            def hids(q):
                for i in range(2):
                    act.wait_ge(hidp, 2 * q + i + 1)
                    if q >= 2:
                        act.wait_ge(cmp_d, q - 1)
                    nc.scalar.activation(hid[:, q % 2, i, 0:M], k.ps[:, 1 + i, 0:M], ACT.Silu, bias=bias1[:, i:i + 1]).then_inc(hidd, 1)
                act.wait_ge(root_in, q + 1)
                nc.scalar.activation(st[0:M, 1:2], st[0:M, 0:1], ACT.Sqrt).then_inc(root, 1)

            act.wait_ge(bias_d, 1)
            for q in range(NQ):
                for b4 in range(1, 4, 2):
                    e = q * 4 + b4
                    act.wait_ge(ktr, NC + e + 1)
                    act.wait_ge(rcp, e)
                    if q >= 2:
                        act.wait_ge(hidp, 2 * (q - 1))
                    nc.scalar.copy(rawT[:, q % 2, b4 * 512:(b4 + 1) * 512], k.ps[:, 3 + e % 2, :]).then_inc(rcp, 1)
                if q:
                    hids(q - 1)
            hids(NQ - 1)

        @block.vector
        def _(dve):
            v = nc.vector
            link = chain(dve, link_s)
            dve.wait_ge(pt, 1)
            v.tensor_copy(peT[:, :], k.ps[:, 0, 0:32])
            v.tensor_copy(b1T[:, :], k.ps[:, 0, 32:34]).then_inc(pcp, 1)
            dve.wait_ge(pt, 2)
            dve.wait_ge(pcp, 1)
            v.tensor_tensor(bias1[:, 0:1], k.ps[:, 1, 0:1], b1T[:, 0:1], ALU.add)
            v.tensor_tensor(bias1[:, 1:2], k.ps[:, 2, 0:1], b1T[:, 1:2], ALU.add).then_inc(bias_d, 1)
            for t in range(NC):
                dve.wait_ge(ktr, t + 1)
                b = k.ps[:, 3 + t % 2, :]
                v.tensor_copy(k.ksel[0:HD, t * P:(t + 1) * P], b[0:HD, 0:P])
                v.tensor_copy(k.kwin[0:HD, t * P:(t + 1) * P], b[0:HD, P:2 * P]).then_inc(kcp, 1)

            def raw_copies(q):
                for b4 in range(0, 4, 2):
                    e = q * 4 + b4
                    dve.wait_ge(ktr, NC + e + 1)
                    if e:
                        dve.wait_ge(rcp, e)
                    if q >= 2:
                        dve.wait_ge(hidp, 2 * (q - 1))
                    v.tensor_copy(rawT[:, q % 2, b4 * 512:(b4 + 1) * 512], k.ps[:, 3 + e % 2, :]).then_inc(rcp, 1)

            raw_copies(0)
            for q in range(NQ):
                if q + 1 < NQ:
                    raw_copies(q + 1)
                dve.wait_ge(cmp_d, q + 1)
                if q >= 2:
                    dve.wait_ge(kct, q - 1)
                c = kc[0:M, q % 2, :]
                link(v.tensor_tensor(c, k.ps[0:M, 5, 0:HD], b2[0:M, 0, :], ALU.add))
                v.tensor_tensor(k.vc[0:M, q, :], k.ps[0:M, 5, HD:2 * HD], b2[0:M, 1, :], ALU.add)
                link(v.tensor_tensor(sq[0:M, :], c, c, ALU.mult))
                link(v.tensor_reduce(st[0:M, 0:1], sq[0:M, :], AX.X, ALU.add))
                link(v.tensor_scalar(st[0:M, 1:2], st[0:M, 0:1], 1.0 / HD, EPS, ALU.mult, ALU.add))
                v.reciprocal(st[0:M, 0:1], st[0:M, 1:2]).then_inc(root_in, 1)
                dve.wait_ge(root, q + 1)
                v.scalar_tensor_tensor(out=c, in0=c, scalar=st[0:M, 1:2], in1=kg[0:M, :], op0=ALU.mult, op1=ALU.mult).then_inc(kcd, 1)
                dve.wait_ge(kct, q + 1)
                v.tensor_copy(k.kcT[0:HD, q, 0:M], k.ps[0:HD, 6, 0:M]).then_inc(kcc, 1)


def stage_attention(nc, k, sem):
    UNITS = [("sel", h) for h in range(H)] + [("win", h) for h in range(H)]
    NU = len(UNITS)
    M = NCMP
    with ExitStack() as ctx:
        def sb(name, shape, dt=F32):
            return ctx.enter_context(nc.sbuf_tensor(name, shape, dt))
        probs = k.hview(2 * T, 2 * T).rearrange("p (b n) -> p b n", b=2)
        pT = k.hview(4 * T, 2 * T).rearrange("p (b n) -> p b n", b=2)
        qaug = k.hview(6 * T, 2 * H * P).rearrange("p (b h q) -> p b h q", b=2, h=H)
        cs = k.hview(6 * T + 1024, H * P).rearrange("p (h c) -> p h c", h=H)
        pcT = k.hview(6 * T + 1536, H * P).rearrange("p (h q) -> p h q", h=H)
        o_tm = k.hview(6 * T + 2048, 2 * W).rearrange("p (b c) -> p b c", b=2)
        pg = k.hview(6 * T + 2560, P + 4)
        sc = k.hview(6 * T + 2700, 3 * NBLK).rearrange("p (a b) -> p a b", a=3)
        m8 = k.hview(6 * T + 2800, 16)
        mx = k.hview(6 * T + 2816, 64)
        (qtr, qcp, cps, cms, cex, cpn, cpt, cptc, cpv, imp, btr, bcp, scr, mxd, exd, ptr, pcp, pvd, osc, otr, ycp, link_s, cgate, ocp) = (
            sem("a_" + n) for n in ("qtr", "qcp", "cps", "cms", "cex", "cpn", "cpt", "cptc", "cpv", "imp", "btr", "bcp", "scr", "mxd",
                                    "exd", "ptr", "pcp", "pvd", "osc", "otr", "ycp", "link", "cgate", "ocp"))
        block = ctx.enter_context(nc.Block())

        def keys(qb, kind):
            return (0, qb + 1) if kind == "sel" else (max(0, qb - 4), qb + 1)

        def fours(n):
            return [(a, min(a + 4, n)) for a in range(0, n, 4)]

        base = []
        total = 0
        for qb in range(NC):
            for kind, h in UNITS:
                base.append(total)
                lo, hi = keys(qb, kind)
                total += len(fours(hi - lo))

        @block.tensor
        def _(pe):
            m = nc.tensor

            def compressed_a(qb):
                if qb:
                    pe.wait_ge(ocp, qb)
                for h in range(H):
                    last = m.transpose(k.ps[0:HD, 6, h * P:(h + 1) * P], k.tm[:, qb, h * HD:(h + 1) * HD], k.ident[:, :])
                last.then_inc(qtr, 1)

            def compressed_b(qb):
                pe.wait_ge(qcp, qb + 1)
                for h in range(H):
                    last = m.matmul(k.ps[:, 6, h * P:h * P + M], qaug[0:HD, qb % 2, h, :], k.kcT[0:HD, 0, 0:M], start=True, stop=True)
                last.then_inc(cps, 1)

            def compressed_c(qb):
                pe.wait_ge(cpn, qb + 1)
                for h in range(H):
                    last = m.transpose(k.ps[0:M, 6, h * P:(h + 1) * P], cs[:, h, 0:M], k.ident[:, :])
                last.then_inc(cpt, 1)
                pe.wait_ge(imp, qb + 1)
                pe.wait_ge(cptc, qb + 1)
                m.transpose(k.ps[0:NBLK, 6, 0:P], sc[:, 0, :], k.ident[:, :]).then_inc(btr, 1)

            def compressed_d(qb):
                pe.wait_ge(bcp, qb + 1)
                for h in range(H):
                    last = m.matmul(k.ps[:, 6, h * HD:(h + 1) * HD], pcT[0:M, h, :], k.vc[0:M, 0, :], start=True, stop=True)
                last.then_inc(cpv, 1)

            def scores(qb, u):
                kind, h = UNITS[u]
                n = qb * NU + u
                lo, hi = keys(qb, kind)
                if n:
                    pe.wait_ge(exd, n)
                if u == 0:
                    pe.wait_ge(bcp, qb + 1)
                rows = HD + NBLK if kind == "sel" else HD
                kt = k.ksel if kind == "sel" else k.kwin
                for a, b in fours(hi - lo):
                    has_end = b == hi - lo
                    has_low = kind == "win" and a == 0 and hi - lo == 5
                    last = m.matmul(k.ps[:, a // 4, 0:(b - a) * P], qaug[0:rows, qb % 2, h, :], kt[0:rows, (lo + a) * P:(lo + b) * P],
                                    start=True, stop=not (has_end or has_low))
                    if has_low:
                        last = m.matmul(k.ps[:, 0, 0:P], k.ident[:, :], k.win_low[:, :], start=False, stop=not has_end)
                    if has_end:
                        e = b - a - 1
                        last = m.matmul(k.ps[:, a // 4, e * P:(e + 1) * P], k.ident[:, :], k.causal[:, :], start=False, stop=True)
                last.then_inc(scr, 1)

            def values(qb, u):
                kind, h = UNITS[u]
                n = qb * NU + u
                lo, hi = keys(qb, kind)
                pe.wait_ge(exd, n + 1)
                banks = fours(hi - lo)

                def turn(i):
                    a, b = banks[i]
                    e = base[n] + i
                    if e >= 2:
                        pe.wait_ge(pcp, e - 1)
                    for t in range(a, b):
                        last = m.transpose(k.ps[:, 4 + e % 2, (t - a) * P:(t - a + 1) * P], probs[:, n % 2, t * P:(t + 1) * P], k.ident[:, :])
                    last.then_inc(ptr, 1)

                turn(0)
                col = W if kind == "sel" else W + 128
                for i, (a, b) in enumerate(banks):
                    if i + 1 < len(banks):
                        turn(i + 1)
                    pe.wait_ge(pcp, base[n] + i + 1)
                    if i == 0 and n >= 1:
                        pe.wait_ge(osc, n)
                    for t in range(a, b):
                        v0 = W + 192 if kind == "sel" else W + 320
                        last = m.matmul(k.ps[:, 7, 0:HD], pT[:, n % 2, t * P:(t + 1) * P], k.tm[:, lo + t, v0:v0 + HD],
                                        start=(t == 0), stop=(t == hi - lo - 1))
                last.then_inc(pvd, 1)

            def finish(qb):
                pe.wait_ge(osc, (qb + 1) * NU)
                for j in range(2):
                    last = m.transpose(k.ps[:, 7, j * P:(j + 1) * P], o_tm[:, qb % 2, j * P:(j + 1) * P], k.ident[:, :])
                last.then_inc(otr, 1)
                pe.wait_ge(ycp, qb + 1)

            STEPS = {0: compressed_a, 1: compressed_b, 3: compressed_c, 5: compressed_d}
            for s in (0, 1, 3, 5):
                STEPS[s](0)
            scores(0, 0)
            for n in range(NC * NU):
                qb, u = divmod(n, NU)
                if u + 1 < NU:
                    scores(qb, u + 1)
                values(qb, u)
                if u in STEPS and qb + 1 < NC:
                    STEPS[u](qb + 1)
                if u == NU - 1:
                    if qb + 1 < NC:
                        scores(qb + 1, 0)
                    finish(qb)

        @block.scalar
        def _(act):
            def compressed_c(qb):
                act.wait_ge(cms, qb + 1)
                for h in range(H):
                    last = nc.scalar.activation(cs[:, h, 0:M], cs[:, h, 0:M], ACT.Exp, scale=SCALE, bias=mx[:, h:h + 1],
                                                accum_out=mx[:, 8 + h:9 + h])
                last.then_inc(cex, 1)

            def exps(qb, u):
                kind, h = UNITS[u]
                n = qb * NU + u
                lo, hi = keys(qb, kind)
                act.wait_ge(mxd, n + 1)
                if n >= 2:
                    act.wait_ge(pvd, n - 1)
                c = 16 + 2 * (n % 2)
                nc.scalar.activation(probs[:, n % 2, 0:(hi - lo) * P], k.scores_ps[:, 0:(hi - lo) * P], ACT.Exp, scale=SCALE,
                                     bias=mx[:, c:c + 1], accum_out=mx[:, c + 1:c + 2]).then_inc(exd, 1)

            def copies(qb, u):
                n = qb * NU + u
                lo, hi = keys(qb, UNITS[u][0])
                for i, (a, b) in enumerate(fours(hi - lo)):
                    e = base[n] + i
                    if e % 2:
                        act.wait_ge(ptr, e + 1)
                        act.wait_ge(pcp, e)
                        if n >= 2:
                            act.wait_ge(pvd, n - 1)
                        nc.scalar.copy(pT[:, n % 2, a * P:b * P], k.ps[:, 5, 0:(b - a) * P]).then_inc(pcp, 1)

            compressed_c(0)
            exps(0, 0)
            for n in range(NC * NU):
                qb, u = divmod(n, NU)
                if u + 1 < NU:
                    exps(qb, u + 1)
                copies(qb, u)
                if u == 2 and qb + 1 < NC:
                    compressed_c(qb + 1)
                if u == NU - 1 and qb + 1 < NC:
                    exps(qb + 1, 0)

        @block.vector
        def _(dve):
            v = nc.vector
            link = chain(dve, link_s)
            link(v.memset(pg[:, :], 0.0))

            def compressed_a(qb):
                dve.wait_ge(qtr, qb + 1)
                v.tensor_copy(qaug[0:HD, qb % 2, :, :].rearrange("p h q -> p (h q)"), k.ps[0:HD, 6, :]).then_inc(qcp, 1)

            def compressed_b(qb):
                dve.wait_ge(cps, qb + 1)
                mask = k.cmp_mask[:, P - 8 * qb:2 * P - 8 * qb]
                link(v.tensor_tensor(cs[:, :, 0:M], k.ps[:, 6, :].rearrange("p (h c) -> p h c", h=H)[:, :, 0:M],
                                     mask[:, 0:M].rearrange("p (o c) -> p o c", o=1).broadcast_to([P, H, M]), ALU.add))
                link(v.tensor_reduce(mx[:, 0:4], cs[:, :, 0:M], AX.X, ALU.max))
                v.tensor_scalar(mx[:, 0:4], mx[:, 0:4], -1e20, -SCALE, ALU.max, ALU.mult).then_inc(cms, 1)

            def compressed_c(qb):
                dve.wait_ge(cex, qb + 1)
                link(v.tensor_scalar(mx[:, 4:8], mx[:, 8:12], 1e-30, None, ALU.max))
                link(v.reciprocal(mx[:, 12:16], mx[:, 4:8]))
                v.tensor_tensor(cs[:, :, 0:M], cs[:, :, 0:M], mx[:, 12:16].rearrange("p (h o) -> p h o", o=1).broadcast_to([P, H, M]),
                                ALU.mult).then_inc(cpn, 1)
                dve.wait_ge(cpn, qb + 1)
                g = pg[:, 1:1 + M]
                link(v.tensor_tensor(g, cs[:, 0, 0:M], cs[:, 1, 0:M], ALU.add))
                link(v.tensor_tensor(g, g, cs[:, 2, 0:M], ALU.add))
                link(v.tensor_tensor(g, g, cs[:, 3, 0:M], ALU.add))
                b, b2, b3 = sc[:, 0, :], sc[:, 1, :], sc[:, 2, :]

                def at(o):
                    return pg[:, 1 + o:1 + o + 4 * (NBLK - 1) + 1:4]
                link(v.scalar_tensor_tensor(out=b, in0=at(-1), scalar=0.5, in1=at(0), op0=ALU.mult, op1=ALU.add))
                link(v.tensor_tensor(b, b, at(1), ALU.add))
                link(v.tensor_tensor(b, b, at(2), ALU.add))
                link(v.scalar_tensor_tensor(out=b, in0=at(3), scalar=0.5, in1=b, op0=ALU.mult, op1=ALU.add))
                link(v.tensor_tensor(b, b, k.sel_mask[:, NBLK - 2 * qb:2 * NBLK - 2 * qb], ALU.add))
                link(v.memset(b[:, 0:1], BIG))
                choose_blocks(link, v, b, b2, b3, m8, imp)
                dve.wait_ge(cpt, qb + 1)
                v.tensor_copy(pcT[0:M, :, :].rearrange("p h q -> p (h q)"), k.ps[0:M, 6, :]).then_inc(cptc, 1)
                dve.wait_ge(btr, qb + 1)
                v.tensor_copy(qaug[HD:HD + NBLK, qb % 2, :, :],
                              k.ps[0:NBLK, 6, 0:P].rearrange("p (o q) -> p o q", o=1).broadcast_to([NBLK, H, P])).then_inc(bcp, 1)

            def compressed_d(qb):
                dve.wait_ge(cpv, qb + 1)
                if qb >= 2:
                    dve.wait_ge(otr, qb - 1)
                gate = k.tm[:, qb, 640:652].rearrange("p (h b) -> p h b", b=3)[:, :, 0:1].broadcast_to([P, H, HD])
                v.tensor_tensor(o_tm[:, qb % 2, :].rearrange("p (h d) -> p h d", d=HD),
                                k.ps[:, 6, 0:W].rearrange("p (h d) -> p h d", d=HD), gate, ALU.mult).then_inc(ocp, 1)

            def maxima(qb, u):
                kind, h = UNITS[u]
                n = qb * NU + u
                lo, hi = keys(qb, kind)
                dve.wait_ge(scr, n + 1)
                c = 16 + 2 * (n % 2)
                link(v.tensor_reduce(mx[:, 20:21], k.scores_ps[:, 0:(hi - lo) * P], AX.X, ALU.max))
                v.tensor_scalar(mx[:, c:c + 1], mx[:, 20:21], -SCALE, None, ALU.mult).then_inc(mxd, 1)

            def copies(qb, u):
                n = qb * NU + u
                lo, hi = keys(qb, UNITS[u][0])
                for i, (a, b) in enumerate(fours(hi - lo)):
                    e = base[n] + i
                    if e % 2 == 0:
                        dve.wait_ge(ptr, e + 1)
                        if e:
                            dve.wait_ge(pcp, e)
                        if n >= 2:
                            dve.wait_ge(pvd, n - 1)
                        v.tensor_copy(pT[:, n % 2, a * P:b * P], k.ps[:, 4, 0:(b - a) * P]).then_inc(pcp, 1)

            def outputs(qb, u):
                kind, h = UNITS[u]
                n = qb * NU + u
                c = 16 + 2 * (n % 2)
                g0 = 640 + 3 * h + (1 if kind == "sel" else 2)
                dve.wait_ge(exd, n + 1)
                link(v.reciprocal(mx[:, 24:25], mx[:, c + 1:c + 2]))
                link(v.tensor_tensor(mx[:, 25:26], mx[:, 24:25], k.tm[:, qb, g0:g0 + 1], ALU.mult))
                dve.wait_ge(pvd, n + 1)
                o = o_tm[:, qb % 2, h * HD:(h + 1) * HD]
                if kind == "sel" and h == 0:
                    dve.wait_ge(ocp, qb + 1)
                v.scalar_tensor_tensor(out=o, in0=k.ps[:, 7, 0:HD], scalar=mx[:, 25:26], in1=o, op0=ALU.mult, op1=ALU.add).then_inc(osc, 1)
                dve.wait_ge(osc, n + 1)

            def finish(qb):
                dve.wait_ge(otr, qb + 1)
                for j in range(2):
                    y = k.yT[6 + j][:, qb * P:(qb + 1) * P]
                    last = v.tensor_tensor(y, k.ps[:, 7, j * P:(j + 1) * P], y, ALU.mult)
                last.then_inc(ycp, 1)

            STEPS = {0: compressed_a, 1: compressed_b, 3: compressed_c, 5: compressed_d}
            for s in (0, 1, 3, 5):
                STEPS[s](0)
            maxima(0, 0)
            for n in range(NC * NU):
                qb, u = divmod(n, NU)
                if u + 1 < NU:
                    maxima(qb, u + 1)
                copies(qb, u)
                outputs(qb, u)
                if u in STEPS and qb + 1 < NC:
                    STEPS[u](qb + 1)
                if u == NU - 1:
                    if qb + 1 < NC:
                        maxima(qb + 1, 0)
                    finish(qb)


def choose_blocks(link, v, score, spare, out, m8, chosen):
    link(v.max(m8[:, 0:8], score))
    link(v.match_replace(spare, m8[:, 0:8], score, -3e38))
    link(v.max(m8[:, 8:16], spare))
    link(v.match_replace(out, m8[:, 8:16], spare, -3e38))
    v.tensor_scalar(score, out, -2e38, NEG, ALU.is_gt, ALU.mult).then_inc(chosen, 1)


def stage_sample_attention(nc, k, sem):
    M, Q = NCMP, NS * H
    GW = 4
    with ExitStack() as ctx:
        def sb(name, shape, dt=F32):
            return ctx.enter_context(nc.sbuf_tensor(name, shape, dt))
        kT = k.hview(0, 2 * T).rearrange("p (b t) -> p b t", b=2)
        kpage = k.hview(2 * T, T).rearrange("p (b g d) -> p b g d", b=2, d=HD)
        vpage = k.hview(3 * T, NS * PAGES * HD).rearrange("p (n g d) -> p n g d", n=NS, d=HD)
        kwin = k.hview(2 * T, T).rearrange("p (n g d) -> p n g d", n=NS, d=HD)
        vwin = k.hview(7 * T, NS * GW * HD).rearrange("p (n g d) -> p n g d", n=NS, d=HD)
        table = sb("table2", [1, NS * PAGES], I32)
        qT = sb("qT_s", [P, NS, H])
        newT = sb("newT_s", [HD, 4, NS])
        gd, gts = sb("gate_diag", [NS, NS, 12]), sb("gates_s", [HD, NS, 12])
        prod = sb("prod_s", [HD, 2, Q])
        snew = sb("snew", [P, 2, Q])
        scT, pc, pcT = sb("scT", [P, Q]), sb("pc_s", [Q, P]), sb("pcT_s", [P, Q])
        pick8 = sb("pick8", [Q, NS])
        st = sb("st_s", [Q, 8])
        pg, sc, m8 = sb("pg_s", [NS, P + 4]), sb("sc_s", [NS, 3, NBLK + 1]), sb("m8_s", [NS, 16])
        cmax = sb("cmax", [P, Q])
        dg = sb("dg_s", [Q, Q])
        M_b, pnew = sb("M_b", [P, Q]), sb("pnew", [P, Q])
        prob = sb("prob_s", [P, NS * PAGES * H])
        o_sum, o_b, l_b = sb("o_sum", [HD, Q]), sb("o_b", [HD, Q]), sb("l_b", [HD, Q])
        o_ch = sb("o_ch", [P, 2, NS])
        names = ("table_in kin0 kin1 vin win_in pk tr0 cp0 gm gcp cs_ csc cst ex nrm pp pcc imp btr bcp oc sn snc ktr kcp skt scd rmx mt dgd mb sub exd2 "
                 "av comb link osum och pick").split()
        z = {n: sem("d_" + n) for n in names}
        kin = [z["kin0"], z["kin1"]]
        block = ctx.enter_context(nc.Block())
        S_ps = k.ps[:, 0, :]
        branches = (("sel", PAGES, 0), ("win", GW, 1))

        @block.sync
        def _(sp):
            sp.dma_start(table[:, :], k.io["page_table"].rearrange("n g -> (n g)").rearrange("(o m) -> o m", o=1)).then_inc(z["table_in"], 16)
            sp.wait_ge(z["table_in"], 16)
            for n in range(NS):
                if n >= 2:
                    sp.wait_ge(z["ktr"], 4 * (n - 1))
                for g in range(PAGES):
                    i = sp.value_load(table[0:1, n * PAGES + g:n * PAGES + g + 1], min_val=0, max_val=k.n_pool - 1)
                    pg_ = k.io["cache_kv"][0, bass.DynSlice(i, 1), :, 2:4, :]
                    sp.dma_start(kpage[:, n % 2, g, :], pg_[:, :, 0, :].rearrange("o p d -> (o p) d")).then_inc(kin[n % 2], 16)
                    sp.dma_start(vpage[:, n, g, :], pg_[:, :, 1, :].rearrange("o p d -> (o p) d")).then_inc(z["vin"], 16)
            sp.wait_ge(z["ktr"], 4 * NS)
            for n in range(NS):
                wv = k.io["cache_win"][0, n].rearrange("(g p) s d -> s p g d", p=P)
                sp.dma_start(kwin[:, n], wv[0]).then_inc(z["win_in"], 16)
                sp.dma_start(vwin[:, n], wv[1]).then_inc(z["win_in"], 16)

        @block.gpsimd
        def _(pool):
            g = nc.gpsimd
            link = chain(pool, z["pick"])
            link(g.memset(pick8[:, :], 1.0))
            link(g.affine_select(out=pick8[:, :], in_=pick8[:, :], pattern=[[-4, NS]], compare_op=ALU.is_ge, fill=0.0, base=0, channel_multiplier=1))
            link(g.affine_select(out=pick8[:, :], in_=pick8[:, :], pattern=[[4, NS]], compare_op=ALU.is_ge, fill=0.0, base=3, channel_multiplier=-1))

        @block.tensor
        def _(pe):
            m = nc.tensor
            one = k.ones
            for h in range(H):
                m.transpose(k.ps[0:HD, 6, h * NS:(h + 1) * NS], k.tm[0:NS, NC, h * HD:(h + 1) * HD], k.ident[0:NS, 0:NS])
            for i, c in enumerate((384, 448, 512, 576)):
                last = m.transpose(k.ps[0:HD, 6, (H + i) * NS:(H + i + 1) * NS], k.tm[0:NS, NC, c:c + HD], k.ident[0:NS, 0:NS])
            last.then_inc(z["tr0"], 1)
            pe.wait_ge(z["gm"], 1)
            m.matmul(k.ps[0:HD, 7, 0:96], one[0:NS, 0:HD], gd[:, :, :].rearrange("a n g -> a (n g)"), start=True, stop=True).then_inc(z["tr0"], 1)
            pe.wait_ge(z["cp0"], 2)
            for n in range(NS):
                last = m.matmul(k.ps[0:M, 5, n * H:(n + 1) * H], k.kcT[0:HD, 1 + n, 0:M], qT[0:HD, n, :], start=True, stop=True)
            last.then_inc(z["cs_"], 1)
            pe.wait_ge(z["sn"], 1)
            pe.wait_ge(z["gcp"], 1)
            m.matmul(k.ps[:, 7, 0:2 * Q], one[0:HD, :], prod[:, :, :].rearrange("d b q -> d (b q)"), start=True, stop=True).then_inc(z["snc"], 1)
            pe.wait_ge(z["csc"], 1)
            m.transpose(k.ps[0:Q, 6, 0:M], scT[0:M, :], k.ident[0:M, 0:M]).then_inc(z["cst"], 1)
            pe.wait_ge(z["nrm"], 1)
            pe.wait_ge(z["pick"], 3)
            m.matmul(k.ps[0:NS, 5, 0:M], pick8[:, :], pc[:, 0:M], start=True, stop=True)
            m.transpose(k.ps[0:M, 6, 0:Q], pc[:, 0:M], k.ident[0:Q, 0:Q]).then_inc(z["pp"], 1)
            pe.wait_ge(z["pcc"], 1)
            for n in range(NS):
                last = m.matmul(k.ps[0:HD, 6, n * H:(n + 1) * H], k.vc[0:M, 1 + n, :], pcT[0:M, n * H:(n + 1) * H], start=True, stop=True)
            last.then_inc(z["oc"], 1)
            pe.wait_ge(z["imp"], 1)
            m.transpose(k.ps[0:NBLK, 5, 0:NS], sc[:, 0, 0:NBLK], k.ident[0:NS, 0:NS]).then_inc(z["btr"], 1)
            pe.wait_ge(z["bcp"], 1)
            pe.wait_ge(z["osum"], 1)

            def pool_max(b):
                pe.wait_ge(z["rmx"], b + 1)
                m.transpose(k.ps[0:Q, 5, 0:P], cmax[:, :], k.ident[:, :]).then_inc(z["mt"], 1)
                pe.wait_ge(z["dgd"], b + 1)
                m.matmul(k.ps[:, 6, 0:Q], one[0:Q, :], dg[:, :], start=True, stop=True).then_inc(z["mb"], 1)

            def pool_values(b, G, v):
                pe.wait_ge(z["exd2"], b + 1)
                p4 = prob[:, 0:NS * G * H].rearrange("p (n g h) -> p n g h", n=NS, h=H)
                for g in range(G):
                    m.matmul(k.ps[0:HD, 5, 0:Q], one[:, 0:HD], p4[:, :, g, :], start=(g == 0), stop=(g == G - 1))
                for n in range(NS):
                    for g in range(G):
                        last = m.matmul(k.ps[0:HD, 7, n * H:(n + 1) * H], v[:, n, g, :], p4[:, n, g, :], start=(g == 0), stop=(g == G - 1))
                last.then_inc(z["av"], 1)

            for n in range(NS):
                pe.wait_ge(kin[n % 2], 16 * PAGES * (n // 2 + 1))
                for b4 in range(4):
                    e = 4 * n + b4
                    if e >= 2:
                        pe.wait_ge(z["kcp"], e - 1)
                    for t in range(4):
                        last = m.transpose(k.ps[0:HD, 3 + e % 2, t * P:(t + 1) * P], kpage[:, n % 2, 4 * b4 + t, :], k.ident[:, :])
                    last.then_inc(z["ktr"], 1)
                pe.wait_ge(z["kcp"], 4 * n + 4)
                for g in range(PAGES):
                    last = m.matmul(S_ps[:, (n * PAGES + g) * H:(n * PAGES + g + 1) * H], kT[0:HD + NBLK, n % 2, g * P:(g + 1) * P],
                                    qT[0:HD + NBLK, n, :], start=True, stop=True)
                last.then_inc(z["scd"], 1)
            pool_max(0)
            pe.wait_ge(z["vin"], 16 * PAGES * NS)
            pool_values(0, PAGES, vpage)
            pe.wait_ge(z["win_in"], 32 * NS)
            for n in range(NS):
                e = 4 * NS + n
                pe.wait_ge(z["kcp"], e - 1)
                for t in range(GW):
                    last = m.transpose(k.ps[0:HD, 3 + e % 2, t * P:(t + 1) * P], kwin[:, n, t, :], k.ident[:, :])
                last.then_inc(z["ktr"], 1)
                pe.wait_ge(z["kcp"], e + 1)
                for g in range(GW):
                    last = m.matmul(S_ps[:, (n * GW + g) * H:(n * GW + g + 1) * H], kT[0:HD, n // 4, (n % 4) * 512 + g * P:(n % 4) * 512 + (g + 1) * P],
                                    qT[0:HD, n, :], start=True, stop=True)
                last.then_inc(z["scd"], 1)
            pe.wait_ge(z["comb"], 1)
            pool_max(1)
            pool_values(1, GW, vwin)

        @block.scalar
        def _(act):
            act.wait_ge(z["ex"], 1)
            nc.scalar.activation(pc[:, 0:M], k.ps[0:Q, 6, 0:M], ACT.Exp, scale=SCALE, bias=st[:, 1:2], accum_out=st[:, 2:3]).then_inc(z["ex"], 1)
            for b, (kind, G, i) in enumerate(branches):
                act.wait_ge(z["sub"], b + 1)
                n = NS * G * H
                nc.scalar.activation(prob[:, 0:n], prob[:, 0:n], ACT.Exp, scale=SCALE)
                nc.scalar.activation(pnew[:, :], pnew[:, :], ACT.Exp, scale=SCALE).then_inc(z["exd2"], 1)

        @block.vector
        def _(dve):
            v = nc.vector
            link = chain(dve, z["link"])
            link(v.memset(pg[:, :], 0.0))
            gate = k.tm[0:NS, NC, 640:652].rearrange("n (o g) -> n o g", o=1).broadcast_to([NS, NS, 12])
            v.tensor_tensor(gd[:, :, :], gate, k.ident[0:NS, 0:NS].rearrange("n (m o) -> n m o", o=1).broadcast_to([NS, NS, 12]), ALU.mult).then_inc(z["gm"], 1)
            dve.wait_ge(z["tr0"], 1)
            v.tensor_copy(qT[0:HD, :, :].rearrange("d n h -> d h n"), k.ps[0:HD, 6, 0:Q].rearrange("d (h n) -> d h n", n=NS)).then_inc(z["cp0"], 1)
            v.tensor_copy(newT[:, :, :].rearrange("d i n -> d (i n)"), k.ps[0:HD, 6, Q:2 * Q]).then_inc(z["cp0"], 1)
            dve.wait_ge(z["cp0"], 2)
            for b in range(2):
                kn = newT[:, 2 * b, :].rearrange("d (n o) -> d n o", o=1).broadcast_to([HD, NS, H])
                last = v.tensor_tensor(prod[:, b, :].rearrange("d (n h) -> d n h", h=H), qT[0:HD, :, :], kn, ALU.mult)
            last.then_inc(z["sn"], 1)
            dve.wait_ge(z["tr0"], 2)
            v.tensor_copy(gts[:, :, :].rearrange("d n g -> d (n g)"), k.ps[0:HD, 7, 0:96]).then_inc(z["gcp"], 1)
            dve.wait_ge(z["cs_"], 1)
            v.tensor_copy(scT[0:M, :], k.ps[0:M, 5, 0:Q]).then_inc(z["csc"], 1)
            dve.wait_ge(z["snc"], 1)
            v.tensor_copy(snew[:, :, :].rearrange("p b q -> p (b q)"), k.ps[:, 7, 0:2 * Q])
            dve.wait_ge(z["cst"], 1)
            link(v.tensor_reduce(st[:, 0:1], k.ps[0:Q, 6, 0:M], AX.X, ALU.max))
            v.tensor_scalar(st[:, 1:2], st[:, 0:1], -SCALE, None, ALU.mult).then_inc(z["ex"], 1)
            dve.wait_ge(z["ex"], 2)
            link(v.reciprocal(st[:, 3:4], st[:, 2:3]))
            v.tensor_scalar(pc[:, 0:M], pc[:, 0:M], st[:, 3:4], None, ALU.mult).then_inc(z["nrm"], 1)
            dve.wait_ge(z["pp"], 1)
            v.tensor_copy(pcT[0:M, :], k.ps[0:M, 6, 0:Q]).then_inc(z["pcc"], 1)
            link(v.tensor_copy(pg[:, 1:1 + M], k.ps[0:NS, 5, 0:M]))

            def at(o):
                return pg[:, 1 + o:1 + o + 4 * (NBLK - 1) + 1:4]
            b = sc[:, 0, 0:NBLK]
            link(v.scalar_tensor_tensor(out=b, in0=at(-1), scalar=0.5, in1=at(0), op0=ALU.mult, op1=ALU.add))
            link(v.tensor_tensor(b, b, at(1), ALU.add))
            link(v.tensor_tensor(b, b, at(2), ALU.add))
            link(v.scalar_tensor_tensor(out=b, in0=at(3), scalar=0.5, in1=b, op0=ALU.mult, op1=ALU.add))
            link(v.memset(sc[:, 0, 0:1], BIG))
            link(v.memset(sc[:, 0, NBLK - 1:NBLK + 1], BIG))
            choose_blocks(link, v, sc[:, 0, :], sc[:, 1, :], sc[:, 2, :], m8, z["imp"])
            dve.wait_ge(z["btr"], 1)
            v.tensor_copy(qT[HD:HD + NBLK, :, :], k.ps[0:NBLK, 5, 0:NS].rearrange("b (n o) -> b n o", o=1).broadcast_to([NBLK, NS, H])).then_inc(z["bcp"], 1)
            dve.wait_ge(z["oc"], 1)
            v.tensor_tensor(o_sum[:, :].rearrange("d (n h) -> d n h", h=H), k.ps[0:HD, 6, 0:Q].rearrange("d (n h) -> d n h", h=H),
                            gts[:, :, 0:12:3], ALU.mult).then_inc(z["osum"], 1)
            link(v.tensor_copy(kT[HD:HD + NBLK, 1, :], kT[HD:HD + NBLK, 0, :]))
            for n in range(NS):
                for b4 in range(4):
                    e = 4 * n + b4
                    dve.wait_ge(z["ktr"], e + 1)
                    if n >= 2:
                        dve.wait_ge(z["scd"], n - 1)
                    v.tensor_copy(kT[0:HD, n % 2, b4 * 512:(b4 + 1) * 512], k.ps[0:HD, 3 + e % 2, :]).then_inc(z["kcp"], 1)

            def softmax(b, G):
                n = NS * G * H
                s4 = S_ps[:, 0:n].rearrange("p (n g h) -> p n g h", n=NS, h=H)
                dve.wait_ge(z["scd"], NS * (b + 1))
                v.tensor_reduce(cmax[:, :].rearrange("p (n h) -> p n h", h=H), s4.rearrange("p n g h -> p n h g"), AX.X, ALU.max).then_inc(z["rmx"], 1)
                dve.wait_ge(z["mt"], b + 1)
                link(v.tensor_reduce(st[:, 4:5], k.ps[0:Q, 5, 0:P], AX.X, ALU.max))
                v.tensor_scalar(dg[:, :], k.ident[0:Q, 0:Q], st[:, 4:5], None, ALU.mult).then_inc(z["dgd"], 1)
                dve.wait_ge(z["mb"], b + 1)
                link(v.tensor_tensor(M_b[:, :], k.ps[:, 6, 0:Q], snew[:, b, :], ALU.max))
                mb = M_b[:, :].rearrange("p (n h) -> p n h", h=H)
                p4 = prob[:, 0:n].rearrange("p (n g h) -> p n g h", n=NS, h=H)
                for g in range(G):
                    v.tensor_tensor(p4[:, :, g, :], s4[:, :, g, :], mb, ALU.subtract)
                v.tensor_tensor(pnew[:, :], snew[:, b, :], M_b[:, :], ALU.subtract).then_inc(z["sub"], 1)

            def combine(b):
                dve.wait_ge(z["av"], b + 1)
                vn = newT[:, 2 * b + 1, :].rearrange("d (n o) -> d n o", o=1).broadcast_to([HD, NS, H])
                ob3 = o_b[:, :].rearrange("d (n h) -> d n h", h=H)
                link(v.tensor_tensor(ob3, pnew[0:HD, :].rearrange("d (n h) -> d n h", h=H), vn, ALU.mult))
                link(v.tensor_tensor(o_b[:, :], k.ps[0:HD, 7, 0:Q], o_b[:, :], ALU.add))
                link(v.tensor_tensor(l_b[:, :], k.ps[0:HD, 5, 0:Q], pnew[0:HD, :], ALU.add))
                link(v.reciprocal(l_b[:, :], l_b[:, :]))
                link(v.tensor_tensor(o_b[:, :], o_b[:, :], l_b[:, :], ALU.mult))
                link(v.tensor_tensor(ob3, ob3, gts[:, :, 1 + b:12:3], ALU.mult))
                v.tensor_tensor(o_sum[:, :], o_sum[:, :], o_b[:, :], ALU.add).then_inc(z["comb"], 1)
                dve.wait_ge(z["comb"], b + 1)

            softmax(0, PAGES)
            combine(0)
            for n in range(NS):
                e = 4 * NS + n
                dve.wait_ge(z["ktr"], e + 1)
                v.tensor_copy(kT[0:HD, n // 4, (n % 4) * 512:(n % 4 + 1) * 512], k.ps[0:HD, 3 + e % 2, :]).then_inc(z["kcp"], 1)
            softmax(1, GW)
            combine(1)
            o3 = o_sum[:, :].rearrange("d (n h) -> d n h", h=H)
            for h in range(H):
                r = slice((h % 2) * HD, (h % 2 + 1) * HD)
                last = v.tensor_copy(o_ch[r, h // 2, :], o3[:, :, h])
            last.then_inc(z["och"], 1)
            dve.wait_ge(z["och"], 1)
            for j in range(2):
                y = k.yT[6 + j][:, T:TT]
                v.tensor_tensor(y, y, o_ch[:, j, :], ALU.mult)


def stage_output(nc, k, sem):
    with ExitStack() as ctx:
        def sb(name, shape, dt=F32):
            return ctx.enter_context(nc.sbuf_tensor(name, shape, dt))
        w_out = k.hview(0, KT * D).rearrange("p (k n) -> p k n", k=KT)
        x_in = k.hview(KT * D, 3 * D).rearrange("p (b n) -> p b n", b=3)
        y_out = k.hview(KT * D + 3 * D, 3 * D).rearrange("p (b n) -> p b n", b=3)
        ys = sb("ys", [NS, D])
        xs = sb("xs", [NS, D])
        w_in, x_s, s_mm, s_v, gated, mm, added, stored, y_s = (sem("o_" + n) for n in ("w_in", "x_s", "s_mm", "s_v", "gated", "mm", "added", "stored", "y_s"))
        x_r = [sem(f"o_x{i}") for i in range(3)]
        out_r = [sem(f"o_stored{i}") for i in range(3)]
        block = ctx.enter_context(nc.Block())
        ROW = {0: 2, 1: 3, 2: 0, 3: 1, 4: 4, 5: 5, 6: 6, 7: 7}

        @block.sync
        def _(sp):
            for i in range(KT):
                sp.dma_start(w_out[:, i, :], k.io["w_out"][0, ROW[i] * P:(ROW[i] + 1) * P, :]).then_inc(w_in, 16)
            sp.dma_start(xs[:, :], k.io["x_sample"][:, 0, :]).then_inc(x_s, 16)
            for t in range(NC):
                if t >= 3:
                    sp.wait_ge(added, t - 2)
                sp.dma_start(x_in[:, t % 3, :], k.io["x_prompt"][0, t * P:(t + 1) * P, :]).then_inc(x_r[t % 3], 16)

        @block.scalar
        def _(act):
            act.wait_ge(y_s, 1)
            act.dma_start(k.io["y_sample"][:, 0, :], ys[:, :]).then_inc(stored, 16)
            for t in range(NC):
                act.wait_ge(added, t + 1)
                act.dma_start(k.io["y_prompt"][0, t * P:(t + 1) * P, :], y_out[:, t % 3, :]).then_inc(out_r[t % 3], 16)
            act.wait_ge(stored, 16)
            for i in range(3):
                act.wait_ge(out_r[i], 16 * len(range(i, NC, 3)))

        @block.tensor
        def _(pe):
            m = nc.tensor
            pe.wait_ge(w_in, 16 * KT)
            for half in range(2):
                for i in range(KT):
                    last = m.matmul(k.ps[0:NS, half, :], k.yT[i][:, T:TT], w_out[:, i, half * 512:(half + 1) * 512], start=(i == 0), stop=(i == KT - 1))
            last.then_inc(s_mm, 1)
            pe.wait_ge(gated, KT)
            for t in range(NC):
                if t >= 2:
                    pe.wait_ge(added, t - 1)
                for half in range(2):
                    for i in range(KT):
                        last = m.matmul(k.ps[:, 2 + 2 * (t % 2) + half, :], k.yT[i][:, t * P:(t + 1) * P], w_out[:, i, half * 512:(half + 1) * 512],
                                        start=(i == 0), stop=(i == KT - 1))
                last.then_inc(mm, 1)

        @block.vector
        def _(dve):
            v = nc.vector
            dve.wait_ge(s_mm, 1)
            for i in range(KT):
                v.tensor_tensor(w_out[:, i, :], w_out[:, i, :], k.gate_p[:, :], ALU.mult).then_inc(gated, 1)
            v.tensor_tensor(ys[:, 0:512], k.ps[0:NS, 0, :], k.gate_s[:, 0:512], ALU.mult)
            v.tensor_tensor(ys[:, 512:D], k.ps[0:NS, 1, :], k.gate_s[:, 512:D], ALU.mult).then_inc(s_v, 1)
            dve.wait_ge(x_s, 16)
            dve.wait_ge(s_v, 1)
            v.tensor_tensor(ys[:, :], ys[:, :], xs[:, :], ALU.add).then_inc(y_s, 1)
            for t in range(NC):
                dve.wait_ge(mm, t + 1)
                dve.wait_ge(x_r[t % 3], 16 * (t // 3 + 1))
                if t >= 3:
                    dve.wait_ge(out_r[t % 3], 16 * (t // 3))
                for half in range(2):
                    c = slice(half * 512, (half + 1) * 512)
                    last = v.tensor_tensor(y_out[:, t % 3, c], k.ps[:, 2 + 2 * (t % 2) + half, :], x_in[:, t % 3, c], ALU.add)
                last.then_inc(added, 1)


_INS = ['x_prompt', 'x_sample', 'cache_kv', 'cache_win', 'state_sconv', 'state_ssm_conv', 'state_ssm', 'state_cconv',
        'page_table', 'c_prompt', 'c_sample', 'norm_g', 'w_ada', 'b_ada', 'w_in', 'w_out', 'sc_w', 'ssd_conv_w', 'ssd_conv_b',
        'ssd_dt_bias', 'ssd_A_log', 'ssd_D', 'ssd_norm_g', 'cf_w', 'cf_b', 'cf_ln_g', 'cf_ln_b', 'q_g', 'k_g',
        'cmp_pe', 'cmp_w1', 'cmp_b1', 'cmp_w2', 'cmp_b2']
_OUTS = [('y_prompt', (1, T, D)), ('y_sample', (NS, 1, D)), ('kv_p', (1, NC, P, 4, HD)), ('kv_s', (1, NS, 1, 4, HD)),
         ('win_p', (1, 1, 512, 2, HD)), ('win_s', (1, NS, 512, 2, HD)), ('sconv_p', (1, 1, 2, W)), ('sconv_s', (1, NS, 2, W)),
         ('ssm_conv_p', (1, 1, 3, CV)), ('ssm_conv_s', (1, NS, 3, CV)), ('ssm_p', (1, 1, SH, SP, SST)),
         ('ssm_s', (1, NS, SH, SP, SST)), ('cconv_p', (1, 1, KCF - 1, W)), ('cconv_s', (1, NS, KCF - 1, W))]


def build(nc, k):
    with ExitStack() as ctx:
        def sb(name, shape):
            return ctx.enter_context(nc.sbuf_tensor(name, shape, F32))

        stores = {name: ctx.enter_context(nc.semaphore(name)) for name in
                  ("xstored", "s_stored", "c_stored", "t_stored", "o_stored", "o_stored0", "o_stored1", "o_stored2")}

        def run(stage):
            own = []

            def sem(name):
                if name in stores:
                    return stores[name]
                own.append(nc.alloc_semaphore(name))
                return own[-1]
            stage(nc, k, sem)
            nc.clear_and_free_semaphores(own)
            nc.all_engine_barrier()
        k.ps = ctx.enter_context(nc.psum_tensor("ps", [P, 8, GT], F32))
        k.scores_ps = k.ps[:, 0:4, :].rearrange("p b n -> p (b n)")
        k.ones, k.ident, k.upper, k.below, k.causal, k.win_low = (
            sb(name, [P, P]) for name in ("ones", "ident", "upper", "below", "causal", "win_low"))
        k.neg_upper = sb("neg_upper", [P, SH * P])
        k.cmp_mask = sb("cmp_mask", [P, 2 * P])
        k.sel_mask = sb("sel_mask", [P, 2 * NBLK])
        k.head_pick = sb("head_pick", [SH, 2, P])
        k.par = sb("par", [P, PEND])
        k.shift, k.scale = sb("shift", [P, KT, NS + 1]), sb("scale", [P, KT, NS + 1])
        k.gate_s, k.gate_p = sb("gate_s", [NS, D]), sb("gate_p", [P, D])
        k.dt = sb("dt", [P, (NC + 1) * SH])
        k.tails_T = sb("tails_T", [P, 6, 3 + NS])
        y_ssd = sb("y_ssd", [P, 2, TT])
        arena = sb("arena", [P, 6, TT])
        k.xbc = arena
        k.yT = [y_ssd[:, j, :] for j in range(2)] + [arena[:, j, :] for j in range(6)]
        h_space = sb("h_space", [P, KT * TT])
        k.hT = h_space[:, :].rearrange("p (k t) -> p k t", k=KT)

        def hview(start, size):
            return h_space[:, start:start + size]
        k.hview = hview
        k.blk_dram = nc.dram_tensor("block_rows", (NBLK, T), F32, kind="Internal").ap()
        run(stage_prepare)
        run(stage_norm)
        run(stage_ssd_inputs)
        run(stage_ssd)
        run(stage_ssd_norm)
        with nc.sbuf_tensor("conf", [P, 2, TT], F32) as conf:
            k.conf = conf
            run(stage_convs)
            run(stage_conformer_norm)
        k.tm = sb("tm", [P, NC + 1, TM])
        run(stage_token_major)
        k.ksel, k.kwin = hview(0, T), hview(T, T)
        k.kcT, k.vc = sb("kcT", [HD, 1 + NS, P]), sb("vc", [P, 1 + NS, HD])
        run(stage_compress)
        run(stage_attention)
        run(stage_sample_attention)
        run(stage_output)


def kernel(**inputs):
    import numpy as np
    import concourse.bacc as bacc
    from concourse.bass_utils import run_bass_kernel_spmd

    nc = bacc.Bacc("TRN2", target_bir_lowering=False, num_devices=1)
    arrays, tensors = {}, {}
    for name in _INS:
        a = np.ascontiguousarray(inputs[name])
        arrays["in_" + name] = a
        tensors[name] = nc.dram_tensor("in_" + name, a.shape, mybir.dt.from_np(a.dtype), kind="ExternalInput").ap()
    for name, shape in _OUTS:
        tensors[name] = nc.dram_tensor("out_" + name, shape, F32, kind="ExternalOutput").ap()
    k = Shared(tensors)
    k.n_pool = inputs["cache_kv"].shape[1]
    build(nc, k)
    r = run_bass_kernel_spmd(nc, [arrays], core_ids=[0])
    return tuple(r.results[0]["out_" + name] for name, _ in _OUTS)
```

```python
from contextlib import ExitStack

import concourse.bass as bass
from concourse import mybir

F32 = mybir.dt.float32
I32 = mybir.dt.int32
ALU = mybir.AluOpType
ACT = mybir.ActivationFunctionType
AX = mybir.AxisListType

P = 128
D = 1024
KT = D // P
W = 256
T = 2048
NC = T // P
NS = 8
TT = T + NS
GT = 512
NG = T // GT
SH, SP, SST = 4, 64, 128
CV = 768
KCF = 31
H, HD = 4, 64
PAST = 2048
PAGES = PAST // P
NCMP = T // 16 - 1
NBLK = T // 64
EPS = 1e-6
NEG = -1e30
BIG = 1e30
SCALE = HD ** -0.5

COL_A = 0
COL_Z = 4 * W
COL_XBC = COL_Z + W
COL_DT = COL_XBC + CV
COL_GLU = COL_DT + SH
COL_CG = COL_GLU + 2 * W
COL_Q = COL_CG + W
COL_KV = COL_Q + W
COL_DG = COL_KV + 6 * HD
COL_BG = COL_DG + W
TM = W + 6 * HD + 3 * H

PA_ROWS, PB_ROWS, PC_ROWS = 5, 38, 4
PA = 0
PB = PA + 6 * PA_ROWS
PC = PB + 2 * PB_ROWS
PEND = PC + 8 * PC_ROWS
B_SC, B_CF, B_CFB, B_LNG, B_LNB, B_SSDG = 0, 3, 34, 35, 36, 37


class Shared:

    def __init__(self, io):
        self.io = io


def chain(eng, sem):
    count = [0]

    def link(ins):
        count[0] += 1
        ins.then_inc(sem, 1)
        eng.wait_ge(sem, count[0])
    return link


def stage_prepare(nc, k, sem):
    NV = NS + 1
    WB = 512
    NB = 3 * D // WB
    with ExitStack() as ctx:
        def sb(name, shape, dt=F32):
            return ctx.enter_context(nc.sbuf_tensor(name, shape, dt))
        c_rows, c_silu = sb("c_rows", [NV, D]), sb("c_silu", [NV, D])
        rows_a, rows_b, rows_c = sb("rows_a", [PA_ROWS, CV]), sb("rows_b", [PB_ROWS, W]), sb("rows_c", [PC_ROWS, D])
        cT = sb("cT", [P, KT, NV])
        w_ada = k.hview(0, 2 * KT * WB).rearrange("p (b k n) -> p b k n", b=2, k=KT)
        pick_prompt = sb("pick_prompt", [NV, P])
        b_gate = sb("b_gate", [NV, D])
        gates = sb("gates", [NV, D])
        blk_rows = k.hview(2 * KT * WB, T)[0:NBLK + 2, :]
        win_rows = k.hview(2 * KT * WB + T, T)[0:NBLK + 2, :]
        rows_in, c_in, bg_in, w_in, silu_done, tr_done, cp_done, w_used, ada_done, gate_done, gsum_done, bc_done, g_done = (
            sem(n) for n in ("rows_in", "c_in", "bg_in", "wada_in", "csilu", "ptr_done", "pcp_done", "wada_used",
                             "ada_done", "gate_done", "gsum_done", "bc_done", "pconst_done"))
        w_in1 = sem("wada_in1")
        blk_sent = sem("blk_sent")
        block = ctx.enter_context(nc.Block())
        par_ps, cT_ps = k.ps[:, 0, 0:PEND], k.ps[:, 1, 0:KT * NV]
        ada_ps = k.ps[:, 2, 0:2 * KT * NV]

        @block.sync
        def _(sp):
            sp.dma_start(c_rows[0:NS, :], k.io["c_sample"]).then_inc(c_in, 16)
            sp.dma_start(c_rows[NS:NV, :], k.io["c_prompt"]).then_inc(c_in, 16)
            for b in range(NB):
                if b >= 2:
                    sp.wait_ge(w_used, b - 1)
                sp.dma_start(w_ada[:, b % 2], k.io["w_ada"][0].rearrange("(k p) n -> p k n", p=P)[:, :, b * WB:(b + 1) * WB]
                             ).then_inc(w_in1 if b % 2 else w_in, 16)

        @block.scalar
        def _(act):
            sc = k.io["sc_w"][0], k.io["cf_w"][0]
            act.dma_start(rows_a[0:4, :], k.io["ssd_conv_w"][0]).then_inc(rows_in, 16)
            act.dma_start(rows_a[4:5, :], k.io["ssd_conv_b"]).then_inc(rows_in, 16)
            act.dma_start(rows_b[B_SC:B_SC + 3, :], sc[0]).then_inc(rows_in, 16)
            act.dma_start(rows_b[B_CF:B_CF + KCF, :], sc[1]).then_inc(rows_in, 16)
            for r, a in ((B_CFB, k.io["cf_b"]), (B_LNG, k.io["cf_ln_g"]), (B_LNB, k.io["cf_ln_b"]), (B_SSDG, k.io["ssd_norm_g"])):
                act.dma_start(rows_b[r:r + 1, :], a).then_inc(rows_in, 16)
            act.dma_start(rows_c[0:1, :], k.io["norm_g"]).then_inc(rows_in, 16)
            act.dma_start(rows_c[1:4, :], k.io["b_ada"][0].rearrange("(r d) -> r d", r=3)).then_inc(rows_in, 16)
            act.dma_start(b_gate[:, :], k.io["b_ada"][0:1, 2 * D:3 * D].broadcast_to([NV, D])).then_inc(bg_in, 16)
            act.wait_ge(c_in, 32)
            nc.scalar.activation(c_silu[:, :], c_rows[:, :], ACT.Silu).then_inc(silu_done, 1)

        @block.gpsimd
        def _(pool):
            g = nc.gpsimd
            link = chain(pool, g_done)
            link(g.memset(k.ones[:, :], 1.0))

            def select(t, src, pattern, base, mult, fill, op=ALU.is_ge):
                link(g.affine_select(out=t, in_=src, pattern=pattern, compare_op=op, fill=fill, base=base,
                                     channel_multiplier=mult))
            one = k.ones[:, :]
            select(k.ident[:, :], one, [[-1, P]], 0, 1, 0.0, ALU.is_equal)
            select(k.upper[:, :], one, [[1, P]], 0, -1, 0.0)
            select(k.below[:, :], one, [[-1, P]], -1, 1, 0.0)
            link(g.memset(k.neg_upper[:, :], 0.0))
            for h in range(SH):
                v = k.neg_upper[:, h * P:(h + 1) * P]
                select(v, v, [[1, P]], 0, -1, NEG)
            link(g.memset(k.causal[:, :], 0.0))
            select(k.causal[:, :], k.causal[:, :], [[-1, P]], 0, 1, NEG)
            link(g.memset(k.win_low[:, :], 0.0))
            select(k.win_low[:, :], k.win_low[:, :], [[1, P]], 0, -1, NEG)
            link(g.memset(k.cmp_mask[:, :], 0.0))
            select(k.cmp_mask[:, :], k.cmp_mask[:, :], [[-16, 2 * P]], 16 * P - 31, 1, NEG)
            link(g.memset(k.sel_mask[:, :], BIG))
            select(k.sel_mask[:, :], k.sel_mask[:, :], [[64, 2 * NBLK]], 64 * (2 - NBLK) - 1, -1, 0.0)
            select(k.sel_mask[:, :], k.sel_mask[:, :], [[-64, 2 * NBLK]], 64 * NBLK, 1, NEG)
            link(g.memset(blk_rows[:, :], 1.0))
            select(blk_rows[:, :], blk_rows[:, :], [[1, T]], 0, -64, 0.0)
            select(blk_rows[:, :], blk_rows[:, :], [[-1, T]], 63, 64, 0.0)
            link(g.memset(blk_rows[NBLK:NBLK + 1, :], 1.0))
            link(g.memset(win_rows[:, :], 1.0))
            select(win_rows[:, :], win_rows[:, :], [[0, T]], -NBLK - 1, 1, 0.0)
            pool.dma_start(k.extra_dram[0], blk_rows[:, :]).then_inc(blk_sent, 16)
            pool.dma_start(k.extra_dram[1], win_rows[:, :]).then_inc(blk_sent, 16)
            link(g.memset(k.low_T[:, :], 0.0))
            for h in range(SH):
                v = k.low_T[:, h * P:(h + 1) * P]
                select(v, v, [[-1, P]], 0, 1, NEG)
            link(g.memset(pick_prompt[:, :], 1.0))
            select(pick_prompt[:, :], pick_prompt[:, :], [[0, P]], -NS, 1, 0.0)
            for j in range(2):
                v = k.head_pick[:, j, :]
                link(g.memset(v, 1.0))
                select(v, v, [[1, P]], 2 * j * SP, -SP, 0.0)
                select(v, v, [[-1, P]], -2 * j * SP + SP - 1, SP, 0.0)
            pool.wait_ge(blk_sent, 32)

        n_const = 1 + 3 + 1 + SH + 2 + 2 + 2 + 3 + 3 + 3 + 1 + SH + 2 + 6

        @block.tensor
        def _(pe):
            m = nc.tensor
            pe.wait_ge(g_done, n_const)
            pe.wait_ge(rows_in, 160)
            for n in range(6):
                m.transpose(par_ps[:, PA + n * PA_ROWS:PA + (n + 1) * PA_ROWS], rows_a[:, n * P:(n + 1) * P],
                            k.ident[0:PA_ROWS, 0:PA_ROWS])
            for n in range(2):
                m.transpose(par_ps[:, PB + n * PB_ROWS:PB + (n + 1) * PB_ROWS], rows_b[:, n * P:(n + 1) * P],
                            k.ident[0:PB_ROWS, 0:PB_ROWS])
            for n in range(8):
                last = m.transpose(par_ps[:, PC + n * PC_ROWS:PC + (n + 1) * PC_ROWS], rows_c[:, n * P:(n + 1) * P],
                                   k.ident[0:PC_ROWS, 0:PC_ROWS])
            last.then_inc(tr_done, 1)
            pe.wait_ge(silu_done, 1)
            for n in range(KT):
                last = m.transpose(cT_ps[:, n * NV:(n + 1) * NV], c_silu[:, n * P:(n + 1) * P], k.ident[0:NV, 0:NV])
            last.then_inc(tr_done, 1)
            pe.wait_ge(cp_done, 2)
            for b in range(NB):
                pe.wait_ge(w_in1 if b % 2 else w_in, 16 * (b // 2 + 1))
                if b < 4:
                    for n in range(4):
                        for kk in range(KT):
                            last = m.matmul(ada_ps[:, (4 * b + n) * NV:(4 * b + n + 1) * NV],
                                            w_ada[:, b % 2, kk, n * P:(n + 1) * P], cT[:, kk, :],
                                            start=(kk == 0), stop=(kk == KT - 1))
                    last.then_inc(w_used, 1)
                else:
                    for kk in range(KT):
                        last = m.matmul(k.ps[0:NV, b - 1, :], cT[:, kk, :], w_ada[:, b % 2, kk, :],
                                        start=(kk == 0), stop=(kk == KT - 1))
                    last.then_inc(w_used, 1)
            pe.wait_ge(gsum_done, 1)
            for n in range(2):
                last = m.matmul(k.ps[:, 5 + n, :], pick_prompt[:, :], gates[:, n * 512:(n + 1) * 512], start=True, stop=True)
            last.then_inc(bc_done, 1)

        @block.vector
        def _(dve):
            v = nc.vector
            dve.wait_ge(tr_done, 1)
            v.tensor_copy(k.par[:, :], par_ps).then_inc(cp_done, 1)
            dve.wait_ge(tr_done, 2)
            v.tensor_copy(cT[:, :, :].rearrange("p k n -> p (k n)"), cT_ps).then_inc(cp_done, 1)
            dve.wait_ge(w_used, 4)
            dve.wait_ge(cp_done, 2)
            pc = k.par[:, PC:PEND].rearrange("p (n r) -> p n r", r=PC_ROWS)
            ada = ada_ps.rearrange("p (n v) -> p n v", v=NV)
            v.tensor_tensor(k.shift[:, :, :], ada[:, 0:KT, :], pc[:, :, 1:2].broadcast_to([P, KT, NV]), ALU.add)
            link = chain(dve, ada_done)
            link(v.tensor_tensor(k.scale[:, :, :], ada[:, KT:2 * KT, :], pc[:, :, 2:3].broadcast_to([P, KT, NV]), ALU.add))
            link(v.tensor_scalar(k.scale[:, :, :], k.scale[:, :, :], 1.0, None, ALU.add))
            link(v.tensor_tensor(k.scale[:, :, :], k.scale[:, :, :], pc[:, :, 0:1].broadcast_to([P, KT, NV]), ALU.mult))
            dve.wait_ge(w_used, NB)
            dve.wait_ge(bg_in, 16)
            link(v.tensor_tensor(gates[:, 0:512], k.ps[0:NV, 3, :], b_gate[:, 0:512], ALU.add))
            v.tensor_tensor(gates[:, 512:D], k.ps[0:NV, 4, :], b_gate[:, 512:D], ALU.add).then_inc(gsum_done, 1)
            dve.wait_ge(gsum_done, 1)
            v.tensor_copy(k.gate_s[:, :], gates[0:NS, :])
            dve.wait_ge(bc_done, 1)
            v.tensor_copy(k.gate_p[:, 0:512], k.ps[:, 5, :])
            v.tensor_copy(k.gate_p[:, 512:D], k.ps[:, 6, :])


def stage_norm(nc, k, sem):
    NX = 3
    with ExitStack() as ctx:
        def sb(name, shape, dt=F32):
            return ctx.enter_context(nc.sbuf_tensor(name, shape, dt))
        x_in = sb("x_in", [P, NX, D])
        x_n = sb("x_n", [P, 2, D])
        junk = sb("junk", [P, D])
        stat = sb("stat", [P, NC + 1, 4])
        x_in0 = [sem(f"x_in{i}") for i in range(NX)]
        sq_done, var_done, root_done, xn_done, tr_done, ev_v, ev_a, link_s, aux = (
            sem(n) for n in ("sq_done", "var_done", "root_done", "xn_done", "xtr_done", "hev_v", "hev_a", "nlink", "naux"))
        block = ctx.enter_context(nc.Block())
        rows = [P] * NC + [NS]

        @block.sync
        def _(sp):
            for t in range(NC + 1):
                if t >= NX:
                    sp.wait_ge(xn_done, t - NX + 1)
                src = k.io["x_prompt"][0, t * P:(t + 1) * P, :] if t < NC else k.io["x_sample"][:, 0, :]
                sp.dma_start(x_in[0:rows[t], t % NX, :], src).then_inc(x_in0[t % NX], 16)

        @block.scalar
        def _(act):
            def head(t):
                r = rows[t]
                act.wait_ge(x_in0[t % NX], 16 * (t // NX + 1))
                if t:
                    act.wait_ge(sq_done, t)
                nc.scalar.activation(junk[0:r, :], x_in[0:r, t % NX, :], ACT.Square,
                                     accum_out=stat[0:r, t, 0:1]).then_inc(sq_done, 1)
                act.wait_ge(var_done, t + 1)
                nc.scalar.activation(stat[0:r, t, 3:4], stat[0:r, t, 2:3], ACT.Sqrt).then_inc(root_done, 1)

            head(0)
            for t in range(NC):
                head(t + 1)
                act.wait_ge(tr_done, t + 1)
                for kk in range(4, 8):
                    last = nc.scalar.activation(k.hT[:, kk, t * P:(t + 1) * P], k.ps[:, 2 * (t % 2) + 1, (kk - 4) * P:(kk - 3) * P],
                                                ACT.Identity, bias=k.shift[:, kk, NS:NS + 1], scale=k.scale[:, kk, NS:NS + 1])
                last.then_inc(ev_a, 1)

        @block.tensor
        def _(pe):
            for t in range(NC + 1):
                r = rows[t]
                pe.wait_ge(xn_done, t + 1)
                if t >= 2:
                    pe.wait_ge(ev_v, t - 1)
                    pe.wait_ge(ev_a, t - 1)
                for kk in range(KT):
                    last = nc.tensor.transpose(k.ps[:, 2 * (t % 2) + kk // 4, (kk % 4) * r:(kk % 4 + 1) * r],
                                               x_n[0:r, t % 2, kk * P:(kk + 1) * P], k.ident[0:r, 0:r])
                last.then_inc(tr_done, 1)

        @block.vector
        def _(dve):
            v = nc.vector
            link = chain(dve, link_s)

            def head(t):
                r = rows[t]
                dve.wait_ge(sq_done, t + 1)
                link(v.tensor_scalar(stat[0:r, t, 1:2], stat[0:r, t, 0:1], 1.0 / D, EPS, ALU.mult, ALU.add))
                v.reciprocal(stat[0:r, t, 2:3], stat[0:r, t, 1:2]).then_inc(var_done, 1)
                dve.wait_ge(root_done, t + 1)
                if t >= 2:
                    dve.wait_ge(tr_done, t - 1)
                v.tensor_scalar(x_n[0:r, t % 2, :], x_in[0:r, t % NX, :], stat[0:r, t, 3:4], None,
                                ALU.mult).then_inc(xn_done, 1)

            head(0)
            for t in range(NC):
                head(t + 1)
                dve.wait_ge(tr_done, t + 1)
                for kk in range(4):
                    last = v.tensor_scalar(k.hT[:, kk, t * P:(t + 1) * P], k.ps[:, 2 * (t % 2), kk * P:(kk + 1) * P],
                                           k.scale[:, kk, NS:NS + 1], k.shift[:, kk, NS:NS + 1], ALU.mult, ALU.add)
                last.then_inc(ev_v, 1)
            dve.wait_ge(tr_done, NC + 1)
            for half in range(2):
                src = k.ps[:, 2 * (NC % 2) + half, 0:4 * NS].rearrange("p (k n) -> p k n", n=NS)
                dst = k.hT[:, 4 * half:4 * half + 4, T:TT]
                link(v.tensor_tensor(dst, src, k.scale[:, 4 * half:4 * half + 4, 0:NS], ALU.mult))
                link(v.tensor_tensor(dst, dst, k.shift[:, 4 * half:4 * half + 4, 0:NS], ALU.add))


def channel_projection(nc, k, eng, cols, w_buf, w_ready, used, unit_done, unit_free):
    for i, c in enumerate(cols):
        eng.wait_ge(w_ready[i % 2], 16 * (i // 2 + 1))
        for g in range(NG + 1):
            u = i * (NG + 1) + g
            if u >= 8:
                unit_free(eng, u - 8)
            n, t0 = (GT, g * GT) if g < NG else (NS, T)
            for kk in range(KT):
                last = nc.tensor.matmul(k.ps[:, u % 8, 0:n], w_buf[:, i % 2, kk, :], k.hT[:, kk, t0:t0 + n],
                                        start=(kk == 0), stop=(kk == KT - 1))
            last.then_inc(unit_done, 1)


def load_tiles(k, sp, cols, w_buf, w_ready, unit_done):
    for i, c in enumerate(cols):
        if i >= 2:
            sp.wait_ge(unit_done, (i - 1) * (NG + 1))
        sp.dma_start(w_buf[:, i % 2], k.io["w_in"][0].rearrange("(k p) n -> p k n", p=P)[:, :, c:c + P]).then_inc(w_ready[i % 2], 16)


def stage_ssd_inputs(nc, k, sem):
    cols = [COL_XBC + P * j for j in range(6)] + [COL_Z, COL_Z + P]
    NJ = 6
    with ExitStack() as ctx:
        def sb(name, shape, dt=F32):
            return ctx.enter_context(nc.sbuf_tensor(name, shape, dt))
        w_buf = sb("w_buf", [P, 2, KT, P])
        w_dt = sb("w_dt", [P, KT, SH])
        raw = sb("raw_xbc", [P, 2, 3 + TT])
        prev_rows = sb("prev_rows", [3 * NS, CV])
        prev = sb("prev_xbc", [P, 6, NS, 3])
        tail = sb("tail_xbc", [P, 2, 3 + NS])
        tails = sb("tails_xbc", [3 + NS, CV])
        w_ready = [sem("wx_ready0"), sem("wx_ready1")]
        dt_in, prev_in, unit_done, evac, conv, silu, link_s, zero, prev_tr, prev_cp, tail_cp, tail_tr, tails_cp, stored, dt_done = (
            sem(n) for n in ("dt_in", "prev_in", "xunit", "xevac", "xconv", "xsilu", "xlink", "xzero", "xprev_tr", "xprev_cp",
                             "xtail_cp", "xtail_tr", "xtails_cp", "xstored", "dt_done"))
        block = ctx.enter_context(nc.Block())
        U = NG + 1

        @block.sync
        def _(sp):
            sp.dma_start(prev_rows[:, :], k.io["state_ssm_conv"][0].rearrange("s r c -> (s r) c")).then_inc(prev_in, 16)
            with nc.allow_non_contiguous_dma(reason="four columns of the projection"):
                sp.dma_start(w_dt[:, :, :], k.io["w_in"][0].rearrange("(k p) n -> p k n", p=P)[:, :, COL_DT:COL_DT + SH]).then_inc(dt_in, 16)
            load_tiles(k, sp, cols, w_buf, w_ready, unit_done)
            sp.dma_start(k.io["ssm_conv_s"][0, :, 0:2, :], k.io["state_ssm_conv"][0, :, 1:3, :]).then_inc(stored, 16)
            sp.wait_ge(tails_cp, 1)
            sp.dma_start(k.io["ssm_conv_p"][0, 0], tails[0:3, :]).then_inc(stored, 16)
            sp.dma_start(k.io["ssm_conv_s"][0, :, 2, :], tails[3:3 + NS, :]).then_inc(stored, 16)
            sp.wait_ge(stored, 48)

        @block.tensor
        def _(pe):
            m = nc.tensor
            pe.wait_ge(prev_in, 16)
            for j in range(NJ):
                last = m.transpose(k.ps[:, 7, j * 24:(j + 1) * 24], prev_rows[:, j * P:(j + 1) * P], k.ident[0:24, 0:24])
            last.then_inc(prev_tr, 1)
            pe.wait_ge(dt_in, 16)
            for t in range(NC + 1):
                r = P if t < NC else NS
                for kk in range(KT):
                    last = m.matmul(k.ps[0:r, 6, t * SH:(t + 1) * SH], k.hT[:, kk, t * P:t * P + r], w_dt[:, kk, :],
                                    start=(kk == 0), stop=(kk == KT - 1))
            last.then_inc(dt_done, 1)
            pe.wait_ge(prev_cp, 3)

            def free(eng, u):
                eng.wait_ge(evac, u + 1)
            channel_projection(nc, k, pe, cols, w_buf, w_ready, None, unit_done, free)
            pe.wait_ge(evac, len(cols) * U)
            for j in range(NJ):
                pe.wait_ge(tail_cp, j + 1)
                m.transpose(k.ps[0:3 + NS, j // 4, (j % 4) * P:(j % 4 + 1) * P], k.tails_T[:, j, :], k.ident[:, :]).then_inc(tail_tr, 1)

        @block.scalar
        def _(act):
            for i in range(len(cols)):
                for g in range(U):
                    n, t0 = (GT, g * GT) if g < NG else (NS, T)
                    u = i * U + g
                    act.wait_ge(unit_done, u + 1)
                    if i < NJ:
                        if i >= 2 and g == 0:
                            act.wait_ge(conv, i - 1)
                            act.wait_ge(tail_cp, i - 1)
                        nc.scalar.copy(raw[:, i % 2, 3 + t0:3 + t0 + n], k.ps[:, u % 8, 0:n]).then_inc(evac, 1)
                    else:
                        nc.scalar.activation(k.yT[i - NJ][:, t0:t0 + n], k.ps[:, u % 8, 0:n], ACT.Silu).then_inc(evac, 1)
                if 1 <= i <= NJ:
                    act.wait_ge(conv, i)
                    b = PA + (i - 1) * PA_ROWS + 4
                    nc.scalar.activation(k.xbc[:, i - 1, :], k.xbc[:, i - 1, :], ACT.Silu, bias=k.par[:, b:b + 1]).then_inc(silu, 1)

        @block.vector
        def _(dve):
            v = nc.vector
            link = chain(dve, link_s)
            link(v.memset(raw[:, :, 0:3], 0.0))
            link(v.memset(k.dt[:, :], 0.0))
            dve.wait_ge(prev_tr, 1)
            v.tensor_copy(prev[:, :, :, :].rearrange("p j s r -> p (j s r)"), k.ps[:, 7, 0:6 * 24]).then_inc(prev_cp, 1)
            dve.wait_ge(dt_done, 1)
            v.tensor_copy(k.dt[:, 0:NC * SH], k.ps[:, 6, 0:NC * SH]).then_inc(prev_cp, 1)
            dve.wait_ge(prev_cp, 2)
            v.tensor_copy(k.dt[0:NS, NC * SH:(NC + 1) * SH], k.ps[0:NS, 6, NC * SH:(NC + 1) * SH]).then_inc(prev_cp, 1)
            dve.wait_ge(prev_cp, 3)
            for j in range(NJ):
                dve.wait_ge(evac, (j + 1) * U)
                wc = [k.par[:, PA + j * PA_ROWS + q:PA + j * PA_ROWS + q + 1] for q in range(4)]
                r = raw[:, j % 2, :]
                o = k.xbc[:, j, 0:T]
                link(v.tensor_scalar(o, r[:, 3:3 + T], wc[3], None, ALU.mult))
                for q in range(3):
                    link(v.scalar_tensor_tensor(out=o, in0=r[:, q:q + T], scalar=wc[q], in1=o, op0=ALU.mult, op1=ALU.add))
                s = k.xbc[:, j, T:TT]
                link(v.tensor_scalar(s, r[:, 3 + T:3 + TT], wc[3], None, ALU.mult))
                for q in range(3):
                    ins = v.scalar_tensor_tensor(out=s, in0=prev[:, j, :, q], scalar=wc[q], in1=s, op0=ALU.mult, op1=ALU.add)
                    if q < 2:
                        link(ins)
                    else:
                        ins.then_inc(conv, 1)
                v.tensor_copy(k.tails_T[:, j, :], r[:, T:3 + TT]).then_inc(tail_cp, 1)
            dve.wait_ge(tail_tr, NJ)
            link(v.tensor_copy(tails[:, 0:512], k.ps[0:3 + NS, 0, :]))
            v.tensor_copy(tails[:, 512:CV], k.ps[0:3 + NS, 1, 0:256]).then_inc(tails_cp, 1)


def stage_ssd(nc, k, sem):
    NT = (NC + 1) * SH
    with ExitStack() as ctx:
        def sb(name, shape, dt=F32):
            return ctx.enter_context(nc.sbuf_tensor(name, shape, dt))
        bias_b, a_neg, d_col = sb("dt_bias_b", [P, SH]), sb("a_neg", [P, SH]), sb("ssd_d_col", [P, 2])
        e_abs, u1, um, zero_m, lnu, da = (sb(n, [P, NT]) for n in ("e_abs", "u1", "um", "zero_m", "lnu", "da"))
        da_exp = sb("da_exp", [NS, SH])
        aU = sb("aU", [P, SH, P])
        dec = sb("dec", [P, 2, SH, P])
        grow = sb("grow", [P, 2, SH, P])
        xdt, xde = sb("xdt", [P, SH, SP]), sb("xde", [P, SH, SP])
        b_tm = sb("b_tm", [P, 2, P])
        mix = sb("mix", [P, SH, P])
        cgrow = sb("cgrow", [P, SH, P])
        state = sb("ssd_state", [P, SH, SP])
        y_sum = sb("y_sum", [P, 2, P])
        st_out = sb("st_out", [P, 2, P])
        h0 = sb("h0", [P, NS, P])
        diag = sb("diag", [P, NS, P])
        hb = sb("hb", [P, NS, P])
        dtT = sb("dtT", [SH, 2, NS])
        dtb = sb("dtb", [P, 2, 2, NS])
        y_s = sb("y_s", [P, NS])
        coef = sb("coef_s", [P, NS])
        small_in, h0_in, dt_a, dt_v, link_s, tr, bt, xd, au, logs, scr, expd, expg, mixd, cg, yd, stn, std, y_fin, fin_tr, fin_cp, stored = (
            sem("s_" + n) for n in ("small_in", "h0_in", "dt_a", "dt_v", "link", "tr", "bt", "xd", "au", "logs", "scr", "expd",
                                    "expg", "mixd", "cg", "yd", "stn", "std", "y_fin", "fin_tr", "fin_cp", "stored"))
        d_pe, d_v, d_alink, h_new = sem("s_d_pe"), sem("s_d_v"), sem("s_alink"), sem("s_h_new")
        h_used = sem("s_h_used")
        btp = k.ps[:, 6, :]
        block = ctx.enter_context(nc.Block())
        tp, sc_ps, log_ps, grow_ps, y_ps, new_ps = (k.ps[:, b, :] for b in range(6))

        @block.sync
        def _(sp):
            sp.dma_start(bias_b[:, :], k.io["ssd_dt_bias"].broadcast_to([P, SH])).then_inc(small_in, 16)
            sp.dma_start(a_neg[:, :], k.io["ssd_A_log"].broadcast_to([P, SH])).then_inc(small_in, 16)
            for h in range(SH):
                sp.dma_start(d_col[(h % 2) * SP:(h % 2 + 1) * SP, h // 2:h // 2 + 1],
                             k.io["ssd_D"][0:1, h:h + 1].broadcast_to([SP, 1])).then_inc(small_in, 16)
            for j in range(2):
                if j:
                    sp.wait_ge(stored, 16)
                    sp.wait_ge(h_used, 1)
                sp.dma_start(h0[:, :, :], k.io["state_ssm"][0].rearrange("n (j h) p s -> j (h p) n s", j=2)[j]).then_inc(h0_in, 16)
                sp.wait_ge(h_new, j + 1)
                sp.dma_start(k.io["ssm_s"][0].rearrange("n (j h) p s -> j (h p) n s", j=2)[j], h0[:, :, :]).then_inc(stored, 16)
            sp.wait_ge(fin_cp, 1)
            sp.dma_start(k.io["ssm_p"][0, 0].rearrange("(j h) p s -> (h p) j s", j=2), st_out[:, :, :]).then_inc(stored, 16)
            sp.wait_ge(stored, 48)

        @block.scalar
        def _(act):
            link = chain(act, d_alink)
            act.wait_ge(dt_v, 1)
            link(nc.scalar.activation(e_abs[:, :], k.dt[:, :], ACT.Abs))
            link(nc.scalar.activation(e_abs[:, :], e_abs[:, :], ACT.Exp, scale=-1.0))
            nc.scalar.activation(a_neg[:, :], a_neg[:, :], ACT.Exp).then_inc(dt_a, 1)
            act.wait_ge(dt_v, 2)
            nc.scalar.activation(lnu[:, :], u1[:, :], ACT.Ln).then_inc(dt_a, 1)
            act.wait_ge(dt_v, 3)
            nc.scalar.activation(da_exp[:, :], da[0:NS, NC * SH:NT], ACT.Exp).then_inc(dt_a, 1)
            for c in range(NC):
                act.wait_ge(tr, c + 1)
                if c:
                    act.wait_ge(stn, c)
                nc.scalar.copy(b_tm[:, :, :].rearrange("p g s -> p (g s)"), btp[:, 0:2 * P]).then_inc(bt, 1)
                act.wait_ge(logs, c + 1)
                if c >= 2:
                    act.wait_ge(std, c - 1)
                nc.scalar.activation(dec[:, c % 2].rearrange("p h l -> p (h l)"), log_ps, ACT.Exp).then_inc(expd, 1)
                nc.scalar.activation(grow[:, c % 2].rearrange("p h l -> p (h l)"), grow_ps, ACT.Exp).then_inc(expg, 1)

        @block.tensor
        def _(pe):
            m = nc.tensor
            for c in range(NC):
                t0 = c * P
                if c:
                    pe.wait_ge(bt, c)
                    pe.wait_ge(xd, c)
                for j in range(4):
                    last = m.transpose((tp if j < 2 else btp)[:, (j % 2) * P:(j % 2 + 1) * P], k.xbc[:, j, t0:t0 + P], k.ident[:, :])
                last.then_inc(tr, 1)
                pe.wait_ge(au, c + 1)
                if c:
                    pe.wait_ge(expg, c)
                m.matmul(log_ps, k.below[:, :], aU[:, :, :].rearrange("p h l -> p (h l)"), start=True, stop=False)
                m.matmul(log_ps, k.ident[:, :], k.neg_upper[:, :], start=False, stop=True)
                m.matmul(grow_ps, k.ones[:, :], aU[:, :, :].rearrange("p h l -> p (h l)"), start=True, stop=True).then_inc(logs, 1)
                if c:
                    pe.wait_ge(mixd, c)
                for g in range(2):
                    last = m.matmul(sc_ps[:, g * P:(g + 1) * P], k.xbc[:, 2 + g, t0:t0 + P], k.xbc[:, 4 + g, t0:t0 + P],
                                    start=True, stop=True)
                last.then_inc(scr, 1)
                pe.wait_ge(mixd, c + 1)
                pe.wait_ge(cg, c + 1)
                if c:
                    pe.wait_ge(yd, c)
                for h in range(SH):
                    o = y_ps[(h % 2) * SP:(h % 2 + 1) * SP, (h // 2) * P:(h // 2 + 1) * P]
                    m.matmul(o, xdt[:, h, :], mix[:, h, :], start=True, stop=(c == 0))
                    if c:
                        m.matmul(o, state[:, h, :], cgrow[:, h, :], start=False, stop=True)
                m.matmul(new_ps[:, 0:P], b_tm[:, 0, :], xde[:, 0:2, :].rearrange("p h s -> p (h s)"), start=True, stop=True)
                m.matmul(new_ps[:, P:2 * P], b_tm[:, 1, :], xde[:, 2:4, :].rearrange("p h s -> p (h s)"),
                         start=True, stop=True).then_inc(stn, 1)
            pe.wait_ge(std, NC)
            for j in range(2):
                last = m.transpose(new_ps[:, j * P:(j + 1) * P], state[:, 2 * j:2 * j + 2, :].rearrange("p h s -> p (h s)"), k.ident[:, :])
            last.then_inc(fin_tr, 1)
            m.transpose(sc_ps[0:SH, 0:NS], k.dt[0:NS, NC * SH:NT], k.ident[0:NS, 0:NS])
            pe.wait_ge(dt_a, 3)
            m.transpose(sc_ps[0:SH, NS:2 * NS], da_exp[:, :], k.ident[0:NS, 0:NS]).then_inc(d_pe, 1)
            pe.wait_ge(d_v, 1)
            for j in range(2):
                last = m.matmul(tp[:, j * 2 * NS:(j + 1) * 2 * NS], k.head_pick[0:SH, j, :], dtT[:, :, :].rearrange("h a n -> h (a n)"),
                                start=True, stop=True)
            last.then_inc(d_pe, 1)
            for n in range(4):
                pe.wait_ge(d_v, 3 + n)
                for half in range(2):
                    last = m.matmul(k.ps[:, 1 + half + 2 * (n % 2), :], k.ones[:, :],
                                    diag[:, 4 * half:4 * half + 4, :].rearrange("p n s -> p (n s)"), start=True, stop=True)
                last.then_inc(d_pe, 1)

        @block.vector
        def _(dve):
            v = nc.vector
            link = chain(dve, link_s)
            dve.wait_ge(small_in, 96)
            dt3 = k.dt[:, :].rearrange("p (t h) -> p t h", h=SH)
            v.tensor_tensor(dt3, dt3, bias_b[:, :].rearrange("p (o h) -> p o h", o=1).broadcast_to([P, NC + 1, SH]), ALU.add).then_inc(dt_v, 1)
            dve.wait_ge(dt_a, 1)
            v.tensor_scalar(u1[:, :], e_abs[:, :], 1.0, None, ALU.add).then_inc(dt_v, 1)
            dve.wait_ge(dt_v, 2)
            link(v.tensor_scalar(um[:, :], u1[:, :], -1.0, None, ALU.add))
            link(v.tensor_scalar(zero_m[:, :], um[:, :], 0.0, None, ALU.is_equal))
            link(v.tensor_tensor(um[:, :], um[:, :], zero_m[:, :], ALU.add))
            link(v.reciprocal(um[:, :], um[:, :]))
            dve.wait_ge(dt_a, 2)
            link(v.tensor_tensor(lnu[:, :], lnu[:, :], zero_m[:, :], ALU.add))
            link(v.tensor_tensor(lnu[:, :], lnu[:, :], um[:, :], ALU.mult))
            link(v.tensor_tensor(lnu[:, :], lnu[:, :], e_abs[:, :], ALU.mult))
            link(v.tensor_scalar(k.dt[:, :], k.dt[:, :], 0.0, None, ALU.max))
            link(v.tensor_tensor(k.dt[:, :], k.dt[:, :], lnu[:, :], ALU.add))
            link(v.tensor_scalar(a_neg[:, :], a_neg[:, :], -1.0, None, ALU.mult))
            da3 = da[:, :].rearrange("p (t h) -> p t h", h=SH)
            v.tensor_tensor(da3, dt3, a_neg[:, :].rearrange("p (o h) -> p o h", o=1).broadcast_to([P, NC + 1, SH]), ALU.mult).then_inc(dt_v, 1)
            dve.wait_ge(dt_v, 3)
            for c in range(NC):
                dtc = k.dt[:, c * SH:(c + 1) * SH].rearrange("p (h o) -> p h o", o=1)
                dac = da3[:, c, :].rearrange("p (h o) -> p h o", o=1)
                if c:
                    dve.wait_ge(logs, c)
                v.tensor_tensor(aU[:, :, :], k.upper[:, :].rearrange("p (o l) -> p o l", o=1).broadcast_to([P, SH, P]),
                                dac.broadcast_to([P, SH, P]), ALU.mult).then_inc(au, 1)
                dve.wait_ge(tr, c + 1)
                if c:
                    dve.wait_ge(stn, c)
                v.tensor_tensor(xdt[:, :, :], tp[:, 0:2 * P].rearrange("p (h s) -> p h s", h=SH),
                                dtc.broadcast_to([P, SH, SP]), ALU.mult).then_inc(xd, 1)
                dve.wait_ge(expd, c + 1)
                dve.wait_ge(scr, c + 1)
                dc, gc = dec[:, c % 2], grow[:, c % 2]
                for g in range(2):
                    last = v.tensor_tensor(mix[:, 2 * g:2 * g + 2, :], sc_ps[:, g * P:(g + 1) * P].rearrange("p (o l) -> p o l", o=1).broadcast_to([P, 2, P]),
                                           dc[:, 2 * g:2 * g + 2, :], ALU.mult)
                last.then_inc(mixd, 1)
                dve.wait_ge(xd, c + 1)
                v.tensor_tensor(xde[:, :, :], xdt[:, :, :], dc[:, :, P - 1:P].broadcast_to([P, SH, SP]), ALU.mult)
                dve.wait_ge(expg, c + 1)
                for g in range(2):
                    last = v.tensor_tensor(cgrow[:, 2 * g:2 * g + 2, :],
                                           k.xbc[:, 4 + g, c * P:(c + 1) * P].rearrange("p (o l) -> p o l", o=1).broadcast_to([P, 2, P]),
                                           gc[:, 2 * g:2 * g + 2, :], ALU.mult)
                last.then_inc(cg, 1)
                dve.wait_ge(stn, c + 1)
                for j in range(2):
                    last = v.scalar_tensor_tensor(out=y_sum[:, j, :], in0=k.xbc[:, j, c * P:(c + 1) * P], scalar=d_col[:, j:j + 1],
                                                  in1=y_ps[:, j * P:(j + 1) * P], op0=ALU.mult, op1=ALU.add)
                last.then_inc(yd, 1)
                if c:
                    link(v.tensor_tensor(state[:, :, :], state[:, :, :], gc[:, :, P - 1:P].broadcast_to([P, SH, SP]), ALU.mult))
                    v.tensor_tensor(state[:, :, :], state[:, :, :], new_ps[:, 0:2 * P].rearrange("p (h s) -> p h s", h=SH), ALU.add).then_inc(std, 1)
                else:
                    v.tensor_copy(state[:, :, :], new_ps[:, 0:2 * P].rearrange("p (h s) -> p h s", h=SH)).then_inc(std, 1)
                dve.wait_ge(yd, c + 1)
                for j in range(2):
                    y = k.yT[j][:, c * P:(c + 1) * P]
                    last = v.tensor_tensor(y, y_sum[:, j, :], y, ALU.mult)
                link(last)
                dve.wait_ge(std, c + 1)
            dve.wait_ge(fin_tr, 1)
            v.tensor_copy(st_out[:, :, :].rearrange("p j s -> p (j s)"), new_ps[:, 0:2 * P]).then_inc(fin_cp, 1)
            dve.wait_ge(d_pe, 1)
            v.tensor_copy(dtT[:, :, :].rearrange("h a n -> h (a n)"), sc_ps[0:SH, 0:2 * NS]).then_inc(d_v, 1)
            dve.wait_ge(d_pe, 2)
            v.tensor_copy(dtb[:, :, :, :].rearrange("p j a n -> p (j a n)"), tp[:, 0:4 * NS]).then_inc(d_v, 1)
            dve.wait_ge(d_v, 2)
            idb = k.ident[:, :].rearrange("p (o s) -> p o s", o=1).broadcast_to([P, NS, P])

            def spread(tile, n):
                if n:
                    dve.wait_ge(d_pe, 2 + n)
                v.tensor_tensor(diag[:, :, :], idb, k.xbc[:, tile, T:TT].rearrange("p (n o) -> p n o", o=1).broadcast_to([P, NS, P]),
                                ALU.mult).then_inc(d_v, 1)

            spread(2, 0)
            for j in range(2):
                xs = k.xbc[:, j, T:TT]
                spread(4 + j, 2 * j + 1)
                dve.wait_ge(h0_in, 16 * (j + 1))
                link(v.tensor_tensor(h0[:, :, :], h0[:, :, :], dtb[:, j, 1, :].rearrange("p (n o) -> p n o", o=1).broadcast_to([P, NS, P]), ALU.mult))
                link(v.tensor_tensor(coef[:, :], xs, dtb[:, j, 0, :], ALU.mult))
                cf = coef[:, :].rearrange("p (n o) -> p n o", o=1)
                for half in range(2):
                    ns = slice(4 * half, 4 * half + 4)
                    last = v.tensor_tensor(hb[:, ns, :], k.ps[:, 1 + half, :].rearrange("p (n s) -> p n s", s=P),
                                           cf[:, ns, :].broadcast_to([P, 4, P]), ALU.mult)
                link(last)
                v.tensor_tensor(h0[:, :, :], h0[:, :, :], hb[:, :, :], ALU.add).then_inc(h_new, 1)
                dve.wait_ge(h_new, j + 1)
                dve.wait_ge(d_pe, 4 + 2 * j)
                if j == 0:
                    spread(3, 2)
                for half in range(2):
                    ns = slice(4 * half, 4 * half + 4)
                    last = v.tensor_tensor(hb[:, ns, :], h0[:, ns, :], k.ps[:, 3 + half, :].rearrange("p (n s) -> p n s", s=P), ALU.mult)
                last.then_inc(h_used, 1)
                dve.wait_ge(h_used, j + 1)
                link(v.tensor_reduce(y_s[:, :], hb[:, :, :], AX.X, ALU.add))
                link(v.scalar_tensor_tensor(out=y_s[:, :], in0=xs, scalar=d_col[:, j:j + 1], in1=y_s[:, :], op0=ALU.mult, op1=ALU.add))
                y = k.yT[j][:, T:TT]
                link(v.tensor_tensor(y, y_s[:, :], y, ALU.mult))


def column_sums(k, pe, m, src, out, n):
    for j in range(2):
        last = m.matmul(out, k.ones[:, :], src[j], start=(j == 0), stop=(j == 1))
    return last


def stage_ssd_norm(nc, k, sem):
    with ExitStack() as ctx:
        sq = ctx.enter_context(nc.sbuf_tensor("rms_sq", [P, 2, 2, GT], F32))
        inv = ctx.enter_context(nc.sbuf_tensor("rms_inv", [P, 2, GT], F32))
        sqd, summed, var, root, link_s = (sem("r_" + n) for n in ("sqd", "summed", "var", "root", "link"))
        block = ctx.enter_context(nc.Block())
        groups = [(g * GT, GT) for g in range(NG)] + [(T, NS)]

        @block.scalar
        def _(act):
            def square(g):
                t0, n = groups[g]
                if g >= 2:
                    act.wait_ge(summed, g - 1)
                for j in range(2):
                    last = nc.scalar.activation(sq[:, g % 2, j, 0:n], k.yT[j][:, t0:t0 + n], ACT.Square)
                last.then_inc(sqd, 1)
            square(0)
            for g, (t0, n) in enumerate(groups):
                if g + 1 < len(groups):
                    square(g + 1)
                act.wait_ge(var, g + 1)
                nc.scalar.activation(inv[:, g % 2, 0:n], inv[:, g % 2, 0:n], ACT.Sqrt).then_inc(root, 1)

        @block.tensor
        def _(pe):
            for g, (t0, n) in enumerate(groups):
                pe.wait_ge(sqd, g + 1)
                if g >= 2:
                    pe.wait_ge(var, g - 1)
                column_sums(k, pe, nc.tensor, [sq[:, g % 2, j, 0:n] for j in range(2)], k.ps[:, g % 2, 0:n], n).then_inc(summed, 1)

        @block.vector
        def _(dve):
            v = nc.vector
            link = chain(dve, link_s)
            for g, (t0, n) in enumerate(groups):
                dve.wait_ge(summed, g + 1)
                link(v.tensor_scalar(inv[:, g % 2, 0:n], k.ps[:, g % 2, 0:n], 1.0 / W, EPS, ALU.mult, ALU.add))
                v.reciprocal(inv[:, g % 2, 0:n], inv[:, g % 2, 0:n]).then_inc(var, 1)
                dve.wait_ge(root, g + 1)
                for j in range(2):
                    y = k.yT[j][:, t0:t0 + n]
                    b = PB + j * PB_ROWS + B_SSDG
                    last = v.scalar_tensor_tensor(out=y, in0=y, scalar=k.par[:, b:b + 1], in1=inv[:, g % 2, 0:n],
                                                  op0=ALU.mult, op1=ALU.mult)
                link(last)


def stage_convs(nc, k, sem):
    cols, kinds = [], []
    for j in range(2):
        cols += [COL_GLU + j * P, COL_GLU + W + j * P, COL_CG + j * P]
        kinds += [("u", j, 0), ("sig", j, 0), ("gate", j, 4)]
    for j in range(2):
        cols += [COL_A + j * P, COL_A + 2 * W + j * P, COL_A + W + j * P, COL_A + 3 * W + j * P]
        kinds += [("u", j, 2), ("v", j, 2), ("b", j, 2), ("gate", j, 2)]
    cols += [COL_DG, COL_DG + P]
    kinds += [("gate", 0, 6), ("gate", 1, 6)]
    U = NG + 1
    PADC = KCF - 1
    with ExitStack() as ctx:
        def sb(name, shape, dt=F32):
            return ctx.enter_context(nc.sbuf_tensor(name, shape, dt))
        w_buf = sb("w_buf2", [P, 2, KT, P])
        first = sb("first", [P, TT])
        second = sb("second", [P, TT])
        padded = sb("padded", [P, PADC + TT])
        acc = k.conf
        prev_rows = sb("prev_rows2", [120, 2, W])
        prev_a_rows = sb("prev_a_rows", [2 * NS, W])
        prev_c = sb("prev_c", [P, 2, NS * PADC])
        prev_a = sb("prev_a", [P, 2, NS, 2])
        prod = sb("prod_c", [P, NS, PADC])
        tailc = sb("tailc", [P, 2, PADC + NS])
        taila = sb("taila", [P, 2, 2 + NS])
        outc = sb("outc", [PADC + NS, W])
        outa = sb("outa", [2 + NS, W])
        w_ready = [sem("wc_ready0"), sem("wc_ready1")]
        prev_in, prev_tr, prev_cp, unit_done, evac, link_s, u_done, convd, tail_cp, tail_tr, tails_cp, stored, pad_free, gated = (
            sem("c_" + n) for n in ("prev_in", "prev_tr", "prev_cp", "unit", "evac", "link", "u_done", "convd", "tail_cp",
                                    "tail_tr", "tails_cp", "stored", "pad_free", "gated"))
        block = ctx.enter_context(nc.Block())

        @block.sync
        def _(sp):
            st = k.io["state_cconv"][0].rearrange("(a s) r c -> (s r) a c", a=2)
            sp.dma_start(prev_rows[:, :, :], st).then_inc(prev_in, 16)
            sp.dma_start(prev_a_rows[:, :], k.io["state_sconv"][0].rearrange("s r c -> (s r) c")).then_inc(prev_in, 16)
            load_tiles(k, sp, cols, w_buf, w_ready, unit_done)
            sp.dma_start(k.io["cconv_s"][0, :, 0:PADC - 1, :], k.io["state_cconv"][0, :, 1:PADC, :]).then_inc(stored, 16)
            sp.dma_start(k.io["sconv_s"][0, :, 0:1, :], k.io["state_sconv"][0, :, 1:2, :]).then_inc(stored, 16)
            sp.wait_ge(tails_cp, 1)
            sp.dma_start(k.io["cconv_p"][0, 0], outc[0:PADC, :]).then_inc(stored, 16)
            sp.dma_start(k.io["cconv_s"][0, :, PADC - 1, :], outc[PADC:PADC + NS, :]).then_inc(stored, 16)
            sp.dma_start(k.io["sconv_p"][0, 0], outa[0:2, :]).then_inc(stored, 16)
            sp.dma_start(k.io["sconv_s"][0, :, 1, :], outa[2:2 + NS, :]).then_inc(stored, 16)
            sp.wait_ge(stored, 96)

        @block.tensor
        def _(pe):
            m = nc.tensor
            pe.wait_ge(prev_in, 32)
            for j in range(2):
                for a in range(2):
                    m.transpose(k.ps[:, 7, (2 * j + a) * 120:(2 * j + a + 1) * 120], prev_rows[:, a, j * P:(j + 1) * P], k.ident[0:120, 0:120])
                last = m.transpose(k.ps[:, 6, j * 16:(j + 1) * 16], prev_a_rows[:, j * P:(j + 1) * P], k.ident[0:16, 0:16])
            last.then_inc(prev_tr, 1)
            pe.wait_ge(prev_cp, 2)

            def free(eng, u):
                eng.wait_ge(evac, u + 1)
            channel_projection(nc, k, pe, cols, w_buf, w_ready, None, unit_done, free)
            pe.wait_ge(evac, len(cols) * U)
            pe.wait_ge(tail_cp, 4)
            for j in range(2):
                m.transpose(k.ps[0:PADC + NS, 0, j * P:(j + 1) * P], tailc[:, j, :], k.ident[:, :])
                last = m.transpose(k.ps[0:2 + NS, 1, j * P:(j + 1) * P], taila[:, j, :], k.ident[:, :])
            last.then_inc(tail_tr, 1)

        @block.scalar
        def _(act):
            nu = 0
            nb = 0
            for i, (kind, j, y0) in enumerate(kinds):
                if kind == "u" and nu:
                    act.wait_ge(u_done, nu)
                if kind == "u" and y0 == 2 and j == 1:
                    act.wait_ge(convd, 3)
                for g in range(U):
                    n, t0 = (GT, g * GT) if g < NG else (NS, T)
                    u = i * U + g
                    act.wait_ge(unit_done, u + 1)
                    src = k.ps[:, u % 8, 0:n]
                    if kind == "u":
                        ins = nc.scalar.copy(first[:, t0:t0 + n], src)
                    elif kind == "v":
                        if g == 0 and j:
                            act.wait_ge(gated, j)
                        ins = nc.scalar.copy(second[:, t0:t0 + n], src)
                    elif kind == "sig":
                        ins = nc.scalar.activation(second[:, t0:t0 + n], src, ACT.Sigmoid)
                    elif kind == "b":
                        if g == 0:
                            act.wait_ge(u_done, nu)
                        ins = nc.scalar.copy(first[:, t0:t0 + n], src)
                    else:
                        ins = nc.scalar.activation(k.yT[y0 + j][:, t0:t0 + n], src, ACT.Silu)
                    ins.then_inc(evac, 1)
                if kind == "u":
                    nu += 1

        @block.vector
        def _(dve):
            v = nc.vector
            link = chain(dve, link_s)
            dve.wait_ge(prev_tr, 1)
            v.tensor_copy(prev_c[:, :, :].rearrange("p j n -> p (j n)"), k.ps[:, 7, 0:480]).then_inc(prev_cp, 1)
            v.tensor_copy(prev_a[:, :, :, :].rearrange("p j s r -> p (j s r)"), k.ps[:, 6, 0:32]).then_inc(prev_cp, 1)
            dve.wait_ge(prev_cp, 2)
            link(v.memset(padded[:, 0:PADC], 0.0))
            for j in range(2):
                cw = [k.par[:, PB + j * PB_ROWS + B_CF + q:PB + j * PB_ROWS + B_CF + q + 1] for q in range(KCF)]
                cb = PB + j * PB_ROWS + B_CFB
                dve.wait_ge(evac, (3 * j + 2) * U)
                v.tensor_tensor(padded[:, PADC:PADC + TT], first[:, :], second[:, :], ALU.mult).then_inc(u_done, 1)
                dve.wait_ge(u_done, j + 1)
                v.tensor_copy(tailc[:, j, :], padded[:, T:T + PADC + NS]).then_inc(tail_cp, 1)
                o, s = acc[:, j, 0:T], acc[:, j, T:TT]
                link(v.tensor_scalar(o, padded[:, PADC:PADC + T], cw[KCF - 1], k.par[:, cb:cb + 1], ALU.mult, ALU.add))
                for q in range(KCF - 1):
                    link(v.scalar_tensor_tensor(out=o, in0=padded[:, q:q + T], scalar=cw[q], in1=o, op0=ALU.mult, op1=ALU.add))
                b = PB + j * PB_ROWS + B_CF
                link(v.tensor_tensor(prod[:, :, :], prev_c[:, j, :].rearrange("p (s r) -> p s r", r=PADC),
                                     k.par[:, b:b + PADC].rearrange("p (o r) -> p o r", o=1).broadcast_to([P, NS, PADC]), ALU.mult))
                link(v.tensor_reduce(s, prod[:, :, :], AX.X, ALU.add))
                link(v.tensor_scalar(s, s, k.par[:, cb:cb + 1], None, ALU.add))
                v.scalar_tensor_tensor(out=s, in0=padded[:, PADC + T:PADC + TT], scalar=cw[KCF - 1], in1=s,
                                       op0=ALU.mult, op1=ALU.add).then_inc(convd, 1)
                dve.wait_ge(convd, j + 1)
            for j in range(2):
                i0 = 6 + 4 * j
                aw = [k.par[:, PB + j * PB_ROWS + B_SC + q:PB + j * PB_ROWS + B_SC + q + 1] for q in range(3)]
                dve.wait_ge(evac, (i0 + 2) * U)
                v.tensor_tensor(padded[:, PADC:PADC + TT], first[:, :], second[:, :], ALU.mult).then_inc(u_done, 1)
                dve.wait_ge(u_done, 3 + j)
                v.tensor_copy(taila[:, j, :], padded[:, T + PADC - 2:T + PADC + NS]).then_inc(tail_cp, 1)
                o, s = second[:, 0:T], second[:, T:TT]
                link(v.tensor_scalar(o, padded[:, PADC:PADC + T], aw[2], None, ALU.mult))
                for q in range(2):
                    link(v.scalar_tensor_tensor(out=o, in0=padded[:, PADC - 2 + q:PADC - 2 + q + T], scalar=aw[q], in1=o,
                                                op0=ALU.mult, op1=ALU.add))
                link(v.tensor_scalar(s, padded[:, PADC + T:PADC + TT], aw[2], None, ALU.mult))
                for q in range(2):
                    link(v.scalar_tensor_tensor(out=s, in0=prev_a[:, j, :, q], scalar=aw[q], in1=s, op0=ALU.mult, op1=ALU.add))
                dve.wait_ge(evac, (i0 + 4) * U)
                y = k.yT[2 + j]
                v.tensor_tensor(second[:, :], second[:, :], first[:, :], ALU.mult).then_inc(convd, 1)
                dve.wait_ge(convd, 3 + j)
                v.tensor_tensor(y[:, :], y[:, :], second[:, :], ALU.mult).then_inc(gated, 1)
            dve.wait_ge(tail_tr, 1)
            v.tensor_copy(outc[:, :], k.ps[0:PADC + NS, 0, 0:W])
            v.tensor_copy(outa[:, :], k.ps[0:2 + NS, 1, 0:W]).then_inc(tails_cp, 1)


def stage_conformer_norm(nc, k, sem):
    with ExitStack() as ctx:
        sq = ctx.enter_context(nc.sbuf_tensor("ln_sq", [P, 2, GT], F32))
        inv = ctx.enter_context(nc.sbuf_tensor("ln_inv", [P, GT], F32))
        mean = ctx.enter_context(nc.sbuf_tensor("ln_mean", [P, GT], F32))
        summed, cen, sqd, sq_sum, var, root, scaled, swished, link_s = (
            sem("ln_" + n) for n in ("summed", "cen", "sqd", "sq_sum", "var", "root", "scaled", "swished", "link"))
        block = ctx.enter_context(nc.Block())
        groups = [(g * GT, GT) for g in range(NG)] + [(T, NS)]
        acc = k.conf

        @block.tensor
        def _(pe):
            for g, (t0, n) in enumerate(groups):
                if g:
                    pe.wait_ge(cen, g)
                column_sums(k, pe, nc.tensor, [acc[:, j, t0:t0 + n] for j in range(2)], k.ps[:, 0, 0:n], n).then_inc(summed, 1)
                pe.wait_ge(sqd, g + 1)
                if g:
                    pe.wait_ge(var, g)
                column_sums(k, pe, nc.tensor, [sq[:, j, 0:n] for j in range(2)], k.ps[:, 1, 0:n], n).then_inc(sq_sum, 1)

        @block.scalar
        def _(act):
            for g, (t0, n) in enumerate(groups):
                act.wait_ge(cen, g + 1)
                if g:
                    act.wait_ge(sq_sum, g)
                for j in range(2):
                    last = nc.scalar.activation(sq[:, j, 0:n], acc[:, j, t0:t0 + n], ACT.Square)
                last.then_inc(sqd, 1)
                act.wait_ge(var, g + 1)
                nc.scalar.activation(inv[:, 0:n], inv[:, 0:n], ACT.Sqrt).then_inc(root, 1)
            act.wait_ge(scaled, len(groups))
            for j in range(2):
                b = PB + j * PB_ROWS
                nc.scalar.activation(acc[:, j, :], acc[:, j, :], ACT.Silu, bias=k.par[:, b + B_LNB:b + B_LNB + 1],
                                     scale=k.par[:, b + B_LNG:b + B_LNG + 1]).then_inc(swished, 1)

        @block.vector
        def _(dve):
            v = nc.vector
            link = chain(dve, link_s)
            for g, (t0, n) in enumerate(groups):
                dve.wait_ge(summed, g + 1)
                link(v.tensor_scalar(mean[:, 0:n], k.ps[:, 0, 0:n], 1.0 / W, None, ALU.mult))
                for j in range(2):
                    last = v.tensor_tensor(acc[:, j, t0:t0 + n], acc[:, j, t0:t0 + n], mean[:, 0:n], ALU.subtract)
                last.then_inc(cen, 1)
                dve.wait_ge(sq_sum, g + 1)
                link(v.tensor_scalar(inv[:, 0:n], k.ps[:, 1, 0:n], 1.0 / W, EPS, ALU.mult, ALU.add))
                v.reciprocal(inv[:, 0:n], inv[:, 0:n]).then_inc(var, 1)
                dve.wait_ge(root, g + 1)
                dve.wait_ge(cen, g + 1)
                for j in range(2):
                    last = v.tensor_tensor(acc[:, j, t0:t0 + n], acc[:, j, t0:t0 + n], inv[:, 0:n], ALU.mult)
                last.then_inc(scaled, 1)
                dve.wait_ge(scaled, g + 1)
            for j in range(2):
                dve.wait_ge(swished, j + 1)
                y = k.yT[4 + j]
                v.tensor_tensor(y[:, :], y[:, :], acc[:, j, :], ALU.mult)


def stage_token_major(nc, k, sem):
    parts = [(0, 384), (384, TM)]
    with ExitStack() as ctx:
        def sb(name, shape, dt=F32):
            return ctx.enter_context(nc.sbuf_tensor(name, shape, dt))
        w_tm = sb("w_tm", [P, KT, 384])
        gains = sb("qk_gains", [P, 6, HD])
        sq = sb("qk_sq", [P, 6, HD])
        ss = sb("qk_ss", [P, (NC + 1) * 6])
        w_in_s, g_in, proj, evac, link_s, ss_done, root, rows_done, stored, mem = (
            sem("t_" + n) for n in ("w_in", "g_in", "proj", "evac", "link", "ss_done", "root", "rows_done", "stored", "mem"))
        block = ctx.enter_context(nc.Block())
        N1 = NC + 1

        @block.sync
        def _(sp):
            for h in range(H):
                sp.dma_start(gains[:, h, :], k.io["q_g"].broadcast_to([P, HD])).then_inc(g_in, 16)
            for i in range(2):
                sp.dma_start(gains[:, H + i, :], k.io["k_g"][0, 1 + i:2 + i, :].broadcast_to([P, HD])).then_inc(g_in, 16)
            wv = k.io["w_in"][0].rearrange("(k p) n -> p k n", p=P)
            sp.dma_start(w_tm[:, :, 0:384], wv[:, :, COL_Q:COL_Q + 384]).then_inc(w_in_s, 16)
            sp.wait_ge(proj, N1)
            sp.dma_start(w_tm[:, :, 0:256], wv[:, :, COL_Q + 384:COL_Q + 640]).then_inc(w_in_s, 16)
            sp.dma_start(w_tm[:, :, 256:268], wv[:, :, COL_BG:COL_BG + 12]).then_inc(w_in_s, 16)
            sp.dma_start(k.io["win_s"][0, :, 0:511], k.io["cache_win"][0, :, 1:512]).then_inc(stored, 16)
            sp.wait_ge(rows_done, 1)
            rows = k.io["kv_p"][0].rearrange("t p s d -> p t (s d)")
            sp.dma_start(rows, k.tm[:, 0:NC, W:W + 256]).then_inc(stored, 16)
            sp.dma_start(k.io["win_p"][0, 0].rearrange("(t p) s d -> p t (s d)", p=P), k.tm[:, NC - 4:NC, 512:640]).then_inc(stored, 16)
            sp.dma_start(k.io["kv_s"][0, :, 0].rearrange("n s d -> n (s d)"), k.tm[0:NS, NC, W:W + 256]).then_inc(stored, 16)
            sp.dma_start(k.io["win_s"][0, :, 511].rearrange("n s d -> n (s d)"), k.tm[0:NS, NC, 512:640]).then_inc(stored, 16)
            sp.wait_ge(stored, 80)

        @block.tensor
        def _(pe):
            for i, (c0, c1) in enumerate(parts):
                pe.wait_ge(w_in_s, 16 if i == 0 else 48)
                for t in range(N1):
                    u = i * N1 + t
                    r = P if t < NC else NS
                    if u >= 4:
                        pe.wait_ge(evac, u - 3)
                    for kk in range(KT):
                        last = nc.tensor.matmul(k.ps[0:r, u % 4, 0:c1 - c0], k.hT[:, kk, t * P:t * P + r], w_tm[:, kk, 0:c1 - c0],
                                                start=(kk == 0), stop=(kk == KT - 1))
                    last.then_inc(proj, 1)

        @block.scalar
        def _(act):
            act.wait_ge(mem, 1)
            for i, (c0, c1) in enumerate(parts):
                for t in range(N1):
                    u = i * N1 + t
                    r = P if t < NC else NS
                    act.wait_ge(proj, u + 1)
                    nc.scalar.copy(k.tm[0:r, t, c0:c1], k.ps[0:r, u % 4, 0:c1 - c0]).then_inc(evac, 1)
            act.wait_ge(ss_done, 1)
            nc.scalar.activation(ss[:, :], ss[:, :], ACT.Sqrt).then_inc(root, 1)
            g = k.tm[:, :, 640:652]
            act.wait_ge(evac, 2 * N1)
            nc.scalar.activation(g, g, ACT.Sigmoid)

        @block.vector
        def _(dve):
            v = nc.vector
            link = chain(dve, link_s)
            v.memset(k.tm[:, NC, :], 0.0).then_inc(mem, 1)
            for t in range(N1):
                q = k.tm[:, t, 0:W]
                kk = k.tm[:, t, 384:640].rearrange("p (i d) -> p i d", d=2 * HD)[:, :, 0:HD]
                dve.wait_ge(evac, N1 + t + 1)
                v.tensor_tensor(sq[:, 0:H, :].rearrange("p h d -> p (h d)"), q, q, ALU.mult)
                link(v.tensor_tensor(sq[:, H:6, :], kk, kk, ALU.mult))
                link(v.tensor_reduce(ss[:, t * 6:(t + 1) * 6], sq[:, :, :], AX.X, ALU.add))
            link(v.tensor_scalar(ss[:, :], ss[:, :], 1.0 / HD, EPS, ALU.mult, ALU.add))
            v.reciprocal(ss[:, :], ss[:, :]).then_inc(ss_done, 1)
            dve.wait_ge(root, 1)
            dve.wait_ge(g_in, 96)
            for t in range(N1):
                q = k.tm[:, t, 0:W].rearrange("p (h d) -> p h d", d=HD)
                kk = k.tm[:, t, 384:640].rearrange("p (i d) -> p i d", d=2 * HD)[:, :, 0:HD]
                s3 = ss[:, t * 6:(t + 1) * 6].rearrange("p (h o) -> p h o", o=1)
                v.tensor_tensor(q, q, s3[:, 0:H, :].broadcast_to([P, H, HD]), ALU.mult)
                link(v.tensor_tensor(kk, kk, s3[:, H:6, :].broadcast_to([P, 2, HD]), ALU.mult))
                v.tensor_tensor(q, q, gains[:, 0:H, :], ALU.mult)
                link(v.tensor_tensor(kk, kk, gains[:, H:6, :], ALU.mult))
            v.memset(sq[:, 0, 0:1], 0.0).then_inc(rows_done, 1)


def stage_compress(nc, k, sem):
    NQ = 1 + NS
    with ExitStack() as ctx:
        def sb(name, shape, dt=F32):
            return ctx.enter_context(nc.sbuf_tensor(name, shape, dt))
        rawT = sb("rawT", [P, 2, T])
        w1 = sb("w1", [P, 32, P])
        page = sb("page", [P, 2, 4, P])
        table = sb("table", [1, NS * PAGES], I32)
        pe_rows = sb("pe_rows", [32, P])
        b1_rows = sb("b1_rows", [2, P])
        peT = sb("peT", [P, 32])
        bias1 = sb("bias1", [P, 2])
        b1T = sb("b1T", [P, 2])
        w2 = sb("w2", [P, 2, HD])
        b2 = sb("b2", [P, 2, HD])
        kg = sb("kg", [P, HD])
        hid = sb("hid", [P, 2, 2, P])
        kc = sb("kc", [P, 2, HD])
        sq = sb("kc_sq", [P, HD])
        st = sb("kc_st", [P, 2])
        table_in, par_in, blk_in, page_in0, page_in1, pt, pcp, bias_d, rcp, hidp, hidd, cmp_d, kcd, kct, kcc, link_s, root, root_in, loaded = (
            sem("k_" + n) for n in ("table_in", "par_in", "blk_in", "page_in0", "page_in1", "pt", "pcp", "bias_d", "rcp",
                                    "hidp", "hidd", "cmp_d", "kcd", "kct", "kcc", "link", "root", "root_in", "loaded"))
        ktr, kcp, kcp2 = sem("k_ktr"), sem("k_kcp"), sem("k_kcp2")
        block = ctx.enter_context(nc.Block())
        M = NCMP
        KB = 2 * NC // 4
        page_in = [[page_in0, sem("k_page_in0p")], [page_in1, sem("k_page_in1p")]]

        def fetch(eng, parity):
            eng.wait_ge(table_in, 16)
            for e in range(4 * NS):
                if e >= 2:
                    eng.wait_ge(ktr, KB + 4 + e - 1)
                for g in range(parity, 4, 2):
                    at = 4 * e + g
                    i = eng.value_load(table[0:1, at:at + 1], min_val=0, max_val=k.n_pool - 1)
                    eng.dma_start(page[:, e % 2, g, :], k.io["cache_kv"][0, bass.DynSlice(i, 1), :, 0:2, :].rearrange("o p s d -> (o p) (s d)")
                                  ).then_inc(page_in[e % 2][parity], 16)

        @block.sync
        def _(sp):
            sp.dma_start(table[:, :], k.io["page_table"].rearrange("n g -> (n g)").rearrange("(o m) -> o m", o=1)).then_inc(table_in, 16)
            sp.dma_start(w1[0:HD], k.io["cmp_w1"][0, 0].rearrange("j d f -> d j f")).then_inc(par_in, 16)
            sp.dma_start(w1[HD:P], k.io["cmp_w1"][0, 1].rearrange("j d f -> d j f")).then_inc(par_in, 16)
            for i in range(2):
                sp.dma_start(pe_rows[:, i * HD:(i + 1) * HD], k.io["cmp_pe"][0, i]).then_inc(par_in, 16)
            sp.dma_start(b1_rows[:, :], k.io["cmp_b1"][0]).then_inc(par_in, 16)
            sp.dma_start(w2[:, :, :], k.io["cmp_w2"][0].rearrange("i f d -> f i d")).then_inc(par_in, 16)
            for i in range(2):
                sp.dma_start(b2[:, i, :], k.io["cmp_b2"][0, i:i + 1, :].broadcast_to([P, HD])).then_inc(par_in, 16)
            sp.dma_start(kg[:, :], k.io["k_g"][0, 0:1, :].broadcast_to([P, HD])).then_inc(par_in, 16)
            for i in range(2):
                sp.dma_start(rawT[HD:HD + NBLK + 2, i, :], k.extra_dram[i]).then_inc(blk_in, 16)
            fetch(sp, 0)

        @block.gpsimd
        def _(pool):
            fetch(pool, 1)

        @block.tensor
        def _(pe):
            m = nc.tensor
            pe.wait_ge(par_in, 144)
            m.transpose(k.ps[:, 0, 0:32], pe_rows[:, :], k.ident[0:32, 0:32])
            m.transpose(k.ps[:, 0, 32:34], b1_rows[:, :], k.ident[0:2, 0:2]).then_inc(pt, 1)
            pe.wait_ge(pcp, 1)
            for i in range(2):
                for j in range(32):
                    r = slice(i * HD, (i + 1) * HD)
                    last = m.matmul(k.ps[:, 1 + i, 0:1], w1[r, j, :], peT[r, j:j + 1], start=(j == 0), stop=(j == 31))
            last.then_inc(pt, 1)
            pe.wait_ge(bias_d, 1)
            for e in range(KB):
                if e >= 2:
                    pe.wait_ge(kcp, e - 1)
                for n in range(4):
                    c = 384 + 128 * (e % 2)
                    last = m.transpose(k.ps[0:HD, 3 + e % 2, n * P:(n + 1) * P], k.tm[:, 4 * (e // 2) + n, c:c + HD], k.ident[:, :])
                last.then_inc(ktr, 1)
            pe.wait_ge(kcp, KB)

            def raw_transposes(q):
                for b4 in range(4):
                    e = q * 4 + b4
                    if q:
                        for landed in page_in[b4 % 2]:
                            pe.wait_ge(landed, 16 * 2 * (2 * (q - 1) + b4 // 2 + 1))
                    if e >= 2:
                        pe.wait_ge(rcp, e - 1)
                    for n in range(4):
                        t = 4 * b4 + n
                        src = k.tm[:, t, W:W + P] if q == 0 else page[:, b4 % 2, n, :]
                        last = m.transpose(k.ps[:, 3 + e % 2, n * P:(n + 1) * P], src, k.ident[:, :])
                    last.then_inc(ktr, 1)

            raw_transposes(0)
            for q in range(NQ):
                if q + 1 < NQ:
                    raw_transposes(q + 1)
                pe.wait_ge(rcp, 4 * (q + 1))
                if q:
                    pe.wait_ge(hidd, 2 * q)
                for i in range(2):
                    r = slice(i * HD, (i + 1) * HD)
                    for j in range(32):
                        last = m.matmul(k.ps[:, 1 + i, 0:M], w1[r, j, :], rawT[r, q % 2, j:j + 16 * (M - 1) + 1:16],
                                        start=(j == 0), stop=(j == 31))
                    last.then_inc(hidp, 1)
                if q:
                    pe.wait_ge(kcc, q)
                for i in range(2):
                    pe.wait_ge(hidd, 2 * q + i + 1)
                    last = m.matmul(k.ps[0:M, 5, i * HD:(i + 1) * HD], hid[:, q % 2, i, 0:M], w2[:, i, :], start=True, stop=True)
                last.then_inc(cmp_d, 1)
                pe.wait_ge(kcd, q + 1)
                m.transpose(k.ps[0:HD, 6, 0:M], kc[0:M, q % 2, :], k.ident[0:M, 0:M]).then_inc(kct, 1)

        @block.scalar
        def _(act):
            def hids(q):
                for i in range(2):
                    act.wait_ge(hidp, 2 * q + i + 1)
                    if q >= 2:
                        act.wait_ge(cmp_d, q - 1)
                    nc.scalar.activation(hid[:, q % 2, i, 0:M], k.ps[:, 1 + i, 0:M], ACT.Silu, bias=bias1[:, i:i + 1]).then_inc(hidd, 1)
                act.wait_ge(root_in, q + 1)
                nc.scalar.activation(st[0:M, 1:2], st[0:M, 0:1], ACT.Sqrt).then_inc(root, 1)

            act.wait_ge(bias_d, 1)
            for q in range(NQ):
                for b4 in range(1, 4, 2):
                    e = q * 4 + b4
                    act.wait_ge(ktr, KB + e + 1)
                    act.wait_ge(rcp, e)
                    if q >= 2:
                        act.wait_ge(hidp, 2 * (q - 1))
                    nc.scalar.copy(rawT[:, q % 2, b4 * 512:(b4 + 1) * 512], k.ps[:, 3 + e % 2, :]).then_inc(rcp, 1)
                if q:
                    hids(q - 1)
            hids(NQ - 1)

        @block.vector
        def _(dve):
            v = nc.vector
            link = chain(dve, link_s)
            dve.wait_ge(pt, 1)
            v.tensor_copy(peT[:, :], k.ps[:, 0, 0:32])
            v.tensor_copy(b1T[:, :], k.ps[:, 0, 32:34]).then_inc(pcp, 1)
            dve.wait_ge(pt, 2)
            dve.wait_ge(pcp, 1)
            v.tensor_tensor(bias1[:, 0:1], k.ps[:, 1, 0:1], b1T[:, 0:1], ALU.add)
            v.tensor_tensor(bias1[:, 1:2], k.ps[:, 2, 0:1], b1T[:, 1:2], ALU.add).then_inc(bias_d, 1)
            dve.wait_ge(blk_in, 32)
            for i, kk in enumerate(k.keys):
                for r in (slice(HD, HD + NBLK), slice(HD + NBLK, HD + NBLK + 2)):
                    v.tensor_copy(kk[0][r, :], rawT[r, i, :])
                    last = v.memset(kk[1][r, :].bitcast(F32), 0.0)
            link(last)
            for e in range(KB):
                dve.wait_ge(ktr, e + 1)
                b = k.ps[0:HD, 3 + e % 2, :]
                hi, lo = (kk[0:HD, (e // 2) * 512:(e // 2 + 1) * 512] for kk in k.keys[e % 2])
                link(v.tensor_copy(hi, b))
                v.tensor_tensor(lo, b, hi.bitcast(F32), ALU.subtract).then_inc(kcp, 1)

            def raw_copies(q):
                for b4 in range(0, 4, 2):
                    e = q * 4 + b4
                    dve.wait_ge(ktr, KB + e + 1)
                    if e:
                        dve.wait_ge(rcp, e)
                    if q >= 2:
                        dve.wait_ge(hidp, 2 * (q - 1))
                    v.tensor_copy(rawT[:, q % 2, b4 * 512:(b4 + 1) * 512], k.ps[:, 3 + e % 2, :]).then_inc(rcp, 1)

            raw_copies(0)
            for q in range(NQ):
                if q + 1 < NQ:
                    raw_copies(q + 1)
                dve.wait_ge(cmp_d, q + 1)
                if q >= 2:
                    dve.wait_ge(kct, q - 1)
                c = kc[0:M, q % 2, :]
                link(v.tensor_tensor(c, k.ps[0:M, 5, 0:HD], b2[0:M, 0, :], ALU.add))
                v.tensor_tensor(k.vc[0:M, q, :], k.ps[0:M, 5, HD:2 * HD], b2[0:M, 1, :], ALU.add)
                link(v.tensor_tensor(sq[0:M, :], c, c, ALU.mult))
                link(v.tensor_reduce(st[0:M, 0:1], sq[0:M, :], AX.X, ALU.add))
                link(v.tensor_scalar(st[0:M, 1:2], st[0:M, 0:1], 1.0 / HD, EPS, ALU.mult, ALU.add))
                v.reciprocal(st[0:M, 0:1], st[0:M, 1:2]).then_inc(root_in, 1)
                dve.wait_ge(root, q + 1)
                v.scalar_tensor_tensor(out=c, in0=c, scalar=st[0:M, 1:2], in1=kg[0:M, :], op0=ALU.mult, op1=ALU.mult).then_inc(kcd, 1)
                dve.wait_ge(kct, q + 1)
                v.tensor_copy(k.kcT[0:HD, q, 0:M], k.ps[0:HD, 6, 0:M]).then_inc(kcc, 1)


def stage_choice(nc, k, sem):
    M = NCMP
    with ExitStack() as ctx:
        def sb(name, shape, dt=F32):
            return ctx.enter_context(nc.sbuf_tensor(name, shape, dt))
        qf, cs, pcT = sb("qf", [HD, 2, H, P]), sb("cs", [P, 2, H, P]), sb("pcT", [P, 2, H, P])
        mx = sb("mx", [P, 2, 16])
        pg = sb("pg", [P, NC, P + 4])
        imp, m8 = sb("imp", [P, NC, NBLK]), sb("m8", [P, NC, 16])
        spare, rest = pg[:, :, 0:NBLK], pg[:, :, NBLK:2 * NBLK]
        names = "va_done q_tr q_cp sc_done masked exp_done probs p_tr p_cp out_done out_read chosen bias_tr link".split()
        z = {n: sem("choice_" + n) for n in names}
        block = ctx.enter_context(nc.Block())

        @block.tensor
        def _(pe):
            m = nc.tensor

            def queries(b):
                if b >= 2:
                    pe.wait_ge(z["q_cp"], b - 1)
                for h in range(H):
                    last = m.transpose(k.ps[0:HD, b % 2, h * P:(h + 1) * P], k.tm[:, b, h * HD:(h + 1) * HD], k.ident[:, :])
                last.then_inc(z["q_tr"], 1)

            def scores(b):
                pe.wait_ge(z["q_cp"], b + 1)
                if b >= 2:
                    pe.wait_ge(z["masked"], b - 1)
                for h in range(H):
                    last = m.matmul(k.ps[:, 2 + b % 2, h * P:h * P + M], qf[:, b % 2, h, :], k.kcT[:, 0, 0:M], start=True, stop=True)
                last.then_inc(z["sc_done"], 1)

            def turn(b):
                pe.wait_ge(z["probs"], b + 1)
                if b >= 2:
                    pe.wait_ge(z["p_cp"], b - 1)
                for h in range(H):
                    last = m.transpose(k.ps[0:M, 4 + b % 2, h * P:(h + 1) * P], cs[:, b % 2, h, 0:M], k.ident[:, :])
                last.then_inc(z["p_tr"], 1)

            def values(b):
                pe.wait_ge(z["p_cp"], b + 1)
                if b >= 2:
                    pe.wait_ge(z["out_read"], b - 1)
                for h in range(H):
                    last = m.matmul(k.ps[:, 6 + b % 2, h * HD:(h + 1) * HD], pcT[0:M, b % 2, h, :], k.vc[0:M, 0, :], start=True, stop=True)
                last.then_inc(z["out_done"], 1)

            for s in range(NC + 3):
                for step, b in ((queries, s), (scores, s - 1), (turn, s - 2), (values, s - 3)):
                    if 0 <= b < NC:
                        step(b)
            pe.wait_ge(z["chosen"], 1)
            for b in range(NC):
                last = m.transpose(k.ps[0:NBLK, b // 4, (b % 4) * P:(b % 4 + 1) * P], imp[:, b, :], k.ident[:, :])
            last.then_inc(z["bias_tr"], 1)

        @block.scalar
        def _(act):
            def queries(b):
                act.wait_ge(z["q_tr"], b + 1)
                if b >= 2:
                    act.wait_ge(z["sc_done"], b - 1)
                nc.scalar.copy(qf[:, b % 2].rearrange("d h q -> d (h q)"), k.ps[0:HD, b % 2, :]).then_inc(z["q_cp"], 1)

            def exps(b):
                act.wait_ge(z["masked"], b + 1)
                for h in range(H):
                    last = nc.scalar.activation(cs[:, b % 2, h, 0:M], cs[:, b % 2, h, 0:M], ACT.Exp, scale=SCALE,
                                                bias=mx[:, b % 2, h:h + 1], accum_out=mx[:, b % 2, 8 + h:9 + h])
                last.then_inc(z["exp_done"], 1)

            def probs(b):
                act.wait_ge(z["p_tr"], b + 1)
                if b >= 2:
                    act.wait_ge(z["out_done"], b - 1)
                nc.scalar.copy(pcT[0:M, b % 2].rearrange("p h q -> p (h q)"), k.ps[0:M, 4 + b % 2, :]).then_inc(z["p_cp"], 1)

            def share(b):
                act.wait_ge(z["out_done"], b + 1)
                for h in range(H):
                    last = nc.scalar.activation(k.tm[:, b, W + h * HD:W + (h + 1) * HD], k.ps[:, 6 + b % 2, h * HD:(h + 1) * HD],
                                                ACT.Copy, scale=k.tm[:, b, 640 + 3 * h:641 + 3 * h])
                last.then_inc(z["out_read"], 1)

            act.wait_ge(z["va_done"], 1)
            for s in range(NC + 3):
                for step, b in ((queries, s), (exps, s - 1), (probs, s - 2), (share, s - 3)):
                    if 0 <= b < NC:
                        step(b)

        @block.vector
        def _(dve):
            v = nc.vector
            link = chain(dve, z["link"])
            v.memset(k.va[:, :, :, HD:HD + 1], 1.0)
            for b in range(2):
                last = v.tensor_copy(k.va[:, :, b, 0:HD], k.tm[:, 0:NC, 448 + 128 * b:512 + 128 * b])
            last.then_inc(z["va_done"], 1)
            link(v.memset(pg[:, :, :], 0.0))

            def mask(b):
                dve.wait_ge(z["sc_done"], b + 1)
                if b >= 2:
                    dve.wait_ge(z["p_tr"], b - 1)
                low = k.cmp_mask[:, P - 8 * b:P - 8 * b + M]
                link(v.tensor_tensor(cs[:, b % 2, :, 0:M], k.ps[:, 2 + b % 2, :].rearrange("p (h c) -> p h c", h=H)[:, :, 0:M],
                                     low.rearrange("p (o c) -> p o c", o=1).broadcast_to([P, H, M]), ALU.add))
                link(v.tensor_reduce(mx[:, b % 2, 0:4], cs[:, b % 2, :, 0:M], AX.X, ALU.max))
                v.tensor_scalar(mx[:, b % 2, 0:4], mx[:, b % 2, 0:4], -1e20, -SCALE, ALU.max, ALU.mult).then_inc(z["masked"], 1)

            def normalise(b):
                dve.wait_ge(z["exp_done"], b + 1)
                r = mx[:, b % 2, 12:16]
                link(v.tensor_scalar(r, mx[:, b % 2, 8:12], 1e-30, None, ALU.max))
                link(v.reciprocal(r, r))
                c = cs[:, b % 2, :, 0:M]
                v.tensor_tensor(c, c, r.rearrange("p (h o) -> p h o", o=1).broadcast_to([P, H, M]), ALU.mult).then_inc(z["probs"], 1)
                dve.wait_ge(z["probs"], b + 1)
                link(v.tensor_reduce(pg[:, b, 1:1 + M], c.rearrange("p h c -> p c h"), AX.X, ALU.add))

            for s in range(NC + 3):
                for step, b in ((normalise, s - 2), (mask, s - 1)):
                    if 0 <= b < NC:
                        step(b)

            def at(o):
                return pg[:, :, 1 + o:1 + o + 4 * (NBLK - 1) + 1:4]
            e = imp[:, :, :]
            link(v.scalar_tensor_tensor(out=e, in0=at(-1), scalar=0.5, in1=at(0), op0=ALU.mult, op1=ALU.add))
            link(v.tensor_tensor(e, e, at(1), ALU.add))
            link(v.tensor_tensor(e, e, at(2), ALU.add))
            link(v.scalar_tensor_tensor(out=e, in0=at(3), scalar=0.5, in1=e, op0=ALU.mult, op1=ALU.add))
            for b in range(NC):
                last = v.tensor_tensor(imp[:, b, :], imp[:, b, :], k.sel_mask[:, NBLK - 2 * b:2 * NBLK - 2 * b], ALU.add)
            link(last)
            link(v.memset(imp[:, :, 0:1], BIG))
            for b in range(NC):
                last = v.max(m8[:, b, 0:8], imp[:, b, :])
            link(last)
            for b in range(NC):
                last = v.match_replace(spare[:, b, :], m8[:, b, 0:8], imp[:, b, :], -3e38)
            link(last)
            for b in range(NC):
                last = v.max(m8[:, b, 8:16], spare[:, b, :])
            link(last)
            for b in range(NC):
                last = v.match_replace(rest[:, b, :], m8[:, b, 8:16], spare[:, b, :], -3e38)
            link(last)
            v.tensor_scalar(e, rest[:, :, :], -2e38, NEG, ALU.is_gt, ALU.mult).then_inc(z["chosen"], 1)
            dve.wait_ge(z["bias_tr"], 1)
            v.tensor_copy(k.biasT[HD:HD + NBLK, :], k.ps[0:NBLK, 0:4, :].rearrange("p b n -> p (b n)"))


def stage_attention(nc, k, sem):
    LAG, NST, NPT = 2, 3, 4
    VW = HD + 1

    def tiles_of(qb):
        return [("sel", t) for t in range(qb + 1)] + [("win", t) for t in range(max(0, qb - 4), qb + 1)]

    def max_units(qb, kind):
        lo = 0 if kind == "sel" else max(0, qb - 4)
        return [("max", kind, h, a, min(a + 4, qb + 1), (a - lo) // 4) for h in range(H) for a in range(lo, qb + 1, 4)]

    def units_of(qb):
        return max_units(qb, "win") + max_units(qb, "sel")

    order, tiles = [("q", 0)] + [(u, 0) for u in units_of(0)] + [("shift", 0)], []
    turns = {}
    for qb in range(NC):
        mine = tiles_of(qb)
        units = units_of(qb + 1) if qb + 1 < NC else []
        first, last = (1, len(mine) - 3) if len(mine) >= 6 else (0, len(mine) - 1)
        done = 0
        for n, (kind, t) in enumerate(mine):
            i = len(tiles)
            tiles.append((qb, kind, t, n == 0 or mine[n - 1][0] != kind, n + 1 == len(mine) or mine[n + 1][0] != kind))
            order.append(("tile", i))
            if i >= LAG and tiles[i - LAG][4]:
                order.append(("part_" + tiles[i - LAG][1], tiles[i - LAG][0]))
                if tiles[i - LAG][1] == "win":
                    turns[i + 2] = tiles[i - LAG][0]
            if i in turns:
                order.append(("out", turns[i]))
            if units:
                if n == 0:
                    order.append(("q", qb + 1))
                upto = 0 if n < first else min(len(units), len(units) * (n - first + 1) // (last - first + 1))
                order += [(u, qb + 1) for u in units[done:upto]]
                done = upto
                if n == len(mine) - 1:
                    order.append(("shift", qb + 1))
    order += [("drain", len(tiles) + i) for i in range(LAG)] + [("part_win", NC - 1), ("out", NC - 1)]

    with ExitStack() as ctx:
        def sb(name, shape, dt=F32):
            return ctx.enter_context(nc.sbuf_tensor(name, shape, dt))
        FR, BF = mybir.dt.float32r, mybir.dt.bfloat16
        qhi, qlo = sb("q_hi", [P, 2, H * P], FR), sb("q_lo", [P, 2, H * P], FR)
        pT = sb("pT", [P, NPT, H, P])
        o_tm, o_part = sb("o_tm", [P, 2, W]), sb("o_part", [P, 2, W])
        part_max = sb("part_max", [P, 2, H, 4])
        shift = sb("row_shift", [P, H, 2])
        wgt = sb("wgt", [P, 2, H])
        id_b, causal_b, low_b = (sb(n, [P, P], BF) for n in ("id_b", "causal_b", "low_b"))
        upper_b, lowT_b = sb("upper_b", [P, H * P], BF), sb("lowT_b", [P, H * P], BF)
        names = "ready st_done exp_done pv_done misc_wr misc_rd mu_done mu_read bias_in shifted part_sel part_win link".split()
        z = {n: sem("a_" + n) for n in names}
        block = ctx.enter_context(nc.Block())
        MISC = 7
        MISC_STEPS = ("q", "shift", "out")
        misc_at = {step: n + 1 for n, step in enumerate(s for s in order if s[0] in MISC_STEPS)}
        n_tiles = {(t[0], t[1]): i + 1 for i, t in enumerate(tiles)}

        @block.tensor
        def _(pe):
            m = nc.tensor
            count = {"mu": 0}
            pe.wait_ge(z["ready"], 6)

            def scores(i):
                qb, kind, t, first, _ = tiles[i]
                if i >= NST:
                    pe.wait_ge(z["exp_done"], i - NST + 1)
                if first and kind == "sel":
                    pe.wait_ge(z["misc_rd"], misc_at["shift", qb])
                hi, lo = k.keys[0 if kind == "sel" else 1]
                R = HD + NBLK + 2
                c, bank = slice(t * P, (t + 1) * P), k.ps[:, i % NST, :]
                low = kind == "win" and t == qb - 4
                m.matmul(bank, hi[0:R, c], qhi[0:R, qb % 2, :], start=True, stop=False)
                m.matmul(bank, hi[0:R, c], qlo[0:R, qb % 2, :], start=False, stop=False)
                last = m.matmul(bank, lo[0:R, c], qhi[0:R, qb % 2, :], start=False, stop=not (low or t == qb))
                if low or t == qb:
                    last = m.matmul(bank, id_b[:, :], (lowT_b if low else upper_b)[:, :], start=False, stop=True)
                last.then_inc(z["st_done"], 1)

            def values(i):
                if i < 0:
                    return
                qb, kind, t, first, end = tiles[i]
                b = 0 if kind == "sel" else 1
                pe.wait_ge(z["exp_done"], i + 1)
                if first and qb:
                    pe.wait_ge(z["part_" + kind], qb)
                for h in range(H):
                    last = m.matmul(k.ps[:, 5 + b, h * VW:(h + 1) * VW], pT[:, i % NPT, h, :], k.va[:, t, b, :],
                                    start=(first and h == 0), stop=(end and h == H - 1), skip_group_check=True)
                last.then_inc(z["pv_done"], 1)

            def max_pass(qb, kind, h, a, b, col):
                n = count["mu"]
                count["mu"] += 1
                if n >= 2:
                    pe.wait_ge(z["mu_read"], n - 1)
                pe.wait_ge(z["misc_rd"], misc_at["q", qb])
                if kind == "sel" and h == 0 and a == 0:
                    pe.wait_ge(z["bias_in"], qb + 1)
                R = HD + NBLK if kind == "sel" else HD
                hi = k.keys[0 if kind == "sel" else 1][0]
                bank = k.ps[:, 3 + n % 2, :]
                low, end = kind == "win" and a == qb - 4, b == qb + 1
                last = m.matmul(bank[:, 0:(b - a) * P], qhi[0:R, qb % 2, h * P:(h + 1) * P], hi[0:R, a * P:b * P],
                                start=True, stop=not (low or end))
                if low:
                    last = m.matmul(bank[:, 0:P], id_b[:, :], low_b[:, :], start=False, stop=not end)
                if end:
                    last = m.matmul(bank[:, (b - a - 1) * P:(b - a) * P], id_b[:, :], causal_b[:, :], start=False, stop=True)
                last.then_inc(z["mu_done"], 1)

            def misc(step, qb):
                bank = k.ps[:, MISC, :]
                n = misc_at[step, qb]
                if n > 1:
                    pe.wait_ge(z["misc_rd"], n - 1)
                if step == "q":
                    for h in range(H):
                        last = m.transpose(bank[0:HD, h * P:(h + 1) * P], k.tm[:, qb, h * HD:(h + 1) * HD], k.ident[:, :])
                elif step == "shift":
                    pe.wait_ge(z["shifted"], qb + 1)
                    for h in range(H):
                        last = m.transpose(bank[0:2, h * P:(h + 1) * P], shift[:, h, :], k.ident[:, :])
                else:
                    pe.wait_ge(z["part_win"], qb + 1)
                    for j in range(2):
                        last = m.transpose(bank[:, j * P:(j + 1) * P], o_tm[:, qb % 2, j * P:(j + 1) * P], k.ident[:, :])
                last.then_inc(z["misc_wr"], 1)

            for what, n in order:
                if what == "tile":
                    scores(n)
                    values(n - LAG)
                elif what == "drain":
                    values(n - LAG)
                elif what in MISC_STEPS:
                    misc(what, n)
                elif what[0] == "max":
                    max_pass(n, *what[1:])

        @block.scalar
        def _(act):
            act.wait_ge(z["ready"], 6)
            for what, n in order:
                if what == "tile":
                    act.wait_ge(z["st_done"], n + 1)
                    if n >= NPT:
                        act.wait_ge(z["pv_done"], n - NPT + 1)
                    nc.scalar.activation(pT[:, n % NPT].rearrange("p h q -> p (h q)"), k.ps[:, n % NST, :], ACT.Exp,
                                         scale=SCALE).then_inc(z["exp_done"], 1)
                elif what == "q":
                    act.wait_ge(z["misc_wr"], misc_at["q", n])
                    nc.scalar.copy(qhi[HD:HD + NBLK, n % 2, :].rearrange("b (h q) -> b h q", h=H),
                                   k.biasT[HD:HD + NBLK, n * P:(n + 1) * P].rearrange("p (o q) -> p o q", o=1).broadcast_to([NBLK, H, P])
                                   ).then_inc(z["bias_in"], 1)

        @block.vector
        def _(dve):
            v = nc.vector
            link = chain(dve, z["link"])
            count = {"mu": 0}
            v.memset(qlo[HD:HD + NBLK, :, :].bitcast(F32), 0.0)
            v.tensor_copy(id_b[:, :], k.ident[:, :]).then_inc(z["ready"], 1)
            v.tensor_copy(causal_b[:, :], k.causal[:, :]).then_inc(z["ready"], 1)
            v.tensor_copy(low_b[:, :], k.win_low[:, :]).then_inc(z["ready"], 1)
            v.tensor_copy(upper_b[:, :], k.neg_upper[:, :]).then_inc(z["ready"], 1)
            v.tensor_copy(lowT_b[:, :], k.low_T[:, :]).then_inc(z["ready"], 1)
            v.memset(part_max[:, :, :, :], 0.0).then_inc(z["ready"], 1)
            dve.wait_ge(z["ready"], 6)

            def misc(step, qb):
                bank = k.ps[:, MISC, :]
                if step == "shift":
                    ns, nw = (qb + 4) // 4, (qb - max(0, qb - 4) + 4) // 4
                    for b, n in ((0, ns), (1, nw)):
                        last = v.tensor_reduce(shift[:, :, b], part_max[:, b, :, 0:n], AX.X, ALU.max)
                    link(last)
                    v.tensor_scalar(shift[:, :, :], shift[:, :, :], -1.0, None, ALU.mult).then_inc(z["shifted"], 1)
                dve.wait_ge(z["misc_wr"], misc_at[step, qb])
                if step == "q":
                    r = slice(0, HD)
                    link(v.tensor_copy(qhi[r, qb % 2, :], bank[r, :]))
                    ins = v.tensor_tensor(qlo[r, qb % 2, :], bank[r, :], qhi[r, qb % 2, :].bitcast(F32), ALU.subtract)
                elif step == "shift":
                    r = slice(HD + NBLK, HD + NBLK + 2)
                    link(v.tensor_copy(qhi[r, qb % 2, :], bank[0:2, :]))
                    ins = v.tensor_tensor(qlo[r, qb % 2, :], bank[0:2, :], qhi[r, qb % 2, :].bitcast(F32), ALU.subtract)
                else:
                    y = [k.yT[6 + j][:, qb * P:(qb + 1) * P] for j in range(2)]
                    link(v.tensor_tensor(y[0], bank[:, 0:P], y[0], ALU.mult))
                    ins = v.tensor_tensor(y[1], bank[:, P:2 * P], y[1], ALU.mult)
                ins.then_inc(z["misc_rd"], 1)

            def part(kind, qb):
                b = 0 if kind == "sel" else 1
                o = k.ps[:, 5 + b, 0:H * VW].rearrange("p (h d) -> p h d", d=VW)
                gates = k.tm[:, qb, 640:652].rearrange("p (h b) -> p h b", b=3)[:, :, 1 + b]
                dve.wait_ge(z["pv_done"], n_tiles[qb, kind])
                link(v.reciprocal(wgt[:, b, :], o[:, :, HD]))
                link(v.tensor_tensor(wgt[:, b, :], wgt[:, b, :], gates, ALU.mult))
                link(v.tensor_tensor(o_part[:, b, :].rearrange("p (h d) -> p h d", d=HD), o[:, :, 0:HD],
                                     wgt[:, b, :].rearrange("p (h o) -> p h o", o=1).broadcast_to([P, H, HD]), ALU.mult))
                t = o_tm[:, qb % 2, :]
                v.tensor_tensor(t, t if b else k.tm[:, qb, W:2 * W], o_part[:, b, :], ALU.add).then_inc(z["part_" + kind], 1)
                dve.wait_ge(z["part_" + kind], qb + 1)

            for what, n in order:
                if what in MISC_STEPS:
                    misc(what, n)
                elif what in ("part_sel", "part_win"):
                    part(what[5:], n)
                elif what[0] == "max":
                    _, kind, h, a, b, col = what
                    i = count["mu"]
                    count["mu"] += 1
                    dve.wait_ge(z["mu_done"], i + 1)
                    c = part_max[:, 0 if kind == "sel" else 1, h, col:col + 1]
                    v.tensor_reduce(c, k.ps[:, 3 + i % 2, 0:(b - a) * P], AX.X, ALU.max).then_inc(z["mu_read"], 1)
                    if kind == "sel" and h == H - 1 and b == n + 1:
                        dve.wait_ge(z["mu_read"], i + 1)


def choose_blocks(link, v, score, spare, out, m8, chosen):
    link(v.max(m8[:, 0:8], score))
    link(v.match_replace(spare, m8[:, 0:8], score, -3e38))
    link(v.max(m8[:, 8:16], spare))
    link(v.match_replace(out, m8[:, 8:16], spare, -3e38))
    v.tensor_scalar(score, out, -2e38, NEG, ALU.is_gt, ALU.mult).then_inc(chosen, 1)


def stage_sample_attention(nc, k, sem):
    M, Q = NCMP, NS * H
    GW = 4
    with ExitStack() as ctx:
        def sb(name, shape, dt=F32):
            return ctx.enter_context(nc.sbuf_tensor(name, shape, dt))
        kT = sb("kT_s", [P, T])
        pages = sb("pages_s", [P, NS, PAGES, P])
        win = k.tm[:, 0:8, :].rearrange("p t c -> p (t c)")[:, 0:NS * GW * P].rearrange("p (n g c) -> p n g c", n=NS, g=GW)
        table = sb("table2", [1, NS * PAGES], I32)
        small = k.tm[:, 8:NC, :].rearrange("p t c -> p (t c)")
        used = [0]

        def sb(name, shape):
            size = 1
            for n in shape[1:]:
                size *= n
            used[0] += size
            t = small[0:shape[0], used[0] - size:used[0]]
            if len(shape) == 2:
                return t
            dims = " ".join("abc"[:len(shape) - 1])
            return t.rearrange(f"p ({dims}) -> p {dims}", **dict(zip("abc", shape[1:])))
        qT = sb("qT_s", [P, NS, H])
        newT = sb("newT_s", [HD, 4, NS])
        gd, gts = sb("gate_diag", [NS, NS, 12]), sb("gates_s", [HD, NS, 12])
        prod = sb("prod_s", [HD, 2, Q])
        snew = sb("snew", [P, 2, Q])
        scT, pc, pcT = sb("scT", [P, Q]), sb("pc_s", [Q, P]), sb("pcT_s", [P, Q])
        pick8 = sb("pick8", [Q, NS])
        st = sb("st_s", [Q, 8])
        pg, sc, m8 = sb("pg_s", [NS, P + 4]), sb("sc_s", [NS, 3, NBLK + 1]), sb("m8_s", [NS, 16])
        cmax = sb("cmax", [P, Q])
        dg = sb("dg_s", [Q, Q])
        M_b, pnew = sb("M_b", [P, Q]), sb("pnew", [P, Q])
        prob = sb("prob_s", [P, NS * PAGES * H])
        o_sum, o_b, l_b = sb("o_sum", [HD, Q]), sb("o_b", [HD, Q]), sb("l_b", [HD, Q])
        o_ch = sb("o_ch", [P, 2, NS])
        names = ("table_in blk_in win_in pk tr0 cp0 gm gcp cs_ csc cst ex nrm pp pcc imp btr bcp oc sn snc ktr kcp skt scd rmx mt dgd mb sub exd2 "
                 "av comb link osum och pick").split()
        z = {n: sem("d_" + n) for n in names}
        kin = [[sem(f"d_kin{n}"), sem(f"d_kin{n}p")] for n in range(NS)]
        block = ctx.enter_context(nc.Block())
        S_ps, W_ps = k.ps[:, 0, :], k.ps[:, 1, :]
        branches = (("sel", PAGES, 0), ("win", GW, 1))

        def scalar_part(act):
            act.wait_ge(z["ex"], 1)
            nc.scalar.activation(pc[:, 0:M], k.ps[0:Q, 6, 0:M], ACT.Exp, scale=SCALE, bias=st[:, 1:2], accum_out=st[:, 2:3]).then_inc(z["ex"], 1)
            for b, (kind, G, i) in enumerate(branches):
                act.wait_ge(z["sub"], b + 1)
                n = NS * G * H
                nc.scalar.activation(prob[:, 0:n], prob[:, 0:n], ACT.Exp, scale=SCALE)
                nc.scalar.activation(pnew[:, :], pnew[:, :], ACT.Exp, scale=SCALE).then_inc(z["exd2"], 1)

        def fetch(eng, parity):
            eng.wait_ge(z["table_in"], 16)
            for at in range(parity, NS * PAGES, 2):
                n, g = divmod(at, PAGES)
                i = eng.value_load(table[0:1, at:at + 1], min_val=0, max_val=k.n_pool - 1)
                eng.dma_start(pages[:, n, g, :], k.io["cache_kv"][0, bass.DynSlice(i, 1), :, 2:4, :].rearrange("o p s d -> (o p) (s d)")
                              ).then_inc(kin[n][parity], 16)

        @block.sync
        def _(sp):
            sp.dma_start(table[:, :], k.io["page_table"].rearrange("n g -> (n g)").rearrange("(o m) -> o m", o=1)).then_inc(z["table_in"], 16)
            fetch(sp, 0)

        @block.scalar
        def _(act):
            act.dma_start(kT[HD:HD + NBLK, :], k.extra_dram[0, 0:NBLK, :]).then_inc(z["blk_in"], 16)
            for n in range(NS):
                act.dma_start(win[:, n], k.io["cache_win"][0, n].rearrange("(g p) s d -> p g (s d)", p=P)).then_inc(z["win_in"], 16)
            scalar_part(act)

        @block.gpsimd
        def _(pool):
            g = nc.gpsimd
            fetch(pool, 1)
            link = chain(pool, z["pick"])
            link(g.memset(pick8[:, :], 1.0))
            link(g.affine_select(out=pick8[:, :], in_=pick8[:, :], pattern=[[-4, NS]], compare_op=ALU.is_ge, fill=0.0, base=0, channel_multiplier=1))
            link(g.affine_select(out=pick8[:, :], in_=pick8[:, :], pattern=[[4, NS]], compare_op=ALU.is_ge, fill=0.0, base=3, channel_multiplier=-1))

        @block.tensor
        def _(pe):
            m = nc.tensor
            one = k.ones
            for h in range(H):
                m.transpose(k.ps[0:HD, 6, h * NS:(h + 1) * NS], k.tm[0:NS, NC, h * HD:(h + 1) * HD], k.ident[0:NS, 0:NS])
            for i, c in enumerate((384, 448, 512, 576)):
                last = m.transpose(k.ps[0:HD, 6, (H + i) * NS:(H + i + 1) * NS], k.tm[0:NS, NC, c:c + HD], k.ident[0:NS, 0:NS])
            last.then_inc(z["tr0"], 1)
            pe.wait_ge(z["gm"], 1)
            m.matmul(k.ps[0:HD, 7, 0:96], one[0:NS, 0:HD], gd[:, :, :].rearrange("a n g -> a (n g)"), start=True, stop=True).then_inc(z["tr0"], 1)
            pe.wait_ge(z["cp0"], 2)
            for n in range(NS):
                last = m.matmul(k.ps[0:M, 5, n * H:(n + 1) * H], k.kcT[0:HD, 1 + n, 0:M], qT[0:HD, n, :], start=True, stop=True)
            last.then_inc(z["cs_"], 1)
            pe.wait_ge(z["sn"], 1)
            pe.wait_ge(z["gcp"], 1)
            m.matmul(k.ps[:, 7, 0:2 * Q], one[0:HD, :], prod[:, :, :].rearrange("d b q -> d (b q)"), start=True, stop=True).then_inc(z["snc"], 1)
            pe.wait_ge(z["csc"], 1)
            m.transpose(k.ps[0:Q, 6, 0:M], scT[0:M, :], k.ident[0:M, 0:M]).then_inc(z["cst"], 1)
            pe.wait_ge(z["nrm"], 1)
            pe.wait_ge(z["pick"], 3)
            m.matmul(k.ps[0:NS, 5, 0:M], pick8[:, :], pc[:, 0:M], start=True, stop=True)
            m.transpose(k.ps[0:M, 6, 0:Q], pc[:, 0:M], k.ident[0:Q, 0:Q]).then_inc(z["pp"], 1)
            pe.wait_ge(z["pcc"], 1)
            for n in range(NS):
                last = m.matmul(k.ps[0:HD, 6, n * H:(n + 1) * H], k.vc[0:M, 1 + n, :], pcT[0:M, n * H:(n + 1) * H], start=True, stop=True)
            last.then_inc(z["oc"], 1)
            pe.wait_ge(z["imp"], 1)
            m.transpose(k.ps[0:NBLK, 5, 0:NS], sc[:, 0, 0:NBLK], k.ident[0:NS, 0:NS]).then_inc(z["btr"], 1)
            pe.wait_ge(z["bcp"], 1)
            pe.wait_ge(z["osum"], 1)

            def pool_max(b):
                pe.wait_ge(z["rmx"], b + 1)
                m.transpose(k.ps[0:Q, 5, 0:P], cmax[:, :], k.ident[:, :]).then_inc(z["mt"], 1)
                pe.wait_ge(z["dgd"], b + 1)
                m.matmul(k.ps[:, 6, 0:Q], one[0:Q, :], dg[:, :], start=True, stop=True).then_inc(z["mb"], 1)

            def pool_values(b, G, v):
                pe.wait_ge(z["exd2"], b + 1)
                p4 = prob[:, 0:NS * G * H].rearrange("p (n g h) -> p n g h", n=NS, h=H)
                for g in range(G):
                    m.matmul(k.ps[0:HD, 5, 0:Q], one[:, 0:HD], p4[:, :, g, :], start=(g == 0), stop=(g == G - 1))
                for n in range(NS):
                    for g in range(G):
                        last = m.matmul(k.ps[0:HD, 7, n * H:(n + 1) * H], v[:, n, g, :], p4[:, n, g, :], start=(g == 0), stop=(g == G - 1))
                last.then_inc(z["av"], 1)

            NE = 4 * NS + NS

            def keys(e):
                if e < 4 * NS:
                    n, b4 = divmod(e, 4)
                    for landed in kin[n]:
                        pe.wait_ge(landed, 16 * PAGES // 2)
                    src = [pages[:, n, 4 * b4 + t, 0:HD] for t in range(4)]
                else:
                    pe.wait_ge(z["win_in"], 16 * NS)
                    src = [win[:, e - 4 * NS, t, 0:HD] for t in range(4)]
                if e >= 2:
                    pe.wait_ge(z["kcp"], e - 1)
                for t in range(4):
                    last = m.transpose(k.ps[0:HD, 3 + e % 2, t * P:(t + 1) * P], src[t], k.ident[:, :])
                last.then_inc(z["ktr"], 1)

            def scores(e):
                pe.wait_ge(z["kcp"], e + 1)
                sel = e < 4 * NS
                rows = HD + NBLK if sel else HD
                n = e // 4 if sel else e - 4 * NS
                at = 4 * e if sel else 4 * n
                for t in range(4):
                    last = m.matmul((S_ps if sel else W_ps)[:, (at + t) * H:(at + t + 1) * H],
                                    kT[0:rows, (e % 4) * 512 + t * P:(e % 4) * 512 + (t + 1) * P], qT[0:rows, n, :], start=True, stop=True)
                last.then_inc(z["scd"], 1)

            keys(0)
            for e in range(NE):
                if e + 1 < NE:
                    keys(e + 1)
                scores(e)
            pool_max(0)
            pool_values(0, PAGES, pages[:, :, :, HD:P])
            pe.wait_ge(z["comb"], 1)
            pool_max(1)
            pool_values(1, GW, win[:, :, :, HD:P])

        @block.vector
        def _(dve):
            v = nc.vector
            link = chain(dve, z["link"])
            link(v.memset(pg[:, :], 0.0))
            gate = k.tm[0:NS, NC, 640:652].rearrange("n (o g) -> n o g", o=1).broadcast_to([NS, NS, 12])
            v.tensor_tensor(gd[:, :, :], gate, k.ident[0:NS, 0:NS].rearrange("n (m o) -> n m o", o=1).broadcast_to([NS, NS, 12]), ALU.mult).then_inc(z["gm"], 1)
            dve.wait_ge(z["tr0"], 1)
            v.tensor_copy(qT[0:HD, :, :].rearrange("d n h -> d h n"), k.ps[0:HD, 6, 0:Q].rearrange("d (h n) -> d h n", n=NS)).then_inc(z["cp0"], 1)
            v.tensor_copy(newT[:, :, :].rearrange("d i n -> d (i n)"), k.ps[0:HD, 6, Q:2 * Q]).then_inc(z["cp0"], 1)
            dve.wait_ge(z["cp0"], 2)
            for b in range(2):
                kn = newT[:, 2 * b, :].rearrange("d (n o) -> d n o", o=1).broadcast_to([HD, NS, H])
                last = v.tensor_tensor(prod[:, b, :].rearrange("d (n h) -> d n h", h=H), qT[0:HD, :, :], kn, ALU.mult)
            last.then_inc(z["sn"], 1)
            dve.wait_ge(z["tr0"], 2)
            v.tensor_copy(gts[:, :, :].rearrange("d n g -> d (n g)"), k.ps[0:HD, 7, 0:96]).then_inc(z["gcp"], 1)
            dve.wait_ge(z["cs_"], 1)
            v.tensor_copy(scT[0:M, :], k.ps[0:M, 5, 0:Q]).then_inc(z["csc"], 1)
            dve.wait_ge(z["snc"], 1)
            v.tensor_copy(snew[:, :, :].rearrange("p b q -> p (b q)"), k.ps[:, 7, 0:2 * Q])
            dve.wait_ge(z["cst"], 1)
            link(v.tensor_reduce(st[:, 0:1], k.ps[0:Q, 6, 0:M], AX.X, ALU.max))
            v.tensor_scalar(st[:, 1:2], st[:, 0:1], -SCALE, None, ALU.mult).then_inc(z["ex"], 1)
            dve.wait_ge(z["ex"], 2)
            link(v.reciprocal(st[:, 3:4], st[:, 2:3]))
            v.tensor_scalar(pc[:, 0:M], pc[:, 0:M], st[:, 3:4], None, ALU.mult).then_inc(z["nrm"], 1)
            dve.wait_ge(z["pp"], 1)
            v.tensor_copy(pcT[0:M, :], k.ps[0:M, 6, 0:Q]).then_inc(z["pcc"], 1)
            link(v.tensor_copy(pg[:, 1:1 + M], k.ps[0:NS, 5, 0:M]))

            def at(o):
                return pg[:, 1 + o:1 + o + 4 * (NBLK - 1) + 1:4]
            b = sc[:, 0, 0:NBLK]
            link(v.scalar_tensor_tensor(out=b, in0=at(-1), scalar=0.5, in1=at(0), op0=ALU.mult, op1=ALU.add))
            link(v.tensor_tensor(b, b, at(1), ALU.add))
            link(v.tensor_tensor(b, b, at(2), ALU.add))
            link(v.scalar_tensor_tensor(out=b, in0=at(3), scalar=0.5, in1=b, op0=ALU.mult, op1=ALU.add))
            link(v.memset(sc[:, 0, 0:1], BIG))
            link(v.memset(sc[:, 0, NBLK - 1:NBLK + 1], BIG))
            choose_blocks(link, v, sc[:, 0, :], sc[:, 1, :], sc[:, 2, :], m8, z["imp"])
            dve.wait_ge(z["btr"], 1)
            v.tensor_copy(qT[HD:HD + NBLK, :, :], k.ps[0:NBLK, 5, 0:NS].rearrange("b (n o) -> b n o", o=1).broadcast_to([NBLK, NS, H])).then_inc(z["bcp"], 1)
            dve.wait_ge(z["oc"], 1)
            v.tensor_tensor(o_sum[:, :].rearrange("d (n h) -> d n h", h=H), k.ps[0:HD, 6, 0:Q].rearrange("d (n h) -> d n h", h=H),
                            gts[:, :, 0:12:3], ALU.mult).then_inc(z["osum"], 1)
            dve.wait_ge(z["blk_in"], 16)
            for e in range(4 * NS + NS):
                dve.wait_ge(z["ktr"], e + 1)
                if e >= 4:
                    dve.wait_ge(z["scd"], e - 3)
                v.tensor_copy(kT[0:HD, (e % 4) * 512:(e % 4 + 1) * 512], k.ps[0:HD, 3 + e % 2, :]).then_inc(z["kcp"], 1)

            def softmax(b, G):
                n = NS * G * H
                s4 = (W_ps if b else S_ps)[:, 0:n].rearrange("p (n g h) -> p n g h", n=NS, h=H)
                dve.wait_ge(z["scd"], 5 * NS)
                v.tensor_reduce(cmax[:, :].rearrange("p (n h) -> p n h", h=H), s4.rearrange("p n g h -> p n h g"), AX.X, ALU.max).then_inc(z["rmx"], 1)
                dve.wait_ge(z["mt"], b + 1)
                link(v.tensor_reduce(st[:, 4:5], k.ps[0:Q, 5, 0:P], AX.X, ALU.max))
                v.tensor_scalar(dg[:, :], k.ident[0:Q, 0:Q], st[:, 4:5], None, ALU.mult).then_inc(z["dgd"], 1)
                dve.wait_ge(z["mb"], b + 1)
                link(v.tensor_tensor(M_b[:, :], k.ps[:, 6, 0:Q], snew[:, b, :], ALU.max))
                mb = M_b[:, :].rearrange("p (n h) -> p n h", h=H)
                p4 = prob[:, 0:n].rearrange("p (n g h) -> p n g h", n=NS, h=H)
                for g in range(G):
                    v.tensor_tensor(p4[:, :, g, :], s4[:, :, g, :], mb, ALU.subtract)
                v.tensor_tensor(pnew[:, :], snew[:, b, :], M_b[:, :], ALU.subtract).then_inc(z["sub"], 1)

            def combine(b):
                dve.wait_ge(z["av"], b + 1)
                vn = newT[:, 2 * b + 1, :].rearrange("d (n o) -> d n o", o=1).broadcast_to([HD, NS, H])
                ob3 = o_b[:, :].rearrange("d (n h) -> d n h", h=H)
                link(v.tensor_tensor(ob3, pnew[0:HD, :].rearrange("d (n h) -> d n h", h=H), vn, ALU.mult))
                link(v.tensor_tensor(o_b[:, :], k.ps[0:HD, 7, 0:Q], o_b[:, :], ALU.add))
                link(v.tensor_tensor(l_b[:, :], k.ps[0:HD, 5, 0:Q], pnew[0:HD, :], ALU.add))
                link(v.reciprocal(l_b[:, :], l_b[:, :]))
                link(v.tensor_tensor(o_b[:, :], o_b[:, :], l_b[:, :], ALU.mult))
                link(v.tensor_tensor(ob3, ob3, gts[:, :, 1 + b:12:3], ALU.mult))
                v.tensor_tensor(o_sum[:, :], o_sum[:, :], o_b[:, :], ALU.add).then_inc(z["comb"], 1)
                dve.wait_ge(z["comb"], b + 1)

            softmax(0, PAGES)
            combine(0)
            softmax(1, GW)
            combine(1)
            o3 = o_sum[:, :].rearrange("d (n h) -> d n h", h=H)
            for h in range(H):
                r = slice((h % 2) * HD, (h % 2 + 1) * HD)
                last = v.tensor_copy(o_ch[r, h // 2, :], o3[:, :, h])
            last.then_inc(z["och"], 1)
            dve.wait_ge(z["och"], 1)
            for j in range(2):
                y = k.yT[6 + j][:, T:TT]
                v.tensor_tensor(y, y, o_ch[:, j, :], ALU.mult)


def stage_output(nc, k, sem):
    with ExitStack() as ctx:
        def sb(name, shape, dt=F32):
            return ctx.enter_context(nc.sbuf_tensor(name, shape, dt))
        w_out = sb("w_out_s", [P, KT, D])
        x_in = sb("x_in2", [P, 3, D])
        y_out = sb("y_out", [P, 3, D])
        ys = sb("ys", [NS, D])
        xs = sb("xs", [NS, D])
        w_in, x_s, s_mm, s_v, gated, mm, added, stored, y_s = (sem("o_" + n) for n in ("w_in", "x_s", "s_mm", "s_v", "gated", "mm", "added", "stored", "y_s"))
        x_r = [sem(f"o_x{i}") for i in range(3)]
        out_r = [sem(f"o_stored{i}") for i in range(3)]
        block = ctx.enter_context(nc.Block())
        ROW = {0: 2, 1: 3, 2: 0, 3: 1, 4: 4, 5: 5, 6: 6, 7: 7}

        @block.sync
        def _(sp):
            for i in range(KT):
                sp.dma_start(w_out[:, i, :], k.io["w_out"][0, ROW[i] * P:(ROW[i] + 1) * P, :]).then_inc(w_in, 16)
            sp.dma_start(xs[:, :], k.io["x_sample"][:, 0, :]).then_inc(x_s, 16)
            for t in range(NC):
                if t >= 3:
                    sp.wait_ge(added, t - 2)
                sp.dma_start(x_in[:, t % 3, :], k.io["x_prompt"][0, t * P:(t + 1) * P, :]).then_inc(x_r[t % 3], 16)

        @block.scalar
        def _(act):
            act.wait_ge(y_s, 1)
            act.dma_start(k.io["y_sample"][:, 0, :], ys[:, :]).then_inc(stored, 16)
            for t in range(NC):
                act.wait_ge(added, t + 1)
                act.dma_start(k.io["y_prompt"][0, t * P:(t + 1) * P, :], y_out[:, t % 3, :]).then_inc(out_r[t % 3], 16)
            act.wait_ge(stored, 16)
            for i in range(3):
                act.wait_ge(out_r[i], 16 * len(range(i, NC, 3)))

        @block.tensor
        def _(pe):
            m = nc.tensor
            pe.wait_ge(w_in, 16 * KT)
            for half in range(2):
                for i in range(KT):
                    last = m.matmul(k.ps[0:NS, half, :], k.yT[i][:, T:TT], w_out[:, i, half * 512:(half + 1) * 512], start=(i == 0), stop=(i == KT - 1))
            last.then_inc(s_mm, 1)
            pe.wait_ge(gated, KT)
            for t in range(NC):
                if t >= 2:
                    pe.wait_ge(added, t - 1)
                for half in range(2):
                    for i in range(KT):
                        last = m.matmul(k.ps[:, 2 + 2 * (t % 2) + half, :], k.yT[i][:, t * P:(t + 1) * P], w_out[:, i, half * 512:(half + 1) * 512],
                                        start=(i == 0), stop=(i == KT - 1))
                last.then_inc(mm, 1)

        @block.vector
        def _(dve):
            v = nc.vector
            dve.wait_ge(s_mm, 1)
            for i in range(KT):
                v.tensor_tensor(w_out[:, i, :], w_out[:, i, :], k.gate_p[:, :], ALU.mult).then_inc(gated, 1)
            v.tensor_tensor(ys[:, 0:512], k.ps[0:NS, 0, :], k.gate_s[:, 0:512], ALU.mult)
            v.tensor_tensor(ys[:, 512:D], k.ps[0:NS, 1, :], k.gate_s[:, 512:D], ALU.mult).then_inc(s_v, 1)
            dve.wait_ge(x_s, 16)
            dve.wait_ge(s_v, 1)
            v.tensor_tensor(ys[:, :], ys[:, :], xs[:, :], ALU.add).then_inc(y_s, 1)
            for t in range(NC):
                dve.wait_ge(mm, t + 1)
                dve.wait_ge(x_r[t % 3], 16 * (t // 3 + 1))
                if t >= 3:
                    dve.wait_ge(out_r[t % 3], 16 * (t // 3))
                for half in range(2):
                    c = slice(half * 512, (half + 1) * 512)
                    last = v.tensor_tensor(y_out[:, t % 3, c], k.ps[:, 2 + 2 * (t % 2) + half, :], x_in[:, t % 3, c], ALU.add)
                last.then_inc(added, 1)


_INS = ['x_prompt', 'x_sample', 'cache_kv', 'cache_win', 'state_sconv', 'state_ssm_conv', 'state_ssm', 'state_cconv',
        'page_table', 'c_prompt', 'c_sample', 'norm_g', 'w_ada', 'b_ada', 'w_in', 'w_out', 'sc_w', 'ssd_conv_w', 'ssd_conv_b',
        'ssd_dt_bias', 'ssd_A_log', 'ssd_D', 'ssd_norm_g', 'cf_w', 'cf_b', 'cf_ln_g', 'cf_ln_b', 'q_g', 'k_g',
        'cmp_pe', 'cmp_w1', 'cmp_b1', 'cmp_w2', 'cmp_b2']
_OUTS = [('y_prompt', (1, T, D)), ('y_sample', (NS, 1, D)), ('kv_p', (1, NC, P, 4, HD)), ('kv_s', (1, NS, 1, 4, HD)),
         ('win_p', (1, 1, 512, 2, HD)), ('win_s', (1, NS, 512, 2, HD)), ('sconv_p', (1, 1, 2, W)), ('sconv_s', (1, NS, 2, W)),
         ('ssm_conv_p', (1, 1, 3, CV)), ('ssm_conv_s', (1, NS, 3, CV)), ('ssm_p', (1, 1, SH, SP, SST)),
         ('ssm_s', (1, NS, SH, SP, SST)), ('cconv_p', (1, 1, KCF - 1, W)), ('cconv_s', (1, NS, KCF - 1, W))]


def build(nc, k):
    with ExitStack() as ctx:
        def sb(name, shape):
            return ctx.enter_context(nc.sbuf_tensor(name, shape, F32))

        stores = {name: ctx.enter_context(nc.semaphore(name)) for name in
                  ("xstored", "s_stored", "c_stored", "t_stored", "o_stored", "o_stored0", "o_stored1", "o_stored2")}

        def run(stage):
            own = []

            def sem(name):
                if name in stores:
                    return stores[name]
                own.append(nc.alloc_semaphore(name))
                return own[-1]
            stage(nc, k, sem)
            nc.clear_and_free_semaphores(own)
            nc.all_engine_barrier()
        k.ps = ctx.enter_context(nc.psum_tensor("ps", [P, 8, GT], F32))
        k.scores_ps = k.ps[:, 0:4, :].rearrange("p b n -> p (b n)")
        k.ones, k.ident, k.upper, k.below, k.causal, k.win_low = (
            sb(name, [P, P]) for name in ("ones", "ident", "upper", "below", "causal", "win_low"))
        k.neg_upper, k.low_T = sb("neg_upper", [P, SH * P]), sb("low_T", [P, SH * P])
        k.cmp_mask = sb("cmp_mask", [P, 2 * P])
        k.sel_mask = sb("sel_mask", [P, 2 * NBLK])
        k.head_pick = sb("head_pick", [SH, 2, P])
        k.par = sb("par", [P, PEND])
        k.shift, k.scale = sb("shift", [P, KT, NS + 1]), sb("scale", [P, KT, NS + 1])
        k.gate_s, k.gate_p = sb("gate_s", [NS, D]), sb("gate_p", [P, D])
        k.dt = sb("dt", [P, (NC + 1) * SH])
        k.tails_T = sb("tails_T", [P, 6, 3 + NS])
        y_ssd = sb("y_ssd", [P, 2, TT])
        arena = sb("arena", [P, 6, TT])
        k.xbc = arena
        k.yT = [y_ssd[:, j, :] for j in range(2)] + [arena[:, j, :] for j in range(6)]
        hold = ctx.enter_context(ExitStack())
        h_space = hold.enter_context(nc.sbuf_tensor("h_space", [P, KT * TT], F32))
        k.hT = h_space[:, :].rearrange("p (k t) -> p k t", k=KT)

        def hview(start, size):
            return h_space[:, start:start + size]
        k.hview = hview
        k.extra_dram = nc.dram_tensor("extra_rows", (2, NBLK + 2, T), F32, kind="Internal").ap()
        run(stage_prepare)
        run(stage_norm)
        run(stage_ssd_inputs)
        run(stage_ssd)
        run(stage_ssd_norm)
        with nc.sbuf_tensor("conf", [P, 2, TT], F32) as conf:
            k.conf = conf
            run(stage_convs)
            run(stage_conformer_norm)
        def right(name, shape):
            return ctx.enter_context(nc.sbuf_tensor(name, shape, F32, side="right"))
        k.tm = right("tm", [P, NC + 1, TM])
        run(stage_token_major)
        hold.close()
        k.kcT, k.vc = right("kcT", [HD, 1 + NS, P]), right("vc", [P, 1 + NS, HD])
        with ExitStack() as held:
            k.keys = [[held.enter_context(nc.sbuf_tensor(f"keys_{b}_{part}", [P, T], mybir.dt.float32r)) for part in ("hi", "lo")]
                      for b in ("sel", "win")]
            run(stage_compress)
            k.va = held.enter_context(nc.sbuf_tensor("values", [P, NC, 2, HD + 1], F32))
            k.biasT = held.enter_context(nc.sbuf_tensor("bias_T", [P, T], F32))
            run(stage_choice)
            run(stage_attention)
        run(stage_sample_attention)
        run(stage_output)


def kernel(**inputs):
    import numpy as np
    import concourse.bacc as bacc
    from concourse.bass_utils import run_bass_kernel_spmd

    nc = bacc.Bacc("TRN2", target_bir_lowering=False, num_devices=1)
    arrays, tensors = {}, {}
    for name in _INS:
        a = np.ascontiguousarray(inputs[name])
        arrays["in_" + name] = a
        tensors[name] = nc.dram_tensor("in_" + name, a.shape, mybir.dt.from_np(a.dtype), kind="ExternalInput").ap()
    for name, shape in _OUTS:
        tensors[name] = nc.dram_tensor("out_" + name, shape, F32, kind="ExternalOutput").ap()
    k = Shared(tensors)
    k.n_pool = inputs["cache_kv"].shape[1]
    build(nc, k)
    r = run_bass_kernel_spmd(nc, [arrays], core_ids=[0])
    return tuple(r.results[0]["out_" + name] for name, _ in _OUTS)
```

```python
from contextlib import ExitStack

import concourse.bass as bass
from concourse import mybir

F32 = mybir.dt.float32
I32 = mybir.dt.int32
ALU = mybir.AluOpType
ACT = mybir.ActivationFunctionType
AX = mybir.AxisListType

P = 128
D = 1024
KT = D // P
W = 256
T = 2048
NC = T // P
NS = 8
TT = T + NS
GT = 512
NG = T // GT
SH, SP, SST = 4, 64, 128
CV = 768
KCF = 31
H, HD = 4, 64
PAST = 2048
PAGES = PAST // P
NCMP = T // 16 - 1
NBLK = T // 64
EPS = 1e-6
NEG = -1e30
BIG = 1e30
SCALE = HD ** -0.5

COL_A = 0
COL_Z = 4 * W
COL_XBC = COL_Z + W
COL_DT = COL_XBC + CV
COL_GLU = COL_DT + SH
COL_CG = COL_GLU + 2 * W
COL_Q = COL_CG + W
COL_KV = COL_Q + W
COL_DG = COL_KV + 6 * HD
COL_BG = COL_DG + W
TM = W + 6 * HD + 3 * H

PA_ROWS, PB_ROWS, PC_ROWS = 5, 38, 4
PA = 0
PB = PA + 6 * PA_ROWS
PC = PB + 2 * PB_ROWS
PEND = PC + 8 * PC_ROWS
B_SC, B_CF, B_CFB, B_LNG, B_LNB, B_SSDG = 0, 3, 34, 35, 36, 37


class Shared:

    def __init__(self, io):
        self.io = io


def chain(eng, sem):
    count = [0]

    def link(ins):
        count[0] += 1
        ins.then_inc(sem, 1)
        eng.wait_ge(sem, count[0])
    return link


def stage_prepare(nc, k, sem):
    NV = NS + 1
    WB = 512
    NB = 3 * D // WB
    NW = 3
    with ExitStack() as ctx:
        def sb(name, shape, dt=F32):
            return ctx.enter_context(nc.sbuf_tensor(name, shape, dt))
        c_rows, c_silu = sb("c_rows", [NV, D]), sb("c_silu", [NV, D])
        rows_a, rows_b, rows_c = sb("rows_a", [PA_ROWS, CV]), sb("rows_b", [PB_ROWS, W]), sb("rows_c", [PC_ROWS, D])
        cT = sb("cT", [P, KT, NV])
        w_ada = k.hview(0, NW * KT * WB).rearrange("p (b k n) -> p b k n", b=NW, k=KT)
        pick_prompt = sb("pick_prompt", [NV, P])
        b_gate = sb("b_gate", [NV, D])
        gates = sb("gates", [NV, D])
        extra = k.xbc[0:NBLK + 2, :, :].rearrange("p j t -> p (j t)")
        blk_rows, win_rows = extra[:, 0:T], extra[:, T:2 * T]
        ada_rows = extra[0:NV, 2 * T:2 * T + 2 * D]
        rows_cp, ada_tr = sem("ada_rows_cp"), sem("ada_tr")
        rows_in, c_in, bg_in, silu_done, tr_done, cp_done, w_used, ada_done, gate_done, gsum_done, bc_done, g_done = (
            sem(n) for n in ("rows_in", "c_in", "bg_in", "csilu", "ptr_done", "pcp_done", "wada_used",
                             "ada_done", "gate_done", "gsum_done", "bc_done", "pconst_done"))
        w_in = [sem(f"wada_in{i}") for i in range(NW)]
        blk_sent = sem("blk_sent")
        block = ctx.enter_context(nc.Block())
        par_ps, cT_ps = k.ps[:, 0, 0:PEND], k.ps[:, 1, 0:KT * NV]
        ada_ps = k.ps[:, 2, 0:2 * KT * NV]

        def load(eng, which):
            for b in which:
                if b >= NW:
                    eng.wait_ge(w_used, b - NW + 1)
                eng.dma_start(w_ada[:, b % NW], k.io["w_ada"][0].rearrange("(k p) n -> p k n", p=P)[:, :, b * WB:(b + 1) * WB]
                              ).then_inc(w_in[b % NW], 16)

        @block.sync
        def _(sp):
            sp.dma_start(c_rows[0:NS, :], k.io["c_sample"]).then_inc(c_in, 16)
            sp.dma_start(c_rows[NS:NV, :], k.io["c_prompt"]).then_inc(c_in, 16)
            load(sp, range(0, NB, 2))

        @block.scalar
        def _(act):
            sc = k.io["sc_w"][0], k.io["cf_w"][0]
            act.dma_start(rows_a[0:4, :], k.io["ssd_conv_w"][0]).then_inc(rows_in, 16)
            act.dma_start(rows_a[4:5, :], k.io["ssd_conv_b"]).then_inc(rows_in, 16)
            act.dma_start(rows_b[B_SC:B_SC + 3, :], sc[0]).then_inc(rows_in, 16)
            act.dma_start(rows_b[B_CF:B_CF + KCF, :], sc[1]).then_inc(rows_in, 16)
            for r, a in ((B_CFB, k.io["cf_b"]), (B_LNG, k.io["cf_ln_g"]), (B_LNB, k.io["cf_ln_b"]), (B_SSDG, k.io["ssd_norm_g"])):
                act.dma_start(rows_b[r:r + 1, :], a).then_inc(rows_in, 16)
            act.dma_start(rows_c[0:1, :], k.io["norm_g"]).then_inc(rows_in, 16)
            act.dma_start(rows_c[1:4, :], k.io["b_ada"][0].rearrange("(r d) -> r d", r=3)).then_inc(rows_in, 16)
            act.dma_start(b_gate[:, :], k.io["b_ada"][0:1, 2 * D:3 * D].broadcast_to([NV, D])).then_inc(bg_in, 16)
            act.wait_ge(c_in, 32)
            nc.scalar.activation(c_silu[:, :], c_rows[:, :], ACT.Silu).then_inc(silu_done, 1)
            load(act, range(1, NB, 2))

        @block.gpsimd
        def _(pool):
            g = nc.gpsimd
            link = chain(pool, g_done)
            link(g.memset(k.ones[:, :], 1.0))

            def select(t, src, pattern, base, mult, fill, op=ALU.is_ge):
                link(g.affine_select(out=t, in_=src, pattern=pattern, compare_op=op, fill=fill, base=base,
                                     channel_multiplier=mult))
            one = k.ones[:, :]
            select(k.ident[:, :], one, [[-1, P]], 0, 1, 0.0, ALU.is_equal)
            select(k.upper[:, :], one, [[1, P]], 0, -1, 0.0)
            select(k.below[:, :], one, [[-1, P]], -1, 1, 0.0)
            link(g.memset(k.neg_upper[:, :], 0.0))
            for h in range(SH):
                v = k.neg_upper[:, h * P:(h + 1) * P]
                select(v, v, [[1, P]], 0, -1, NEG)
            link(g.memset(k.causal[:, :], 0.0))
            select(k.causal[:, :], k.causal[:, :], [[-1, P]], 0, 1, NEG)
            link(g.memset(k.win_low[:, :], 0.0))
            select(k.win_low[:, :], k.win_low[:, :], [[1, P]], 0, -1, NEG)
            link(g.memset(k.cmp_mask[:, :], 0.0))
            select(k.cmp_mask[:, :], k.cmp_mask[:, :], [[-16, 2 * P]], 16 * P - 31, 1, NEG)
            link(g.memset(k.sel_mask[:, :], BIG))
            select(k.sel_mask[:, :], k.sel_mask[:, :], [[64, 2 * NBLK]], 64 * (2 - NBLK) - 1, -1, 0.0)
            select(k.sel_mask[:, :], k.sel_mask[:, :], [[-64, 2 * NBLK]], 64 * NBLK, 1, NEG)
            link(g.memset(blk_rows[:, :], 1.0))
            select(blk_rows[:, :], blk_rows[:, :], [[1, T]], 0, -64, 0.0)
            select(blk_rows[:, :], blk_rows[:, :], [[-1, T]], 63, 64, 0.0)
            link(g.memset(blk_rows[NBLK:NBLK + 1, :], 1.0))
            link(g.memset(win_rows[:, :], 1.0))
            select(win_rows[:, :], win_rows[:, :], [[0, T]], -NBLK - 1, 1, 0.0)
            pool.dma_start(k.extra_dram[0], blk_rows[:, :]).then_inc(blk_sent, 16)
            pool.dma_start(k.extra_dram[1], win_rows[:, :]).then_inc(blk_sent, 16)
            link(g.memset(k.low_T[:, :], 0.0))
            for h in range(SH):
                v = k.low_T[:, h * P:(h + 1) * P]
                select(v, v, [[-1, P]], 0, 1, NEG)
            link(g.memset(pick_prompt[:, :], 1.0))
            select(pick_prompt[:, :], pick_prompt[:, :], [[0, P]], -NS, 1, 0.0)
            for j in range(2):
                v = k.head_pick[:, j, :]
                link(g.memset(v, 1.0))
                select(v, v, [[1, P]], 2 * j * SP, -SP, 0.0)
                select(v, v, [[-1, P]], -2 * j * SP + SP - 1, SP, 0.0)
            pool.wait_ge(blk_sent, 32)

        n_const = 1 + 3 + 1 + SH + 2 + 2 + 2 + 3 + 3 + 3 + 1 + SH + 2 + 6

        @block.tensor
        def _(pe):
            m = nc.tensor
            pe.wait_ge(g_done, 2)
            pe.wait_ge(rows_in, 160)
            for n in range(6):
                m.transpose(par_ps[:, PA + n * PA_ROWS:PA + (n + 1) * PA_ROWS], rows_a[:, n * P:(n + 1) * P],
                            k.ident[0:PA_ROWS, 0:PA_ROWS])
            for n in range(2):
                m.transpose(par_ps[:, PB + n * PB_ROWS:PB + (n + 1) * PB_ROWS], rows_b[:, n * P:(n + 1) * P],
                            k.ident[0:PB_ROWS, 0:PB_ROWS])
            for n in range(8):
                last = m.transpose(par_ps[:, PC + n * PC_ROWS:PC + (n + 1) * PC_ROWS], rows_c[:, n * P:(n + 1) * P],
                                   k.ident[0:PC_ROWS, 0:PC_ROWS])
            last.then_inc(tr_done, 1)
            pe.wait_ge(silu_done, 1)
            for n in range(KT):
                last = m.transpose(cT_ps[:, n * NV:(n + 1) * NV], c_silu[:, n * P:(n + 1) * P], k.ident[0:NV, 0:NV])
            last.then_inc(tr_done, 1)
            pe.wait_ge(cp_done, 2)
            for b in range(NB):
                pe.wait_ge(w_in[b % NW], 16 * (b // NW + 1))
                for kk in range(KT):
                    last = m.matmul(k.ps[0:NV, (3 + b) % 8, :], cT[:, kk, :], w_ada[:, b % NW, kk, :],
                                    start=(kk == 0), stop=(kk == KT - 1))
                last.then_inc(w_used, 1)
            pe.wait_ge(rows_cp, 4)
            for n in range(2 * KT):
                last = m.transpose(ada_ps[:, n * NV:(n + 1) * NV], ada_rows[:, n * P:(n + 1) * P], k.ident[0:NV, 0:NV])
            last.then_inc(ada_tr, 1)
            pe.wait_ge(g_done, n_const)
            pe.wait_ge(gsum_done, 1)
            for n in range(2):
                last = m.matmul(k.ps[:, 5 + n, :], pick_prompt[:, :], gates[:, n * 512:(n + 1) * 512], start=True, stop=True)
            last.then_inc(bc_done, 1)

        @block.vector
        def _(dve):
            v = nc.vector
            dve.wait_ge(tr_done, 1)
            v.tensor_copy(k.par[:, :], par_ps).then_inc(cp_done, 1)
            dve.wait_ge(tr_done, 2)
            v.tensor_copy(cT[:, :, :].rearrange("p k n -> p (k n)"), cT_ps).then_inc(cp_done, 1)
            for b in range(4):
                dve.wait_ge(w_used, b + 1)
                v.tensor_copy(ada_rows[:, b * WB:(b + 1) * WB], k.ps[0:NV, 3 + b, :]).then_inc(rows_cp, 1)
            dve.wait_ge(ada_tr, 1)
            dve.wait_ge(cp_done, 2)
            pc = k.par[:, PC:PEND].rearrange("p (n r) -> p n r", r=PC_ROWS)
            ada = ada_ps.rearrange("p (n v) -> p n v", v=NV)
            v.tensor_tensor(k.shift[:, :, :], ada[:, 0:KT, :], pc[:, :, 1:2].broadcast_to([P, KT, NV]), ALU.add)
            link = chain(dve, ada_done)
            link(v.tensor_tensor(k.scale[:, :, :], ada[:, KT:2 * KT, :], pc[:, :, 2:3].broadcast_to([P, KT, NV]), ALU.add))
            link(v.tensor_scalar(k.scale[:, :, :], k.scale[:, :, :], 1.0, None, ALU.add))
            link(v.tensor_tensor(k.scale[:, :, :], k.scale[:, :, :], pc[:, :, 0:1].broadcast_to([P, KT, NV]), ALU.mult))
            dve.wait_ge(w_used, NB)
            dve.wait_ge(bg_in, 16)
            link(v.tensor_tensor(gates[:, 0:512], k.ps[0:NV, 7, :], b_gate[:, 0:512], ALU.add))
            v.tensor_tensor(gates[:, 512:D], k.ps[0:NV, 0, :], b_gate[:, 512:D], ALU.add).then_inc(gsum_done, 1)
            dve.wait_ge(gsum_done, 1)
            v.tensor_copy(k.gate_s[:, :], gates[0:NS, :])
            dve.wait_ge(bc_done, 1)
            v.tensor_copy(k.gate_p[:, 0:512], k.ps[:, 5, :])
            v.tensor_copy(k.gate_p[:, 512:D], k.ps[:, 6, :])


def stage_norm(nc, k, sem):
    NX = 3
    with ExitStack() as ctx:
        def sb(name, shape, dt=F32):
            return ctx.enter_context(nc.sbuf_tensor(name, shape, dt))
        x_in = sb("x_in", [P, NX, D])
        x_n = sb("x_n", [P, 2, D])
        junk = sb("junk", [P, D])
        stat = sb("stat", [P, NC + 1, 4])
        x_in0 = [sem(f"x_in{i}") for i in range(NX)]
        sq_done, var_done, root_done, xn_done, tr_done, ev_v, ev_a, link_s, aux = (
            sem(n) for n in ("sq_done", "var_done", "root_done", "xn_done", "xtr_done", "hev_v", "hev_a", "nlink", "naux"))
        block = ctx.enter_context(nc.Block())
        rows = [P] * NC + [NS]

        @block.sync
        def _(sp):
            for t in range(NC + 1):
                if t >= NX:
                    sp.wait_ge(xn_done, t - NX + 1)
                src = k.io["x_prompt"][0, t * P:(t + 1) * P, :] if t < NC else k.io["x_sample"][:, 0, :]
                sp.dma_start(x_in[0:rows[t], t % NX, :], src).then_inc(x_in0[t % NX], 16)

        @block.scalar
        def _(act):
            def head(t):
                r = rows[t]
                act.wait_ge(x_in0[t % NX], 16 * (t // NX + 1))
                if t:
                    act.wait_ge(sq_done, t)
                nc.scalar.activation(junk[0:r, :], x_in[0:r, t % NX, :], ACT.Square,
                                     accum_out=stat[0:r, t, 0:1]).then_inc(sq_done, 1)
                act.wait_ge(var_done, t + 1)
                nc.scalar.activation(stat[0:r, t, 3:4], stat[0:r, t, 2:3], ACT.Sqrt).then_inc(root_done, 1)

            head(0)
            for t in range(NC):
                head(t + 1)
                act.wait_ge(tr_done, t + 1)
                for kk in range(4, 8):
                    last = nc.scalar.activation(k.hT[:, kk, t * P:(t + 1) * P], k.ps[:, 2 * (t % 2) + 1, (kk - 4) * P:(kk - 3) * P],
                                                ACT.Identity, bias=k.shift[:, kk, NS:NS + 1], scale=k.scale[:, kk, NS:NS + 1])
                last.then_inc(ev_a, 1)

        @block.tensor
        def _(pe):
            for t in range(NC + 1):
                r = rows[t]
                pe.wait_ge(xn_done, t + 1)
                if t >= 2:
                    pe.wait_ge(ev_v, t - 1)
                    pe.wait_ge(ev_a, t - 1)
                for kk in range(KT):
                    last = nc.tensor.transpose(k.ps[:, 2 * (t % 2) + kk // 4, (kk % 4) * r:(kk % 4 + 1) * r],
                                               x_n[0:r, t % 2, kk * P:(kk + 1) * P], k.ident[0:r, 0:r])
                last.then_inc(tr_done, 1)

        @block.vector
        def _(dve):
            v = nc.vector
            link = chain(dve, link_s)

            def head(t):
                r = rows[t]
                dve.wait_ge(sq_done, t + 1)
                link(v.tensor_scalar(stat[0:r, t, 1:2], stat[0:r, t, 0:1], 1.0 / D, EPS, ALU.mult, ALU.add))
                v.reciprocal(stat[0:r, t, 2:3], stat[0:r, t, 1:2]).then_inc(var_done, 1)
                dve.wait_ge(root_done, t + 1)
                if t >= 2:
                    dve.wait_ge(tr_done, t - 1)
                v.tensor_scalar(x_n[0:r, t % 2, :], x_in[0:r, t % NX, :], stat[0:r, t, 3:4], None,
                                ALU.mult).then_inc(xn_done, 1)

            head(0)
            for t in range(NC):
                head(t + 1)
                dve.wait_ge(tr_done, t + 1)
                for kk in range(4):
                    last = v.tensor_scalar(k.hT[:, kk, t * P:(t + 1) * P], k.ps[:, 2 * (t % 2), kk * P:(kk + 1) * P],
                                           k.scale[:, kk, NS:NS + 1], k.shift[:, kk, NS:NS + 1], ALU.mult, ALU.add)
                last.then_inc(ev_v, 1)
            dve.wait_ge(tr_done, NC + 1)
            for half in range(2):
                src = k.ps[:, 2 * (NC % 2) + half, 0:4 * NS].rearrange("p (k n) -> p k n", n=NS)
                dst = k.hT[:, 4 * half:4 * half + 4, T:TT]
                link(v.tensor_tensor(dst, src, k.scale[:, 4 * half:4 * half + 4, 0:NS], ALU.mult))
                link(v.tensor_tensor(dst, dst, k.shift[:, 4 * half:4 * half + 4, 0:NS], ALU.add))


def channel_projection(nc, k, eng, cols, w_buf, w_ready, used, unit_done, unit_free):
    for i, c in enumerate(cols):
        eng.wait_ge(w_ready[i % 2], 16 * (i // 2 + 1))
        for g in range(NG + 1):
            u = i * (NG + 1) + g
            if u >= 8:
                unit_free(eng, u - 8)
            n, t0 = (GT, g * GT) if g < NG else (NS, T)
            for kk in range(KT):
                last = nc.tensor.matmul(k.ps[:, u % 8, 0:n], w_buf[:, i % 2, kk, :], k.hT[:, kk, t0:t0 + n],
                                        start=(kk == 0), stop=(kk == KT - 1))
            last.then_inc(unit_done, 1)


def load_tiles(k, sp, cols, w_buf, w_ready, unit_done):
    for i, c in enumerate(cols):
        if i >= 2:
            sp.wait_ge(unit_done, (i - 1) * (NG + 1))
        sp.dma_start(w_buf[:, i % 2], k.io["w_in"][0].rearrange("(k p) n -> p k n", p=P)[:, :, c:c + P]).then_inc(w_ready[i % 2], 16)


def stage_ssd_inputs(nc, k, sem):
    cols = [COL_XBC + P * j for j in range(6)] + [COL_Z, COL_Z + P]
    NJ = 6
    with ExitStack() as ctx:
        def sb(name, shape, dt=F32):
            return ctx.enter_context(nc.sbuf_tensor(name, shape, dt))
        w_buf = sb("w_buf", [P, 2, KT, P])
        w_dt = sb("w_dt", [P, KT, SH])
        raw = sb("raw_xbc", [P, 2, 3 + TT])
        prev_rows = sb("prev_rows", [3 * NS, CV])
        prev = sb("prev_xbc", [P, 6, NS, 3])
        tail = sb("tail_xbc", [P, 2, 3 + NS])
        tails = sb("tails_xbc", [3 + NS, CV])
        dt_rows = k.xbc[0:SH, 5, :]
        w_ready = [sem("wx_ready0"), sem("wx_ready1")]
        dt_mm, dt_cp = sem("dt_mm"), sem("dt_cp")
        dt_in, prev_in, unit_done, evac, conv, silu, link_s, zero, prev_tr, prev_cp, tail_cp, tail_tr, tails_cp, stored, dt_done = (
            sem(n) for n in ("dt_in", "prev_in", "xunit", "xevac", "xconv", "xsilu", "xlink", "xzero", "xprev_tr", "xprev_cp",
                             "xtail_cp", "xtail_tr", "xtails_cp", "xstored", "dt_done"))
        block = ctx.enter_context(nc.Block())
        U = NG + 1

        @block.sync
        def _(sp):
            sp.dma_start(prev_rows[:, :], k.io["state_ssm_conv"][0].rearrange("s r c -> (s r) c")).then_inc(prev_in, 16)
            with nc.allow_non_contiguous_dma(reason="four columns of the projection"):
                sp.dma_start(w_dt[:, :, :], k.io["w_in"][0].rearrange("(k p) n -> p k n", p=P)[:, :, COL_DT:COL_DT + SH]).then_inc(dt_in, 16)
            load_tiles(k, sp, cols, w_buf, w_ready, unit_done)
            sp.dma_start(k.io["ssm_conv_s"][0, :, 0:2, :], k.io["state_ssm_conv"][0, :, 1:3, :]).then_inc(stored, 16)
            sp.wait_ge(tails_cp, 1)
            sp.dma_start(k.io["ssm_conv_p"][0, 0], tails[0:3, :]).then_inc(stored, 16)
            sp.dma_start(k.io["ssm_conv_s"][0, :, 2, :], tails[3:3 + NS, :]).then_inc(stored, 16)
            sp.wait_ge(stored, 48)

        @block.tensor
        def _(pe):
            m = nc.tensor
            pe.wait_ge(prev_in, 16)
            for j in range(NJ):
                last = m.transpose(k.ps[:, 7, j * 24:(j + 1) * 24], prev_rows[:, j * P:(j + 1) * P], k.ident[0:24, 0:24])
            last.then_inc(prev_tr, 1)
            pe.wait_ge(dt_in, 16)
            for g in range(U):
                n, t0 = (GT, g * GT) if g < NG else (NS, T)
                for kk in range(KT):
                    last = m.matmul(k.ps[0:SH, g, 0:n], w_dt[:, kk, :], k.hT[:, kk, t0:t0 + n], start=(kk == 0), stop=(kk == KT - 1))
                last.then_inc(dt_mm, 1)
            pe.wait_ge(dt_cp, U)
            for t in range(NC + 1):
                r = P if t < NC else NS
                last = m.transpose(k.ps[0:r, 6, t * SH:(t + 1) * SH], dt_rows[:, t * P:t * P + r], k.ident[0:SH, 0:SH])
            last.then_inc(dt_done, 1)
            pe.wait_ge(prev_cp, 3)

            def free(eng, u):
                eng.wait_ge(evac, u + 1)
            channel_projection(nc, k, pe, cols, w_buf, w_ready, None, unit_done, free)
            pe.wait_ge(evac, len(cols) * U)
            for j in range(NJ):
                pe.wait_ge(tail_cp, j + 1)
                m.transpose(k.ps[0:3 + NS, j // 4, (j % 4) * P:(j % 4 + 1) * P], k.tails_T[:, j, :], k.ident[:, :]).then_inc(tail_tr, 1)

        @block.scalar
        def _(act):
            for i in range(len(cols)):
                for g in range(U):
                    n, t0 = (GT, g * GT) if g < NG else (NS, T)
                    u = i * U + g
                    act.wait_ge(unit_done, u + 1)
                    if i < NJ:
                        if i >= 2 and g == 0:
                            act.wait_ge(conv, i - 1)
                            act.wait_ge(tail_cp, i - 1)
                        nc.scalar.copy(raw[:, i % 2, 3 + t0:3 + t0 + n], k.ps[:, u % 8, 0:n]).then_inc(evac, 1)
                    else:
                        nc.scalar.activation(k.yT[i - NJ][:, t0:t0 + n], k.ps[:, u % 8, 0:n], ACT.Silu).then_inc(evac, 1)
                if 1 <= i <= NJ:
                    act.wait_ge(conv, i)
                    b = PA + (i - 1) * PA_ROWS + 4
                    nc.scalar.activation(k.xbc[:, i - 1, :], k.xbc[:, i - 1, :], ACT.Silu, bias=k.par[:, b:b + 1]).then_inc(silu, 1)

        @block.vector
        def _(dve):
            v = nc.vector
            link = chain(dve, link_s)
            link(v.memset(raw[:, :, 0:3], 0.0))
            link(v.memset(k.dt[:, :], 0.0))
            dve.wait_ge(prev_tr, 1)
            v.tensor_copy(prev[:, :, :, :].rearrange("p j s r -> p (j s r)"), k.ps[:, 7, 0:6 * 24]).then_inc(prev_cp, 1)
            for g in range(U):
                n, t0 = (GT, g * GT) if g < NG else (NS, T)
                dve.wait_ge(dt_mm, g + 1)
                v.tensor_copy(dt_rows[:, t0:t0 + n], k.ps[0:SH, g, 0:n]).then_inc(dt_cp, 1)
            dve.wait_ge(dt_done, 1)
            v.tensor_copy(k.dt[:, 0:NC * SH], k.ps[:, 6, 0:NC * SH]).then_inc(prev_cp, 1)
            dve.wait_ge(prev_cp, 2)
            v.tensor_copy(k.dt[0:NS, NC * SH:(NC + 1) * SH], k.ps[0:NS, 6, NC * SH:(NC + 1) * SH]).then_inc(prev_cp, 1)
            dve.wait_ge(prev_cp, 3)
            for j in range(NJ):
                dve.wait_ge(evac, (j + 1) * U)
                wc = [k.par[:, PA + j * PA_ROWS + q:PA + j * PA_ROWS + q + 1] for q in range(4)]
                r = raw[:, j % 2, :]
                o = k.xbc[:, j, 0:T]
                link(v.tensor_scalar(o, r[:, 3:3 + T], wc[3], None, ALU.mult))
                for q in range(3):
                    link(v.scalar_tensor_tensor(out=o, in0=r[:, q:q + T], scalar=wc[q], in1=o, op0=ALU.mult, op1=ALU.add))
                s = k.xbc[:, j, T:TT]
                link(v.tensor_scalar(s, r[:, 3 + T:3 + TT], wc[3], None, ALU.mult))
                for q in range(3):
                    ins = v.scalar_tensor_tensor(out=s, in0=prev[:, j, :, q], scalar=wc[q], in1=s, op0=ALU.mult, op1=ALU.add)
                    if q < 2:
                        link(ins)
                    else:
                        ins.then_inc(conv, 1)
                v.tensor_copy(k.tails_T[:, j, :], r[:, T:3 + TT]).then_inc(tail_cp, 1)
            dve.wait_ge(tail_tr, NJ)
            link(v.tensor_copy(tails[:, 0:512], k.ps[0:3 + NS, 0, :]))
            v.tensor_copy(tails[:, 512:CV], k.ps[0:3 + NS, 1, 0:256]).then_inc(tails_cp, 1)


def stage_ssd(nc, k, sem):
    NT = (NC + 1) * SH
    with ExitStack() as ctx:
        def sb(name, shape, dt=F32):
            return ctx.enter_context(nc.sbuf_tensor(name, shape, dt))
        bias_b, a_neg, d_col = sb("dt_bias_b", [P, SH]), sb("a_neg", [P, SH]), sb("ssd_d_col", [P, 2])
        e_abs, u1, um, zero_m, lnu, da = (sb(n, [P, NT]) for n in ("e_abs", "u1", "um", "zero_m", "lnu", "da"))
        da_exp = sb("da_exp", [NS, SH])
        aU = sb("aU", [P, SH, P])
        dec = sb("dec", [P, 2, SH, P])
        grow = sb("grow", [P, 2, SH, P])
        xdt, xde = sb("xdt", [P, 2, SH, SP]), sb("xde", [P, SH, SP])
        b_tm = sb("b_tm", [P, 2, 2, P])
        mix = sb("mix", [P, SH, P])
        cgrow = sb("cgrow", [P, SH, P])
        state = sb("ssd_state", [P, SH, SP])
        y_sum = sb("y_sum", [P, 2, P])
        st_out = sb("st_out", [P, 2, P])
        h0 = sb("h0", [P, NS, P])
        diag = sb("diag", [P, NS, P])
        hb = sb("hb", [P, NS, P])
        dtT = sb("dtT", [SH, 2, NS])
        dtb = sb("dtb", [P, 2, 2, NS])
        y_s = sb("y_s", [P, NS])
        coef = sb("coef_s", [P, NS])
        small_in, h0_in, dt_a, dt_v, link_s, tr, bt, xd, au, logs, scr, expd, expg, mixd, cg, yd, stn, std, y_fin, fin_tr, fin_cp, stored = (
            sem("s_" + n) for n in ("small_in", "h0_in", "dt_a", "dt_v", "link", "tr", "bt", "xd", "au", "logs", "scr", "expd",
                                    "expg", "mixd", "cg", "yd", "stn", "std", "y_fin", "fin_tr", "fin_cp", "stored"))
        d_pe, d_v, d_alink, h_new = sem("s_d_pe"), sem("s_d_v"), sem("s_alink"), sem("s_h_new")
        h_used = sem("s_h_used")
        btp = k.ps[:, 6, :]
        block = ctx.enter_context(nc.Block())
        tp, sc_ps, log_ps, grow_ps, y_ps, new_ps = (k.ps[:, b, :] for b in range(6))

        @block.sync
        def _(sp):
            sp.dma_start(bias_b[:, :], k.io["ssd_dt_bias"].broadcast_to([P, SH])).then_inc(small_in, 16)
            sp.dma_start(a_neg[:, :], k.io["ssd_A_log"].broadcast_to([P, SH])).then_inc(small_in, 16)
            for h in range(SH):
                sp.dma_start(d_col[(h % 2) * SP:(h % 2 + 1) * SP, h // 2:h // 2 + 1],
                             k.io["ssd_D"][0:1, h:h + 1].broadcast_to([SP, 1])).then_inc(small_in, 16)
            for j in range(2):
                if j:
                    sp.wait_ge(stored, 16)
                    sp.wait_ge(h_used, 1)
                sp.dma_start(h0[:, :, :], k.io["state_ssm"][0].rearrange("n (j h) p s -> j (h p) n s", j=2)[j]).then_inc(h0_in, 16)
                sp.wait_ge(h_new, j + 1)
                sp.dma_start(k.io["ssm_s"][0].rearrange("n (j h) p s -> j (h p) n s", j=2)[j], h0[:, :, :]).then_inc(stored, 16)
            sp.wait_ge(fin_cp, 1)
            sp.dma_start(k.io["ssm_p"][0, 0].rearrange("(j h) p s -> (h p) j s", j=2), st_out[:, :, :]).then_inc(stored, 16)
            sp.wait_ge(stored, 48)

        @block.scalar
        def _(act):
            link = chain(act, d_alink)
            act.wait_ge(dt_v, 1)
            link(nc.scalar.activation(e_abs[:, :], k.dt[:, :], ACT.Abs))
            link(nc.scalar.activation(e_abs[:, :], e_abs[:, :], ACT.Exp, scale=-1.0))
            nc.scalar.activation(a_neg[:, :], a_neg[:, :], ACT.Exp).then_inc(dt_a, 1)
            act.wait_ge(dt_v, 2)
            nc.scalar.activation(lnu[:, :], u1[:, :], ACT.Ln).then_inc(dt_a, 1)
            act.wait_ge(dt_v, 3)
            nc.scalar.activation(da_exp[:, :], da[0:NS, NC * SH:NT], ACT.Exp).then_inc(dt_a, 1)
            for c in range(NC):
                act.wait_ge(tr, c + 1)
                if c >= 2:
                    act.wait_ge(stn, c - 1)
                nc.scalar.copy(b_tm[:, c % 2].rearrange("p g s -> p (g s)"), btp[:, 0:2 * P]).then_inc(bt, 1)
                act.wait_ge(logs, c + 1)
                if c >= 2:
                    act.wait_ge(std, c - 1)
                nc.scalar.activation(dec[:, c % 2].rearrange("p h l -> p (h l)"), log_ps, ACT.Exp).then_inc(expd, 1)
                nc.scalar.activation(grow[:, c % 2].rearrange("p h l -> p (h l)"), grow_ps, ACT.Exp).then_inc(expg, 1)

        @block.tensor
        def _(pe):
            m = nc.tensor

            def turn(c):
                if c:
                    pe.wait_ge(bt, c)
                    pe.wait_ge(xd, c)
                for j in range(4):
                    last = m.transpose((tp if j < 2 else btp)[:, (j % 2) * P:(j % 2 + 1) * P], k.xbc[:, j, c * P:(c + 1) * P], k.ident[:, :])
                last.then_inc(tr, 1)

            def decays(c):
                pe.wait_ge(au, c + 1)
                if c:
                    pe.wait_ge(expg, c)
                m.matmul(log_ps, k.below[:, :], aU[:, :, :].rearrange("p h l -> p (h l)"), start=True, stop=False)
                m.matmul(log_ps, k.ident[:, :], k.neg_upper[:, :], start=False, stop=True)
                m.matmul(grow_ps, k.ones[:, :], aU[:, :, :].rearrange("p h l -> p (h l)"), start=True, stop=True).then_inc(logs, 1)

            turn(0)
            decays(0)
            for c in range(NC):
                t0 = c * P
                if c:
                    pe.wait_ge(mixd, c)
                for g in range(2):
                    last = m.matmul(sc_ps[:, g * P:(g + 1) * P], k.xbc[:, 2 + g, t0:t0 + P], k.xbc[:, 4 + g, t0:t0 + P],
                                    start=True, stop=True)
                last.then_inc(scr, 1)
                if c + 1 < NC:
                    turn(c + 1)
                    decays(c + 1)
                pe.wait_ge(mixd, c + 1)
                pe.wait_ge(cg, c + 1)
                if c:
                    pe.wait_ge(yd, c)
                for h in range(SH):
                    o = y_ps[(h % 2) * SP:(h % 2 + 1) * SP, (h // 2) * P:(h // 2 + 1) * P]
                    m.matmul(o, xdt[:, c % 2, h, :], mix[:, h, :], start=True, stop=(c == 0))
                    if c:
                        m.matmul(o, state[:, h, :], cgrow[:, h, :], start=False, stop=True)
                for g in range(2):
                    last = m.matmul(new_ps[:, g * P:(g + 1) * P], b_tm[:, c % 2, g, :], xde[:, 2 * g:2 * g + 2, :].rearrange("p h s -> p (h s)"),
                                    start=True, stop=True)
                last.then_inc(stn, 1)
            pe.wait_ge(std, NC)
            for j in range(2):
                last = m.transpose(new_ps[:, j * P:(j + 1) * P], state[:, 2 * j:2 * j + 2, :].rearrange("p h s -> p (h s)"), k.ident[:, :])
            last.then_inc(fin_tr, 1)
            m.transpose(sc_ps[0:SH, 0:NS], k.dt[0:NS, NC * SH:NT], k.ident[0:NS, 0:NS])
            pe.wait_ge(dt_a, 3)
            m.transpose(sc_ps[0:SH, NS:2 * NS], da_exp[:, :], k.ident[0:NS, 0:NS]).then_inc(d_pe, 1)
            pe.wait_ge(d_v, 1)
            for j in range(2):
                last = m.matmul(tp[:, j * 2 * NS:(j + 1) * 2 * NS], k.head_pick[0:SH, j, :], dtT[:, :, :].rearrange("h a n -> h (a n)"),
                                start=True, stop=True)
            last.then_inc(d_pe, 1)
            for n in range(4):
                pe.wait_ge(d_v, 3 + n)
                for half in range(2):
                    last = m.matmul(k.ps[:, 1 + half + 2 * (n % 2), :], k.ones[:, :],
                                    diag[:, 4 * half:4 * half + 4, :].rearrange("p n s -> p (n s)"), start=True, stop=True)
                last.then_inc(d_pe, 1)

        @block.vector
        def _(dve):
            v = nc.vector
            link = chain(dve, link_s)
            dve.wait_ge(small_in, 96)
            dt3 = k.dt[:, :].rearrange("p (t h) -> p t h", h=SH)
            v.tensor_tensor(dt3, dt3, bias_b[:, :].rearrange("p (o h) -> p o h", o=1).broadcast_to([P, NC + 1, SH]), ALU.add).then_inc(dt_v, 1)
            dve.wait_ge(dt_a, 1)
            v.tensor_scalar(u1[:, :], e_abs[:, :], 1.0, None, ALU.add).then_inc(dt_v, 1)
            dve.wait_ge(dt_v, 2)
            link(v.tensor_scalar(um[:, :], u1[:, :], -1.0, None, ALU.add))
            link(v.tensor_scalar(zero_m[:, :], um[:, :], 0.0, None, ALU.is_equal))
            link(v.tensor_tensor(um[:, :], um[:, :], zero_m[:, :], ALU.add))
            link(v.reciprocal(um[:, :], um[:, :]))
            dve.wait_ge(dt_a, 2)
            link(v.tensor_tensor(lnu[:, :], lnu[:, :], zero_m[:, :], ALU.add))
            link(v.tensor_tensor(lnu[:, :], lnu[:, :], um[:, :], ALU.mult))
            link(v.tensor_tensor(lnu[:, :], lnu[:, :], e_abs[:, :], ALU.mult))
            link(v.tensor_scalar(k.dt[:, :], k.dt[:, :], 0.0, None, ALU.max))
            link(v.tensor_tensor(k.dt[:, :], k.dt[:, :], lnu[:, :], ALU.add))
            link(v.tensor_scalar(a_neg[:, :], a_neg[:, :], -1.0, None, ALU.mult))
            da3 = da[:, :].rearrange("p (t h) -> p t h", h=SH)
            v.tensor_tensor(da3, dt3, a_neg[:, :].rearrange("p (o h) -> p o h", o=1).broadcast_to([P, NC + 1, SH]), ALU.mult).then_inc(dt_v, 1)
            dve.wait_ge(dt_v, 3)

            def steps(c):
                if c:
                    dve.wait_ge(logs, c)
                v.tensor_tensor(aU[:, :, :], k.upper[:, :].rearrange("p (o l) -> p o l", o=1).broadcast_to([P, SH, P]),
                                da3[:, c, :].rearrange("p (h o) -> p h o", o=1).broadcast_to([P, SH, P]), ALU.mult).then_inc(au, 1)

            def inputs(c):
                dve.wait_ge(tr, c + 1)
                v.tensor_tensor(xdt[:, c % 2], tp[:, 0:2 * P].rearrange("p (h s) -> p h s", h=SH),
                                k.dt[:, c * SH:(c + 1) * SH].rearrange("p (h o) -> p h o", o=1).broadcast_to([P, SH, SP]), ALU.mult).then_inc(xd, 1)

            steps(0)
            inputs(0)
            steps(1)
            for c in range(NC):
                dve.wait_ge(expd, c + 1)
                dve.wait_ge(scr, c + 1)
                dc, gc = dec[:, c % 2], grow[:, c % 2]
                for g in range(2):
                    last = v.tensor_tensor(mix[:, 2 * g:2 * g + 2, :], sc_ps[:, g * P:(g + 1) * P].rearrange("p (o l) -> p o l", o=1).broadcast_to([P, 2, P]),
                                           dc[:, 2 * g:2 * g + 2, :], ALU.mult)
                last.then_inc(mixd, 1)
                dve.wait_ge(xd, c + 1)
                v.tensor_tensor(xde[:, :, :], xdt[:, c % 2], dc[:, :, P - 1:P].broadcast_to([P, SH, SP]), ALU.mult)
                dve.wait_ge(expg, c + 1)
                for g in range(2):
                    last = v.tensor_tensor(cgrow[:, 2 * g:2 * g + 2, :],
                                           k.xbc[:, 4 + g, c * P:(c + 1) * P].rearrange("p (o l) -> p o l", o=1).broadcast_to([P, 2, P]),
                                           gc[:, 2 * g:2 * g + 2, :], ALU.mult)
                last.then_inc(cg, 1)
                if c + 1 < NC:
                    inputs(c + 1)
                if c + 2 < NC:
                    steps(c + 2)
                dve.wait_ge(stn, c + 1)
                for j in range(2):
                    last = v.scalar_tensor_tensor(out=y_sum[:, j, :], in0=k.xbc[:, j, c * P:(c + 1) * P], scalar=d_col[:, j:j + 1],
                                                  in1=y_ps[:, j * P:(j + 1) * P], op0=ALU.mult, op1=ALU.add)
                last.then_inc(yd, 1)
                if c:
                    link(v.tensor_tensor(state[:, :, :], state[:, :, :], gc[:, :, P - 1:P].broadcast_to([P, SH, SP]), ALU.mult))
                    v.tensor_tensor(state[:, :, :], state[:, :, :], new_ps[:, 0:2 * P].rearrange("p (h s) -> p h s", h=SH), ALU.add).then_inc(std, 1)
                else:
                    v.tensor_copy(state[:, :, :], new_ps[:, 0:2 * P].rearrange("p (h s) -> p h s", h=SH)).then_inc(std, 1)
                dve.wait_ge(yd, c + 1)
                for j in range(2):
                    y = k.yT[j][:, c * P:(c + 1) * P]
                    last = v.tensor_tensor(y, y_sum[:, j, :], y, ALU.mult)
                link(last)
                dve.wait_ge(std, c + 1)
            dve.wait_ge(fin_tr, 1)
            v.tensor_copy(st_out[:, :, :].rearrange("p j s -> p (j s)"), new_ps[:, 0:2 * P]).then_inc(fin_cp, 1)
            dve.wait_ge(d_pe, 1)
            v.tensor_copy(dtT[:, :, :].rearrange("h a n -> h (a n)"), sc_ps[0:SH, 0:2 * NS]).then_inc(d_v, 1)
            dve.wait_ge(d_pe, 2)
            v.tensor_copy(dtb[:, :, :, :].rearrange("p j a n -> p (j a n)"), tp[:, 0:4 * NS]).then_inc(d_v, 1)
            dve.wait_ge(d_v, 2)
            idb = k.ident[:, :].rearrange("p (o s) -> p o s", o=1).broadcast_to([P, NS, P])

            def spread(tile, n):
                if n:
                    dve.wait_ge(d_pe, 2 + n)
                v.tensor_tensor(diag[:, :, :], idb, k.xbc[:, tile, T:TT].rearrange("p (n o) -> p n o", o=1).broadcast_to([P, NS, P]),
                                ALU.mult).then_inc(d_v, 1)

            spread(2, 0)
            for j in range(2):
                xs = k.xbc[:, j, T:TT]
                spread(4 + j, 2 * j + 1)
                dve.wait_ge(h0_in, 16 * (j + 1))
                link(v.tensor_tensor(h0[:, :, :], h0[:, :, :], dtb[:, j, 1, :].rearrange("p (n o) -> p n o", o=1).broadcast_to([P, NS, P]), ALU.mult))
                link(v.tensor_tensor(coef[:, :], xs, dtb[:, j, 0, :], ALU.mult))
                cf = coef[:, :].rearrange("p (n o) -> p n o", o=1)
                for half in range(2):
                    ns = slice(4 * half, 4 * half + 4)
                    last = v.tensor_tensor(hb[:, ns, :], k.ps[:, 1 + half, :].rearrange("p (n s) -> p n s", s=P),
                                           cf[:, ns, :].broadcast_to([P, 4, P]), ALU.mult)
                link(last)
                v.tensor_tensor(h0[:, :, :], h0[:, :, :], hb[:, :, :], ALU.add).then_inc(h_new, 1)
                dve.wait_ge(h_new, j + 1)
                dve.wait_ge(d_pe, 4 + 2 * j)
                if j == 0:
                    spread(3, 2)
                for half in range(2):
                    ns = slice(4 * half, 4 * half + 4)
                    last = v.tensor_tensor(hb[:, ns, :], h0[:, ns, :], k.ps[:, 3 + half, :].rearrange("p (n s) -> p n s", s=P), ALU.mult)
                last.then_inc(h_used, 1)
                dve.wait_ge(h_used, j + 1)
                link(v.tensor_reduce(y_s[:, :], hb[:, :, :], AX.X, ALU.add))
                link(v.scalar_tensor_tensor(out=y_s[:, :], in0=xs, scalar=d_col[:, j:j + 1], in1=y_s[:, :], op0=ALU.mult, op1=ALU.add))
                y = k.yT[j][:, T:TT]
                link(v.tensor_tensor(y, y_s[:, :], y, ALU.mult))


def column_sums(k, pe, m, src, out, n):
    for j in range(2):
        last = m.matmul(out, k.ones[:, :], src[j], start=(j == 0), stop=(j == 1))
    return last


def stage_ssd_norm(nc, k, sem):
    with ExitStack() as ctx:
        sq = ctx.enter_context(nc.sbuf_tensor("rms_sq", [P, 2, 2, GT], F32))
        inv = ctx.enter_context(nc.sbuf_tensor("rms_inv", [P, 2, GT], F32))
        sqd, summed, var, root, link_s = (sem("r_" + n) for n in ("sqd", "summed", "var", "root", "link"))
        block = ctx.enter_context(nc.Block())
        groups = [(g * GT, GT) for g in range(NG)] + [(T, NS)]

        @block.scalar
        def _(act):
            def square(g):
                t0, n = groups[g]
                if g >= 2:
                    act.wait_ge(summed, g - 1)
                for j in range(2):
                    last = nc.scalar.activation(sq[:, g % 2, j, 0:n], k.yT[j][:, t0:t0 + n], ACT.Square)
                last.then_inc(sqd, 1)
            square(0)
            for g, (t0, n) in enumerate(groups):
                if g + 1 < len(groups):
                    square(g + 1)
                act.wait_ge(var, g + 1)
                nc.scalar.activation(inv[:, g % 2, 0:n], inv[:, g % 2, 0:n], ACT.Sqrt).then_inc(root, 1)

        @block.tensor
        def _(pe):
            for g, (t0, n) in enumerate(groups):
                pe.wait_ge(sqd, g + 1)
                if g >= 2:
                    pe.wait_ge(var, g - 1)
                column_sums(k, pe, nc.tensor, [sq[:, g % 2, j, 0:n] for j in range(2)], k.ps[:, g % 2, 0:n], n).then_inc(summed, 1)

        @block.vector
        def _(dve):
            v = nc.vector
            link = chain(dve, link_s)
            for g, (t0, n) in enumerate(groups):
                dve.wait_ge(summed, g + 1)
                link(v.tensor_scalar(inv[:, g % 2, 0:n], k.ps[:, g % 2, 0:n], 1.0 / W, EPS, ALU.mult, ALU.add))
                v.reciprocal(inv[:, g % 2, 0:n], inv[:, g % 2, 0:n]).then_inc(var, 1)
                dve.wait_ge(root, g + 1)
                for j in range(2):
                    y = k.yT[j][:, t0:t0 + n]
                    b = PB + j * PB_ROWS + B_SSDG
                    last = v.scalar_tensor_tensor(out=y, in0=y, scalar=k.par[:, b:b + 1], in1=inv[:, g % 2, 0:n],
                                                  op0=ALU.mult, op1=ALU.mult)
                link(last)


def stage_convs(nc, k, sem):
    cols, kinds = [], []
    for j in range(2):
        cols += [COL_GLU + j * P, COL_GLU + W + j * P, COL_CG + j * P]
        kinds += [("u", j, 0), ("sig", j, 0), ("gate", j, 4)]
    for j in range(2):
        cols += [COL_A + j * P, COL_A + 2 * W + j * P, COL_A + W + j * P, COL_A + 3 * W + j * P]
        kinds += [("u", j, 2), ("v", j, 2), ("b", j, 2), ("gate", j, 2)]
    cols += [COL_DG, COL_DG + P]
    kinds += [("gate", 0, 6), ("gate", 1, 6)]
    U = NG + 1
    PADC = KCF - 1
    with ExitStack() as ctx:
        def sb(name, shape, dt=F32):
            return ctx.enter_context(nc.sbuf_tensor(name, shape, dt))
        w_buf = sb("w_buf2", [P, 2, KT, P])
        first = sb("first", [P, TT])
        second = sb("second", [P, TT])
        padded = sb("padded", [P, PADC + TT])
        acc = k.conf
        prev_rows = sb("prev_rows2", [120, 2, W])
        prev_a_rows = sb("prev_a_rows", [2 * NS, W])
        prev_c = sb("prev_c", [P, 2, NS * PADC])
        prev_a = sb("prev_a", [P, 2, NS, 2])
        prod = sb("prod_c", [P, NS, PADC])
        tailc = sb("tailc", [P, 2, PADC + NS])
        taila = sb("taila", [P, 2, 2 + NS])
        outc = sb("outc", [PADC + NS, W])
        outa = sb("outa", [2 + NS, W])
        w_ready = [sem("wc_ready0"), sem("wc_ready1")]
        prev_in, prev_tr, prev_cp, unit_done, evac, link_s, u_done, convd, tail_cp, tail_tr, tails_cp, stored, pad_free, gated = (
            sem("c_" + n) for n in ("prev_in", "prev_tr", "prev_cp", "unit", "evac", "link", "u_done", "convd", "tail_cp",
                                    "tail_tr", "tails_cp", "stored", "pad_free", "gated"))
        block = ctx.enter_context(nc.Block())

        @block.sync
        def _(sp):
            st = k.io["state_cconv"][0].rearrange("(a s) r c -> (s r) a c", a=2)
            sp.dma_start(prev_rows[:, :, :], st).then_inc(prev_in, 16)
            sp.dma_start(prev_a_rows[:, :], k.io["state_sconv"][0].rearrange("s r c -> (s r) c")).then_inc(prev_in, 16)
            load_tiles(k, sp, cols, w_buf, w_ready, unit_done)
            sp.dma_start(k.io["cconv_s"][0, :, 0:PADC - 1, :], k.io["state_cconv"][0, :, 1:PADC, :]).then_inc(stored, 16)
            sp.dma_start(k.io["sconv_s"][0, :, 0:1, :], k.io["state_sconv"][0, :, 1:2, :]).then_inc(stored, 16)
            sp.wait_ge(tails_cp, 1)
            sp.dma_start(k.io["cconv_p"][0, 0], outc[0:PADC, :]).then_inc(stored, 16)
            sp.dma_start(k.io["cconv_s"][0, :, PADC - 1, :], outc[PADC:PADC + NS, :]).then_inc(stored, 16)
            sp.dma_start(k.io["sconv_p"][0, 0], outa[0:2, :]).then_inc(stored, 16)
            sp.dma_start(k.io["sconv_s"][0, :, 1, :], outa[2:2 + NS, :]).then_inc(stored, 16)
            sp.wait_ge(stored, 96)

        @block.tensor
        def _(pe):
            m = nc.tensor
            pe.wait_ge(prev_in, 32)
            for j in range(2):
                for a in range(2):
                    m.transpose(k.ps[:, 7, (2 * j + a) * 120:(2 * j + a + 1) * 120], prev_rows[:, a, j * P:(j + 1) * P], k.ident[0:120, 0:120])
                last = m.transpose(k.ps[:, 6, j * 16:(j + 1) * 16], prev_a_rows[:, j * P:(j + 1) * P], k.ident[0:16, 0:16])
            last.then_inc(prev_tr, 1)
            pe.wait_ge(prev_cp, 2)

            def free(eng, u):
                eng.wait_ge(evac, u + 1)
            channel_projection(nc, k, pe, cols, w_buf, w_ready, None, unit_done, free)
            pe.wait_ge(evac, len(cols) * U)
            pe.wait_ge(tail_cp, 4)
            for j in range(2):
                m.transpose(k.ps[0:PADC + NS, 0, j * P:(j + 1) * P], tailc[:, j, :], k.ident[:, :])
                last = m.transpose(k.ps[0:2 + NS, 1, j * P:(j + 1) * P], taila[:, j, :], k.ident[:, :])
            last.then_inc(tail_tr, 1)

        @block.scalar
        def _(act):
            nu = 0
            nb = 0
            for i, (kind, j, y0) in enumerate(kinds):
                if kind == "u" and nu:
                    act.wait_ge(u_done, nu)
                if kind == "u" and y0 == 2 and j == 1:
                    act.wait_ge(convd, 3)
                for g in range(U):
                    n, t0 = (GT, g * GT) if g < NG else (NS, T)
                    u = i * U + g
                    act.wait_ge(unit_done, u + 1)
                    src = k.ps[:, u % 8, 0:n]
                    if kind == "u":
                        ins = nc.scalar.copy(first[:, t0:t0 + n], src)
                    elif kind == "v":
                        if g == 0 and j:
                            act.wait_ge(gated, j)
                        ins = nc.scalar.copy(second[:, t0:t0 + n], src)
                    elif kind == "sig":
                        ins = nc.scalar.activation(second[:, t0:t0 + n], src, ACT.Sigmoid)
                    elif kind == "b":
                        if g == 0:
                            act.wait_ge(u_done, nu)
                        ins = nc.scalar.copy(first[:, t0:t0 + n], src)
                    else:
                        ins = nc.scalar.activation(k.yT[y0 + j][:, t0:t0 + n], src, ACT.Silu)
                    ins.then_inc(evac, 1)
                if kind == "u":
                    nu += 1

        @block.vector
        def _(dve):
            v = nc.vector
            link = chain(dve, link_s)
            dve.wait_ge(prev_tr, 1)
            v.tensor_copy(prev_c[:, :, :].rearrange("p j n -> p (j n)"), k.ps[:, 7, 0:480]).then_inc(prev_cp, 1)
            v.tensor_copy(prev_a[:, :, :, :].rearrange("p j s r -> p (j s r)"), k.ps[:, 6, 0:32]).then_inc(prev_cp, 1)
            dve.wait_ge(prev_cp, 2)
            link(v.memset(padded[:, 0:PADC], 0.0))
            for j in range(2):
                cw = [k.par[:, PB + j * PB_ROWS + B_CF + q:PB + j * PB_ROWS + B_CF + q + 1] for q in range(KCF)]
                cb = PB + j * PB_ROWS + B_CFB
                dve.wait_ge(evac, (3 * j + 2) * U)
                v.tensor_tensor(padded[:, PADC:PADC + TT], first[:, :], second[:, :], ALU.mult).then_inc(u_done, 1)
                dve.wait_ge(u_done, j + 1)
                v.tensor_copy(tailc[:, j, :], padded[:, T:T + PADC + NS]).then_inc(tail_cp, 1)
                o, s = acc[:, j, 0:T], acc[:, j, T:TT]
                link(v.tensor_scalar(o, padded[:, PADC:PADC + T], cw[KCF - 1], k.par[:, cb:cb + 1], ALU.mult, ALU.add))
                for q in range(KCF - 1):
                    link(v.scalar_tensor_tensor(out=o, in0=padded[:, q:q + T], scalar=cw[q], in1=o, op0=ALU.mult, op1=ALU.add))
                b = PB + j * PB_ROWS + B_CF
                link(v.tensor_tensor(prod[:, :, :], prev_c[:, j, :].rearrange("p (s r) -> p s r", r=PADC),
                                     k.par[:, b:b + PADC].rearrange("p (o r) -> p o r", o=1).broadcast_to([P, NS, PADC]), ALU.mult))
                link(v.tensor_reduce(s, prod[:, :, :], AX.X, ALU.add))
                link(v.tensor_scalar(s, s, k.par[:, cb:cb + 1], None, ALU.add))
                v.scalar_tensor_tensor(out=s, in0=padded[:, PADC + T:PADC + TT], scalar=cw[KCF - 1], in1=s,
                                       op0=ALU.mult, op1=ALU.add).then_inc(convd, 1)
                dve.wait_ge(convd, j + 1)
            for j in range(2):
                i0 = 6 + 4 * j
                aw = [k.par[:, PB + j * PB_ROWS + B_SC + q:PB + j * PB_ROWS + B_SC + q + 1] for q in range(3)]
                dve.wait_ge(evac, (i0 + 2) * U)
                v.tensor_tensor(padded[:, PADC:PADC + TT], first[:, :], second[:, :], ALU.mult).then_inc(u_done, 1)
                dve.wait_ge(u_done, 3 + j)
                v.tensor_copy(taila[:, j, :], padded[:, T + PADC - 2:T + PADC + NS]).then_inc(tail_cp, 1)
                o, s = second[:, 0:T], second[:, T:TT]
                link(v.tensor_scalar(o, padded[:, PADC:PADC + T], aw[2], None, ALU.mult))
                for q in range(2):
                    link(v.scalar_tensor_tensor(out=o, in0=padded[:, PADC - 2 + q:PADC - 2 + q + T], scalar=aw[q], in1=o,
                                                op0=ALU.mult, op1=ALU.add))
                link(v.tensor_scalar(s, padded[:, PADC + T:PADC + TT], aw[2], None, ALU.mult))
                for q in range(2):
                    link(v.scalar_tensor_tensor(out=s, in0=prev_a[:, j, :, q], scalar=aw[q], in1=s, op0=ALU.mult, op1=ALU.add))
                dve.wait_ge(evac, (i0 + 4) * U)
                y = k.yT[2 + j]
                v.tensor_tensor(second[:, :], second[:, :], first[:, :], ALU.mult).then_inc(convd, 1)
                dve.wait_ge(convd, 3 + j)
                v.tensor_tensor(y[:, :], y[:, :], second[:, :], ALU.mult).then_inc(gated, 1)
            dve.wait_ge(tail_tr, 1)
            v.tensor_copy(outc[:, :], k.ps[0:PADC + NS, 0, 0:W])
            v.tensor_copy(outa[:, :], k.ps[0:2 + NS, 1, 0:W]).then_inc(tails_cp, 1)


def stage_conformer_norm(nc, k, sem):
    with ExitStack() as ctx:
        sq = ctx.enter_context(nc.sbuf_tensor("ln_sq", [P, 2, GT], F32))
        inv = ctx.enter_context(nc.sbuf_tensor("ln_inv", [P, GT], F32))
        mean = ctx.enter_context(nc.sbuf_tensor("ln_mean", [P, GT], F32))
        summed, cen, sqd, sq_sum, var, root, scaled, swished, link_s = (
            sem("ln_" + n) for n in ("summed", "cen", "sqd", "sq_sum", "var", "root", "scaled", "swished", "link"))
        block = ctx.enter_context(nc.Block())
        groups = [(g * GT, GT) for g in range(NG)] + [(T, NS)]
        acc = k.conf

        @block.tensor
        def _(pe):
            for g, (t0, n) in enumerate(groups):
                if g:
                    pe.wait_ge(cen, g)
                column_sums(k, pe, nc.tensor, [acc[:, j, t0:t0 + n] for j in range(2)], k.ps[:, 0, 0:n], n).then_inc(summed, 1)
                pe.wait_ge(sqd, g + 1)
                if g:
                    pe.wait_ge(var, g)
                column_sums(k, pe, nc.tensor, [sq[:, j, 0:n] for j in range(2)], k.ps[:, 1, 0:n], n).then_inc(sq_sum, 1)

        @block.scalar
        def _(act):
            for g, (t0, n) in enumerate(groups):
                act.wait_ge(cen, g + 1)
                if g:
                    act.wait_ge(sq_sum, g)
                for j in range(2):
                    last = nc.scalar.activation(sq[:, j, 0:n], acc[:, j, t0:t0 + n], ACT.Square)
                last.then_inc(sqd, 1)
                act.wait_ge(var, g + 1)
                nc.scalar.activation(inv[:, 0:n], inv[:, 0:n], ACT.Sqrt).then_inc(root, 1)
            act.wait_ge(scaled, len(groups))
            for j in range(2):
                b = PB + j * PB_ROWS
                nc.scalar.activation(acc[:, j, :], acc[:, j, :], ACT.Silu, bias=k.par[:, b + B_LNB:b + B_LNB + 1],
                                     scale=k.par[:, b + B_LNG:b + B_LNG + 1]).then_inc(swished, 1)

        @block.vector
        def _(dve):
            v = nc.vector
            link = chain(dve, link_s)
            for g, (t0, n) in enumerate(groups):
                dve.wait_ge(summed, g + 1)
                link(v.tensor_scalar(mean[:, 0:n], k.ps[:, 0, 0:n], 1.0 / W, None, ALU.mult))
                for j in range(2):
                    last = v.tensor_tensor(acc[:, j, t0:t0 + n], acc[:, j, t0:t0 + n], mean[:, 0:n], ALU.subtract)
                last.then_inc(cen, 1)
                dve.wait_ge(sq_sum, g + 1)
                link(v.tensor_scalar(inv[:, 0:n], k.ps[:, 1, 0:n], 1.0 / W, EPS, ALU.mult, ALU.add))
                v.reciprocal(inv[:, 0:n], inv[:, 0:n]).then_inc(var, 1)
                dve.wait_ge(root, g + 1)
                dve.wait_ge(cen, g + 1)
                for j in range(2):
                    last = v.tensor_tensor(acc[:, j, t0:t0 + n], acc[:, j, t0:t0 + n], inv[:, 0:n], ALU.mult)
                last.then_inc(scaled, 1)
                dve.wait_ge(scaled, g + 1)
            for j in range(2):
                dve.wait_ge(swished, j + 1)
                y = k.yT[4 + j]
                v.tensor_tensor(y[:, :], y[:, :], acc[:, j, :], ALU.mult)


def stage_token_major(nc, k, sem):
    parts = [(0, 384), (384, TM)]
    with ExitStack() as ctx:
        def sb(name, shape, dt=F32):
            return ctx.enter_context(nc.sbuf_tensor(name, shape, dt))
        w_tm = sb("w_tm", [P, KT, 384])
        gains = sb("qk_gains", [P, 6, HD])
        sq = sb("qk_sq", [P, 6, HD])
        ss = sb("q_ss", [P, NC + 1, H])
        ss_k = sb("k_ss", [P, NC + 1, 2])
        w_in_s, g_in, proj, evac, link_s, ss_done, root, rows_done, stored, mem = (
            sem("t_" + n) for n in ("w_in", "g_in", "proj", "evac", "link", "ss_done", "root", "rows_done", "stored", "mem"))
        block = ctx.enter_context(nc.Block())
        N1 = NC + 1

        @block.sync
        def _(sp):
            for h in range(H):
                sp.dma_start(gains[:, h, :], k.io["q_g"].broadcast_to([P, HD])).then_inc(g_in, 16)
            for i in range(2):
                sp.dma_start(gains[:, H + i, :], k.io["k_g"][0, 1 + i:2 + i, :].broadcast_to([P, HD])).then_inc(g_in, 16)
            wv = k.io["w_in"][0].rearrange("(k p) n -> p k n", p=P)
            sp.dma_start(w_tm[:, :, 0:384], wv[:, :, COL_Q:COL_Q + 384]).then_inc(w_in_s, 16)
            sp.wait_ge(proj, N1)
            sp.dma_start(w_tm[:, :, 0:256], wv[:, :, COL_Q + 384:COL_Q + 640]).then_inc(w_in_s, 16)
            sp.dma_start(w_tm[:, :, 256:268], wv[:, :, COL_BG:COL_BG + 12]).then_inc(w_in_s, 16)
            sp.dma_start(k.io["win_s"][0, :, 0:511], k.io["cache_win"][0, :, 1:512]).then_inc(stored, 16)
            sp.wait_ge(rows_done, 2)
            rows = k.io["kv_p"][0].rearrange("t p s d -> p t (s d)")
            sp.dma_start(rows, k.tm[:, 0:NC, W:W + 256]).then_inc(stored, 16)
            sp.dma_start(k.io["win_p"][0, 0].rearrange("(t p) s d -> p t (s d)", p=P), k.tm[:, NC - 4:NC, 512:640]).then_inc(stored, 16)
            sp.dma_start(k.io["kv_s"][0, :, 0].rearrange("n s d -> n (s d)"), k.tm[0:NS, NC, W:W + 256]).then_inc(stored, 16)
            sp.dma_start(k.io["win_s"][0, :, 511].rearrange("n s d -> n (s d)"), k.tm[0:NS, NC, 512:640]).then_inc(stored, 16)
            sp.wait_ge(stored, 80)

        @block.tensor
        def _(pe):
            for i, (c0, c1) in enumerate(parts):
                pe.wait_ge(w_in_s, 16 if i == 0 else 48)
                for t in range(N1):
                    u = i * N1 + t
                    r = P if t < NC else NS
                    if u >= 4:
                        pe.wait_ge(evac, u - 3)
                    for kk in range(KT):
                        last = nc.tensor.matmul(k.ps[0:r, u % 4, 0:c1 - c0], k.hT[:, kk, t * P:t * P + r], w_tm[:, kk, 0:c1 - c0],
                                                start=(kk == 0), stop=(kk == KT - 1))
                    last.then_inc(proj, 1)

        @block.scalar
        def _(act):
            act.wait_ge(mem, 1)
            for i, (c0, c1) in enumerate(parts):
                for t in range(N1):
                    u = i * N1 + t
                    r = P if t < NC else NS
                    act.wait_ge(proj, u + 1)
                    nc.scalar.copy(k.tm[0:r, t, c0:c1], k.ps[0:r, u % 4, 0:c1 - c0]).then_inc(evac, 1)
                act.wait_ge(ss_done, i + 1)
                sums = (ss, ss_k)[i][:, :, :]
                nc.scalar.activation(sums, sums, ACT.Sqrt).then_inc(root, 1)
            g = k.tm[:, :, 640:652]
            act.wait_ge(evac, 2 * N1)
            nc.scalar.activation(g, g, ACT.Sigmoid)

        @block.vector
        def _(dve):
            v = nc.vector
            link = chain(dve, link_s)
            v.memset(k.tm[:, NC, :], 0.0).then_inc(mem, 1)

            def inverse(sums):
                link(v.tensor_scalar(sums, sums, 1.0 / HD, EPS, ALU.mult, ALU.add))
                v.reciprocal(sums, sums).then_inc(ss_done, 1)

            for t in range(N1):
                dve.wait_ge(evac, t + 1)
                q = k.tm[:, t, 0:W]
                link(v.tensor_tensor(sq[:, 0:H, :].rearrange("p h d -> p (h d)"), q, q, ALU.mult))
                last = v.tensor_reduce(ss[:, t, :], sq[:, 0:H, :], AX.X, ALU.add)
                link(last)
            inverse(ss[:, :, :])
            dve.wait_ge(root, 1)
            dve.wait_ge(g_in, 96)
            for t in range(N1):
                q = k.tm[:, t, 0:W].rearrange("p (h d) -> p h d", d=HD)
                link(v.tensor_tensor(q, q, ss[:, t, :].rearrange("p (h o) -> p h o", o=1).broadcast_to([P, H, HD]), ALU.mult))
                v.tensor_tensor(q, q, gains[:, 0:H, :], ALU.mult)
            for t in range(N1):
                dve.wait_ge(evac, N1 + t + 1)
                kk = k.tm[:, t, 384:640].rearrange("p (i d) -> p i d", d=2 * HD)[:, :, 0:HD]
                link(v.tensor_tensor(sq[:, H:6, :], kk, kk, ALU.mult))
                link(v.tensor_reduce(ss_k[:, t, :], sq[:, H:6, :], AX.X, ALU.add))
            inverse(ss_k[:, :, :])
            dve.wait_ge(root, 2)
            for i in range(2):
                c = 384 + 2 * HD * i
                kk = k.tm[:, :, c:c + HD]
                link(v.tensor_tensor(kk, kk, ss_k[:, :, i:i + 1].broadcast_to([P, N1, HD]), ALU.mult))
                g = gains[:, H + i:H + i + 1, :].broadcast_to([P, N1, HD])
                v.tensor_tensor(kk, kk, g, ALU.mult).then_inc(rows_done, 1)


def stage_compress(nc, k, sem):
    NQ = 1 + NS
    NB = 3
    PAIRS = T // 2
    with ExitStack() as ctx:
        def sb(name, shape, dt=F32):
            return ctx.enter_context(nc.sbuf_tensor(name, shape, dt))
        rawT = sb("rawT", [P, 2, 2, PAIRS])
        w1 = sb("w1", [P, 2, 16, P])
        page = sb("page", [P, NB, 2, 2, P])
        table = sb("table", [1, NS * PAGES], I32)
        pe_rows = sb("pe_rows", [16, 2, P])
        b1_rows = sb("b1_rows", [2, P])
        peT = sb("peT", [P, 2, 16])
        bias1 = sb("bias1", [P, 2])
        b1T = sb("b1T", [P, 2])
        w2 = sb("w2", [P, 2, HD])
        b2 = sb("b2", [P, 2, HD])
        kg = sb("kg", [P, HD])
        kc = k.tm[:, 0:NQ, W:W + HD]
        hid = k.tm[:, NQ:NQ + 4, W:W + P].rearrange("p (b i) c -> p b i c", b=2)
        sq = sb("kc_sq", [P, HD])
        st = sb("kc_st", [P, 3, NQ])
        names = ("table_in par_in blk_in pt pcp bias_d rcp hidp hidd cmp_d cmp_e kct link root root_in "
                 "scaled ktr kcp staged").split()
        z = {n: sem("k_" + n) for n in names}
        page_in = [[sem(f"k_page_in{b}_{e}") for e in ("sp", "pool")] for b in range(NB)]
        block = ctx.enter_context(nc.Block())
        M = NCMP
        KB = 2 * NC // 4
        staging = rawT[:, 1].rearrange("p i n -> p (i n)")
        stage_rows = (slice(HD, HD + NBLK + 2), slice(0, NBLK + 2))

        def fetch(eng, half):
            eng.wait_ge(z["table_in"], 16)
            for u in range(4 * NS):
                if u >= NB:
                    eng.wait_ge(z["ktr"], KB + 4 + u - NB + 1)
                for pair in range(2):
                    at = 4 * u + 2 * pair + half
                    i = eng.value_load(table[0:1, at:at + 1], min_val=0, max_val=k.n_pool - 1)
                    eng.dma_start(page[half * HD:(half + 1) * HD, u % NB, pair],
                                  k.io["cache_kv"][0, bass.DynSlice(i, 1), :, 0:2, :].rearrange("o (p t) s d -> (o p) t (s d)", t=2)
                                  ).then_inc(page_in[u % NB][half], 16)

        @block.sync
        def _(sp):
            sp.dma_start(table[:, :], k.io["page_table"].rearrange("n g -> (n g)").rearrange("(o m) -> o m", o=1)).then_inc(z["table_in"], 16)
            for i in range(2):
                for t in range(2):
                    sp.dma_start(w1[t * HD:(t + 1) * HD, i], k.io["cmp_w1"][0, i].rearrange("(j t) d f -> t d j f", t=2)[t]).then_inc(z["par_in"], 16)
                sp.dma_start(pe_rows[:, i, :], k.io["cmp_pe"][0, i].rearrange("(j t) d -> j (t d)", t=2)).then_inc(z["par_in"], 16)
                sp.dma_start(b2[:, i, :], k.io["cmp_b2"][0, i:i + 1, :].broadcast_to([P, HD])).then_inc(z["par_in"], 16)
                sp.dma_start(staging[stage_rows[i], :], k.extra_dram[i]).then_inc(z["blk_in"], 16)
            sp.dma_start(b1_rows[:, :], k.io["cmp_b1"][0]).then_inc(z["par_in"], 16)
            sp.dma_start(w2[:, :, :], k.io["cmp_w2"][0].rearrange("i f d -> f i d")).then_inc(z["par_in"], 16)
            sp.dma_start(kg[:, :], k.io["k_g"][0, 0:1, :].broadcast_to([P, HD])).then_inc(z["par_in"], 16)
            fetch(sp, 0)

        @block.gpsimd
        def _(pool):
            fetch(pool, 1)

        @block.tensor
        def _(pe):
            m = nc.tensor
            for e in range(KB):
                if e >= 2:
                    pe.wait_ge(z["kcp"], e - 1)
                for n in range(4):
                    c = 384 + 128 * (e % 2)
                    last = m.transpose(k.ps[0:HD, 3 + e % 2, n * P:(n + 1) * P], k.tm[:, 4 * (e // 2) + n, c:c + HD], k.ident[:, :])
                last.then_inc(z["ktr"], 1)
            pe.wait_ge(z["kcp"], KB)

            def raw_transposes(q):
                for b4 in range(4):
                    e = q * 4 + b4
                    if q:
                        u = e - 4
                        for landed in page_in[u % NB]:
                            pe.wait_ge(landed, 32 * (u // NB + 1))
                    if e >= 2:
                        pe.wait_ge(z["rcp"], e - 1)
                    bank = k.ps[:, 3 + e % 2, :]
                    for n in range(4):
                        if q == 0:
                            src = k.tm[:, 4 * b4 + n, W:W + P]
                        else:
                            src = page[:, u % NB, n % 2, n // 2, :]
                        last = m.transpose(bank[:, n * P:(n + 1) * P], src, k.ident[:, :])
                    last.then_inc(z["ktr"], 1)

            def second_layer(q):
                if q >= 2:
                    pe.wait_ge(z["cmp_e"], q - 1)
                for i in range(2):
                    pe.wait_ge(z["hidd"], 2 * q + i + 1)
                    last = m.matmul(k.ps[0:M, 5 + q % 2, i * HD:(i + 1) * HD], hid[:, q % 2, i, 0:M], w2[:, i, :], start=True, stop=True)
                last.then_inc(z["cmp_d"], 1)

            raw_transposes(0)
            pe.wait_ge(z["par_in"], 16 * 11)
            for i in range(2):
                m.transpose(k.ps[:, 0, 16 * i:16 * (i + 1)], pe_rows[:, i, :], k.ident[0:16, 0:16])
            m.transpose(k.ps[:, 0, 32:34], b1_rows[:, :], k.ident[0:2, 0:2]).then_inc(z["pt"], 1)
            pe.wait_ge(z["pcp"], 1)
            for i in range(2):
                for j in range(16):
                    last = m.matmul(k.ps[:, 7, i:i + 1], w1[:, i, j, :], peT[:, i, j:j + 1], start=(j == 0), stop=(j == 15))
            last.then_inc(z["pt"], 1)
            for q in range(NQ):
                if q + 1 < NQ:
                    raw_transposes(q + 1)
                pe.wait_ge(z["rcp"], 4 * (q + 1))
                if q >= 2:
                    pe.wait_ge(z["hidd"], 2 * (q - 1))
                for i in range(2):
                    for j in range(16):
                        last = m.matmul(k.ps[:, 1 + q % 2, i * P:i * P + M], w1[:, i, j, :], rawT[:, q % 2, i, j:j + 8 * (M - 1) + 1:8],
                                        start=(j == 0), stop=(j == 15))
                last.then_inc(z["hidp"], 1)
                if q:
                    second_layer(q - 1)
            second_layer(NQ - 1)
            for q in range(NQ):
                pe.wait_ge(z["scaled"], q + 1)
                last = m.transpose(k.ps[0:HD, (0, 7, 5)[q // 4], (q % 4) * P:(q % 4) * P + M], kc[0:M, q, :], k.ident[0:M, 0:M])
                if q % 4 == 3 or q == NQ - 1:
                    last.then_inc(z["kct"], 1)

        def raw_copy(copy, q, b4):
            bank, c = k.ps[:, 3 + b4 % 2, :], slice(b4 * 256, (b4 + 1) * 256)
            for i in range(2):
                for t in range(2):
                    src = slice(t * 256, (t + 1) * 256) if q else slice(t, GT, 2)
                    last = copy(rawT[t * HD:(t + 1) * HD, q % 2, i, c], bank[i * HD:(i + 1) * HD, src])
            return last

        @block.scalar
        def _(act):
            def hids(q):
                act.wait_ge(z["hidp"], q + 1)
                if q >= 2:
                    act.wait_ge(z["cmp_d"], q - 1)
                for i in range(2):
                    nc.scalar.activation(hid[:, q % 2, i, 0:M], k.ps[:, 1 + q % 2, i * P:i * P + M], ACT.Silu, bias=bias1[:, i:i + 1]).then_inc(z["hidd"], 1)

            for q in range(NQ):
                for b4 in range(1, 4, 2):
                    e = q * 4 + b4
                    act.wait_ge(z["ktr"], KB + e + 1)
                    act.wait_ge(z["rcp"], e)
                    if q == 1:
                        act.wait_ge(z["staged"], 1)
                    if q >= 2:
                        act.wait_ge(z["hidp"], q - 1)
                    raw_copy(nc.scalar.copy, q, b4).then_inc(z["rcp"], 1)
                if q == 1:
                    act.wait_ge(z["bias_d"], 1)
                if q:
                    hids(q - 1)
            hids(NQ - 1)
            act.wait_ge(z["root_in"], 1)
            nc.scalar.activation(st[0:M, 2, :], st[0:M, 1, :], ACT.Sqrt).then_inc(z["root"], 1)

        def second(q, v, link, dve):
            dve.wait_ge(z["cmp_d"], q + 1)
            c, bank = kc[0:M, q, :], k.ps[0:M, 5 + q % 2, :]
            link(v.tensor_tensor(c, bank[:, 0:HD], b2[0:M, 0, :], ALU.add))
            v.tensor_tensor(k.vc[0:M, q, :], bank[:, HD:2 * HD], b2[0:M, 1, :], ALU.add).then_inc(z["cmp_e"], 1)
            link(v.tensor_tensor(sq[0:M, :], c, c, ALU.mult))
            link(v.tensor_reduce(st[0:M, 0, q:q + 1], sq[0:M, :], AX.X, ALU.add))

        @block.vector
        def _(dve):
            v = nc.vector
            link = chain(dve, z["link"])
            for e in range(KB):
                dve.wait_ge(z["ktr"], e + 1)
                b = k.ps[0:HD, 3 + e % 2, :]
                hi, lo = (kk[0:HD, (e // 2) * 512:(e // 2 + 1) * 512] for kk in k.keys[e % 2])
                link(v.tensor_copy(hi, b))
                v.tensor_tensor(lo, b, hi.bitcast(F32), ALU.subtract).then_inc(z["kcp"], 1)

            def raw_copies(q):
                for b4 in range(0, 4, 2):
                    e = q * 4 + b4
                    dve.wait_ge(z["ktr"], KB + e + 1)
                    if e:
                        dve.wait_ge(z["rcp"], e)
                    if q >= 2:
                        dve.wait_ge(z["hidp"], q - 1)
                    raw_copy(v.tensor_copy, q, b4).then_inc(z["rcp"], 1)

            raw_copies(0)
            dve.wait_ge(z["pt"], 1)
            v.tensor_copy(peT[:, :, :].rearrange("p i j -> p (i j)"), k.ps[:, 0, 0:32])
            v.tensor_copy(b1T[:, :], k.ps[:, 0, 32:34]).then_inc(z["pcp"], 1)
            dve.wait_ge(z["blk_in"], 32)
            for i, kk in enumerate(k.keys):
                for n, size in ((0, NBLK), (NBLK, 2)):
                    r = slice(HD + n, HD + n + size)
                    src = slice(stage_rows[i].start + n, stage_rows[i].start + n + size)
                    v.tensor_copy(kk[0][r, :], staging[src, :])
                    last = v.memset(kk[1][r, :].bitcast(F32), 0.0)
            last.then_inc(z["staged"], 1)
            dve.wait_ge(z["staged"], 1)
            dve.wait_ge(z["pt"], 2)
            dve.wait_ge(z["pcp"], 1)
            v.tensor_tensor(bias1[:, :], k.ps[:, 7, 0:2], b1T[:, :], ALU.add).then_inc(z["bias_d"], 1)
            for q in range(NQ):
                if q + 1 < NQ:
                    raw_copies(q + 1)
                if q:
                    second(q - 1, v, link, dve)
            second(NQ - 1, v, link, dve)
            link(v.tensor_scalar(st[0:M, 1, :], st[0:M, 0, :], 1.0 / HD, EPS, ALU.mult, ALU.add))
            v.reciprocal(st[0:M, 1, :], st[0:M, 1, :]).then_inc(z["root_in"], 1)
            dve.wait_ge(z["root"], 1)
            for q in range(NQ):
                v.scalar_tensor_tensor(out=kc[0:M, q, :], in0=kc[0:M, q, :], scalar=st[0:M, 2, q:q + 1], in1=kg[0:M, :],
                                       op0=ALU.mult, op1=ALU.mult).then_inc(z["scaled"], 1)
            for n in range(3):
                q, size = 4 * n, min(4, NQ - 4 * n)
                dve.wait_ge(z["kct"], n + 1)
                v.tensor_copy(k.kcT[0:HD, q:q + size, 0:M],
                              k.ps[0:HD, (0, 7, 5)[n], 0:size * P].rearrange("d (q c) -> d q c", c=P)[:, :, 0:M])


def stage_choice(nc, k, sem):
    M = NCMP
    with ExitStack() as ctx:
        def sb(name, shape, dt=F32):
            return ctx.enter_context(nc.sbuf_tensor(name, shape, dt))
        qf, cs, pcT = sb("qf", [HD, 2, H, P]), sb("cs", [P, 2, H, P]), sb("pcT", [P, 2, H, P])
        mx = sb("mx", [P, 2, 16])
        pg = sb("pg", [P, NC, P + 4])
        imp, m8 = sb("imp", [P, NC, NBLK]), sb("m8", [P, NC, 16])
        spare, rest = pg[:, :, 0:NBLK], pg[:, :, NBLK:2 * NBLK]
        names = "va_done q_tr q_cp sc_done masked exp_done probs p_tr p_cp out_done out_read chosen bias_tr link".split()
        z = {n: sem("choice_" + n) for n in names}
        block = ctx.enter_context(nc.Block())

        @block.tensor
        def _(pe):
            m = nc.tensor

            def queries(b):
                if b >= 2:
                    pe.wait_ge(z["q_cp"], b - 1)
                for h in range(H):
                    last = m.transpose(k.ps[0:HD, b % 2, h * P:(h + 1) * P], k.tm[:, b, h * HD:(h + 1) * HD], k.ident[:, :])
                last.then_inc(z["q_tr"], 1)

            def scores(b):
                pe.wait_ge(z["q_cp"], b + 1)
                if b >= 2:
                    pe.wait_ge(z["masked"], b - 1)
                for h in range(H):
                    last = m.matmul(k.ps[:, 2 + b % 2, h * P:h * P + M], qf[:, b % 2, h, :], k.kcT[:, 0, 0:M], start=True, stop=True)
                last.then_inc(z["sc_done"], 1)

            def turn(b):
                pe.wait_ge(z["probs"], b + 1)
                if b >= 2:
                    pe.wait_ge(z["p_cp"], b - 1)
                for h in range(H):
                    last = m.transpose(k.ps[0:M, 4 + b % 2, h * P:(h + 1) * P], cs[:, b % 2, h, 0:M], k.ident[:, :])
                last.then_inc(z["p_tr"], 1)

            def values(b):
                pe.wait_ge(z["p_cp"], b + 1)
                if b >= 2:
                    pe.wait_ge(z["out_read"], b - 1)
                for h in range(H):
                    last = m.matmul(k.ps[:, 6 + b % 2, h * HD:(h + 1) * HD], pcT[0:M, b % 2, h, :], k.vc[0:M, 0, :], start=True, stop=True)
                last.then_inc(z["out_done"], 1)

            for s in range(NC + 3):
                for step, b in ((queries, s), (scores, s - 1), (turn, s - 2), (values, s - 3)):
                    if 0 <= b < NC:
                        step(b)
            pe.wait_ge(z["chosen"], 1)
            for b in range(NC):
                last = m.transpose(k.ps[0:NBLK, b // 4, (b % 4) * P:(b % 4 + 1) * P], imp[:, b, :], k.ident[:, :])
            last.then_inc(z["bias_tr"], 1)

        @block.scalar
        def _(act):
            def queries(b):
                act.wait_ge(z["q_tr"], b + 1)
                if b >= 2:
                    act.wait_ge(z["sc_done"], b - 1)
                nc.scalar.copy(qf[:, b % 2].rearrange("d h q -> d (h q)"), k.ps[0:HD, b % 2, :]).then_inc(z["q_cp"], 1)

            def exps(b):
                act.wait_ge(z["masked"], b + 1)
                for h in range(H):
                    last = nc.scalar.activation(cs[:, b % 2, h, 0:M], cs[:, b % 2, h, 0:M], ACT.Exp, scale=SCALE,
                                                bias=mx[:, b % 2, h:h + 1], accum_out=mx[:, b % 2, 8 + h:9 + h])
                last.then_inc(z["exp_done"], 1)

            def probs(b):
                act.wait_ge(z["p_tr"], b + 1)
                if b >= 2:
                    act.wait_ge(z["out_done"], b - 1)
                nc.scalar.copy(pcT[0:M, b % 2].rearrange("p h q -> p (h q)"), k.ps[0:M, 4 + b % 2, :]).then_inc(z["p_cp"], 1)

            def share(b):
                act.wait_ge(z["out_done"], b + 1)
                for h in range(H):
                    last = nc.scalar.activation(k.tm[:, b, W + h * HD:W + (h + 1) * HD], k.ps[:, 6 + b % 2, h * HD:(h + 1) * HD],
                                                ACT.Copy, scale=k.tm[:, b, 640 + 3 * h:641 + 3 * h])
                last.then_inc(z["out_read"], 1)

            act.wait_ge(z["va_done"], 1)
            for s in range(NC + 3):
                for step, b in ((queries, s), (exps, s - 1), (probs, s - 2), (share, s - 3)):
                    if 0 <= b < NC:
                        step(b)

        @block.vector
        def _(dve):
            v = nc.vector
            link = chain(dve, z["link"])
            v.memset(k.va[:, :, :, HD:HD + 1], 1.0)
            for b in range(2):
                last = v.tensor_copy(k.va[:, :, b, 0:HD], k.tm[:, 0:NC, 448 + 128 * b:512 + 128 * b])
            last.then_inc(z["va_done"], 1)
            link(v.memset(pg[:, :, :], 0.0))

            def mask(b):
                dve.wait_ge(z["sc_done"], b + 1)
                if b >= 2:
                    dve.wait_ge(z["p_tr"], b - 1)
                low = k.cmp_mask[:, P - 8 * b:P - 8 * b + M]
                link(v.tensor_tensor(cs[:, b % 2, :, 0:M], k.ps[:, 2 + b % 2, :].rearrange("p (h c) -> p h c", h=H)[:, :, 0:M],
                                     low.rearrange("p (o c) -> p o c", o=1).broadcast_to([P, H, M]), ALU.add))
                link(v.tensor_reduce(mx[:, b % 2, 0:4], cs[:, b % 2, :, 0:M], AX.X, ALU.max))
                v.tensor_scalar(mx[:, b % 2, 0:4], mx[:, b % 2, 0:4], -1e20, -SCALE, ALU.max, ALU.mult).then_inc(z["masked"], 1)

            def normalise(b):
                dve.wait_ge(z["exp_done"], b + 1)
                r = mx[:, b % 2, 12:16]
                link(v.tensor_scalar(r, mx[:, b % 2, 8:12], 1e-30, None, ALU.max))
                link(v.reciprocal(r, r))
                c = cs[:, b % 2, :, 0:M]
                v.tensor_tensor(c, c, r.rearrange("p (h o) -> p h o", o=1).broadcast_to([P, H, M]), ALU.mult).then_inc(z["probs"], 1)
                dve.wait_ge(z["probs"], b + 1)
                link(v.tensor_reduce(pg[:, b, 1:1 + M], c.rearrange("p h c -> p c h"), AX.X, ALU.add))

            for s in range(NC + 3):
                for step, b in ((normalise, s - 2), (mask, s - 1)):
                    if 0 <= b < NC:
                        step(b)

            def at(o):
                return pg[:, :, 1 + o:1 + o + 4 * (NBLK - 1) + 1:4]
            e = imp[:, :, :]
            link(v.scalar_tensor_tensor(out=e, in0=at(-1), scalar=0.5, in1=at(0), op0=ALU.mult, op1=ALU.add))
            link(v.tensor_tensor(e, e, at(1), ALU.add))
            link(v.tensor_tensor(e, e, at(2), ALU.add))
            link(v.scalar_tensor_tensor(out=e, in0=at(3), scalar=0.5, in1=e, op0=ALU.mult, op1=ALU.add))
            for b in range(NC):
                last = v.tensor_tensor(imp[:, b, :], imp[:, b, :], k.sel_mask[:, NBLK - 2 * b:2 * NBLK - 2 * b], ALU.add)
            link(last)
            link(v.memset(imp[:, :, 0:1], BIG))
            for b in range(NC):
                last = v.max(m8[:, b, 0:8], imp[:, b, :])
            link(last)
            for b in range(NC):
                last = v.match_replace(spare[:, b, :], m8[:, b, 0:8], imp[:, b, :], -3e38)
            link(last)
            for b in range(NC):
                last = v.max(m8[:, b, 8:16], spare[:, b, :])
            link(last)
            for b in range(NC):
                last = v.match_replace(rest[:, b, :], m8[:, b, 8:16], spare[:, b, :], -3e38)
            link(last)
            v.tensor_scalar(e, rest[:, :, :], -2e38, NEG, ALU.is_gt, ALU.mult).then_inc(z["chosen"], 1)
            dve.wait_ge(z["bias_tr"], 1)
            v.tensor_copy(k.biasT[HD:HD + NBLK, :], k.ps[0:NBLK, 0:4, :].rearrange("p b n -> p (b n)"))


def stage_attention(nc, k, sem):
    LAG, NST, NPT = 2, 3, 3
    VW = HD + 1

    def tiles_of(qb):
        return [("sel", t) for t in range(qb + 1)] + [("win", t) for t in range(max(0, qb - 4), qb + 1)]

    def max_units(qb, kind):
        lo = 0 if kind == "sel" else max(0, qb - 4)
        return [("max", kind, h, a, min(a + 4, qb + 1), (a - lo) // 4) for h in range(H) for a in range(lo, qb + 1, 4)]

    def units_of(qb):
        return max_units(qb, "win") + max_units(qb, "sel")

    order, tiles = [("q", 0)] + [(u, 0) for u in units_of(0)] + [("shift", 0)], []
    later = {}
    for qb in range(NC):
        mine = tiles_of(qb)
        units = units_of(qb + 1) if qb + 1 < NC else []
        first, last, ready = (1, len(mine) - 4, len(mine) - 2) if len(mine) >= 6 else (0, len(mine) - 1, len(mine) - 1)
        done = 0
        for n, (kind, t) in enumerate(mine):
            i = len(tiles)
            tiles.append((qb, kind, t, n == 0 or mine[n - 1][0] != kind, n + 1 == len(mine) or mine[n + 1][0] != kind))
            order.append(("tile", i))
            if i >= LAG and tiles[i - LAG][4]:
                b, kind = tiles[i - LAG][0:2]
                order.append(("evac_" + kind, b))
                later.setdefault(i + 1, []).append(("part_" + kind, b))
                if kind == "win":
                    later.setdefault(i + 3, []).append(("out", b))
            order += later.get(i, [])
            if units:
                if n == 0:
                    order.append(("q", qb + 1))
                upto = 0 if n < first else min(len(units), len(units) * (n - first + 1) // (last - first + 1))
                order += [(u, qb + 1) for u in units[done:upto]]
                done = upto
                if n == ready:
                    order.append(("shift", qb + 1))
    order += [("drain", len(tiles) + i) for i in range(LAG)] + [("evac_win", NC - 1), ("part_win", NC - 1), ("out", NC - 1)]

    with ExitStack() as ctx:
        def sb(name, shape, dt=F32):
            return ctx.enter_context(nc.sbuf_tensor(name, shape, dt))
        FR, BF = mybir.dt.float32r, mybir.dt.bfloat16
        qhi, qlo = sb("q_hi", [P, 2, H * P], FR), sb("q_lo", [P, 2, H * P], FR)
        pT = sb("pT", [P, NPT, H, P])
        oT = sb("oT", [VW, 2, H * P])
        o_tm, o_part = sb("o_tm", [P, 2, W]), sb("o_part", [P, 2, W])
        part_max = sb("part_max", [P, 2, H, 4])
        shift = sb("row_shift", [P, H, 2])
        wgt = sb("wgt", [P, 2, H])
        id_b, causal_b, low_b = (sb(n, [P, P], BF) for n in ("id_b", "causal_b", "low_b"))
        upper_b, lowT_b = sb("upper_b", [P, H * P], BF), sb("lowT_b", [P, H * P], BF)
        names = "ready st_done exp_done pv_done misc_wr misc_rd mu_done mu_read bias_in shifted evac_sel evac_win summed link".split()
        z = {n: sem("a_" + n) for n in names}
        block = ctx.enter_context(nc.Block())
        MISC = 7
        MISC_STEPS = ("q", "shift", "part_sel", "part_win", "out")
        misc_at = {step: n + 1 for n, step in enumerate(s for s in order if s[0] in MISC_STEPS)}
        n_tiles = {(t[0], t[1]): i + 1 for i, t in enumerate(tiles)}

        @block.tensor
        def _(pe):
            m = nc.tensor
            count = {"mu": 0}
            pe.wait_ge(z["ready"], 6)

            def scores(i):
                qb, kind, t, first, _ = tiles[i]
                if i >= NST:
                    pe.wait_ge(z["exp_done"], i - NST + 1)
                if first and kind == "sel":
                    pe.wait_ge(z["misc_rd"], misc_at["shift", qb])
                hi, lo = k.keys[0 if kind == "sel" else 1]
                R = HD + NBLK + 2
                c, bank = slice(t * P, (t + 1) * P), k.ps[:, i % NST, :]
                low = kind == "win" and t == qb - 4
                m.matmul(bank, hi[0:R, c], qhi[0:R, qb % 2, :], start=True, stop=False)
                m.matmul(bank, hi[0:R, c], qlo[0:R, qb % 2, :], start=False, stop=False)
                last = m.matmul(bank, lo[0:R, c], qhi[0:R, qb % 2, :], start=False, stop=not (low or t == qb))
                if low or t == qb:
                    last = m.matmul(bank, id_b[:, :], (lowT_b if low else upper_b)[:, :], start=False, stop=True)
                last.then_inc(z["st_done"], 1)

            def values(i):
                if i < 0:
                    return
                qb, kind, t, first, end = tiles[i]
                b = 0 if kind == "sel" else 1
                pe.wait_ge(z["exp_done"], i + 1)
                if first and qb:
                    pe.wait_ge(z["evac_" + kind], qb)
                m.matmul(k.ps[0:VW, 5 + b, :], k.va[:, t, b, :], pT[:, i % NPT].rearrange("p h q -> p (h q)"),
                         start=first, stop=end).then_inc(z["pv_done"], 1)

            def max_pass(qb, kind, h, a, b, col):
                n = count["mu"]
                count["mu"] += 1
                if n >= 2:
                    pe.wait_ge(z["mu_read"], n - 1)
                pe.wait_ge(z["misc_rd"], misc_at["q", qb])
                if kind == "sel" and h == 0 and a == 0:
                    pe.wait_ge(z["bias_in"], qb + 1)
                R = HD + NBLK if kind == "sel" else HD
                hi = k.keys[0 if kind == "sel" else 1][0]
                bank = k.ps[:, 3 + n % 2, :]
                low, end = kind == "win" and a == qb - 4, b == qb + 1
                last = m.matmul(bank[:, 0:(b - a) * P], qhi[0:R, qb % 2, h * P:(h + 1) * P], hi[0:R, a * P:b * P],
                                start=True, stop=not (low or end))
                if low:
                    last = m.matmul(bank[:, 0:P], id_b[:, :], low_b[:, :], start=False, stop=not end)
                if end:
                    last = m.matmul(bank[:, (b - a - 1) * P:(b - a) * P], id_b[:, :], causal_b[:, :], start=False, stop=True)
                last.then_inc(z["mu_done"], 1)

            def misc(step, qb):
                bank = k.ps[:, MISC, :]
                n = misc_at[step, qb]
                if n > 1:
                    pe.wait_ge(z["misc_rd"], n - 1)
                if step == "q":
                    for h in range(H):
                        last = m.transpose(bank[0:HD, h * P:(h + 1) * P], k.tm[:, qb, h * HD:(h + 1) * HD], k.ident[:, :])
                elif step == "shift":
                    pe.wait_ge(z["shifted"], qb + 1)
                    for h in range(H):
                        last = m.transpose(bank[0:2, h * P:(h + 1) * P], shift[:, h, :], k.ident[:, :])
                elif step in ("part_sel", "part_win"):
                    pe.wait_ge(z["evac_" + step[5:]], qb + 1)
                    for h in range(H):
                        last = m.transpose(bank[:, h * VW:(h + 1) * VW], oT[:, 0 if step == "part_sel" else 1, h * P:(h + 1) * P],
                                           k.ident[0:VW, 0:VW])
                else:
                    pe.wait_ge(z["summed"], qb + 1)
                    for j in range(2):
                        last = m.transpose(bank[:, j * P:(j + 1) * P], o_tm[:, qb % 2, j * P:(j + 1) * P], k.ident[:, :])
                last.then_inc(z["misc_wr"], 1)

            for what, n in order:
                if what == "tile":
                    scores(n)
                    values(n - LAG)
                elif what == "drain":
                    values(n - LAG)
                elif what in MISC_STEPS:
                    misc(what, n)
                elif what[0] == "max":
                    max_pass(n, *what[1:])

        @block.scalar
        def _(act):
            act.wait_ge(z["ready"], 6)
            for what, n in order:
                if what == "tile":
                    act.wait_ge(z["st_done"], n + 1)
                    if n >= NPT:
                        act.wait_ge(z["pv_done"], n - NPT + 1)
                    nc.scalar.activation(pT[:, n % NPT].rearrange("p h q -> p (h q)"), k.ps[:, n % NST, :], ACT.Exp,
                                         scale=SCALE).then_inc(z["exp_done"], 1)
                elif what in ("evac_sel", "evac_win"):
                    b = 0 if what == "evac_sel" else 1
                    act.wait_ge(z["pv_done"], n_tiles[n, what[5:]])
                    if n:
                        act.wait_ge(z["misc_rd"], misc_at["part_" + what[5:], n - 1])
                    nc.scalar.copy(oT[:, b, :], k.ps[0:VW, 5 + b, :]).then_inc(z[what], 1)
                elif what == "q":
                    act.wait_ge(z["misc_wr"], misc_at["q", n])
                    nc.scalar.copy(qhi[HD:HD + NBLK, n % 2, :].rearrange("b (h q) -> b h q", h=H),
                                   k.biasT[HD:HD + NBLK, n * P:(n + 1) * P].rearrange("p (o q) -> p o q", o=1).broadcast_to([NBLK, H, P])
                                   ).then_inc(z["bias_in"], 1)

        @block.vector
        def _(dve):
            v = nc.vector
            link = chain(dve, z["link"])
            count = {"mu": 0}
            v.memset(qlo[HD:HD + NBLK, :, :].bitcast(F32), 0.0)
            v.tensor_copy(id_b[:, :], k.ident[:, :]).then_inc(z["ready"], 1)
            v.tensor_copy(causal_b[:, :], k.causal[:, :]).then_inc(z["ready"], 1)
            v.tensor_copy(low_b[:, :], k.win_low[:, :]).then_inc(z["ready"], 1)
            v.tensor_copy(upper_b[:, :], k.neg_upper[:, :]).then_inc(z["ready"], 1)
            v.tensor_copy(lowT_b[:, :], k.low_T[:, :]).then_inc(z["ready"], 1)
            v.memset(part_max[:, :, :, :], 0.0).then_inc(z["ready"], 1)
            dve.wait_ge(z["ready"], 6)

            def misc(step, qb):
                bank = k.ps[:, MISC, :]
                if step == "shift":
                    ns, nw = (qb + 4) // 4, (qb - max(0, qb - 4) + 4) // 4
                    for b, n in ((0, ns), (1, nw)):
                        last = v.tensor_reduce(shift[:, :, b], part_max[:, b, :, 0:n], AX.X, ALU.max)
                    link(last)
                    v.tensor_scalar(shift[:, :, :], shift[:, :, :], -1.0, None, ALU.mult).then_inc(z["shifted"], 1)
                dve.wait_ge(z["misc_wr"], misc_at[step, qb])
                if step == "q":
                    r = slice(0, HD)
                    link(v.tensor_copy(qhi[r, qb % 2, :], bank[r, :]))
                    ins = v.tensor_tensor(qlo[r, qb % 2, :], bank[r, :], qhi[r, qb % 2, :].bitcast(F32), ALU.subtract)
                elif step == "shift":
                    r = slice(HD + NBLK, HD + NBLK + 2)
                    link(v.tensor_copy(qhi[r, qb % 2, :], bank[0:2, :]))
                    ins = v.tensor_tensor(qlo[r, qb % 2, :], bank[0:2, :], qhi[r, qb % 2, :].bitcast(F32), ALU.subtract)
                elif step in ("part_sel", "part_win"):
                    b = 0 if step == "part_sel" else 1
                    o = bank[:, 0:H * VW].rearrange("p (h d) -> p h d", d=VW)
                    gates = k.tm[:, qb, 640:652].rearrange("p (h b) -> p h b", b=3)[:, :, 1 + b]
                    link(v.reciprocal(wgt[:, b, :], o[:, :, HD]))
                    link(v.tensor_tensor(wgt[:, b, :], wgt[:, b, :], gates, ALU.mult))
                    ins = v.tensor_tensor(o_part[:, b, :].rearrange("p (h d) -> p h d", d=HD), o[:, :, 0:HD],
                                          wgt[:, b, :].rearrange("p (h o) -> p h o", o=1).broadcast_to([P, H, HD]), ALU.mult)
                else:
                    y = [k.yT[6 + j][:, qb * P:(qb + 1) * P] for j in range(2)]
                    link(v.tensor_tensor(y[0], bank[:, 0:P], y[0], ALU.mult))
                    ins = v.tensor_tensor(y[1], bank[:, P:2 * P], y[1], ALU.mult)
                ins.then_inc(z["misc_rd"], 1)
                if step in ("part_sel", "part_win"):
                    dve.wait_ge(z["misc_rd"], misc_at[step, qb])
                    t = o_tm[:, qb % 2, :]
                    if b == 0:
                        link(v.tensor_tensor(t, k.tm[:, qb, W:2 * W], o_part[:, 0, :], ALU.add))
                    else:
                        v.tensor_tensor(t, t, o_part[:, 1, :], ALU.add).then_inc(z["summed"], 1)

            for what, n in order:
                if what in MISC_STEPS:
                    misc(what, n)
                elif what[0] == "max":
                    _, kind, h, a, b, col = what
                    i = count["mu"]
                    count["mu"] += 1
                    dve.wait_ge(z["mu_done"], i + 1)
                    c = part_max[:, 0 if kind == "sel" else 1, h, col:col + 1]
                    v.tensor_reduce(c, k.ps[:, 3 + i % 2, 0:(b - a) * P], AX.X, ALU.max).then_inc(z["mu_read"], 1)
                    if kind == "sel" and h == H - 1 and b == n + 1:
                        dve.wait_ge(z["mu_read"], i + 1)


def choose_blocks(link, v, score, spare, out, m8, chosen):
    link(v.max(m8[:, 0:8], score))
    link(v.match_replace(spare, m8[:, 0:8], score, -3e38))
    link(v.max(m8[:, 8:16], spare))
    link(v.match_replace(out, m8[:, 8:16], spare, -3e38))
    v.tensor_scalar(score, out, -2e38, NEG, ALU.is_gt, ALU.mult).then_inc(chosen, 1)


def stage_sample_attention(nc, k, sem):
    M, Q = NCMP, NS * H
    GW = 4
    with ExitStack() as ctx:
        def sb(name, shape, dt=F32):
            return ctx.enter_context(nc.sbuf_tensor(name, shape, dt))
        kT = sb("kT_s", [P, T])
        pages = sb("pages_s", [P, NS, PAGES, P])
        win = k.tm[:, 0:8, :].rearrange("p t c -> p (t c)")[:, 0:NS * GW * P].rearrange("p (n g c) -> p n g c", n=NS, g=GW)
        table = sb("table2", [1, NS * PAGES], I32)
        small = k.tm[:, 8:NC, :].rearrange("p t c -> p (t c)")
        used = [0]

        def sb(name, shape):
            size = 1
            for n in shape[1:]:
                size *= n
            used[0] += size
            t = small[0:shape[0], used[0] - size:used[0]]
            if len(shape) == 2:
                return t
            dims = " ".join("abc"[:len(shape) - 1])
            return t.rearrange(f"p ({dims}) -> p {dims}", **dict(zip("abc", shape[1:])))
        qT = sb("qT_s", [P, NS, H])
        newT = sb("newT_s", [HD, 4, NS])
        gd, gts = sb("gate_diag", [NS, NS, 12]), sb("gates_s", [HD, NS, 12])
        prod = sb("prod_s", [HD, 2, Q])
        snew = sb("snew", [P, 2, Q])
        scT, pc, pcT = sb("scT", [P, Q]), sb("pc_s", [Q, P]), sb("pcT_s", [P, Q])
        pick8 = sb("pick8", [Q, NS])
        st = sb("st_s", [Q, 8])
        pg, sc, m8 = sb("pg_s", [NS, P + 4]), sb("sc_s", [NS, 3, NBLK + 1]), sb("m8_s", [NS, 16])
        cmax = sb("cmax", [P, Q])
        dg = sb("dg_s", [Q, Q])
        M_b, pnew = sb("M_b", [P, Q]), sb("pnew", [P, Q])
        prob = sb("prob_s", [P, NS * PAGES * H])
        o_sum, o_b, l_b = sb("o_sum", [HD, Q]), sb("o_b", [HD, Q]), sb("l_b", [HD, Q])
        o_ch = sb("o_ch", [P, 2, NS])
        names = ("table_in blk_in win_in pk tr0 cp0 gm gcp cs_ csc cst ex nrm pp pcc imp btr bcp oc sn snc ktr kcp skt scd rmx mt dgd mb sub exd2 "
                 "av comb link osum och pick").split()
        z = {n: sem("d_" + n) for n in names}
        kin = [[sem(f"d_kin{n}"), sem(f"d_kin{n}p")] for n in range(NS)]
        block = ctx.enter_context(nc.Block())
        S_ps, W_ps = k.ps[:, 0, :], k.ps[:, 1, :]
        branches = (("sel", PAGES, 0), ("win", GW, 1))

        def scalar_part(act):
            act.wait_ge(z["ex"], 1)
            nc.scalar.activation(pc[:, 0:M], k.ps[0:Q, 6, 0:M], ACT.Exp, scale=SCALE, bias=st[:, 1:2], accum_out=st[:, 2:3]).then_inc(z["ex"], 1)
            for b, (kind, G, i) in enumerate(branches):
                act.wait_ge(z["sub"], b + 1)
                n = NS * G * H
                nc.scalar.activation(prob[:, 0:n], prob[:, 0:n], ACT.Exp, scale=SCALE)
                nc.scalar.activation(pnew[:, :], pnew[:, :], ACT.Exp, scale=SCALE).then_inc(z["exd2"], 1)

        shares = ([g for g in range(PAGES) if g % 3 < 2], [g for g in range(PAGES) if g % 3 == 2])

        def fetch(eng, parity):
            eng.wait_ge(z["table_in"], 16)
            for n, g in ((n, g) for n in range(NS) for g in shares[parity]):
                at = n * PAGES + g
                i = eng.value_load(table[0:1, at:at + 1], min_val=0, max_val=k.n_pool - 1)
                eng.dma_start(pages[:, n, g, :], k.io["cache_kv"][0, bass.DynSlice(i, 1), :, 2:4, :].rearrange("o p s d -> (o p) (s d)")
                              ).then_inc(kin[n][parity], 16)

        @block.sync
        def _(sp):
            sp.dma_start(table[:, :], k.io["page_table"].rearrange("n g -> (n g)").rearrange("(o m) -> o m", o=1)).then_inc(z["table_in"], 16)
            fetch(sp, 0)

        @block.scalar
        def _(act):
            act.dma_start(kT[HD:HD + NBLK, :], k.extra_dram[0, 0:NBLK, :]).then_inc(z["blk_in"], 16)
            for n in range(NS):
                act.dma_start(win[:, n], k.io["cache_win"][0, n].rearrange("(g p) s d -> p g (s d)", p=P)).then_inc(z["win_in"], 16)
            scalar_part(act)

        @block.gpsimd
        def _(pool):
            g = nc.gpsimd
            link = chain(pool, z["pick"])
            link(g.memset(pick8[:, :], 1.0))
            link(g.affine_select(out=pick8[:, :], in_=pick8[:, :], pattern=[[-4, NS]], compare_op=ALU.is_ge, fill=0.0, base=0, channel_multiplier=1))
            link(g.affine_select(out=pick8[:, :], in_=pick8[:, :], pattern=[[4, NS]], compare_op=ALU.is_ge, fill=0.0, base=3, channel_multiplier=-1))
            fetch(pool, 1)

        @block.tensor
        def _(pe):
            m = nc.tensor
            one = k.ones
            for h in range(H):
                m.transpose(k.ps[0:HD, 6, h * NS:(h + 1) * NS], k.tm[0:NS, NC, h * HD:(h + 1) * HD], k.ident[0:NS, 0:NS])
            for i, c in enumerate((384, 448, 512, 576)):
                last = m.transpose(k.ps[0:HD, 6, (H + i) * NS:(H + i + 1) * NS], k.tm[0:NS, NC, c:c + HD], k.ident[0:NS, 0:NS])
            last.then_inc(z["tr0"], 1)
            pe.wait_ge(z["gm"], 1)
            m.matmul(k.ps[0:HD, 7, 0:96], one[0:NS, 0:HD], gd[:, :, :].rearrange("a n g -> a (n g)"), start=True, stop=True).then_inc(z["tr0"], 1)
            pe.wait_ge(z["cp0"], 2)
            for n in range(NS):
                last = m.matmul(k.ps[0:M, 5, n * H:(n + 1) * H], k.kcT[0:HD, 1 + n, 0:M], qT[0:HD, n, :], start=True, stop=True)
            last.then_inc(z["cs_"], 1)
            pe.wait_ge(z["sn"], 1)
            pe.wait_ge(z["gcp"], 1)
            m.matmul(k.ps[:, 7, 0:2 * Q], one[0:HD, :], prod[:, :, :].rearrange("d b q -> d (b q)"), start=True, stop=True).then_inc(z["snc"], 1)
            pe.wait_ge(z["csc"], 1)
            m.transpose(k.ps[0:Q, 6, 0:M], scT[0:M, :], k.ident[0:M, 0:M]).then_inc(z["cst"], 1)
            pe.wait_ge(z["nrm"], 1)
            pe.wait_ge(z["pick"], 3)
            m.matmul(k.ps[0:NS, 5, 0:M], pick8[:, :], pc[:, 0:M], start=True, stop=True)
            m.transpose(k.ps[0:M, 6, 0:Q], pc[:, 0:M], k.ident[0:Q, 0:Q]).then_inc(z["pp"], 1)
            pe.wait_ge(z["pcc"], 1)
            for n in range(NS):
                last = m.matmul(k.ps[0:HD, 6, n * H:(n + 1) * H], k.vc[0:M, 1 + n, :], pcT[0:M, n * H:(n + 1) * H], start=True, stop=True)
            last.then_inc(z["oc"], 1)
            pe.wait_ge(z["imp"], 1)
            m.transpose(k.ps[0:NBLK, 5, 0:NS], sc[:, 0, 0:NBLK], k.ident[0:NS, 0:NS]).then_inc(z["btr"], 1)
            pe.wait_ge(z["bcp"], 1)
            pe.wait_ge(z["osum"], 1)

            def pool_max(b):
                pe.wait_ge(z["rmx"], b + 1)
                m.transpose(k.ps[0:Q, 5, 0:P], cmax[:, :], k.ident[:, :]).then_inc(z["mt"], 1)
                pe.wait_ge(z["dgd"], b + 1)
                m.matmul(k.ps[:, 6, 0:Q], one[0:Q, :], dg[:, :], start=True, stop=True).then_inc(z["mb"], 1)

            def pool_values(b, G, v):
                pe.wait_ge(z["exd2"], b + 1)
                p4 = prob[:, 0:NS * G * H].rearrange("p (n g h) -> p n g h", n=NS, h=H)
                for g in range(G):
                    m.matmul(k.ps[0:HD, 5, 0:Q], one[:, 0:HD], p4[:, :, g, :], start=(g == 0), stop=(g == G - 1))
                for n in range(NS):
                    for g in range(G):
                        last = m.matmul(k.ps[0:HD, 7, n * H:(n + 1) * H], v[:, n, g, :], p4[:, n, g, :], start=(g == 0), stop=(g == G - 1))
                last.then_inc(z["av"], 1)

            NE = 4 * NS + NS

            def keys(e):
                if e < 4 * NS:
                    n, b4 = divmod(e, 4)
                    for landed, share in zip(kin[n], shares):
                        pe.wait_ge(landed, 16 * len(share))
                    src = [pages[:, n, 4 * b4 + t, 0:HD] for t in range(4)]
                else:
                    pe.wait_ge(z["win_in"], 16 * NS)
                    src = [win[:, e - 4 * NS, t, 0:HD] for t in range(4)]
                if e >= 2:
                    pe.wait_ge(z["kcp"], e - 1)
                for t in range(4):
                    last = m.transpose(k.ps[0:HD, 3 + e % 2, t * P:(t + 1) * P], src[t], k.ident[:, :])
                last.then_inc(z["ktr"], 1)

            def scores(e):
                pe.wait_ge(z["kcp"], e + 1)
                sel = e < 4 * NS
                rows = HD + NBLK if sel else HD
                n = e // 4 if sel else e - 4 * NS
                at = 4 * e if sel else 4 * n
                for t in range(4):
                    last = m.matmul((S_ps if sel else W_ps)[:, (at + t) * H:(at + t + 1) * H],
                                    kT[0:rows, (e % 4) * 512 + t * P:(e % 4) * 512 + (t + 1) * P], qT[0:rows, n, :], start=True, stop=True)
                last.then_inc(z["scd"], 1)

            keys(0)
            for e in range(NE):
                if e + 1 < NE:
                    keys(e + 1)
                scores(e)
            pool_max(0)
            pool_values(0, PAGES, pages[:, :, :, HD:P])
            pe.wait_ge(z["comb"], 1)
            pool_max(1)
            pool_values(1, GW, win[:, :, :, HD:P])

        @block.vector
        def _(dve):
            v = nc.vector
            link = chain(dve, z["link"])
            link(v.memset(pg[:, :], 0.0))
            gate = k.tm[0:NS, NC, 640:652].rearrange("n (o g) -> n o g", o=1).broadcast_to([NS, NS, 12])
            v.tensor_tensor(gd[:, :, :], gate, k.ident[0:NS, 0:NS].rearrange("n (m o) -> n m o", o=1).broadcast_to([NS, NS, 12]), ALU.mult).then_inc(z["gm"], 1)
            dve.wait_ge(z["tr0"], 1)
            v.tensor_copy(qT[0:HD, :, :].rearrange("d n h -> d h n"), k.ps[0:HD, 6, 0:Q].rearrange("d (h n) -> d h n", n=NS)).then_inc(z["cp0"], 1)
            v.tensor_copy(newT[:, :, :].rearrange("d i n -> d (i n)"), k.ps[0:HD, 6, Q:2 * Q]).then_inc(z["cp0"], 1)
            dve.wait_ge(z["cp0"], 2)
            for b in range(2):
                kn = newT[:, 2 * b, :].rearrange("d (n o) -> d n o", o=1).broadcast_to([HD, NS, H])
                last = v.tensor_tensor(prod[:, b, :].rearrange("d (n h) -> d n h", h=H), qT[0:HD, :, :], kn, ALU.mult)
            last.then_inc(z["sn"], 1)
            dve.wait_ge(z["tr0"], 2)
            v.tensor_copy(gts[:, :, :].rearrange("d n g -> d (n g)"), k.ps[0:HD, 7, 0:96]).then_inc(z["gcp"], 1)
            dve.wait_ge(z["cs_"], 1)
            v.tensor_copy(scT[0:M, :], k.ps[0:M, 5, 0:Q]).then_inc(z["csc"], 1)
            dve.wait_ge(z["snc"], 1)
            v.tensor_copy(snew[:, :, :].rearrange("p b q -> p (b q)"), k.ps[:, 7, 0:2 * Q])
            dve.wait_ge(z["cst"], 1)
            link(v.tensor_reduce(st[:, 0:1], k.ps[0:Q, 6, 0:M], AX.X, ALU.max))
            v.tensor_scalar(st[:, 1:2], st[:, 0:1], -SCALE, None, ALU.mult).then_inc(z["ex"], 1)
            dve.wait_ge(z["ex"], 2)
            link(v.reciprocal(st[:, 3:4], st[:, 2:3]))
            v.tensor_scalar(pc[:, 0:M], pc[:, 0:M], st[:, 3:4], None, ALU.mult).then_inc(z["nrm"], 1)
            dve.wait_ge(z["pp"], 1)
            v.tensor_copy(pcT[0:M, :], k.ps[0:M, 6, 0:Q]).then_inc(z["pcc"], 1)
            link(v.tensor_copy(pg[:, 1:1 + M], k.ps[0:NS, 5, 0:M]))

            def at(o):
                return pg[:, 1 + o:1 + o + 4 * (NBLK - 1) + 1:4]
            b = sc[:, 0, 0:NBLK]
            link(v.scalar_tensor_tensor(out=b, in0=at(-1), scalar=0.5, in1=at(0), op0=ALU.mult, op1=ALU.add))
            link(v.tensor_tensor(b, b, at(1), ALU.add))
            link(v.tensor_tensor(b, b, at(2), ALU.add))
            link(v.scalar_tensor_tensor(out=b, in0=at(3), scalar=0.5, in1=b, op0=ALU.mult, op1=ALU.add))
            link(v.memset(sc[:, 0, 0:1], BIG))
            link(v.memset(sc[:, 0, NBLK - 1:NBLK + 1], BIG))
            choose_blocks(link, v, sc[:, 0, :], sc[:, 1, :], sc[:, 2, :], m8, z["imp"])
            dve.wait_ge(z["btr"], 1)
            v.tensor_copy(qT[HD:HD + NBLK, :, :], k.ps[0:NBLK, 5, 0:NS].rearrange("b (n o) -> b n o", o=1).broadcast_to([NBLK, NS, H])).then_inc(z["bcp"], 1)
            dve.wait_ge(z["oc"], 1)
            v.tensor_tensor(o_sum[:, :].rearrange("d (n h) -> d n h", h=H), k.ps[0:HD, 6, 0:Q].rearrange("d (n h) -> d n h", h=H),
                            gts[:, :, 0:12:3], ALU.mult).then_inc(z["osum"], 1)
            dve.wait_ge(z["blk_in"], 16)
            for e in range(4 * NS + NS):
                dve.wait_ge(z["ktr"], e + 1)
                if e >= 4:
                    dve.wait_ge(z["scd"], e - 3)
                v.tensor_copy(kT[0:HD, (e % 4) * 512:(e % 4 + 1) * 512], k.ps[0:HD, 3 + e % 2, :]).then_inc(z["kcp"], 1)

            def softmax(b, G):
                n = NS * G * H
                s4 = (W_ps if b else S_ps)[:, 0:n].rearrange("p (n g h) -> p n g h", n=NS, h=H)
                dve.wait_ge(z["scd"], 5 * NS)
                v.tensor_reduce(cmax[:, :].rearrange("p (n h) -> p n h", h=H), s4.rearrange("p n g h -> p n h g"), AX.X, ALU.max).then_inc(z["rmx"], 1)
                dve.wait_ge(z["mt"], b + 1)
                link(v.tensor_reduce(st[:, 4:5], k.ps[0:Q, 5, 0:P], AX.X, ALU.max))
                v.tensor_scalar(dg[:, :], k.ident[0:Q, 0:Q], st[:, 4:5], None, ALU.mult).then_inc(z["dgd"], 1)
                dve.wait_ge(z["mb"], b + 1)
                link(v.tensor_tensor(M_b[:, :], k.ps[:, 6, 0:Q], snew[:, b, :], ALU.max))
                mb = M_b[:, :].rearrange("p (n h) -> p n h", h=H)
                p4 = prob[:, 0:n].rearrange("p (n g h) -> p n g h", n=NS, h=H)
                for g in range(G):
                    v.tensor_tensor(p4[:, :, g, :], s4[:, :, g, :], mb, ALU.subtract)
                v.tensor_tensor(pnew[:, :], snew[:, b, :], M_b[:, :], ALU.subtract).then_inc(z["sub"], 1)

            def combine(b):
                dve.wait_ge(z["av"], b + 1)
                vn = newT[:, 2 * b + 1, :].rearrange("d (n o) -> d n o", o=1).broadcast_to([HD, NS, H])
                ob3 = o_b[:, :].rearrange("d (n h) -> d n h", h=H)
                link(v.tensor_tensor(ob3, pnew[0:HD, :].rearrange("d (n h) -> d n h", h=H), vn, ALU.mult))
                link(v.tensor_tensor(o_b[:, :], k.ps[0:HD, 7, 0:Q], o_b[:, :], ALU.add))
                link(v.tensor_tensor(l_b[:, :], k.ps[0:HD, 5, 0:Q], pnew[0:HD, :], ALU.add))
                link(v.reciprocal(l_b[:, :], l_b[:, :]))
                link(v.tensor_tensor(o_b[:, :], o_b[:, :], l_b[:, :], ALU.mult))
                link(v.tensor_tensor(ob3, ob3, gts[:, :, 1 + b:12:3], ALU.mult))
                v.tensor_tensor(o_sum[:, :], o_sum[:, :], o_b[:, :], ALU.add).then_inc(z["comb"], 1)
                dve.wait_ge(z["comb"], b + 1)

            softmax(0, PAGES)
            combine(0)
            softmax(1, GW)
            combine(1)
            o3 = o_sum[:, :].rearrange("d (n h) -> d n h", h=H)
            for h in range(H):
                r = slice((h % 2) * HD, (h % 2 + 1) * HD)
                last = v.tensor_copy(o_ch[r, h // 2, :], o3[:, :, h])
            last.then_inc(z["och"], 1)
            dve.wait_ge(z["och"], 1)
            for j in range(2):
                y = k.yT[6 + j][:, T:TT]
                v.tensor_tensor(y, y, o_ch[:, j, :], ALU.mult)


def stage_output(nc, k, sem):
    FR = mybir.dt.float32r
    NR = 3
    ROW = {0: 2, 1: 3, 2: 0, 3: 1, 4: 4, 5: 5, 6: 6, 7: 7}
    with ExitStack() as ctx:
        def sb(name, shape, dt=FR):
            return ctx.enter_context(nc.sbuf_tensor(name, shape, dt))
        w_hi, w_lo = sb("w_out_hi", [P, KT, D]), sb("w_out_lo", [P, KT, D])
        y_hi, y_lo = sb("y_hi", [P, 2, KT, P]), sb("y_lo", [P, 2, KT, P])
        w_raw, x_in, y_out = (k.tm[:, :, :].rearrange("p t c -> p (t c)")[:, n * NR * D:(n + 1) * NR * D].rearrange("p (b c) -> p b c", b=NR)
                              for n in range(3))
        names = "w_hi_done w_split y_hi_done y_split mm gated added".split()
        z = {n: sem("o_" + n) for n in names}
        w_in = [sem(f"o_w{i}") for i in range(NR)]
        x_r = [sem(f"o_x{i}") for i in range(NR)]
        out_r = [sem(f"o_stored{i}") for i in range(NR)]
        block = ctx.enter_context(nc.Block())
        rows = [P] * NC + [NS]
        split = ((k.y_ssd, 0, 2), (k.xbc, 2, KT))

        @block.sync
        def _(sp):
            def load_x(t):
                src = k.io["x_prompt"][0, t * P:(t + 1) * P, :] if t < NC else k.io["x_sample"][:, 0, :]
                sp.dma_start(x_in[0:rows[t], t % NR, :], src).then_inc(x_r[t % NR], 16)

            for i in range(KT):
                if i >= NR:
                    sp.wait_ge(z["w_split"], i - NR + 1)
                sp.dma_start(w_raw[:, i % NR, :], k.io["w_out"][0, ROW[i] * P:(ROW[i] + 1) * P, :]).then_inc(w_in[i % NR], 16)
            for t in range(NR):
                load_x(t)
            for t in range(NC + 1):
                sp.wait_ge(z["added"], t + 1)
                dst = k.io["y_prompt"][0, t * P:(t + 1) * P, :] if t < NC else k.io["y_sample"][:, 0, :]
                sp.dma_start(dst, y_out[0:rows[t], t % NR, :]).then_inc(out_r[t % NR], 16)
                if t + NR <= NC:
                    load_x(t + NR)
            for i in range(NR):
                sp.wait_ge(out_r[i], 16 * len(range(i, NC + 1, NR)))

        @block.scalar
        def _(act):
            def hi_y(t):
                if t >= 2:
                    act.wait_ge(z["mm"], t - 1)
                r = rows[t]
                for src, a, b in split:
                    last = nc.scalar.copy(y_hi[:, t % 2, a:b, 0:r], src[:, 0:b - a, t * P:t * P + r])
                last.then_inc(z["y_hi_done"], 1)

            hi_y(0)
            for i in range(KT):
                act.wait_ge(w_in[i % NR], 16 * (i // NR + 1))
                nc.scalar.copy(w_hi[:, i, :], w_raw[:, i % NR, :]).then_inc(z["w_hi_done"], 1)
            for t in range(1, NC + 1):
                hi_y(t)

        @block.tensor
        def _(pe):
            m = nc.tensor
            for t in range(NC + 1):
                r = rows[t]
                pe.wait_ge(z["y_split"], t + 1)
                if t >= 2:
                    pe.wait_ge(z["gated"], t - 1)
                for half in range(2):
                    bank, c = k.ps[0:r, 2 * (t % 2) + half, :], slice(half * 512, (half + 1) * 512)
                    for i in range(KT):
                        if t == 0:
                            pe.wait_ge(z["w_split"], i + 1)
                        hi, lo = y_hi[:, t % 2, i, 0:r], y_lo[:, t % 2, i, 0:r]
                        m.matmul(bank, hi, w_hi[:, i, c], start=(i == 0), stop=False)
                        m.matmul(bank, hi, w_lo[:, i, c], start=False, stop=False)
                        last = m.matmul(bank, lo, w_hi[:, i, c], start=False, stop=(i == KT - 1))
                last.then_inc(z["mm"], 1)

        @block.vector
        def _(dve):
            v = nc.vector

            def lo_y(t):
                dve.wait_ge(z["y_hi_done"], t + 1)
                r = rows[t]
                for src, a, b in split:
                    last = v.tensor_tensor(y_lo[:, t % 2, a:b, 0:r], src[:, 0:b - a, t * P:t * P + r],
                                           y_hi[:, t % 2, a:b, 0:r].bitcast(F32), ALU.subtract)
                last.then_inc(z["y_split"], 1)

            lo_y(0)
            for i in range(KT):
                dve.wait_ge(z["w_hi_done"], i + 1)
                v.tensor_tensor(w_lo[:, i, :], w_raw[:, i % NR, :], w_hi[:, i, :].bitcast(F32), ALU.subtract).then_inc(z["w_split"], 1)
            for t in range(NC + 1):
                if t < NC:
                    lo_y(t + 1)
                r = rows[t]
                dve.wait_ge(z["mm"], t + 1)
                if t >= NR:
                    dve.wait_ge(out_r[t % NR], 16 * (t // NR))
                out = y_out[0:r, t % NR, :]
                gate = k.gate_p if t < NC else k.gate_s
                banks = k.ps[0:r, 2 * (t % 2):2 * (t % 2) + 2, :].rearrange("p b n -> p (b n)")
                v.tensor_tensor(out, banks, gate[0:r, :], ALU.mult).then_inc(z["gated"], 1)
                dve.wait_ge(z["gated"], t + 1)
                dve.wait_ge(x_r[t % NR], 16 * (t // NR + 1))
                v.tensor_tensor(out, out, x_in[0:r, t % NR, :], ALU.add).then_inc(z["added"], 1)


_INS = ['x_prompt', 'x_sample', 'cache_kv', 'cache_win', 'state_sconv', 'state_ssm_conv', 'state_ssm', 'state_cconv',
        'page_table', 'c_prompt', 'c_sample', 'norm_g', 'w_ada', 'b_ada', 'w_in', 'w_out', 'sc_w', 'ssd_conv_w', 'ssd_conv_b',
        'ssd_dt_bias', 'ssd_A_log', 'ssd_D', 'ssd_norm_g', 'cf_w', 'cf_b', 'cf_ln_g', 'cf_ln_b', 'q_g', 'k_g',
        'cmp_pe', 'cmp_w1', 'cmp_b1', 'cmp_w2', 'cmp_b2']
_OUTS = [('y_prompt', (1, T, D)), ('y_sample', (NS, 1, D)), ('kv_p', (1, NC, P, 4, HD)), ('kv_s', (1, NS, 1, 4, HD)),
         ('win_p', (1, 1, 512, 2, HD)), ('win_s', (1, NS, 512, 2, HD)), ('sconv_p', (1, 1, 2, W)), ('sconv_s', (1, NS, 2, W)),
         ('ssm_conv_p', (1, 1, 3, CV)), ('ssm_conv_s', (1, NS, 3, CV)), ('ssm_p', (1, 1, SH, SP, SST)),
         ('ssm_s', (1, NS, SH, SP, SST)), ('cconv_p', (1, 1, KCF - 1, W)), ('cconv_s', (1, NS, KCF - 1, W))]


def build(nc, k):
    with ExitStack() as ctx:
        def sb(name, shape):
            return ctx.enter_context(nc.sbuf_tensor(name, shape, F32))

        stores = {name: ctx.enter_context(nc.semaphore(name)) for name in
                  ("xstored", "s_stored", "c_stored", "t_stored", "o_stored0", "o_stored1", "o_stored2")}

        def run(stage):
            own = []

            def sem(name):
                if name in stores:
                    return stores[name]
                own.append(nc.alloc_semaphore(name))
                return own[-1]
            stage(nc, k, sem)
            nc.clear_and_free_semaphores(own)
            nc.all_engine_barrier()
        k.ps = ctx.enter_context(nc.psum_tensor("ps", [P, 8, GT], F32))
        k.scores_ps = k.ps[:, 0:4, :].rearrange("p b n -> p (b n)")
        k.ones, k.ident, k.upper, k.below, k.causal, k.win_low = (
            sb(name, [P, P]) for name in ("ones", "ident", "upper", "below", "causal", "win_low"))
        k.neg_upper, k.low_T = sb("neg_upper", [P, SH * P]), sb("low_T", [P, SH * P])
        k.cmp_mask = sb("cmp_mask", [P, 2 * P])
        k.sel_mask = sb("sel_mask", [P, 2 * NBLK])
        k.head_pick = sb("head_pick", [SH, 2, P])
        k.par = sb("par", [P, PEND])
        k.shift, k.scale = sb("shift", [P, KT, NS + 1]), sb("scale", [P, KT, NS + 1])
        k.gate_s, k.gate_p = sb("gate_s", [NS, D]), sb("gate_p", [P, D])
        k.dt = sb("dt", [P, (NC + 1) * SH])
        k.tails_T = sb("tails_T", [P, 6, 3 + NS])
        y_ssd = sb("y_ssd", [P, 2, TT])
        arena = sb("arena", [P, 6, TT])
        k.xbc, k.y_ssd = arena, y_ssd
        k.yT = [y_ssd[:, j, :] for j in range(2)] + [arena[:, j, :] for j in range(6)]
        hold = ctx.enter_context(ExitStack())
        h_space = hold.enter_context(nc.sbuf_tensor("h_space", [P, KT * TT], F32))
        k.hT = h_space[:, :].rearrange("p (k t) -> p k t", k=KT)

        def hview(start, size):
            return h_space[:, start:start + size]
        k.hview = hview
        k.extra_dram = nc.dram_tensor("extra_rows", (2, NBLK + 2, T), F32, kind="Internal").ap()
        run(stage_prepare)
        run(stage_norm)
        run(stage_ssd_inputs)
        run(stage_ssd)
        run(stage_ssd_norm)
        with nc.sbuf_tensor("conf", [P, 2, TT], F32) as conf:
            k.conf = conf
            run(stage_convs)
            run(stage_conformer_norm)
        compressed = ctx.enter_context(ExitStack())

        def right(name, shape, until=ctx):
            return until.enter_context(nc.sbuf_tensor(name, shape, F32, side="right"))
        k.tm = right("tm", [P, NC + 1, TM])
        run(stage_token_major)
        hold.close()
        k.kcT, k.vc = right("kcT", [HD, 1 + NS, P], compressed), right("vc", [P, 1 + NS, HD], compressed)
        with ExitStack() as held:
            k.keys = [[held.enter_context(nc.sbuf_tensor(f"keys_{b}_{part}", [P, T], mybir.dt.float32r)) for part in ("hi", "lo")]
                      for b in ("sel", "win")]
            run(stage_compress)
            k.va = held.enter_context(nc.sbuf_tensor("values", [P, NC, 2, HD + 1], F32))
            k.biasT = held.enter_context(nc.sbuf_tensor("bias_T", [P, T], F32))
            run(stage_choice)
            run(stage_attention)
        run(stage_sample_attention)
        compressed.close()
        run(stage_output)


def kernel(**inputs):
    import numpy as np
    import concourse.bacc as bacc
    from concourse.bass_utils import run_bass_kernel_spmd

    nc = bacc.Bacc("TRN2", target_bir_lowering=False, num_devices=1)
    arrays, tensors = {}, {}
    for name in _INS:
        a = np.ascontiguousarray(inputs[name])
        arrays["in_" + name] = a
        tensors[name] = nc.dram_tensor("in_" + name, a.shape, mybir.dt.from_np(a.dtype), kind="ExternalInput").ap()
    for name, shape in _OUTS:
        tensors[name] = nc.dram_tensor("out_" + name, shape, F32, kind="ExternalOutput").ap()
    k = Shared(tensors)
    k.n_pool = inputs["cache_kv"].shape[1]
    build(nc, k)
    r = run_bass_kernel_spmd(nc, [arrays], core_ids=[0])
    return tuple(r.results[0]["out_" + name] for name, _ in _OUTS)
```
